# Optimizing a Trainium2 kernel written in Bass

```python
import jax, jax.numpy as jnp
from jax import lax
import numpy as np

D_MODEL = 1024
BATCH = 1
SEQ = 256
DEPTH = 1

D_MIX = D_MODEL
ATTN_HEAD_DIM = 64
ATTN_HEADS = (D_MIX // 2) // ATTN_HEAD_DIM
ATTN_KV_HEADS = 2
ATTN_WIDTH = ATTN_HEADS * ATTN_HEAD_DIM
ATTN_KV_WIDTH = ATTN_KV_HEADS * ATTN_HEAD_DIM
WINDOW = 128
BLOCK = 128
ROPE_THETA = 10000.0

GLA_HEADS = 4
GLA_WIDTH = D_MIX - ATTN_WIDTH
GLA_DV = GLA_WIDTH // GLA_HEADS
GLA_DK = GLA_DV // 2
GLA_QK_WIDTH = GLA_HEADS * GLA_DK
GLA_GATE_RANK = 16
GLA_GATE_TAU = 16.0
GLA_CHUNK = 64

D_FF = 2816
PLE_DIM = 256
EPS = 1e-6

IN_SIZES = (ATTN_WIDTH, ATTN_KV_WIDTH, ATTN_KV_WIDTH,
            GLA_QK_WIDTH, GLA_QK_WIDTH, GLA_WIDTH, GLA_GATE_RANK, GLA_WIDTH)
D_IN = sum(IN_SIZES)


def rmsnorm(x, g):
    xf = x.astype(jnp.float32)
    y = xf * lax.rsqrt(jnp.mean(xf * xf, axis=-1, keepdims=True) + EPS)
    return (y * g.astype(jnp.float32)).astype(x.dtype)

def swiglu(x, w_gate, w_up, w_down):
    return (jax.nn.silu(x @ w_gate) * (x @ w_up)) @ w_down

def rope(x, pos):
    dh = x.shape[-1]
    inv_freq = ROPE_THETA ** (-jnp.arange(0, dh, 2, dtype=jnp.float32) / dh)
    ang = pos.astype(jnp.float32)[:, None] * inv_freq[None, :]
    cos = jnp.cos(ang)[None, :, None, :]
    sin = jnp.sin(ang)[None, :, None, :]
    xf = x.astype(jnp.float32)
    x1, x2 = xf[..., : dh // 2], xf[..., dh // 2:]
    out = jnp.concatenate([x1 * cos - x2 * sin, x2 * cos + x1 * sin], axis=-1)
    return out.astype(x.dtype)

def split_cols(z):
    points = np.cumsum(IN_SIZES)[:-1].tolist()
    return jnp.split(z, points, axis=-1)

def sliding_window_attention(q, k, v, sinks):
    B, S, H, Dh = q.shape
    KVH = k.shape[2]
    G = H // KVH
    NB = S // BLOCK
    qb = q.reshape(B, NB, BLOCK, KVH, G, Dh)

    def band(t):
        tb = t.reshape(B, NB, BLOCK, KVH, Dh)
        prev = jnp.pad(tb[:, :-1], ((0, 0), (1, 0), (0, 0), (0, 0), (0, 0)))
        return jnp.concatenate([prev, tb], axis=2)

    kb, vb = band(k), band(v)
    scores = jnp.einsum('bnqhgd,bnkhd->bnhgqk', qb, kb).astype(jnp.float32) * (Dh ** -0.5)
    qi = jnp.arange(BLOCK)[:, None]
    kj = jnp.arange(2 * BLOCK)[None, :]
    rel = kj - BLOCK - qi
    in_band = (rel <= 0) & (rel > -WINDOW)
    kpos = jnp.arange(NB)[:, None, None] * BLOCK + kj[None] - BLOCK
    valid = in_band[None] & (kpos >= 0)
    scores = jnp.where(valid[None, :, None, None], scores, -jnp.inf)
    sink = sinks.astype(jnp.float32).reshape(KVH, G)[None, None, :, :, None, None]
    m = jnp.maximum(jnp.max(scores, axis=-1, keepdims=True), sink)
    e = jnp.exp(scores - m)
    denom = jnp.sum(e, axis=-1, keepdims=True) + jnp.exp(sink - m)
    probs = (e / denom).astype(v.dtype)
    out = jnp.einsum('bnhgqk,bnkhd->bnqhgd', probs, vb)
    return out.reshape(B, S, H * Dh)

def gla_chunked(q, k, v, log_alpha):
    B, S, H, DK = q.shape
    DV = v.shape[-1]
    C = GLA_CHUNK
    NC = S // C

    def chunks(t):
        return t.astype(jnp.float32).reshape(B, NC, C, H, t.shape[-1]).transpose(1, 0, 3, 2, 4)

    qc = chunks(q) * (DK ** -0.5)
    kc, vc, gc = chunks(k), chunks(v), chunks(log_alpha)
    causal = jnp.tril(jnp.ones((C, C), dtype=bool))[None, None, :, :, None]

    def step(state, inp):
        qi, ki, vi, gi = inp
        b = jnp.cumsum(gi, axis=2)
        b_last = b[:, :, -1:, :]
        diff = b[:, :, :, None, :] - b[:, :, None, :, :]
        decay = jnp.exp(jnp.where(causal, diff, -jnp.inf))
        attn = jnp.einsum('bhid,bhjd,bhijd->bhij', qi, ki, decay)
        o = (jnp.einsum('bhij,bhjv->bhiv', attn, vi)
             + jnp.einsum('bhid,bhdv->bhiv', qi * jnp.exp(b), state))
        new_state = (jnp.swapaxes(jnp.exp(b_last), 2, 3) * state
                     + jnp.einsum('bhjd,bhjv->bhdv', ki * jnp.exp(b_last - b), vi))
        return new_state, o

    s0 = jnp.zeros((B, H, DK, DV), jnp.float32)
    _, o = lax.scan(step, s0, (qc, kc, vc, gc))
    return o.transpose(1, 0, 3, 2, 4).reshape(B, S, H, DV).astype(v.dtype)

def first_inputs(seed: int = 0) -> dict:
    key = jax.random.key(seed)
    ks = jax.random.split(key, 24)
    L, D, F = DEPTH, D_MODEL, D_FF

    def w(k, shape, fan_in):
        return jax.random.normal(k, shape, jnp.float32) * (fan_in ** -0.5)

    def gain(k, shape):
        return 1.0 + 0.05 * jax.random.normal(k, shape, jnp.float32)

    return {
        "x": jax.random.normal(ks[0], (BATCH, SEQ, D), jnp.float32),
        "p": jax.random.normal(ks[1], (L, BATCH, SEQ, PLE_DIM), jnp.float32),
        "ffn1_norm": gain(ks[2], (L, D)),
        "ffn1_w_gate": w(ks[3], (L, D, F), D),
        "ffn1_w_up": w(ks[4], (L, D, F), D),
        "ffn1_w_down": w(ks[5], (L, F, D), F),
        "mix_norm": gain(ks[6], (L, D)),
        "w_in": w(ks[7], (L, D, D_IN), D),
        "q_norm": gain(ks[8], (L, ATTN_HEAD_DIM)),
        "k_norm": gain(ks[9], (L, ATTN_HEAD_DIM)),
        "attn_sinks": 0.5 * jax.random.normal(ks[10], (L, ATTN_HEADS), jnp.float32),
        "gla_w_gate_up": w(ks[11], (L, GLA_GATE_RANK, GLA_QK_WIDTH), GLA_GATE_RANK),
        "gla_b_gate": 0.1 * jax.random.normal(ks[12], (L, GLA_QK_WIDTH), jnp.float32),
        "gla_out_norm": gain(ks[13], (L, GLA_DV)),
        "w_out": w(ks[14], (L, D_MIX, D), D_MIX),
        "ffn2_norm": gain(ks[15], (L, D)),
        "ffn2_w_gate": w(ks[16], (L, D, F), D),
        "ffn2_w_up": w(ks[17], (L, D, F), D),
        "ffn2_w_down": w(ks[18], (L, F, D), F),
        "ple_gate_norm": gain(ks[19], (L, D)),
        "ple_w_gate": w(ks[20], (L, D, D), D),
        "ple_w_proj": w(ks[21], (L, PLE_DIM, D), PLE_DIM),
        "ple_norm": gain(ks[22], (L, D)),
    }

def first_block(x, p, ffn1_norm, ffn1_w_gate, ffn1_w_up, ffn1_w_down, mix_norm, w_in,
              q_norm, k_norm, attn_sinks, gla_w_gate_up, gla_b_gate, gla_out_norm, w_out,
              ffn2_norm, ffn2_w_gate, ffn2_w_up, ffn2_w_down,
              ple_gate_norm, ple_w_gate, ple_w_proj, ple_norm):
    B, S, _ = x.shape
    pos = jnp.arange(S)
    h = x
    for i in range(DEPTH):
        h = h + 0.5 * swiglu(rmsnorm(h, ffn1_norm[i]), ffn1_w_gate[i], ffn1_w_up[i], ffn1_w_down[i])

        n = rmsnorm(h, mix_norm[i])
        aq, ak, av, gq, gk, gv, glr, gog = split_cols(n @ w_in[i])

        aq = rope(rmsnorm(aq.reshape(B, S, ATTN_HEADS, ATTN_HEAD_DIM), q_norm[i]), pos)
        ak = rope(rmsnorm(ak.reshape(B, S, ATTN_KV_HEADS, ATTN_HEAD_DIM), k_norm[i]), pos)
        av = av.reshape(B, S, ATTN_KV_HEADS, ATTN_HEAD_DIM)
        attn_o = sliding_window_attention(aq, ak, av, attn_sinks[i])

        log_alpha = jax.nn.log_sigmoid(
            (glr @ gla_w_gate_up[i] + gla_b_gate[i]).astype(jnp.float32)) / GLA_GATE_TAU
        gla_o = gla_chunked(gq.reshape(B, S, GLA_HEADS, GLA_DK),
                            gk.reshape(B, S, GLA_HEADS, GLA_DK),
                            gv.reshape(B, S, GLA_HEADS, GLA_DV),
                            log_alpha.reshape(B, S, GLA_HEADS, GLA_DK))
        gla_o = rmsnorm(gla_o, gla_out_norm[i]) * jax.nn.silu(gog.reshape(B, S, GLA_HEADS, GLA_DV))
        gla_o = gla_o.reshape(B, S, GLA_WIDTH)

        h = h + jnp.concatenate([attn_o, gla_o], axis=-1) @ w_out[i]

        h = h + 0.5 * swiglu(rmsnorm(h, ffn2_norm[i]), ffn2_w_gate[i], ffn2_w_up[i], ffn2_w_down[i])

        gate = jax.nn.sigmoid(rmsnorm(h, ple_gate_norm[i]) @ ple_w_gate[i])
        emb = rmsnorm(p[i] @ ple_w_proj[i], ple_norm[i])
        h = h + gate * emb
    return h


DEPTH_2 = 2

N_AB_LAYERS = (DEPTH_2 + 1) // 2
N_C_LAYERS = DEPTH_2 // 2

M_HEADS = 4
M_QK_DIM = 64
M_V_DIM = 128
M_CHUNK = 64
GATE_SOFTCAP = 15.0
G_HEADS = 4
G_K_DIM = 128
G_V_DIM = 128
G_CHUNK = 64
SHORT_CONV = 4
C_HEADS = 8
C_K_DIM = D_MODEL // C_HEADS
C_V_DIM = D_MODEL // C_HEADS
C_CHUNK = 32
FFN_CONV = 3

M_QK = M_HEADS * M_QK_DIM
M_V = M_HEADS * M_V_DIM
G_QK = G_HEADS * G_K_DIM
G_V = G_HEADS * G_V_DIM
AB_SPLITS = (M_QK, M_QK, M_V, M_V, M_HEADS, M_HEADS, G_QK, G_QK, G_V, G_V, G_HEADS, G_HEADS)
AB_SPLIT_IDX = tuple(int(s) for s in np.cumsum(AB_SPLITS)[:-1])
AB_IN = sum(AB_SPLITS)
AB_MIX = M_V + G_V
C_K_TOTAL = C_HEADS * C_K_DIM
C_MIX = C_HEADS * C_V_DIM
C_IN = 2 * C_K_TOTAL + 2 * C_MIX


def rms_norm(x, gain):
    xf = x.astype(jnp.float32)
    y = xf * lax.rsqrt(jnp.mean(jnp.square(xf), -1, keepdims=True) + EPS)
    return (y * gain.astype(jnp.float32)).astype(x.dtype)

def head_rms_norm(x, gain):
    B, S, H, d = x.shape
    y = x * lax.rsqrt(jnp.mean(jnp.square(x), -1, keepdims=True) + EPS)
    return y.reshape(B, S, H * d) * gain.astype(jnp.float32)

def l2_norm(x):
    return x * lax.rsqrt(jnp.sum(jnp.square(x), -1, keepdims=True) + EPS)

def softcap(x, cap):
    return cap * jnp.tanh(x / cap)

def causal_dwconv(x, w):
    K, C = w.shape
    return lax.conv_general_dilated(
        x, w[:, None, :].astype(x.dtype), window_strides=(1,), padding=[(K - 1, 0)],
        dimension_numbers=("NWC", "WIO", "NWC"), feature_group_count=C)

def to_heads(t, n_heads):
    B, S, C = t.shape
    return t.reshape(B, S, n_heads, C // n_heads)

def to_chunks(t, L):
    B, S, H = t.shape[:3]
    t = t.reshape((B, S // L, L, H) + t.shape[3:])
    return jnp.moveaxis(t, (1, 3), (0, 2))

def from_chunks(t):
    N, B, H, L = t.shape[:4]
    t = jnp.moveaxis(t, (0, 2), (1, 3))
    return t.reshape((B, N * L, H) + t.shape[4:])

def mlstm_chunkwise(q, k, v, i_pre, f_pre):
    B, S, H, DK = q.shape
    DV = v.shape[-1]
    L = M_CHUNK
    q = q * DK ** -0.5
    qc, kc, vc = to_chunks(q, L), to_chunks(k, L), to_chunks(v, L)
    lfc = to_chunks(jax.nn.log_sigmoid(f_pre), L)
    igc = to_chunks(i_pre, L)
    causal = jnp.tril(jnp.ones((L, L), bool))

    def step(carry, inp):
        C, n, m = carry
        q_, k_, v_, lf_, ig_ = inp
        b = jnp.cumsum(lf_, -1)
        log_d = jnp.where(causal, b[..., :, None] - b[..., None, :] + ig_[..., None, :], -jnp.inf)
        log_inter = b + m[..., None]
        m_t = jnp.maximum(jnp.max(log_d, -1), log_inter)
        d = jnp.exp(log_d - m_t[..., None])
        w_inter = jnp.exp(log_inter - m_t)
        s = jnp.einsum("bhld,bhsd->bhls", q_, k_) * d
        num = jnp.einsum("bhls,bhsv->bhlv", s, v_) + w_inter[..., None] * jnp.einsum("bhld,bhdv->bhlv", q_, C)
        den = jnp.sum(s, -1) + w_inter * jnp.einsum("bhld,bhd->bhl", q_, n)
        h = num / jnp.maximum(jnp.abs(den), jnp.exp(-m_t))[..., None]
        b_last = b[..., -1]
        log_w = b_last[..., None] - b + ig_
        m_new = jnp.maximum(b_last + m, jnp.max(log_w, -1))
        wk = jnp.exp(log_w - m_new[..., None])
        carry_decay = jnp.exp(b_last + m - m_new)
        C = carry_decay[..., None, None] * C + jnp.einsum("bhl,bhld,bhlv->bhdv", wk, k_, v_)
        n = carry_decay[..., None] * n + jnp.einsum("bhl,bhld->bhd", wk, k_)
        return (C, n, m_new), h

    init = (jnp.zeros((B, H, DK, DV), jnp.float32), jnp.zeros((B, H, DK), jnp.float32),
            jnp.zeros((B, H), jnp.float32))
    _, h = lax.scan(step, init, (qc, kc, vc, lfc, igc))
    return from_chunks(h)

def gated_delta_chunkwise(q, k, v, g, beta):
    B, S, H, DK = q.shape
    DV = v.shape[-1]
    L = G_CHUNK
    q = q * DK ** -0.5
    qc, kc, vc = to_chunks(q, L), to_chunks(k, L), to_chunks(v, L)
    bc = to_chunks(beta, L)
    G = jnp.cumsum(to_chunks(g, L), -1)
    incl = jnp.tril(jnp.ones((L, L), bool))
    strict = jnp.tril(jnp.ones((L, L), bool), -1)
    diff = G[..., :, None] - G[..., None, :]
    decay = jnp.where(incl, jnp.exp(jnp.where(incl, diff, 0.0)), 0.0)
    kk = jnp.einsum("nbhld,nbhsd->nbhls", kc, kc)
    a_mat = jnp.where(strict, bc[..., :, None] * kk * decay, 0.0) + jnp.eye(L, dtype=jnp.float32)
    rhs = jnp.concatenate([vc * bc[..., None], kc * (bc * jnp.exp(G))[..., None]], -1)
    sol = lax.linalg.triangular_solve(a_mat, rhs, left_side=True, lower=True, unit_diagonal=True)
    u, w = sol[..., :DV], sol[..., DV:]
    attn = jnp.einsum("nbhld,nbhsd->nbhls", qc, kc) * decay
    q_dec = qc * jnp.exp(G)[..., None]
    k_dec = kc * jnp.exp(G[..., -1:] - G)[..., None]
    g_last = jnp.exp(G[..., -1])

    def step(state, inp):
        u_, w_, attn_, qd_, kd_, gl_ = inp
        v_new = u_ - jnp.einsum("bhld,bhdv->bhlv", w_, state)
        o = jnp.einsum("bhld,bhdv->bhlv", qd_, state) + jnp.einsum("bhls,bhsv->bhlv", attn_, v_new)
        state = gl_[..., None, None] * state + jnp.einsum("bhld,bhlv->bhdv", kd_, v_new)
        return state, o

    _, o = lax.scan(step, jnp.zeros((B, H, DK, DV), jnp.float32), (u, w, attn, q_dec, k_dec, g_last))
    return from_chunks(o)

def hgrn2_chunkwise(q, k, v, log_f):
    B, S, H, DK = q.shape
    DV = v.shape[-1]
    L = C_CHUNK
    q = q * DK ** -0.5
    qc, kc, vc = to_chunks(q, L), to_chunks(k, L), to_chunks(v, L)
    G = jnp.cumsum(to_chunks(log_f, L), -2)
    q_dec = qc * jnp.exp(G)
    k_dec = kc * jnp.exp(G[..., -1:, :] - G)
    g_last = jnp.exp(G[..., -1, :])
    incl = jnp.tril(jnp.ones((L, L), bool))[:, :, None]

    def step(state, inp):
        q_, k_, v_, G_, qd_, kd_, gl_ = inp
        diff = G_[..., :, None, :] - G_[..., None, :, :]
        pair_decay = jnp.exp(jnp.where(incl, diff, -jnp.inf))
        attn = jnp.einsum("bhld,bhlsd,bhsd->bhls", q_, pair_decay, k_)
        o = jnp.einsum("bhld,bhdv->bhlv", qd_, state) + jnp.einsum("bhls,bhsv->bhlv", attn, v_)
        state = gl_[..., :, None] * state + jnp.einsum("bhld,bhlv->bhdv", kd_, v_)
        return state, o

    _, o = lax.scan(step, jnp.zeros((B, H, DK, DV), jnp.float32), (qc, kc, vc, G, q_dec, k_dec, g_last))
    return from_chunks(o)

def hgrn_lower_bounds(lb_logits):
    p = jax.nn.softmax(lb_logits.astype(jnp.float32), axis=0)
    return jnp.cumsum(p, axis=0) - p[0]

def ab_mixer(u, w_in, conv_m, m_gate_bias, m_norm, conv_g, g_a_log, g_dt_bias, g_norm, w_out):
    f32 = jnp.float32
    proj = u @ w_in
    m_q, m_k, m_v, m_o, m_i, m_f, g_q, g_k, g_v, g_gate, g_a, g_b = jnp.split(proj, AB_SPLIT_IDX, axis=-1)
    m_qk = jax.nn.silu(causal_dwconv(jnp.concatenate([m_q, m_k], -1), conv_m))
    m_q, m_k = jnp.split(m_qk, 2, axis=-1)
    gb = m_gate_bias.astype(f32)
    i_pre = softcap(m_i.astype(f32) + gb[0], GATE_SOFTCAP)
    f_pre = softcap(m_f.astype(f32) + gb[1], GATE_SOFTCAP)
    h_m = mlstm_chunkwise(to_heads(m_q, M_HEADS).astype(f32), to_heads(m_k, M_HEADS).astype(f32),
                          to_heads(m_v, M_HEADS).astype(f32), i_pre, f_pre)
    y_m = jax.nn.sigmoid(m_o.astype(f32)) * head_rms_norm(h_m, m_norm)
    g_qkv = jax.nn.silu(causal_dwconv(jnp.concatenate([g_q, g_k, g_v], -1), conv_g))
    g_q, g_k, g_v = jnp.split(g_qkv, 3, axis=-1)
    log_decay = -jnp.exp(g_a_log.astype(f32)) * jax.nn.softplus(g_a.astype(f32) + g_dt_bias.astype(f32))
    beta = jax.nn.sigmoid(g_b.astype(f32))
    h_g = gated_delta_chunkwise(l2_norm(to_heads(g_q, G_HEADS).astype(f32)),
                                l2_norm(to_heads(g_k, G_HEADS).astype(f32)),
                                to_heads(g_v, G_HEADS).astype(f32), log_decay, beta)
    y_g = head_rms_norm(h_g, g_norm) * jax.nn.silu(g_gate.astype(f32))
    y = jnp.concatenate([y_m, y_g], -1).astype(u.dtype)
    return y @ w_out

def hgrn2_mixer(u, w_in, lower_bound, norm_gain, w_out):
    f32 = jnp.float32
    q, f, i, gate = jnp.split(u @ w_in, [C_K_TOTAL, 2 * C_K_TOTAL, 2 * C_K_TOTAL + C_MIX], axis=-1)
    lb = lower_bound.astype(f32)
    ff = f.astype(f32)
    log_f = jnp.logaddexp(jnp.log(lb), jnp.log1p(-lb) + jax.nn.log_sigmoid(ff))
    k = (1.0 - lb) * jax.nn.sigmoid(-ff)
    o = hgrn2_chunkwise(to_heads(jax.nn.silu(q.astype(f32)), C_HEADS), to_heads(k, C_HEADS),
                        to_heads(i.astype(f32), C_HEADS), to_heads(log_f, C_HEADS))
    y = head_rms_norm(o, norm_gain) * jax.nn.silu(gate.astype(f32))
    return y.astype(u.dtype) @ w_out

def conv_ffn(u, w_up, conv_w, conv_b, w_down):
    hdn = causal_dwconv(u @ w_up, conv_w) + conv_b
    gate, val = jnp.split(hdn, 2, axis=-1)
    return (jax.nn.silu(gate) * val) @ w_down

def second_inputs(seed: int = 0) -> dict:
    key = jax.random.key(seed)
    ks = jax.random.split(key, 24)
    f32 = jnp.float32

    def nrm(k, shape, scale):
        return jax.random.normal(k, shape, f32) * scale

    dt = jnp.exp(jax.random.uniform(ks[9], (N_AB_LAYERS, G_HEADS), f32, np.log(1e-3), np.log(1e-1)))
    return {
        "x": nrm(ks[0], (BATCH, SEQ, D_MODEL), 1.0),
        "norm_gains": 1.0 + nrm(ks[1], (DEPTH_2, 4, D_MODEL), 0.05),
        "ab_w_in": nrm(ks[2], (N_AB_LAYERS, D_MODEL, AB_IN), D_MODEL ** -0.5),
        "ab_conv_m": nrm(ks[3], (N_AB_LAYERS, SHORT_CONV, 2 * M_QK), SHORT_CONV ** -0.5),
        "ab_m_gate_bias": jnp.stack([nrm(ks[4], (N_AB_LAYERS, M_HEADS), 0.1),
                                     jnp.linspace(3.0, 6.0, M_HEADS, dtype=f32) + nrm(ks[5], (N_AB_LAYERS, M_HEADS), 0.1)], axis=1),
        "ab_m_norm": 1.0 + nrm(ks[6], (N_AB_LAYERS, M_V), 0.05),
        "ab_conv_g": nrm(ks[7], (N_AB_LAYERS, SHORT_CONV, 2 * G_QK + G_V), SHORT_CONV ** -0.5),
        "ab_g_a_log": jnp.log(jax.random.uniform(ks[8], (N_AB_LAYERS, G_HEADS), f32, 1.0, 16.0)),
        "ab_g_dt_bias": dt + jnp.log(-jnp.expm1(-dt)),
        "ab_g_norm": 1.0 + nrm(ks[10], (N_AB_LAYERS, G_V), 0.05),
        "ab_w_out": nrm(ks[11], (N_AB_LAYERS, AB_MIX, D_MODEL), AB_MIX ** -0.5),
        "c_w_in": nrm(ks[12], (N_C_LAYERS, D_MODEL, C_IN), D_MODEL ** -0.5),
        "c_lb_logits": nrm(ks[13], (DEPTH_2, C_K_TOTAL), 0.5),
        "c_norm": 1.0 + nrm(ks[14], (N_C_LAYERS, C_MIX), 0.05),
        "c_w_out": nrm(ks[15], (N_C_LAYERS, C_MIX, D_MODEL), C_MIX ** -0.5),
        "ffn_w_up": nrm(ks[16], (DEPTH_2, D_MODEL, 2 * D_FF), D_MODEL ** -0.5),
        "ffn_conv_w": nrm(ks[17], (DEPTH_2, FFN_CONV, 2 * D_FF), FFN_CONV ** -0.5),
        "ffn_conv_b": nrm(ks[18], (DEPTH_2, 2 * D_FF), 0.02),
        "ffn_w_down": nrm(ks[19], (DEPTH_2, D_FF, D_MODEL), D_FF ** -0.5),
    }

def second_block(x, norm_gains, ab_w_in, ab_conv_m, ab_m_gate_bias, ab_m_norm, ab_conv_g, ab_g_a_log,
              ab_g_dt_bias, ab_g_norm, ab_w_out, c_w_in, c_lb_logits, c_norm, c_w_out,
              ffn_w_up, ffn_conv_w, ffn_conv_b, ffn_w_down):
    lower_bounds = hgrn_lower_bounds(c_lb_logits)
    for layer in range(DEPTH_2):
        j = layer // 2
        u = rms_norm(x, norm_gains[layer, 0])
        if layer % 2 == 0:
            mix = ab_mixer(u, ab_w_in[j], ab_conv_m[j], ab_m_gate_bias[j], ab_m_norm[j], ab_conv_g[j],
                           ab_g_a_log[j], ab_g_dt_bias[j], ab_g_norm[j], ab_w_out[j])
        else:
            mix = hgrn2_mixer(u, c_w_in[j], lower_bounds[layer], c_norm[j], c_w_out[j])
        x = x + rms_norm(mix, norm_gains[layer, 1])
        u = rms_norm(x, norm_gains[layer, 2])
        ff = conv_ffn(u, ffn_w_up[layer], ffn_conv_w[layer], ffn_conv_b[layer], ffn_w_down[layer])
        x = x + rms_norm(ff, norm_gains[layer, 3])
    return x


def setup_inputs(seed=0):
    out = dict(first_inputs(seed))
    for name, value in second_inputs(seed + 1).items():
        if name != "x":
            out[name + "_2"] = value
    return out


def reference(
    x, p, ffn1_norm, ffn1_w_gate, ffn1_w_up, ffn1_w_down, mix_norm, w_in, q_norm, k_norm,
    attn_sinks, gla_w_gate_up, gla_b_gate, gla_out_norm, w_out, ffn2_norm, ffn2_w_gate,
    ffn2_w_up, ffn2_w_down, ple_gate_norm, ple_w_gate, ple_w_proj, ple_norm, norm_gains_2,
    ab_w_in_2, ab_conv_m_2, ab_m_gate_bias_2, ab_m_norm_2, ab_conv_g_2, ab_g_a_log_2,
    ab_g_dt_bias_2, ab_g_norm_2, ab_w_out_2, c_w_in_2, c_lb_logits_2, c_norm_2, c_w_out_2,
    ffn_w_up_2, ffn_conv_w_2, ffn_conv_b_2, ffn_w_down_2,
):
    x = first_block(
        x, p, ffn1_norm, ffn1_w_gate, ffn1_w_up, ffn1_w_down, mix_norm, w_in, q_norm, k_norm,
        attn_sinks, gla_w_gate_up, gla_b_gate, gla_out_norm, w_out, ffn2_norm, ffn2_w_gate,
        ffn2_w_up, ffn2_w_down, ple_gate_norm, ple_w_gate, ple_w_proj, ple_norm,
    )
    return second_block(
        x, norm_gains_2, ab_w_in_2, ab_conv_m_2, ab_m_gate_bias_2, ab_m_norm_2, ab_conv_g_2,
        ab_g_a_log_2, ab_g_dt_bias_2, ab_g_norm_2, ab_w_out_2, c_w_in_2, c_lb_logits_2,
        c_norm_2, c_w_out_2, ffn_w_up_2, ffn_conv_w_2, ffn_conv_b_2, ffn_w_down_2,
    )


_drawn_inputs = setup_inputs


def setup_inputs(seed=0):
    import zlib

    import numpy as np

    out = dict(_drawn_inputs(seed))
    spreads = {}
    factors = {'q_norm': 6.104,
     'k_norm': 5.215,
     'attn_sinks': 31.34,
     'ple_gate_norm': 3.801,
     'ffn_conv_b_2': 2.739}
    for name, (base, spread) in spreads.items():
        noise = np.random.default_rng([zlib.crc32(name.encode()), seed]).standard_normal(out[name].shape)
        drawn = base * np.exp(spread * noise) if base else spread * noise
        out[name] = __import__('jax').numpy.asarray(drawn.astype(out[name].dtype))
    for name, factor in factors.items():
        out[name] = (out[name] * factor).astype(out[name].dtype)
    return out
```

```python
from contextlib import ExitStack

import numpy as np
import concourse.bass as bass
from concourse import mybir

F32 = mybir.dt.float32
F32R = mybir.dt.float32r
U32 = mybir.dt.uint32
ALU = mybir.AluOpType
ACT = mybir.ActivationFunctionType
AX_X = mybir.AxisListType.X

P = 128
SEQ = 256
NT = SEQ // P
D = 1024
KC = D // P
F = 2816
FC = F // P
GROUP = 256
GROUPS = F // GROUP
BANK = 512
RING = 6
SLOT = 2048
PIECE = SLOT // 2
EPS = 1e-6
BIG = 1.0e30
PARTS = [("ffn0", 3 * GROUPS), ("mix0", 10), ("mix0o", 4), ("ffn1", 3 * GROUPS), ("emb", 1), ("ple", 4),
         ("ab", 15), ("abo", 4), ("ffn2", 3 * GROUPS), ("hg", 16), ("hgo", 4), ("ffn3", 3 * GROUPS)]
LEVELS = [64, 32, 16, 8, 4, 2, 1]

MQ, MV, MO, MI, DQ, DK, DV, DG, DA = 0, 512, 1024, 1536, 1544, 2056, 2568, 3080, 3592
AQ, AK, AV, GQ, GK, GV, GR, GO = 0, 512, 640, 768, 1024, 1280, 1792, 1808


def shape_constants():
    j = np.arange(P)[:, None]
    i = np.arange(P)[None, :]
    parts = {"ident": (j == i), "upper": (j <= i)}
    for h in LEVELS:
        parts[f"level{h}"] = (j // (2 * h) == i // (2 * h)) & (j % (2 * h) < h) & (i % (2 * h) >= h)
    parts["prev"] = np.where(i > j, 0.0, -BIG)
    parts["own"] = np.where(i <= j, 0.0, -BIG)
    freq = np.float32(10000.0) ** (-np.arange(0, 64, 2, dtype=np.float32) / np.float32(64))
    ang = (np.arange(SEQ, dtype=np.float32)[:, None] * freq[None, :]).reshape(NT, P, 32)
    for name, f in (("cos", np.cos), ("sin", np.sin)):
        for t in range(NT):
            parts[f"{name}{t}"] = f(ang[t].astype(np.float64))
    at, cols, n = {}, [], 0
    for name, a in parts.items():
        at[name] = n
        n += a.shape[1]
        cols.append(a.astype(np.float32))
    return at, np.ascontiguousarray(np.concatenate(cols, axis=1))


class Steps:

    def __init__(self, nc, ctx, numbered):
        self.nc, self.ctx, self.numbered = nc, ctx, numbered
        self.sems, self.count, self.made = {}, {}, {}

    def sem(self, name):
        if name not in self.sems:
            self.sems[name] = self.ctx.enter_context(self.nc.semaphore(name))
        return self.sems[name]

    def did(self, engine, name):
        assert name not in self.made, name
        self.count[engine] = self.count.get(engine, 0) + 1
        self.made[name] = (f"{engine}_done", self.count[engine])
        return self.sem(f"{engine}_done"), 1

    def after(self, name):
        if self.numbered is None:
            return self.sem("pe_done"), 1
        s, n = self.numbered[name]
        return self.sem(s), n


def build(nc, A, out, numbered, stop=None):
    const_at, _ = shape_constants()
    ctx = ExitStack()
    with ctx:
        steps = Steps(nc, ctx, numbered)
        after = steps.after

        def sb(name, shape, dt=F32):
            return ctx.enter_context(nc.sbuf_tensor(name, shape, dt))

        def sem(name):
            return ctx.enter_context(nc.semaphore(name))

        raw = sb("raw", [P, RING, SLOT])
        whi = sb("whi", [P, RING, PIECE], F32R)
        wlo = sb("wlo", [P, RING, PIECE], F32R)
        xh = sb("xh", [P, KC, SEQ], F32R)
        xl = sb("xl", [P, KC, SEQ], F32R)
        hidh = sb("hidh", [P, 2, 2, SEQ], F32R)
        hidl = sb("hidl", [P, 2, 2, SEQ], F32R)
        h = sb("h", [P, NT, D])
        gain = sb("gain", [P, 2, D])
        const = sb("const", [P, A["const"].shape[1]])
        small = sb("small", [P, 1792])
        zero_r = sb("zero_r", [P, P], F32R)
        arena = sb("arena", [P, 13824])
        psum = ctx.enter_context(nc.psum_tensor("psum", [P, 8, BANK], F32))

        class Columns:
            def __init__(self, tile):
                self.tile, self.n = tile, 0

            def take(self, n, parts=P):
                a = self.tile[0:parts, self.n:self.n + n]
                self.n += n
                assert self.n <= self.tile.shape[1], self.n
                return a

        few = Columns(small)

        def cst(name, n=P):
            return const[:, const_at[name]:const_at[name] + n]

        ident = cst("ident")

        sg = arena[:, 0:1024].rearrange("p (a c t) -> p a c t", a=2, c=2)
        hp = arena[:, 1024:2048].rearrange("p (a c t) -> p a c t", a=2, c=2)
        cg = arena[:, 2048:4096].rearrange("p (a g c t) -> p a g c t", a=2, g=2, c=2)
        nrm = arena[:, 11776:13824].rearrange("p (t d) -> p t d", t=NT)
        taps = sb("taps", [P, 2, 4, 2 * FC])

        loaded = [sem(f"loaded{n}") for n in range(RING)]
        hi_done = sem("hi_done")
        lo_done = sem("lo_done")
        used = sem("used")
        sg_ready = sem("sg_ready")
        hp_ready = sem("hp_ready")
        hid_hi = sem("hid_hi")
        hid_lo = sem("hid_lo")
        conv_mid = sem("conv_mid")
        conv_one = sem("conv_one")
        conv_all = sem("conv_all")
        params = sem("params")
        x_in = sem("x_in")
        gains_in = [sem(f"gain_in{n}") for n in range(2)]
        out_sem = sem("stored")

        ng = A["norm_gains_2"]
        GAINS = [("ffn0", [A["ffn1_norm"][0]], "ffn0.n1"), ("mix0", [A["mix_norm"][0]], "mix0.n1"),
                 ("ffn1", [A["ffn2_norm"][0]], "ffn1.n1"), ("emb", [A["ple_norm"][0]], "emb.e1"),
                 ("ple", [A["ple_gate_norm"][0]], "ple.n1"),
                 ("ab", [ng[0, 0]], "ab.n1"), ("abh", [A["ab_m_norm_2"][0], A["ab_g_norm_2"][0]], "ab.last"),
                 ("abp", [ng[0, 1]], "abo.p1"),
                 ("ffn2", [ng[0, 2]], "ffn2.n1"), ("ffn2p", [ng[0, 3]], "ffn2.p1"),
                 ("hg", [ng[1, 0]], "hg.n1"), ("hgh", [A["c_norm_2"][0]], "hg.last"), ("hgp", [ng[1, 1]], "hgo.p1"),
                 ("ffn3", [ng[1, 2]], "ffn3.n1"), ("ffn3p", [ng[1, 3]], "ffn3.p1")]
        gain_at, counts = {}, [0, 0]
        for n, (name, parts, last_use) in enumerate(GAINS):
            counts[n % 2] += 16 * len(parts)
            gain_at[name] = (n, counts[n % 2])

        def pool_gain(pool, name):
            n, _ = gain_at[name]
            if n >= 2:
                pool.wait_ge(*after(GAINS[n - 2][2]))
            at = 0
            for v in GAINS[n][1]:
                pool.dma_start(gain[:, n % 2, at:at + v.shape[0]], v.partition_broadcast(P)).then_inc(gains_in[n % 2], 16)
                at += v.shape[0]

        def next_gain(pool, gains):
            name = next(gains, None)
            if name:
                pool_gain(pool, name)

        def gain_of(dve, name):
            n, value = gain_at[name]
            dve.wait_ge(gains_in[n % 2], value)
            return gain[:, n % 2, :]

        SWIGLU = [(A["ffn1_w_gate"][0], A["ffn1_w_up"][0], A["ffn1_w_down"][0]),
                  (A["ffn2_w_gate"][0], A["ffn2_w_up"][0], A["ffn2_w_down"][0])]
        CONVFF = [(A["ffn_w_up_2"][l][:, 0:F], A["ffn_w_up_2"][l][:, F:2 * F], A["ffn_w_down_2"][l]) for l in range(2)]
        FFN = SWIGLU + CONVFF

        first_slot, total_slots = {}, 0
        for part, slots in PARTS:
            first_slot[part] = total_slots
            total_slots += slots

        def sp_slot(sp, s, i, shape, parts):
            if not (isinstance(i, int) and s + RING * i < RING):
                sp.wait_ge(lo_done, 2 * (s - RING) + 2 + 2 * RING * i)
            a, b = shape
            view = raw[:, s % RING, 0:a * b].rearrange("p (a b) -> p a b", a=a)
            for where, src in parts:
                dst = view[where] if isinstance(where, tuple) else view[:, where, :]
                sp.dma_start(dst, src).then_inc(loaded[s % RING], 16)

        def sp_gate_up(sp, s, i, n, g):
            wg, wu, _ = FFN[n]
            for k in range(2):
                sp_slot(sp, s + k, i, (4, 512), [
                    ((slice(None), slice(None), slice(256 * j, 256 * j + 256)),
                     w.rearrange("(k p) n -> p k n", p=P)[:, 4 * k:4 * k + 4, bass.ds(g * GROUP, GROUP)])
                    for j, w in enumerate((wg, wu))])

        def sp_down(sp, s, i, n, g):
            wd = FFN[n][2].rearrange("(f p) n -> p f n", p=P)
            sp_slot(sp, s, i, (2, D), [(slice(c, c + 1), wd[:, bass.ds(g * 2 + c, 1), :]) for c in range(2)])

        def sp_ffn(sp, n):
            s = first_slot[f"ffn{n}"] + 2
            sp_gate_up(sp, s - 2, 0, n, 0)

            def body(i):
                for half in range(2):
                    sp_gate_up(sp, s + 3 * half, i, n, i * 2 + half + 1)
                    sp_down(sp, s + 3 * half + 2, i, n, i * 2 + half)
            body(0)
            with sp.Fori(1, GROUPS // 2) as i:
                body(i)
            sp_down(sp, s + 3 * (GROUPS - 1), 0, n, GROUPS - 1)

        def piece_of(p, shape):
            a, b = shape[0] // 2, shape[1]
            r = raw[:, (p // 2) % RING, (p % 2) * a * b:(p % 2 + 1) * a * b]
            return r, whi[:, p % RING, 0:a * b], wlo[:, p % RING, 0:a * b]

        def split_hi(act, p, shape=(4, 512), i=0):
            if p % 2 == 0:
                act.wait_ge(loaded[(p // 2) % RING], 32 * (p // 2 // RING + 1) + 32 * i)
            if not (isinstance(i, int) and p + 2 * RING * i < RING):
                act.wait_ge(used, p - RING + 1 + 2 * RING * i)
            r, hi, _ = piece_of(p, shape)
            nc.scalar.activation(hi, r, ACT.Copy).then_inc(hi_done, 1)

        def split_lo(dve, p, shape=(4, 512), i=0):
            dve.wait_ge(hi_done, p + 1 + 2 * RING * i)
            r, hi, lo = piece_of(p, shape)
            nc.vector.tensor_tensor(lo, r, hi.bitcast(F32), ALU.subtract).then_inc(lo_done, 1)

        def weights(p, a, b):
            return (whi[:, p % RING, 0:a * b].rearrange("p (a b) -> p a b", a=a),
                    wlo[:, p % RING, 0:a * b].rearrange("p (a b) -> p a b", a=a))

        def three(pe_out, sh, sl, mh, ml, start, stop):
            nc.tensor.matmul(pe_out, sh, mh, start=start, stop=False, skip_group_check=True)
            nc.tensor.matmul(pe_out, sh, ml, start=False, stop=False, skip_group_check=True)
            return nc.tensor.matmul(pe_out, sl, mh, start=False, stop=stop, skip_group_check=True)

        def pe_turn(pe, X, tile, chunks=KC, ready=None):
            for t in range(NT):
                pe.wait_ge(*after(ready or f"{X}.n{t}"))
                for b in range((chunks + 3) // 4):
                    for c in range(4 * b, min(4 * b + 4, chunks)):
                        last = nc.tensor.transpose(psum[:, 4 + 2 * t + b, (c % 4) * P:(c % 4) * P + P],
                                                   tile[:, t, c * P:c * P + P], ident)
                    last.then_inc(*steps.did("pe", f"{X}.T{t}{b}"))

        def turned(t, b, chunks):
            n = min(4, chunks - 4 * b)
            return (psum[:, 4 + 2 * t + b, 0:n * P].rearrange("p (c t) -> p c t", c=n),
                    xh[:, 4 * b:4 * b + n, t * P:t * P + P], xl[:, 4 * b:4 * b + n, t * P:t * P + P])

        def act_turn(act, X, chunks=KC):
            for t in range(NT):
                for b in range((chunks + 3) // 4):
                    src, hi, _ = turned(t, b, chunks)
                    act.wait_ge(*after(f"{X}.T{t}{b}"))
                    nc.scalar.activation(hi, src, ACT.Copy).then_inc(*steps.did("act", f"{X}.xh{t}{b}"))

        def dve_turn(dve, X, chunks=KC):
            for t in range(NT):
                for b in range((chunks + 3) // 4):
                    src, hi, lo = turned(t, b, chunks)
                    dve.wait_ge(*after(f"{X}.xh{t}{b}"))
                    last = nc.vector.tensor_tensor(lo, src, hi.bitcast(F32), ALU.subtract)
                    last.then_inc(*steps.did("dve", f"{X}.xl{t}{b}"))
                    final = f"{X}.xl{t}{b}"
            return final

        def turn_end(X, chunks=KC):
            return f"{X}.xl{NT - 1}{(chunks + 3) // 4 - 1}"

        half_power = few.take(64)
        junk, junk2 = few.take(1), few.take(1)

        def pool_rstd(pool, name, total, n, count, scratch):
            nc.gpsimd.tensor_scalar(scratch, total, 1.0 / count, EPS, ALU.mult, ALU.add)\
                .then_inc(*steps.did("pool", f"{name}.mean"))
            pool.wait_ge(*after(f"{name}.mean"))
            nc.gpsimd.tensor_tensor(scratch, scratch, half_power[:, 0:n], ALU.pow)\
                .then_inc(*steps.did("pool", name))

        square_sums = {}

        def sums(X, n):
            if X not in square_sums:
                square_sums[X] = (few.take(n), few.take(n))
            return square_sums[X]

        def act_norm(act, X, src):
            total, _ = sums(X, NT)
            for t in range(NT):
                act.wait_ge(*after(f"{src}.h{t}"))
                nc.scalar.activation(nrm[:, t, :], h[:, t, :], ACT.Square, accum_out=total[:, t:t + 1])\
                    .then_inc(*steps.did("act", f"{X}.ss{t}"))
            act_turn(act, X)

        def pool_norm(pool, X):
            total, r = sums(X, NT)
            for t in range(NT):
                pool.wait_ge(*after(f"{X}.ss{t}"))
                pool_rstd(pool, f"{X}.r{t}", total[:, t:t + 1], 1, D, r[:, t:t + 1])

        def dve_norm(dve, X):
            _, r = sums(X, NT)
            g = gain_of(dve, X)
            for t in range(NT):
                dve.wait_ge(*after(f"{X}.r{t}"))
                nc.vector.scalar_tensor_tensor(nrm[:, t, :], h[:, t, :], r[:, t:t + 1], g, ALU.mult, ALU.mult)\
                    .then_inc(*steps.did("dve", f"{X}.n{t}"))
            dve_turn(dve, X)

        def pe_unit(pe, p, rows=(), columns=(), shape=(4, 512), which=(0, 1, 2, 3)):
            for k in which:
                pe.wait_ge(lo_done, p + k + 1)
                wh, wl = weights(p + k, shape[0] // 2, shape[1])
                for kk in range(2):
                    kc = 2 * k + kk
                    for c0, c1, outs, starts in rows:
                        for t in range(NT):
                            tok = slice(t * P, t * P + P)
                            last = three(outs[t], xh[:, kc, tok], xl[:, kc, tok], wh[:, kk, c0:c1], wl[:, kk, c0:c1],
                                         start=(kc == 0 and starts[t]), stop=(kc == KC - 1))
                    for c0, o, starts in columns:
                        last = three(o, wh[:, kk, c0:c0 + P], wl[:, kk, c0:c0 + P], xh[:, kc, :], xl[:, kc, :],
                                     start=(kc == 0 and starts), stop=(kc == KC - 1))
                last.then_inc(used, 1)

        def split4(fn, eng, p, shape=(4, 512), which=(0, 1, 2, 3)):
            for k in which:
                fn(eng, p + k, shape)

        def pe_gate_up(pe, n, g, q, p, i):
            if not isinstance(g, int) or n * GROUPS + g >= 2:
                pe.wait_ge(hid_lo, g + n * GROUPS - 1)
            for k in range(4):
                pe.wait_ge(lo_done, p + k + 1 + 2 * RING * i)
                wh, wl = weights(p + k, 2, 512)
                for kk in range(2):
                    kc = 2 * k + kk
                    for c in range(2):
                        for j in range(2):
                            col = slice(256 * j + 128 * c, 256 * j + 128 * c + 128)
                            last = three(psum[:, 4 + 2 * q + c, 256 * j:256 * j + 256], wh[:, kk, col],
                                         wl[:, kk, col], xh[:, kc, :], xl[:, kc, :],
                                         start=(kc == 0 and j == 0), stop=(kc == KC - 1))
                last.then_inc(used, 1)

        def pe_down(pe, n, g, q, p, i):
            pe.wait_ge(hid_lo, g + n * GROUPS + 1)
            for c in range(2):
                pe.wait_ge(lo_done, p + c + 1 + 2 * RING * i)
                wh, wl = weights(p + c, 1, D)
                for t in range(NT):
                    for half in range(2):
                        tok, col = slice(t * P, t * P + P), slice(half * BANK, half * BANK + BANK)
                        last = three(psum[:, 2 * t + half, :], hidh[:, q, c, tok], hidl[:, q, c, tok],
                                     wh[:, 0, col], wl[:, 0, col], start=False, stop=True)
                last.then_inc(used, 1)

        def ffn_loop(eng, body):
            body(0)
            with eng.Fori(1, GROUPS // 2) as i:
                body(i)

        def pe_ffn(pe, n):
            X = f"ffn{n}"
            pe_turn(pe, X, nrm)
            pe.wait_ge(*after(turn_end(X)))
            for b in range(4):
                nc.tensor.matmul(psum[:, b, :], zero_r[:, :], xh[:, 0:2, :], start=True, stop=True, skip_group_check=True)
            p = 2 * first_slot[X]
            pe_gate_up(pe, n, 0, 0, p, 0)

            def body(i):
                for half in range(2):
                    q = p + 4 + 6 * half
                    pe_gate_up(pe, n, i * 2 + half + 1, (half + 1) % 2, q, i)
                    pe_down(pe, n, i * 2 + half, half, q + 4, i)
            ffn_loop(pe, body)
            pe_down(pe, n, GROUPS - 1, 0, p + 4 + 6 * (GROUPS - 1), 0)

        def act_hidden(act, n, g, q, p, i):
            G0 = n * GROUPS
            first = isinstance(g, int) and g == 0
            act.wait_ge(used, p + 2 * RING * i - (0 if first else 2))
            if n < 2:
                nc.scalar.activation(sg[:, q], psum[:, 4 + 2 * q:6 + 2 * q, 0:256], ACT.Silu).then_inc(sg_ready, 1)
                return
            for j in range(2):
                for c in range(2):
                    f = g * 2 + (FC * j + c)
                    last = nc.scalar.activation(cg[:, q, j, c, :], psum[:, 4 + 2 * q + c, 256 * j:256 * j + 256],
                                                ACT.Identity, scale=tap(n, 2, f), bias=tap(n, 3, f))
            last.then_inc(conv_mid, 1)
            act.wait_ge(conv_all, g + (G0 - 2 * GROUPS) + 1)
            nc.scalar.activation(sg[:, q], cg[:, q, 0], ACT.Silu).then_inc(sg_ready, 1)

        def tap(n, k, f):
            return taps[:, n - 2, k, bass.ds(f, 1)]

        def dve_hidden(dve, n, g, q, i):
            G0 = n * GROUPS
            if n < 2:
                dve.wait_ge(sg_ready, g + G0 + 1)
                nc.vector.tensor_tensor(hp[:, q], psum[:, 4 + 2 * q:6 + 2 * q, 256:512], sg[:, q], ALU.mult)\
                    .then_inc(hp_ready, 1)
                return
            dve.wait_ge(conv_mid, g + (G0 - 2 * GROUPS) + 1)
            for k, done in ((1, conv_one), (0, conv_all)):
                if k == 0:
                    dve.wait_ge(conv_one, g + (G0 - 2 * GROUPS) + 1)
                lag = 2 - k
                for j in range(2):
                    for c in range(2):
                        y = cg[:, q, j, c, lag:SEQ]
                        last = nc.vector.scalar_tensor_tensor(
                            y, psum[:, 4 + 2 * q + c, 256 * j:256 * j + SEQ - lag], tap(n, k, g * 2 + (FC * j + c)), y,
                            ALU.mult, ALU.add)
                last.then_inc(done, 1)
            dve.wait_ge(sg_ready, g + G0 + 1)
            nc.vector.tensor_tensor(hp[:, q], cg[:, q, 1], sg[:, q], ALU.mult).then_inc(hp_ready, 1)

        def act_hid_hi(act, n, g, q, p, i):
            act.wait_ge(hp_ready, g + n * GROUPS + 1)
            if not (isinstance(g, int) and g < 2):
                act.wait_ge(used, p - 6 + 2 * RING * i)
            nc.scalar.activation(hidh[:, q], hp[:, q], ACT.Copy).then_inc(hid_hi, 1)

        def dve_hid_lo(dve, n, g, q):
            dve.wait_ge(hid_hi, g + n * GROUPS + 1)
            nc.vector.tensor_tensor(hidl[:, q], hp[:, q], hidh[:, q].bitcast(F32), ALU.subtract).then_inc(hid_lo, 1)

        def act_ffn(act, n, src):
            act_norm(act, f"ffn{n}", src)
            p = 2 * first_slot[f"ffn{n}"]
            split4(split_hi, act, p)

            def body(i):
                for half in range(2):
                    q, g = p + 4 + 6 * half, i * 2 + half
                    for k in range(2):
                        split_hi(act, q + k, i=i)
                    act_hidden(act, n, g, half, q, i)
                    for k in range(2, 4):
                        split_hi(act, q + k, i=i)
                    act_hid_hi(act, n, g, half, q, i)
                    for k in range(4, 6):
                        split_hi(act, q + k, shape=(2, D), i=i)
            ffn_loop(act, body)
            q, g = p + 4 + 6 * (GROUPS - 1), GROUPS - 1
            for k in range(2):
                split_hi(act, q + k, shape=(2, D))
            act_hidden(act, n, g, 0, q, 0)
            act_hid_hi(act, n, g, 0, q, 0)

        def dve_ffn(dve, n):
            dve_norm(dve, f"ffn{n}")
            p = 2 * first_slot[f"ffn{n}"]
            split4(split_lo, dve, p)

            def body(i):
                for half in range(2):
                    q, g = p + 4 + 6 * half, i * 2 + half
                    for k in range(2):
                        split_lo(dve, q + k, i=i)
                    dve_hidden(dve, n, g, half, i)
                    for k in range(2, 4):
                        split_lo(dve, q + k, i=i)
                    dve_hid_lo(dve, n, g, half)
                    for k in range(4, 6):
                        split_lo(dve, q + k, shape=(2, D), i=i)
            ffn_loop(dve, body)
            q, g = p + 4 + 6 * (GROUPS - 1), GROUPS - 1
            for k in range(2):
                split_lo(dve, q + k, shape=(2, D))
            dve_hidden(dve, n, g, 0, 0)
            dve_hid_lo(dve, n, g, 0)
            if n < 2:
                dve_add(dve, f"ffn{n}", 0.5, 2 * (first_slot[f"ffn{n}"] + 3 * GROUPS))

        def acc(t):
            return psum[:, 2 * t:2 * t + 2, :]

        def rows(a):
            return a.rearrange("p (b n) -> p b n", b=2)

        def dve_add(dve, X, factor, pieces):
            dve.wait_ge(used, pieces)
            for t in range(NT):
                nc.vector.scalar_tensor_tensor(rows(h[:, t, :]), acc(t), factor, rows(h[:, t, :]), ALU.mult, ALU.add)\
                    .then_inc(*steps.did("dve", f"{X}.h{t}"))

        def act_post(act, X, pieces):
            total, _ = sums(X + ".p", NT)
            act.wait_ge(used, pieces)
            for t in range(NT):
                nc.scalar.activation(rows(nrm[:, t, :]), acc(t), ACT.Square, accum_out=total[:, t:t + 1])\
                    .then_inc(*steps.did("act", f"{X}.ps{t}"))

        def pool_post(pool, X):
            total, r = sums(X + ".p", NT)
            for t in range(NT):
                pool.wait_ge(*after(f"{X}.ps{t}"))
                pool_rstd(pool, f"{X}.pr{t}", total[:, t:t + 1], 1, D, r[:, t:t + 1])

        def dve_post(dve, X):
            _, r = sums(X + ".p", NT)
            g = gain_of(dve, {"abo": "abp", "hgo": "hgp"}.get(X, X + "p"))
            for t in range(NT):
                dve.wait_ge(*after(f"{X}.pr{t}"))
                nc.vector.scalar_tensor_tensor(rows(nrm[:, t, :]), acc(t), r[:, t:t + 1], rows(g), ALU.mult, ALU.mult)\
                    .then_inc(*steps.did("dve", f"{X}.p{t}"))
                dve.wait_ge(*after(f"{X}.p{t}"))
                nc.vector.tensor_tensor(h[:, t, :], h[:, t, :], nrm[:, t, :], ALU.add)\
                    .then_inc(*steps.did("dve", f"{X}.h{t}"))

        ALL = slice(None)

        def unit(w, *cols):
            wv = w.rearrange("(k p) n -> p k n", p=P)
            width = sum(b - a for a, b in cols)
            if len(cols) == 1:
                a, b = cols[0]
                return [((4, width), [(slice(2 * m, 2 * m + 2), wv[:, 4 * k + 2 * m:4 * k + 2 * m + 2, a:b])
                                      for m in range(2)]) for k in range(2)]
            (a, b), (c, d) = cols
            return [((4, width), [((ALL, ALL, slice(0, b - a)), wv[:, 4 * k:4 * k + 4, a:b]),
                                  ((ALL, ALL, slice(b - a, width)), wv[:, 4 * k:4 * k + 4, c:d])]) for k in range(2)]

        w_in, w_ple, ab_in, c_in = A["w_in"][0], A["ple_w_gate"][0], A["ab_w_in_2"][0], A["c_w_in_2"][0]
        w_emb = A["ple_w_proj"][0].rearrange("(k p) n -> p k n", p=P)
        PROJ = {
            "mix0": [unit(w_in, (AQ, AK)), unit(w_in, (AK, GK)), unit(w_in, (GK, GV), (GR, GO)),
                     unit(w_in, (GV, GR)), unit(w_in, (GO, GO + 512))],
            "mix0o": [unit(A["w_out"][0], (n, n + 512)) for n in (0, 512)],
            "emb": [[((2, D), [(slice(c, c + 1), w_emb[:, c:c + 1, :]) for c in range(2)])]],
            "ple": [unit(w_ple, (n, n + 512)) for n in (0, 512)],
            "abo": [unit(A["ab_w_out_2"][0], (n, n + 512)) for n in (0, 512)],
            "hgo": [unit(A["c_w_out_2"][0], (n, n + 512)) for n in (0, 512)],
            "ab": [[((8, 16), [((ALL, ALL, slice(8 * m, 8 * m + 8)), ab_in.rearrange("(k p) n -> p k n", p=P)[:, :, a:a + 8])
                               for m, a in enumerate((MI, DA))])],
                   unit(ab_in, (MQ, MV)), unit(ab_in, (MV, MO)), unit(ab_in, (DK, DV)), unit(ab_in, (DQ, DK)),
                   unit(ab_in, (DV, DG)), unit(ab_in, (MO, MI)), unit(ab_in, (DG, DA))],
            "hg": [unit(c_in, (n, n + 512)) for n in (1024, 1536, 0, 512, 2048, 2560, 3072, 3584)],
        }

        def sp_proj(sp, part):
            s = first_slot[part]
            for slots in PROJ[part]:
                for shape, loads in slots:
                    sp_slot(sp, s, 0, shape, loads)
                    s += 1

        def piece_at(part, u):
            return 2 * (first_slot[part] + 2 * u)

        def bank(b, a=0, n=BANK):
            return psum[:, b, a:a + n]

        def out_units(pe, part):
            for u in range(2):
                pe_unit(pe, piece_at(part, u), rows=[(0, 512, [bank(u), bank(2 + u)], (True, True))])

        mix = nrm
        PAIR = 4
        sqa, qn, kn = arena[:, 0:1280], arena[:, 1280:2304], arena[:, 2304:2560]
        qr, kr, kd, tmp = arena[:, 2560:3584], arena[:, 3584:3840], arena[:, 3840:4352], arena[:, 4352:4864]
        av = arena[:, 4992:5248].rearrange("p (t n) -> p t n", t=NT)
        qT, kT = arena[:, 5248:6272], arena[:, 6272:6784]
        s0 = arena[:, 6784:7808].rearrange("p (k n) -> p k n", k=8)
        s1 = arena[:, 7808:9856].rearrange("p (k n) -> p k n", k=8)
        eT = arena[:, 0:3072].rearrange("p (s k n) -> p s k n", s=3, k=8)
        a_ss, a_r = few.take(20), few.take(20)
        a_max, a_neg, a_den, a_exs = few.take(16), few.take(16), few.take(16), few.take(16)

        def pe_a_proj(pe):
            X = "mix0"
            pe_turn(pe, X, nrm)
            pe.wait_ge(*after(turn_end(X)))
            pe_unit(pe, piece_at(X, 0), rows=[(0, 512, [bank(0), bank(1)], (True, True))])
            pe_unit(pe, piece_at(X, 1), rows=[(0, 256, [bank(2, 0, 256), bank(3, 0, 256)], (True, True))],
                    columns=[(256, bank(4, 0, 256), True), (384, bank(4, 256, 256), False)])
            pe_unit(pe, piece_at(X, 2), columns=[(0, bank(5, 0, 256), True), (128, bank(5, 256, 256), False)],
                    rows=[(256, 272, [bank(6, 0, 16), bank(6, 16, 16)], (True, False))], shape=(4, 272))

        def act_a_rows(act):
            act.wait_ge(used, piece_at("mix0", 2))
            sq = sqa.rearrange("p (t n) -> p t n", t=NT)
            nc.scalar.activation(sq[:, :, 0:512], psum[:, 0:2, :], ACT.Square).then_inc(*steps.did("act", "a.sq"))
            nc.scalar.activation(sq[:, :, 512:640], psum[:, 2:4, 0:128], ACT.Square).then_inc(*steps.did("act", "a.sk"))
            nc.scalar.activation(av, psum[:, 2:4, 128:256], ACT.Copy).then_inc(*steps.did("act", "a.v"))

        def pool_a(pool):
            pool.wait_ge(*after("a.ss"))
            pool_rstd(pool, "a.r", a_ss, 20, 64, a_r)

        def dve_a_rows(dve):
            sq = sqa.rearrange("p (t n) -> p t n", t=NT)
            ss = a_ss.rearrange("p (t k) -> p t k", t=NT)
            r = a_r.rearrange("p (t k) -> p t k", t=NT)
            dve.wait_ge(*after("a.sk"))
            nc.vector.tensor_reduce(ss, sq.rearrange("p t (k d) -> p t k d", d=64), AX_X, ALU.add)\
                .then_inc(*steps.did("dve", "a.ss"))
            dve.wait_ge(*after("a.r"))
            dve.wait_ge(*after("a.v"))
            nc.vector.tensor_tensor(kn.rearrange("p (t k d) -> p t k d", t=2, k=2),
                                    psum[:, 2:4, 0:128].rearrange("p t (k d) -> p t k d", k=2),
                                    r[:, :, 8:10].unsqueeze(3).broadcast_to([P, 2, 2, 64]), ALU.mult)\
                .then_inc(*steps.did("dve", "a.kn"))
            nc.vector.tensor_tensor(qn.rearrange("p (t k d) -> p t k d", t=2, k=8),
                                    psum[:, 0:2, :].rearrange("p t (k d) -> p t k d", k=8),
                                    r[:, :, 0:8].unsqueeze(3).broadcast_to([P, 2, 8, 64]), ALU.mult)\
                .then_inc(*steps.did("dve", "a.qn"))
            for name, n, heads, g in (("k", kn, 4, "k_norm"), ("q", qn, 16, "q_norm")):
                v = n.rearrange("p (k d) -> p k d", d=64)
                dve.wait_ge(*after(f"a.{name}n"))
                nc.vector.tensor_tensor(v, v, spread[g].unsqueeze(1).broadcast_to([P, heads, 64]), ALU.mult)\
                    .then_inc(*steps.did("dve", f"a.{name}g"))
            cos, sin = (cst(f"{f}0", 64).rearrange("p (t d) -> p t d", t=2) for f in ("cos", "sin"))
            for name, n, out_, heads in (("k", kn, kr, 2), ("q", qn, qr, 8)):
                v = n.rearrange("p (t k d) -> p t k d", t=2, k=heads)
                o = out_.rearrange("p (t k d) -> p t k d", t=2, k=heads)
                t_ = tmp[:, 0:64 * heads].rearrange("p (t k d) -> p t k d", t=2, k=heads)
                c, s = (a.unsqueeze(2).broadcast_to([P, 2, heads, 32]) for a in (cos, sin))
                lo, hi = slice(0, 32), slice(32, 64)
                dve.wait_ge(*after(f"a.{name}g"))
                nc.vector.tensor_tensor(o[:, :, :, lo], v[:, :, :, lo], c, ALU.mult).then_inc(*steps.did("dve", f"a.{name}1"))
                nc.vector.tensor_tensor(o[:, :, :, hi], v[:, :, :, hi], c, ALU.mult).then_inc(*steps.did("dve", f"a.{name}2"))
                if name == "q":
                    dve.wait_ge(*after("a.kr"))
                nc.vector.tensor_tensor(t_, v[:, :, :, hi], s, ALU.mult).then_inc(*steps.did("dve", f"a.{name}3"))
                dve.wait_ge(*after(f"a.{name}3"))
                nc.vector.tensor_tensor(o[:, :, :, lo], o[:, :, :, lo], t_, ALU.subtract).then_inc(*steps.did("dve", f"a.{name}4"))
                dve.wait_ge(*after(f"a.{name}4"))
                nc.vector.tensor_tensor(t_, v[:, :, :, lo], s, ALU.mult).then_inc(*steps.did("dve", f"a.{name}5"))
                dve.wait_ge(*after(f"a.{name}5"))
                nc.vector.tensor_tensor(o[:, :, :, hi], o[:, :, :, hi], t_, ALU.add).then_inc(*steps.did("dve", f"a.{name}r"))

        def act_a_dup(act):
            act.wait_ge(*after("a.kr"))
            nc.scalar.activation(kd.rearrange("p (k a d) -> p k a d", k=4, a=2),
                                 kr.rearrange("p (k d) -> p k d", k=4).unsqueeze(2).broadcast_to([P, 4, 2, 64]), ACT.Copy)\
                .then_inc(*steps.did("act", "a.kd"))

        def pe_a_turn(pe):
            pe.wait_ge(*after("a.qr"))
            pe.wait_ge(*after("a.kd"))
            for t in range(NT):
                for pair in range(4):
                    nc.tensor.transpose(bank(pair // 2, (pair % 2) * 256 + t * P, P),
                                        qr[:, t * 512 + pair * P:t * 512 + pair * P + P], ident)
                for kv in range(2):
                    last = nc.tensor.transpose(bank(2, kv * 256 + t * P, P),
                                               kd[:, (2 * t + kv) * P:(2 * t + kv) * P + P], ident)
            last.then_inc(*steps.did("pe", "a.T"))

        def act_a_turned(act):
            act.wait_ge(*after("a.T"))
            nc.scalar.activation(rows(qT), psum[:, 0:2, :], ACT.Copy).then_inc(*steps.did("act", "a.qT"))

        def dve_a_turned(dve):
            dve.wait_ge(*after("a.T"))
            nc.vector.tensor_copy(kT, bank(2)).then_inc(*steps.did("dve", "a.kT"))

        SCORE_BANKS = [[2, 4], [5, 6]]

        def pe_a_scores(pe):
            for name in ("a.qT", "a.kT", "g.q", "g.k", "g.glr"):
                pe.wait_ge(*after(name))
            for par in range(2):
                part = slice(64 * par, 64 * par + 64)
                for i in range(4):
                    pair, kv = i, i // 2
                    nc.tensor.matmul(bank(par, i * P, P), qT[part, pair * 256:pair * 256 + P],
                                     kT[part, kv * 256:kv * 256 + P], start=True, stop=True)
                    last = nc.tensor.matmul(bank(SCORE_BANKS[par][i // 2], (i % 2) * 256, 256),
                                            qT[part, pair * 256 + P:pair * 256 + 2 * P],
                                            kT[part, kv * 256:kv * 256 + 256], start=True, stop=True)
            last.then_inc(*steps.did("pe", "a.S"))

        def dve_a_softmax(dve):
            dve.wait_ge(*after("a.S"))
            for par in range(2):
                nc.vector.scalar_tensor_tensor(s0[:, 4 * par:4 * par + 4, :], bank(par).rearrange("p (k n) -> p k n", k=4), 0.125,
                                               cst("own").unsqueeze(1).broadcast_to([P, 4, P]), ALU.mult, ALU.add)
                for m in range(2):
                    last = nc.vector.scalar_tensor_tensor(
                        s1[:, 4 * par + 2 * m:4 * par + 2 * m + 2, :],
                        bank(SCORE_BANKS[par][m]).rearrange("p (k n) -> p k n", k=2), 0.125,
                        cst("prev", 256).unsqueeze(1).broadcast_to([P, 2, 256]), ALU.mult, ALU.add)
            last.then_inc(*steps.did("dve", "a.masked"))
            dve.wait_ge(*after("a.masked"))
            nc.vector.tensor_reduce(a_max[:, 0:8], s0, AX_X, ALU.max).then_inc(*steps.did("dve", "a.m0"))
            nc.vector.tensor_reduce(a_max[:, 8:16], s1, AX_X, ALU.max).then_inc(*steps.did("dve", "a.m1"))
            dve.wait_ge(*after("a.m1"))
            sink = spread["attn_sinks"].rearrange("p (i q) -> p q i", q=2).unsqueeze(1).broadcast_to([P, 2, 2, 4])
            by_head = lambda a: a.rearrange("p (t q i) -> p t q i", t=2, q=2)
            nc.vector.tensor_tensor(by_head(a_max), by_head(a_max), sink, ALU.max).then_inc(*steps.did("dve", "a.m"))
            dve.wait_ge(*after("a.m"))
            nc.vector.tensor_scalar(a_neg, a_max, -1.0, None, ALU.mult).then_inc(*steps.did("dve", "a.neg"))
            nc.vector.tensor_tensor(by_head(a_exs), sink, by_head(a_max), ALU.subtract).then_inc(*steps.did("dve", "a.sm"))

        def act_a_exp(act):
            act.wait_ge(*after("a.neg"))
            for k in range(8):
                nc.scalar.activation(s0[:, k, :], s0[:, k, :], ACT.Exp, bias=a_neg[:, k:k + 1],
                                     accum_out=a_den[:, k:k + 1]).then_inc(*steps.did("act", f"a.e0{k}"))
            act.wait_ge(*after("a.sm"))
            nc.scalar.activation(a_exs, a_exs, ACT.Exp).then_inc(*steps.did("act", "a.exs"))
            for k in range(8):
                nc.scalar.activation(s1[:, k, :], s1[:, k, :], ACT.Exp, bias=a_neg[:, 8 + k:9 + k],
                                     accum_out=a_den[:, 8 + k:9 + k]).then_inc(*steps.did("act", f"a.e1{k}"))

        def dve_a_den(dve):
            dve.wait_ge(*after("a.e17"))
            nc.vector.tensor_tensor(a_den, a_den, a_exs, ALU.add).then_inc(*steps.did("dve", "a.den"))
            dve.wait_ge(*after("a.den"))
            nc.vector.reciprocal(a_den, a_den).then_inc(*steps.did("dve", "a.rden"))

        def pe_a_probs(pe):
            pe.wait_ge(*after("a.masked"))
            for g, (src, at, b) in enumerate(((s0, 0, (0, 1)), (s1, 0, (2, 4)), (s1, P, (5, 6)))):
                pe.wait_ge(*after("a.e07" if g == 0 else "a.e17"))
                for k in range(8):
                    last = nc.tensor.transpose(bank(b[k // 4], (k % 4) * P, P), src[:, k, at:at + P], ident)
                    if k % 4 == 3:
                        last.then_inc(*steps.did("pe", f"a.eT{g}{k // 4}"))

        def act_a_probs(act):
            for g, b in ((0, 0), (1, 2), (2, 5)):
                act.wait_ge(*after(f"a.eT{g}0"))
                nc.scalar.activation(eT[:, g, 0:4, :], bank(b).rearrange("p (k n) -> p k n", k=4), ACT.Copy)\
                    .then_inc(*steps.did("act", f"a.pT{g}0"))

        def dve_a_probs(dve):
            for g, b in ((0, 1), (1, 4), (2, 6)):
                dve.wait_ge(*after(f"a.eT{g}1"))
                nc.vector.tensor_copy(eT[:, g, 4:8, :], bank(b).rearrange("p (k n) -> p k n", k=4))\
                    .then_inc(*steps.did("dve", f"a.pT{g}1"))

        def pe_a_out(pe):
            pe.wait_ge(*after("a.v"))
            for g, t, tv in ((0, 0, 0), (1, 1, 0), (2, 1, 1)):
                for name in ("a.pT00", "a.pT01") if g == 0 else ("a.pT20", "a.pT21"):
                    pe.wait_ge(*after(name))
                if g == 2:
                    continue
                for k in range(8):
                    hd = (k % 4) * 2 + k // 4
                    kv = hd // 4
                    last = nc.tensor.matmul(bank(t, hd * 64, 64), eT[:, g, k, :], av[:, tv, kv * 64:kv * 64 + 64],
                                            start=True, stop=(g == 0))
                    if g == 1:
                        last = nc.tensor.matmul(bank(t, hd * 64, 64), eT[:, 2, k, :], av[:, 1, kv * 64:kv * 64 + 64],
                                                start=False, stop=True)
                if g == 0:
                    pe.wait_ge(*after("a.pT20"))
                    pe.wait_ge(*after("a.pT21"))
            last.then_inc(*steps.did("pe", "a.O"))

        def dve_a_out(dve):
            dve.wait_ge(*after("a.O"))
            for t in range(NT):
                heads = lambda a: a.rearrange("p (i q d) -> p q i d", q=2, d=64)
                nc.vector.tensor_tensor(heads(mix[:, t, 0:512]), heads(bank(t)),
                                        a_den[:, 8 * t:8 * t + 8].rearrange("p (q i) -> p q i", q=2).unsqueeze(3)
                                        .broadcast_to([P, 2, 4, 64]), ALU.mult).then_inc(*steps.did("dve", f"a.mix{t}"))

        gq, gk = arena[:, 9856:10368], arena[:, 10368:10880]
        glr, glrT = arena[:, 10880:10912], arena[0:16, 10912:11168]
        gv = arena[:, 3072:4096].rearrange("p (t n) -> p t n", t=NT)
        sil = arena[:, 8832:9856].rearrange("p (t n) -> p t n", t=NT)
        la, gb = arena[:, 4096:4608], arena[:, 6272:6784]
        lt = arena[:, 9344:9856]
        g_e, g_l = arena[:, 5248:5760], (arena[:, 5760:6272], arena[:, 6784:7296])
        g_at = arena[:, 7296:8320].rearrange("p (q n) -> p q n", q=2)
        g_cross = arena[:, 8320:8832].rearrange("p (q n) -> p q n", q=2)
        osq = arena[:, 0:1024]
        ones = few.take(1)
        g_ss, g_r = few.take(8), few.take(8)

        def act_g_q(act):
            act.wait_ge(used, piece_at("mix0", 2))
            nc.scalar.activation(gq, bank(4), ACT.Copy, scale=0.125).then_inc(*steps.did("act", "g.q"))

        def dve_g_k(dve):
            dve.wait_ge(used, piece_at("mix0", 3))
            nc.vector.tensor_copy(gk, bank(5)).then_inc(*steps.did("dve", "g.k"))
            nc.vector.tensor_copy(glr, bank(6, 0, 32)).then_inc(*steps.did("dve", "g.glr"))

        def pe_g_v(pe):
            pe.wait_ge(*after("a.kn"))
            pe_unit(pe, piece_at("mix0", 3), rows=[(0, 512, [bank(3), bank(7)], (True, True))])

        def act_g_v(act):
            act.wait_ge(used, piece_at("mix0", 4))
            act.wait_ge(*after("a.T"))
            for t, b in ((0, 3), (1, 7)):
                nc.scalar.activation(gv[:, t, :], bank(b), ACT.Copy).then_inc(*steps.did("act", f"g.v{t}"))

        def pe_g_gate(pe):
            pe.wait_ge(*after("g.v1"))
            pe_unit(pe, piece_at("mix0", 4), rows=[(0, 512, [bank(3), bank(7)], (True, True))])

        def pe_g_alpha(pe):
            pe.wait_ge(*after("a.pT21"))
            for t in range(NT):
                last = nc.tensor.transpose(psum[0:16, 6, t * P:t * P + P], glr[:, t * 16:t * 16 + 16], ident)
            last.then_inc(*steps.did("pe", "g.glrT"))
            pe.wait_ge(*after("g.rT"))
            for c in range(2):
                last = nc.tensor.matmul(bank(6, c * 256, 256), gate_up[:, c * P:c * P + P], glrT, start=(c == 0), stop=True,
                                        skip_group_check=True)
            last.then_inc(*steps.did("pe", "g.z"))

        def dve_g_alpha(dve):
            dve.wait_ge(*after("g.glrT"))
            nc.vector.tensor_copy(glrT, psum[0:16, 6, 0:256]).then_inc(*steps.did("dve", "g.rT"))
            dve.wait_ge(*after("g.z"))
            for c in range(2):
                nc.vector.tensor_scalar(la[:, c * 256:c * 256 + 256], bank(6, c * 256, 256), gate_bias[:, c:c + 1], None, ALU.add)\
                    .then_inc(*steps.did("dve", f"g.y{c}"))

        def act_g_alpha(act):
            act.wait_ge(*after("g.y1"))
            act.wait_ge(*after("a.eT21"))
            nc.scalar.activation(lt, la, ACT.Abs).then_inc(*steps.did("act", "g.abs"))
            act.wait_ge(*after("g.abs"))
            nc.scalar.activation(lt, lt, ACT.Exp, scale=-1.0).then_inc(*steps.did("act", "g.exp"))
            act.wait_ge(*after("g.exp"))
            nc.scalar.activation(lt, lt, ACT.Ln, bias=1.0).then_inc(*steps.did("act", "g.ln"))

        def dve_g_sum(dve):
            dve.wait_ge(*after("g.ln"))
            nc.vector.scalar_tensor_tensor(la, la, 0.0, lt, ALU.min, ALU.subtract).then_inc(*steps.did("dve", "g.la"))
            dve.wait_ge(*after("g.la"))
            for c in range(2):
                part = slice(c * 256, c * 256 + 256)
                nc.vector.tensor_tensor_scan(gb[:, part], ones.broadcast_to([P, 256]), la[:, part], 0.0, ALU.mult, ALU.add)\
                    .then_inc(*steps.did("dve", f"g.cum{c}"))
            dve.wait_ge(*after("g.cum1"))
            nc.vector.tensor_scalar(gb, gb, 1.0 / 16.0, None, ALU.mult).then_inc(*steps.did("dve", "g.b"))

        def dve_level_x(dve, X, n, half, b, e, ready):
            blocks = lambda a: a.rearrange("p (m r) -> p m r", r=2 * half)
            left, right = slice(0, half), slice(half, 2 * half)
            for name in ready:
                dve.wait_ge(*after(name))
            ref = blocks(b)[:, :, half - 1:half].broadcast_to([P, b.shape[1] // (2 * half), half])
            nc.vector.tensor_tensor(blocks(e)[:, :, right], blocks(b)[:, :, right], ref, ALU.subtract)\
                .then_inc(*steps.did("dve", f"{X}.x{n}r"))
            nc.vector.tensor_tensor(blocks(e)[:, :, left], ref, blocks(b)[:, :, left], ALU.subtract)\
                .then_inc(*steps.did("dve", f"{X}.x{n}"))

        def dve_level_l(dve, X, n, half, q, k, e, l, ready=()):
            blocks = lambda a: a.rearrange("p (m r) -> p m r", r=2 * half)
            left, right = slice(0, half), slice(half, 2 * half)
            for name in ready:
                dve.wait_ge(*after(name))
            dve.wait_ge(*after(f"{X}.e{n}"))
            nc.vector.tensor_tensor(blocks(l)[:, :, right], blocks(q)[:, :, right], blocks(e)[:, :, right], ALU.mult)\
                .then_inc(*steps.did("dve", f"{X}.l{n}r"))
            nc.vector.tensor_tensor(blocks(l)[:, :, left], blocks(k)[:, :, left], blocks(e)[:, :, left], ALU.mult)\
                .then_inc(*steps.did("dve", f"{X}.l{n}"))

        def act_level(act, X, n, e):
            act.wait_ge(*after(f"{X}.x{n}"))
            nc.scalar.activation(e, e, ACT.Exp).then_inc(*steps.did("act", f"{X}.e{n}"))

        ALL_LEVELS = [P] + LEVELS
        BANKS2 = ((0, 1), (2, 3))

        def pe_g_levels(pe):
            for n in range(len(ALL_LEVELS) + 1):
                pe.wait_ge(*after("a.mix1" if n < 2 else f"g.put{n - 2}"))
                if n == 1:
                    pe.wait_ge(*after("g.sil1"))
                if n < len(ALL_LEVELS):
                    pe.wait_ge(*after(f"g.l{n}"))
                    l = r = g_l[n % 2]
                else:
                    l, r = gk, gq
                for par in range(2):
                    part = slice(64 * par, 64 * par + 64)
                    for c in range(2):
                        if n == 0:
                            last = nc.tensor.matmul(bank(BANKS2[0][par], c * P, P), l[part, c * 256:c * 256 + P],
                                                    r[part, c * 256 + P:c * 256 + 256], start=True, stop=True)
                            continue
                        for t in range(NT):
                            tok = slice(c * 256 + t * P, c * 256 + t * P + P)
                            last = nc.tensor.matmul(bank(BANKS2[n % 2][par], (2 * c + t) * P, P), l[part, tok], r[part, tok],
                                                    start=True, stop=True)
                last.then_inc(*steps.did("pe", f"g.P{n}"))

        def dve_g_put(dve, n):
            dve.wait_ge(*after(f"g.P{n}"))
            if n == 0:
                nc.vector.tensor_copy(g_cross, psum[:, 0:2, 0:256]).then_inc(*steps.did("dve", "g.put0"))
                return
            if n == 1:
                dve.wait_ge(*after("g.at0"))
            else:
                dve.wait_ge(*after(f"g.put{n - 1}"))
            mask = cst(f"level{ALL_LEVELS[n]}") if n < len(ALL_LEVELS) else ident
            for par in range(2):
                four = lambda a: a.rearrange("p (m i) -> p m i", m=4)
                last = nc.vector.copy_predicated(four(g_at[:, par, :]), mask.bitcast(U32).unsqueeze(1).broadcast_to([P, 4, P]),
                                                 four(bank(BANKS2[n % 2][par])))
            last.then_inc(*steps.did("dve", f"g.put{n}"))

        def dve_g_levels(dve):
            for n, half in enumerate(ALL_LEVELS):
                ready = ["g.b", "g.q"] if n == 0 else [f"g.l{n - 1}"]
                if n == 0:
                    ready.append("a.S")
                dve_level_x(dve, "g", n, half, gb, g_e, ready)
                if n >= 1:
                    dve_g_put(dve, n - 1)
                dve_level_l(dve, "g", n, half, gq, gk, g_e, g_l[n % 2], ([f"g.P{n - 2}"] if n >= 2 else []) + (["a.eT21"] if n == 1 else []))
            dve_g_put(dve, len(ALL_LEVELS) - 1)
            dve_g_put(dve, len(ALL_LEVELS))

        def act_g_levels(act):
            for n in range(len(ALL_LEVELS)):
                act_level(act, "g", n, g_e)

        def act_g_gate(act):
            act.wait_ge(used, piece_at("mix0o", 0))
            act.wait_ge(*after("a.eT21"))
            act.wait_ge(*after("g.la"))
            for t, b in ((0, 3), (1, 7)):
                nc.scalar.activation(sil[:, t, :], bank(b), ACT.Silu).then_inc(*steps.did("act", f"g.sil{t}"))

        def pe_g_out(pe):
            pe.wait_ge(*after(f"g.put{len(ALL_LEVELS)}"))
            pe.wait_ge(*after("g.v1"))
            for t in range(NT):
                for hd in range(4):
                    par, c = hd % 2, hd // 2
                    o = bank(4 + t, hd * P, P)
                    last = nc.tensor.matmul(o, g_at[:, par, (2 * c + t) * P:(2 * c + t) * P + P], gv[:, t, hd * P:hd * P + P],
                                            start=True, stop=(t == 0))
                    if t == 1:
                        last = nc.tensor.matmul(o, g_cross[:, par, c * P:c * P + P], gv[:, 0, hd * P:hd * P + P],
                                                start=False, stop=True)
            last.then_inc(*steps.did("pe", "g.O"))

        def act_heads(act, X, src, sq, done):
            act.wait_ge(*after(done))
            nc.scalar.activation(sq, src, ACT.Square).then_inc(*steps.did("act", f"{X}.osq"))

        def dve_g_out(dve):
            dve.wait_ge(*after("g.osq"))
            v = osq.rearrange("p (k d) -> p k d", d=P)
            nc.vector.tensor_reduce(g_ss, v, AX_X, ALU.add).then_inc(*steps.did("dve", "g.oss"))
            dve.wait_ge(*after("g.or"))
            o4 = psum[:, 4:6, :].rearrange("p t (k d) -> p t k d", d=P)
            r4 = g_r.rearrange("p (t k) -> p t k", t=NT).unsqueeze(3).broadcast_to([P, NT, 4, P])
            nc.vector.tensor_tensor(osq.rearrange("p (t k d) -> p t k d", t=NT, d=P), o4, r4, ALU.mult)\
                .then_inc(*steps.did("dve", "g.on"))
            dve.wait_ge(*after("g.on"))
            nc.vector.tensor_tensor(v, v, spread["gla_out_norm"].unsqueeze(1).broadcast_to([P, 8, P]), ALU.mult)\
                .then_inc(*steps.did("dve", "g.og"))
            dve.wait_ge(*after("g.og"))
            for t in range(NT):
                nc.vector.tensor_tensor(mix[:, t, 512:1024], osq[:, t * 512:t * 512 + 512], sil[:, t, :], ALU.mult)\
                    .then_inc(*steps.did("dve", f"mix0o.n{t}"))

        def sp_mix0(sp):
            sp_proj(sp, "mix0")
            sp_proj(sp, "mix0o")

        def pool_mix0(pool):
            pool_norm(pool, "mix0")
            pool_a(pool)
            pool.wait_ge(*after("a.eT21"))
            nc.gpsimd.memset(arena[:, 7296:8320], 0.0).then_inc(*steps.did("pool", "g.at0"))
            pool.wait_ge(*after("g.oss"))
            pool_rstd(pool, "g.or", g_ss, 8, P, g_r)

        def pe_mix0(pe):
            pe_a_proj(pe)
            pe_a_turn(pe)
            pe_g_v(pe)
            pe_a_scores(pe)
            pe_g_gate(pe)
            pe_a_probs(pe)
            pe_g_alpha(pe)
            pe_a_out(pe)
            pe_g_levels(pe)
            pe_g_out(pe)
            pe.wait_ge(*after("mix0o.n1"))
            pe_turn(pe, "mix0o", mix)
            pe.wait_ge(*after(turn_end("mix0o")))
            out_units(pe, "mix0o")

        def act_mix0(act, src):
            act_norm(act, "mix0", src)
            M = lambda u: piece_at("mix0", u)
            split4(split_hi, act, M(0))
            split4(split_hi, act, M(1))
            split4(split_hi, act, M(2), (4, 272), (0, 1))
            act_a_rows(act)
            act_g_q(act)
            split4(split_hi, act, M(2), (4, 272), (2, 3))
            act_a_dup(act)
            split4(split_hi, act, M(3))
            act_a_turned(act)
            split4(split_hi, act, M(4), which=(0, 1, 2))
            act_g_v(act)
            split4(split_hi, act, M(4), which=(3,))
            act_a_exp(act)
            act_a_probs(act)
            act_g_alpha(act)
            act_g_gate(act)
            act_g_levels(act)
            act_heads(act, "g", psum[:, 4:6, :], osq.rearrange("p (t n) -> p t n", t=NT), "g.O")
            split4(split_hi, act, piece_at("mix0o", 0))
            act_turn(act, "mix0o")
            split4(split_hi, act, piece_at("mix0o", 1))

        def dve_mix0(dve):
            dve_norm(dve, "mix0")
            M = lambda u: piece_at("mix0", u)
            split4(split_lo, dve, M(0))
            split4(split_lo, dve, M(1))
            split4(split_lo, dve, M(2), (4, 272), (0, 1))
            dve_a_rows(dve)
            split4(split_lo, dve, M(2), (4, 272), (2, 3))
            split4(split_lo, dve, M(3), which=(0, 1))
            dve_g_k(dve)
            dve_a_turned(dve)
            split4(split_lo, dve, M(3), which=(2, 3))
            split4(split_lo, dve, M(4), which=(0, 1, 2))
            dve_a_softmax(dve)
            split4(split_lo, dve, M(4), which=(3,))
            dve_a_den(dve)
            dve_a_probs(dve)
            dve_g_alpha(dve)
            dve_g_sum(dve)
            dve_a_out(dve)
            dve_g_levels(dve)
            dve_g_out(dve)
            split4(split_lo, dve, piece_at("mix0o", 0))
            dve_turn(dve, "mix0o")
            split4(split_lo, dve, piece_at("mix0o", 1))
            dve_add(dve, "mix0", 1.0, 2 * (first_slot["mix0o"] + 4))

        emb = arena[:, 0:2048].rearrange("p (t d) -> p t d", t=NT)
        sgm = arena[:, 2048:4096].rearrange("p (t d) -> p t d", t=NT)

        def pe_ple(pe):
            pe.wait_ge(hid_lo, 2 * GROUPS)
            pe_turn(pe, "emb", p_rows, chunks=2, ready="params")
            pe.wait_ge(*after(turn_end("emb", 2)))
            pe.wait_ge(*after("ffn1.h1"))
            p = 2 * first_slot["emb"]
            for c in range(2):
                pe.wait_ge(lo_done, p + c + 1)
                wh, wl = weights(p + c, 1, D)
                for t in range(NT):
                    for half in range(2):
                        tok, col = slice(t * P, t * P + P), slice(half * BANK, half * BANK + BANK)
                        last = three(bank(2 * t + half), xh[:, c, tok], xl[:, c, tok], wh[:, 0, col], wl[:, 0, col],
                                     start=(c == 0), stop=(c == 1))
                last.then_inc(used, 1)
            pe_turn(pe, "ple", nrm)
            pe.wait_ge(*after(turn_end("ple")))
            pe.wait_ge(*after("emb.e1"))
            out_units(pe, "ple")

        def act_ple(act):
            act_turn(act, "emb", chunks=2)
            for k in range(2):
                split_hi(act, 2 * first_slot["emb"] + k, (2, D))
            total, _ = sums("emb", NT)
            act.wait_ge(used, 2 * first_slot["ple"])
            for t in range(NT):
                nc.scalar.activation(rows(sgm[:, t, :]), acc(t), ACT.Square, accum_out=total[:, t:t + 1])\
                    .then_inc(*steps.did("act", f"emb.ss{t}"))
            act_norm(act, "ple", "ffn1")
            for u in range(2):
                split4(split_hi, act, piece_at("ple", u))
            act.wait_ge(used, 2 * first_slot["ab"])
            act.wait_ge(*after("emb.ss1"))
            for t in range(NT):
                nc.scalar.activation(rows(sgm[:, t, :]), acc(t), ACT.Sigmoid).then_inc(*steps.did("act", f"ple.g{t}"))

        def pool_ple(pool):
            total, r = sums("emb", NT)
            for t in range(NT):
                pool.wait_ge(*after(f"emb.ss{t}"))
                pool_rstd(pool, f"emb.r{t}", total[:, t:t + 1], 1, D, r[:, t:t + 1])
            pool_norm(pool, "ple")

        def dve_ple(dve):
            dve_turn(dve, "emb", chunks=2)
            for k in range(2):
                split_lo(dve, 2 * first_slot["emb"] + k, (2, D))
            _, r = sums("emb", NT)
            g = gain_of(dve, "emb")
            for t in range(NT):
                dve.wait_ge(*after(f"emb.r{t}"))
                nc.vector.scalar_tensor_tensor(rows(emb[:, t, :]), acc(t), r[:, t:t + 1], rows(g), ALU.mult, ALU.mult)\
                    .then_inc(*steps.did("dve", f"emb.e{t}"))
            dve_norm(dve, "ple")
            for u in range(2):
                split4(split_lo, dve, piece_at("ple", u))
            for t in range(NT):
                dve.wait_ge(*after(f"ple.g{t}"))
                nc.vector.tensor_tensor(sgm[:, t, :], sgm[:, t, :], emb[:, t, :], ALU.mult).then_inc(*steps.did("dve", f"ple.m{t}"))
                dve.wait_ge(*after(f"ple.m{t}"))
                nc.vector.tensor_tensor(h[:, t, :], h[:, t, :], sgm[:, t, :], ALU.add).then_inc(*steps.did("dve", f"ple.h{t}"))

        ab_p = {"small": 2 * first_slot["ab"]}
        for n, name in enumerate(("mqk", "mv", "dk", "dq", "dv", "mo", "dg")):
            ab_p[name] = ab_p["small"] + 2 + 4 * n
        Y = {"dk": arena[:, 0:1024], "dq": arena[:, 1024:2048], "dv": arena[:, 2048:3072], "mqk": arena[:, 8192:9216]}
        krow, qrow, vb = arena[:, 3072:4096], arena[:, 4096:5120], arena[:, 5120:6144]
        kb, kbT, kT2, qT2 = arena[:, 6144:7168], arena[:, 7168:8192], arena[:, 0:1024], arena[:, 1024:2048]
        mE, mvE = arena[:, 9216:10752], arena[:, 10752:11776]
        m_sq = arena[:, 8192:9216]
        dE, dNT, dat = arena[:, 8192:9216], arena[:, 9216:10240], arena[:, 2048:3072]
        dN, dXT, dX, dV = arena[:, 6144:7168], arena[:, 7168:8192], arena[:, 4096:5120], arena[:, 9216:10240]
        u0, dS, u1 = arena[:, 10240:10752], arena[:, 10752:11264], arena[:, 11264:11776]
        gtmp, d_sq = arena[:, 8192:9216], arena[:, 6144:7168]
        gz, gth, gcap, gex = few.take(32), few.take(16), few.take(16), few.take(24)
        glog, gcum, gbeta, gei, gt4 = few.take(16), few.take(16), few.take(8), few.take(8), few.take(8)
        m_den, m_ss, m_r, k_ss, k_r, q_ss, q_r, d_ss, d_r = (few.take(8) for _ in range(9))
        exa, glast, kdecay, eg1, beg = (few.take(4) for _ in range(5))
        by_t = lambda a: a.rearrange("p (t n) -> p t n", t=NT)
        heads4 = lambda a: a.rearrange("p (t k d) -> p t k d", t=NT, d=P)
        ones_sq = ones.broadcast_to([P, P])

        def spread_heads(a, t=None):
            return a.rearrange("p (t k) -> p t k", k=4).unsqueeze(3).broadcast_to([P, a.shape[1] // 4, 4, P])

        def conv_banks(name):
            return {"mqk": (0, 1), "dk": (0, 1), "dq": (6, 7), "dv": (0, 1)}[name]

        def conv_tap(name, k, c):
            if name == "mqk":
                return conv_m[:, k * 4 + c:k * 4 + c + 1]
            c += {"dq": 0, "dk": 4, "dv": 8}[name]
            return conv_g[:, k * 12 + c:k * 12 + c + 1]

        def pe_conv_unit(pe, name, ready=()):
            for r in ready:
                pe.wait_ge(*after(r))
            b = conv_banks(name)
            pe_unit(pe, ab_p[name], columns=[(c * P, bank(b[c // 2], (c % 2) * 256, 256), c % 2 == 0) for c in range(4)])

        def act_conv_first(act, name):
            act.wait_ge(used, ab_p[name] + 4)
            b = conv_banks(name)
            for c in range(4):
                last = nc.scalar.activation(Y[name][:, c * 256:c * 256 + 256], bank(b[c // 2], (c % 2) * 256, 256), ACT.Identity,
                                            scale=conv_tap(name, 3, c))
            last.then_inc(*steps.did("act", f"{name}.c3"))

        def dve_conv_rest(dve, name):
            b = conv_banks(name)
            for k in (2, 1, 0):
                dve.wait_ge(*after(f"{name}.c{k + 1}"))
                lag = 3 - k
                for c in range(4):
                    y = Y[name][:, c * 256 + lag:c * 256 + 256]
                    last = nc.vector.scalar_tensor_tensor(y, bank(b[c // 2], (c % 2) * 256, 256 - lag), conv_tap(name, k, c), y,
                                                          ALU.mult, ALU.add)
                last.then_inc(*steps.did("dve", f"{name}.c{k}"))

        def act_conv_silu(act, name):
            act.wait_ge(*after(f"{name}.c0"))
            nc.scalar.activation(Y[name], Y[name], ACT.Silu).then_inc(*steps.did("act", f"{name}.y"))

        def pe_ab_first(pe):
            pe_turn(pe, "ab", nrm)
            pe.wait_ge(*after(turn_end("ab")))
            for k in range(2):
                pe.wait_ge(lo_done, ab_p["small"] + k + 1)
                wh, wl = weights(ab_p["small"] + k, 4, 16)
                for kk in range(4):
                    kc = 4 * k + kk
                    for t in range(NT):
                        tok = slice(t * P, t * P + P)
                        last = three(bank(7, t * 16, 16), xh[:, kc, tok], xl[:, kc, tok], wh[:, kk, :], wl[:, kk, :],
                                     start=(kc == 0 and t == 0), stop=(kc == KC - 1))
                last.then_inc(used, 1)
            pe.wait_ge(*after("ple.m1"))
            pe_conv_unit(pe, "mqk")
            pe_unit(pe, ab_p["mv"], rows=[(0, 512, [bank(2), bank(3)], (True, True))])

        def dve_gates(dve):
            dve.wait_ge(used, ab_p["small"] + 2)
            z, src = by_t(gz), bank(7, 0, 32).rearrange("p (t n) -> p t n", t=NT)
            b = spread["ab_m_gate_bias_2"].unsqueeze(1).broadcast_to([P, NT, 8])
            nc.vector.tensor_tensor(z[:, :, 0:8], src[:, :, 0:8], b, ALU.add).then_inc(*steps.did("dve", "gate.if"))
            dt = spread["ab_g_dt_bias_2"].unsqueeze(1).broadcast_to([P, NT, 4])
            nc.vector.tensor_tensor(z[:, :, 8:12], src[:, :, 8:12], dt, ALU.add).then_inc(*steps.did("dve", "gate.a"))
            nc.vector.tensor_copy(z[:, :, 12:16], src[:, :, 12:16]).then_inc(*steps.did("dve", "gate.b"))

        def act_gates(act):
            act.wait_ge(*after("gate.b"))
            nc.scalar.activation(by_t(gth), by_t(gz)[:, :, 0:8], ACT.Tanh, scale=1.0 / 15.0).then_inc(*steps.did("act", "gate.th"))
            e = by_t(gex)
            nc.scalar.activation(e[:, :, 4:8], by_t(gz)[:, :, 8:12], ACT.Abs).then_inc(*steps.did("act", "gate.abs"))
            act.wait_ge(*after("gate.abs"))
            act.wait_ge(*after("gate.cap"))
            nc.scalar.activation(e[:, :, 4:8], e[:, :, 4:8], ACT.Exp, scale=-1.0).then_inc(*steps.did("act", "gate.ea"))
            nc.scalar.activation(e[:, :, 0:4], by_t(gcap)[:, :, 4:8], ACT.Exp, scale=-1.0).then_inc(*steps.did("act", "gate.ef"))
            nc.scalar.activation(e[:, :, 8:12], by_t(gz)[:, :, 12:16], ACT.Exp, scale=-1.0).then_inc(*steps.did("act", "gate.eb"))
            nc.scalar.activation(by_t(gei), by_t(gcap)[:, :, 0:4], ACT.Exp).then_inc(*steps.did("act", "gate.ei"))
            nc.scalar.activation(exa, spread["ab_g_a_log_2"], ACT.Exp).then_inc(*steps.did("act", "gate.exa"))
            act.wait_ge(*after("gate.ef"))
            nc.scalar.activation(e[:, :, 0:8], e[:, :, 0:8], ACT.Ln, bias=1.0).then_inc(*steps.did("act", "gate.ln"))

        def dve_gate_logs(dve):
            dve.wait_ge(*after("gate.th"))
            nc.vector.tensor_scalar(gcap, gth, 15.0, None, ALU.mult).then_inc(*steps.did("dve", "gate.cap"))
            e, l = by_t(gex), by_t(glog)
            dve.wait_ge(*after("gate.ln"))
            nc.vector.tensor_scalar(l[:, :, 0:4], e[:, :, 0:4], -1.0, None, ALU.mult).then_inc(*steps.did("dve", "gate.lf"))
            nc.vector.scalar_tensor_tensor(l[:, :, 4:8], by_t(gz)[:, :, 8:12], 0.0, e[:, :, 4:8], ALU.max, ALU.add)\
                .then_inc(*steps.did("dve", "gate.sp"))
            dve.wait_ge(*after("gate.sp"))
            nc.vector.scalar_tensor_tensor(l[:, :, 4:8], l[:, :, 4:8], -1.0, exa.unsqueeze(1).broadcast_to([P, NT, 4]),
                                           ALU.mult, ALU.mult).then_inc(*steps.did("dve", "gate.g"))
            nc.vector.tensor_scalar(by_t(gbeta), e[:, :, 8:12], 1.0, None, ALU.add).then_inc(*steps.did("dve", "gate.1b"))
            dve.wait_ge(*after("gate.1b"))
            nc.vector.reciprocal(gbeta, gbeta).then_inc(*steps.did("dve", "gate.beta"))

        def pe_gate_sums(pe):
            upper, l = cst("upper"), by_t(glog)
            pe.wait_ge(*after("gate.g"))
            pe.wait_ge(*after("gate.lf"))
            pe.wait_ge(*after("gate.b"))
            nc.tensor.matmul(bank(7, 0, 8), upper, l[:, 0, :], start=True, stop=True, skip_group_check=True)
            nc.tensor.matmul(bank(7, 8, 4), ones_sq, l[:, 0, 0:4], start=False, stop=False, skip_group_check=True)
            nc.tensor.matmul(bank(7, 8, 4), upper, l[:, 1, 0:4], start=False, stop=True, skip_group_check=True)
            nc.tensor.matmul(bank(7, 12, 4), upper, l[:, 1, 4:8], start=False, stop=True, skip_group_check=True)\
                .then_inc(*steps.did("pe", "gate.cum"))
            for x in range(4):
                lf = [l[:, t, x:x + 1].broadcast_to([P, P]) for t in range(NT)]
                o = lambda t: bank(4 + x // 2, (x % 2) * 256 + t * P, P)
                nc.tensor.matmul(o(0), lf[0], upper, start=(x % 2 == 0), stop=True, skip_group_check=True)
                nc.tensor.matmul(o(1), lf[0], ones_sq, start=False, stop=False, skip_group_check=True)
                last = nc.tensor.matmul(o(1), lf[1], upper, start=False, stop=True, skip_group_check=True)
            last.then_inc(*steps.did("pe", "gate.rowm"))
            pe.wait_ge(*after("gate.col"))
            for t in range(NT):
                for x in range(4):
                    last = nc.tensor.matmul(bank(6 + t, x * P, P), l[:, t, 4 + x:5 + x].broadcast_to([P, P]), upper,
                                            start=(x == 0), stop=True, skip_group_check=True)
            last.then_inc(*steps.did("pe", "gate.rowg"))

        def dve_gate_rows(dve):
            dve.wait_ge(*after("gate.cum"))
            nc.vector.tensor_copy(gcum, bank(7, 0, 16)).then_inc(*steps.did("dve", "gate.col"))
            dve.wait_ge(*after("gate.col"))
            dve.wait_ge(*after("gate.rowm"))
            c, x4 = by_t(gcum), mE.rearrange("p (k n) -> p k n", k=4)
            r4 = psum[:, 4:6, :].rearrange("p b (k n) -> p (b k) n", k=2)
            nc.vector.tensor_tensor(x4[:, :, 0:256], r4, c[:, 0, 0:4].unsqueeze(2).broadcast_to([P, 4, 256]), ALU.subtract)\
                .then_inc(*steps.did("dve", "mx0"))
            nc.vector.tensor_tensor(x4[:, :, 256:384], r4[:, :, P:256], c[:, 1, 0:4].unsqueeze(2).broadcast_to([P, 4, P]), ALU.subtract)\
                .then_inc(*steps.did("dve", "mx1"))

        def dve_delta_exponents(dve):
            dve.wait_ge(*after("gate.rowg"))
            c = by_t(gcum)
            nc.vector.tensor_copy(glast, bank(6).rearrange("p (k n) -> p k n", k=4)[:, :, P - 1]).then_inc(*steps.did("dve", "glast"))
            nc.vector.tensor_tensor(heads4(dE0), psum[:, 6:8, :].rearrange("p t (k d) -> p t k d", k=4),
                                    c[:, :, 4:8].unsqueeze(3).broadcast_to([P, NT, 4, P]), ALU.subtract)\
                .then_inc(*steps.did("dve", "dx"))
            dve.wait_ge(*after("glast"))
            nc.vector.tensor_tensor(glast, glast, c[:, 0, 4:8], ALU.subtract).then_inc(*steps.did("dve", "dlast"))

        dE0 = arena[:, 6144:7168]

        def pool_ab_masks(pool):
            pool.wait_ge(*after("mx1"))
            x4 = mE.rearrange("p (k n) -> p k n", k=4)
            for at, name in ((0, "mm0"), (256, "mm1")):
                nc.gpsimd.affine_select(out=x4[:, :, at:at + P], in_=x4[:, :, at:at + P], compare_op=ALU.is_ge, fill=-BIG,
                                        base=0, pattern=[[0, 4], [1, P]], channel_multiplier=-1).then_inc(*steps.did("pool", name))
            pool.wait_ge(*after("dx"))
            v = dE0.rearrange("p (k n) -> p k n", k=8)
            nc.gpsimd.affine_select(out=v, in_=v, compare_op=ALU.is_ge, fill=-BIG, base=0, pattern=[[0, 8], [1, P]],
                                    channel_multiplier=-1).then_inc(*steps.did("pool", "dm"))

        def act_ab_decays(act):
            act.wait_ge(*after("mm1"))
            nc.scalar.activation(mE, mE, ACT.Exp).then_inc(*steps.did("act", "mE"))
            act.wait_ge(*after("dm"))
            nc.scalar.activation(dE0, dE0, ACT.Exp).then_inc(*steps.did("act", "dE0"))
            act.wait_ge(*after("dlast"))
            nc.scalar.activation(kdecay, glast, ACT.Exp).then_inc(*steps.did("act", "kdecay"))
            nc.scalar.activation(eg1, by_t(gcum)[:, 1, 4:8], ACT.Exp).then_inc(*steps.did("act", "eg1"))

        def dve_m_v(dve):
            dve.wait_ge(used, ab_p["mv"] + 4)
            dve.wait_ge(*after("gate.ei"))
            nc.vector.tensor_tensor(heads4(mvE), psum[:, 2:4, :].rearrange("p t (k d) -> p t k d", k=4), spread_heads(gei), ALU.mult)\
                .then_inc(*steps.did("dve", "mvE"))

        M_BANKS = (2, 4, 3, 5)

        def pe_m_scores(pe):
            for name in ("mqk.y", "mvE", "mx1"):
                pe.wait_ge(*after(name))
            y = Y["mqk"]
            for par in range(2):
                part = slice(64 * par, 64 * par + 64)
                for c in range(2):
                    x = 2 * c + par
                    q, k = y[part, c * 256:c * 256 + 256], y[part, 512 + c * 256:512 + c * 256 + 256]
                    nc.tensor.matmul(bank(M_BANKS[x], 0, 256), k[:, 0:P], q, start=True, stop=True)
                    last = nc.tensor.matmul(bank(M_BANKS[x], 256, P), k[:, P:256], q[:, P:256], start=True, stop=True)
            last.then_inc(*steps.did("pe", "mS"))

        def dve_m_matrix(dve):
            dve.wait_ge(*after("mS"))
            dve.wait_ge(*after("mE"))
            for x in range(4):
                e = mE[:, x * 384:x * 384 + 384]
                last = nc.vector.scalar_tensor_tensor(e, bank(M_BANKS[x], 0, 384), 0.125, e, ALU.mult, ALU.mult)
            last.then_inc(*steps.did("dve", "mA"))

        def pe_m_out(pe):
            pe.wait_ge(*after("mA"))
            last = None
            for den in range(2):
                for x in range(4):
                    a = mE[:, x * 384:x * 384 + 384]
                    for t in range(NT):
                        o = bank(4, t * 4 + x, 1) if den else bank(2 + t, x * P, P)
                        rhs = lambda s: by_t(gei)[:, s, x:x + 1] if den else mvE[:, s * 512 + x * P:s * 512 + x * P + P]
                        nc.tensor.matmul(o, a[:, t * P:t * P + P], rhs(0), start=True, stop=(t == 0))
                        if t == 1:
                            last = nc.tensor.matmul(o, a[:, 256:384], rhs(1), start=False, stop=True)
            last.then_inc(*steps.did("pe", "mO"))

        def dve_m_out(dve):
            dve.wait_ge(*after("mO"))
            nc.vector.tensor_scalar(m_den, bank(4, 0, 8), -1.0, None, ALU.mult).then_inc(*steps.did("dve", "m.nden"))
            dve.wait_ge(*after("m.nden"))
            nc.vector.scalar_tensor_tensor(m_den, bank(4, 0, 8), 1.0, m_den, ALU.max, ALU.max).then_inc(*steps.did("dve", "m.den"))
            dve.wait_ge(*after("m.den"))
            nc.vector.reciprocal(m_den, m_den).then_inc(*steps.did("dve", "m.rden"))
            dve.wait_ge(*after("m.rden"))
            m4 = mix[:, :, 0:512].rearrange("p t (k d) -> p t k d", k=4)
            nc.vector.tensor_tensor(m4, psum[:, 2:4, :].rearrange("p t (k d) -> p t k d", k=4), spread_heads(m_den), ALU.mult)\
                .then_inc(*steps.did("dve", "m.h"))

        def act_m_square(act):
            act.wait_ge(*after("m.h"))
            nc.scalar.activation(by_t(m_sq), mix[:, :, 0:512], ACT.Square).then_inc(*steps.did("act", "m.sq"))

        def dve_m_norm(dve):
            dve.wait_ge(*after("m.sq"))
            nc.vector.tensor_reduce(m_ss, m_sq.rearrange("p (k d) -> p k d", d=P), AX_X, ALU.add).then_inc(*steps.did("dve", "m.ss"))
            dve.wait_ge(*after("m.r"))
            m4 = mix[:, :, 0:512].rearrange("p t (k d) -> p t k d", k=4)
            nc.vector.tensor_tensor(m4, m4, spread_heads(m_r), ALU.mult).then_inc(*steps.did("dve", "m.n"))
            g = gain_of(dve, "abh")
            dve.wait_ge(*after("m.n"))
            nc.vector.tensor_tensor(mix[:, :, 0:512], mix[:, :, 0:512], g[:, 0:512].unsqueeze(1).broadcast_to([P, NT, 512]), ALU.mult)\
                .then_inc(*steps.did("dve", "m.g"))

        ROW_BANKS = {"dk": 4, "dq": 2, "dv": 6}

        def pe_rows(pe, name, ready):
            for r in ready:
                pe.wait_ge(*after(r))
            for t in range(NT):
                for c in range(4):
                    last = nc.tensor.transpose(bank(ROW_BANKS[name] + t, c * P, P), Y[name][:, c * 256 + t * P:c * 256 + t * P + P], ident)
            last.then_inc(*steps.did("pe", f"{name}.R"))

        def act_row_squares(act, name, sq):
            act.wait_ge(*after(f"{name}.R"))
            b = ROW_BANKS[name]
            nc.scalar.activation(by_t(sq), psum[:, b:b + 2, :], ACT.Square).then_inc(*steps.did("act", f"{name}.sq"))

        def dve_row_sums(dve, name, sq, ss):
            dve.wait_ge(*after(f"{name}.sq"))
            nc.vector.tensor_reduce(ss, sq.rearrange("p (k d) -> p k d", d=P), AX_X, ALU.add).then_inc(*steps.did("dve", f"{name}.ss"))

        def dve_row_scale(dve, name, dst, r, ready, done):
            b = ROW_BANKS[name]
            for x in ready:
                dve.wait_ge(*after(x))
            nc.vector.tensor_tensor(heads4(dst), psum[:, b:b + 2, :].rearrange("p t (k d) -> p t k d", k=4), spread_heads(r), ALU.mult)\
                .then_inc(*steps.did("dve", done))

        def pool_delta(pool):
            pool.wait_ge(*after("m.ss"))
            pool_rstd(pool, "m.r", m_ss, 8, P, m_r)
            for name, ss, r in (("dk", k_ss, k_r), ("dq", q_ss, q_r)):
                pool.wait_ge(*after(f"{name}.ss"))
                pool_rstd(pool, f"{name}.rr", ss, 8, 1, r)
            pool.wait_ge(*after("dq.rr"))
            nc.gpsimd.tensor_scalar(q_r, q_r, float(P) ** -0.5, None, ALU.mult).then_inc(*steps.did("pool", "dq.rs"))
            pool.wait_ge(*after("d.ss"))
            pool_rstd(pool, "d.r", d_ss, 8, P, d_r)

        def pe_cols(pe, name, src, b, ready):
            for r in ready:
                pe.wait_ge(*after(r))
            for x in range(4):
                for t in range(NT):
                    last = nc.tensor.transpose(bank(b + x // 2, (x % 2) * 256 + t * P, P), src[:, t * 512 + x * P:t * 512 + x * P + P], ident)
            last.then_inc(*steps.did("pe", name))

        def per_tile(pe, b, lhs, rhs, name):
            for t in range(NT):
                for x in range(4):
                    last = nc.tensor.matmul(bank(b + t, x * P, P), lhs(t, x), rhs(t, x), start=True, stop=True)
            last.then_inc(*steps.did("pe", name))

        tok_head = lambda a: lambda t, x: a[:, t * 512 + x * P:t * 512 + x * P + P]
        head_tok = lambda a: lambda t, x: a[:, x * 256 + t * P:x * 256 + t * P + P]

        def pe_delta_matrices(pe):
            pe.wait_ge(*after("kT2"))
            pe.wait_ge(*after("qT2"))
            pe.wait_ge(*after("kbT"))
            per_tile(pe, 2, head_tok(kT2), head_tok(kbT), "dNT.p")
            per_tile(pe, 4, head_tok(kT2), head_tok(qT2), "dat.p")

        def dve_delta_matrices(dve):
            dve.wait_ge(*after("dE"))
            for name, b, dst in (("dNT", 2, dNT), ("dat", 4, dat)):
                dve.wait_ge(*after(f"{name}.p"))
                nc.vector.tensor_tensor(by_t(dst), psum[:, b:b + 2, :], by_t(dE), ALU.mult).then_inc(*steps.did("dve", name))
            dve.wait_ge(*after("dNT"))
            eight = lambda a: a.rearrange("p (k n) -> p k n", k=8)
            nc.vector.tensor_tensor(eight(dXT), eight(dNT), cst("level1").unsqueeze(1).broadcast_to([P, 8, P]), ALU.mult)\
                .then_inc(*steps.did("dve", "dXT.m"))
            dve.wait_ge(*after("dXT.m"))
            nc.vector.tensor_tensor(eight(dXT), ident.unsqueeze(1).broadcast_to([P, 8, P]), eight(dXT), ALU.subtract)\
                .then_inc(*steps.did("dve", "dXT"))

        SOLVE = LEVELS[::-1][1:]

        def pe_delta_start(pe):
            pe.wait_ge(*after("dNT"))
            for t in range(NT):
                for x in range(4):
                    last = nc.tensor.transpose(bank(t, x * P, P), tok_head(dNT)(t, x), ident)
            last.then_inc(*steps.did("pe", "dN.T"))
            pe.wait_ge(*after("dXT"))
            pe.wait_ge(*after("dat"))
            for t in range(NT):
                for x in range(4):
                    last = nc.tensor.transpose(bank(2 + t, x * P, P), tok_head(dXT)(t, x), ident)
            last.then_inc(*steps.did("pe", "dX.T"))

        def act_delta_start(act):
            for name, dst, b in (("dN", dN, 0), ("dX", dX, 2)):
                act.wait_ge(*after(f"{name}.T"))
                nc.scalar.activation(by_t(dst), psum[:, b:b + 2, :], ACT.Copy).then_inc(*steps.did("act", name))

        def solved(n, t):
            return f"dX.{n}{t}"

        def pe_delta_level(pe, n, part):
            for t in range(NT):
                if part == 0:
                    for name in ("dN", "dX") if n == 0 else (f"dXTn{n - 1}{t}",):
                        pe.wait_ge(*after(name))
                    for x in range(4):
                        last = nc.tensor.matmul(bank(t, x * P, P), tok_head(dN)(t, x), tok_head(dXT)(t, x), start=True, stop=True)
                    last.then_inc(*steps.did("pe", f"dV.p{n}{t}"))
                    continue
                pe.wait_ge(*after(f"dV{n}{t}"))
                if n > 0:
                    pe.wait_ge(*after(f"dXn{n - 1}{t}"))
                for x in range(4):
                    last = nc.tensor.matmul(bank(2 + t, x * P, P), tok_head(dX)(t, x), tok_head(dV)(t, x), start=True, stop=True)
                last.then_inc(*steps.did("pe", f"dXT.p{n}{t}"))
                if n < len(SOLVE) - 1:
                    for x in range(4):
                        last = nc.tensor.matmul(bank(4 + t, x * P, P), tok_head(dV)(t, x), tok_head(dX)(t, x), start=True, stop=True)
                    last.then_inc(*steps.did("pe", f"dX.p{n}{t}"))

        def dve_delta_level(dve, n):
            four = lambda a: a.rearrange("p (k n) -> p k n", k=4)
            mask = cst(f"level{SOLVE[n]}").unsqueeze(1).broadcast_to([P, 4, P])
            half = lambda a, t: a[:, t * 512:t * 512 + 512]
            for t in range(NT):
                dve.wait_ge(*after(f"dV.p{n}{t}"))
                nc.vector.tensor_tensor(four(half(dV, t)), four(bank(t)), mask, ALU.mult).then_inc(*steps.did("dve", f"dV{n}{t}"))
            for t in range(NT):
                dve.wait_ge(*after(f"dXT.p{n}{t}"))
                if n > 0:
                    dve.wait_ge(*after(f"dXTn{n - 1}{t}"))
                nc.vector.tensor_tensor(half(dXT, t), half(dXT, t), bank(2 + t), ALU.subtract).then_inc(*steps.did("dve", f"dXTn{n}{t}"))
                if n < len(SOLVE) - 1:
                    dve.wait_ge(*after(f"dX.p{n}{t}"))
                    nc.vector.tensor_tensor(half(dX, t), half(dX, t), bank(4 + t), ALU.subtract).then_inc(*steps.did("dve", f"dXn{n}{t}"))

        def four_heads(pe, b, lhs, rhs, name):
            for x in range(4):
                last = nc.tensor.matmul(bank(b, x * P, P), lhs(x), rhs(x), start=True, stop=True)
            last.then_inc(*steps.did("pe", name))

        head = lambda a: lambda x: a[:, x * P:x * P + P]

        def pe_delta_out(pe):
            n = len(SOLVE) - 1
            pe.wait_ge(*after(f"dXTn{n}0"))
            four_heads(pe, 0, head(dXT[:, 0:512]), head(vb[:, 0:512]), "d.u0p")
            pe.wait_ge(*after("d.u0"))
            pe.wait_ge(*after("d.kdec"))
            four_heads(pe, 1, head(krow[:, 0:512]), head(u0), "d.Sp")
            four_heads(pe, 5, head(dat[:, 0:512]), head(u0), "d.o0p")
            pe.wait_ge(*after("d.S"))
            pe.wait_ge(*after(f"dXTn{n}1"))
            four_heads(pe, 2, lambda x: head_tok(kT2)(1, x), head(dS), "d.kSp")
            four_heads(pe, 3, lambda x: head_tok(qT2)(1, x), head(dS), "d.qSp")
            pe.wait_ge(*after("d.rhs"))
            four_heads(pe, 0, head(dXT[:, 512:1024]), head(u1), "d.u1p")
            pe.wait_ge(*after("d.u1"))
            four_heads(pe, 1, head(dat[:, 512:1024]), head(u1), "d.o1p")

        def dve_delta_prep(dve):
            four = lambda a: a.rearrange("p (k n) -> p k n", k=4)
            dve.wait_ge(*after("kdecay"))
            dve.wait_ge(*after("kT2.T"))
            nc.vector.tensor_tensor(four(krow[:, 0:512]), four(krow[:, 0:512]), kdecay.unsqueeze(2).broadcast_to([P, 4, P]), ALU.mult)\
                .then_inc(*steps.did("dve", "d.kdec"))
            dve.wait_ge(*after("eg1"))
            nc.vector.tensor_tensor(beg, eg1, gbeta[:, 4:8], ALU.mult).then_inc(*steps.did("dve", "beg"))

        def dve_delta_out(dve):
            four = lambda a: a.rearrange("p (k n) -> p k n", k=4)
            wide = lambda a: a.unsqueeze(2).broadcast_to([P, 4, P])
            dve.wait_ge(*after("d.u0p"))
            nc.vector.tensor_copy(u0, bank(0)).then_inc(*steps.did("dve", "d.u0"))
            dve.wait_ge(*after("d.Sp"))
            nc.vector.tensor_copy(dS, bank(1)).then_inc(*steps.did("dve", "d.S"))
            dve.wait_ge(*after("d.kSp"))
            dve.wait_ge(*after("beg"))
            nc.vector.tensor_tensor(four(u1), four(bank(2)), wide(beg), ALU.mult).then_inc(*steps.did("dve", "d.ks"))
            dve.wait_ge(*after("d.ks"))
            nc.vector.tensor_tensor(u1, vb[:, 512:1024], u1, ALU.subtract).then_inc(*steps.did("dve", "d.rhs"))
            m = mix[:, 1, 512:1024]
            dve.wait_ge(*after("d.qSp"))
            nc.vector.tensor_tensor(four(m), four(bank(3)), wide(eg1), ALU.mult).then_inc(*steps.did("dve", "d.qs"))
            dve.wait_ge(*after("d.u1p"))
            nc.vector.tensor_copy(u1, bank(0)).then_inc(*steps.did("dve", "d.u1"))
            nc.vector.tensor_copy(mix[:, 0, 512:1024], bank(5)).then_inc(*steps.did("dve", "d.o0"))
            dve.wait_ge(*after("d.o1p"))
            dve.wait_ge(*after("d.qs"))
            nc.vector.tensor_tensor(m, m, bank(1), ALU.add).then_inc(*steps.did("dve", "d.o1"))
            dve.wait_ge(*after("d.osq"))
            nc.vector.tensor_reduce(d_ss, d_sq.rearrange("p (k d) -> p k d", d=P), AX_X, ALU.add).then_inc(*steps.did("dve", "d.ss"))
            dve.wait_ge(*after("d.r"))
            m4 = mix[:, :, 512:1024].rearrange("p t (k d) -> p t k d", k=4)
            nc.vector.tensor_tensor(m4, m4, spread_heads(d_r), ALU.mult).then_inc(*steps.did("dve", "d.n"))
            g = gain_of(dve, "abh")
            dve.wait_ge(*after("d.n"))
            nc.vector.tensor_tensor(mix[:, :, 512:1024], mix[:, :, 512:1024], g[:, 512:1024].unsqueeze(1).broadcast_to([P, NT, 512]),
                                    ALU.mult).then_inc(*steps.did("dve", "ab.last"))
            dve.wait_ge(*after("ab.last"))
            dve.wait_ge(*after("d.gate"))
            for t in range(NT):
                nc.vector.tensor_tensor(mix[:, t, 512:1024], mix[:, t, 512:1024], gtmp[:, t * 512:t * 512 + 512], ALU.mult)\
                    .then_inc(*steps.did("dve", f"abo.n{t}"))

        def pe_ab(pe):
            pe_ab_first(pe)
            pe_gate_sums(pe)
            pe_conv_unit(pe, "dk", ["mqk.c0"])
            pe_m_scores(pe)
            pe_conv_unit(pe, "dq", ["dx", "glast"])
            pe_m_out(pe)
            pe_conv_unit(pe, "dv", ["dk.c0"])
            pe_rows(pe, "dk", ["dk.y", "m.h"])
            pe_rows(pe, "dq", ["dq.y"])
            pe.wait_ge(*after("dv.c0"))
            pe_unit(pe, ab_p["mo"], rows=[(0, 512, [bank(0), bank(1)], (True, True))])
            pe_rows(pe, "dv", ["dv.y", "dq.c0"])
            pe_cols(pe, "kT2.T", krow, 4, ["krow"])
            pe_cols(pe, "kbT.T", kb, 2, ["kb", "qrow"])
            pe_cols(pe, "qT2.T", qrow, 6, ["vb"])
            pe.wait_ge(*after("m.gate"))
            pe_delta_matrices(pe)
            pe_delta_start(pe)
            for n in range(len(SOLVE)):
                pe_delta_level(pe, n, 0)
                if n < 4:
                    if n == 0:
                        pe.wait_ge(*after("qT2"))
                    pe_unit(pe, ab_p["dg"], rows=[(0, 512, [bank(6), bank(7)], (True, True))], which=(n,))
                pe_delta_level(pe, n, 1)
            pe_delta_out(pe)
            pe_turn_after(pe)

        def pe_turn_after(pe):
            pe.wait_ge(*after("d.gate"))
            pe_turn(pe, "abo", mix, ready="abo.n1")
            pe.wait_ge(*after(turn_end("abo")))
            out_units(pe, "abo")

        def act_ab(act, src):
            act_norm(act, "ab", src)
            for k in range(2):
                split_hi(act, ab_p["small"] + k, (8, 16))
            S = lambda name, which=(0, 1, 2, 3): split4(split_hi, act, ab_p[name], which=which)
            S("mqk", (0, 1, 2))
            act_gates(act)
            S("mqk", (3,))
            S("mv", (0, 1, 2))
            act_conv_first(act, "mqk")
            S("mv", (3,))
            S("dk", (0,))
            act_conv_silu(act, "mqk")
            S("dk", (1, 2, 3))
            act_ab_decays(act)
            S("dq", (0, 1))
            act_conv_first(act, "dk")
            S("dq", (2,))
            act_conv_silu(act, "dk")
            S("dq", (3,))
            S("dv", (0, 1))
            act_conv_first(act, "dq")
            S("dv", (2,))
            act_conv_silu(act, "dq")
            act_m_square(act)
            S("dv", (3,))
            S("mo", (0, 1, 2))
            act_conv_first(act, "dv")
            act_row_squares(act, "dk", arena[:, 9216:10240])
            act_conv_silu(act, "dv")
            act_row_squares(act, "dq", arena[:, 10240:11264])
            S("mo", (3,))
            act.wait_ge(*after("krow"))
            act.wait_ge(*after("m.ss"))
            act.wait_ge(*after("m.g"))
            act.wait_ge(used, ab_p["mo"] + 4)
            act.wait_ge(*after("dk.ss"))
            nc.scalar.activation(by_t(arena[:, 9216:10240]), psum[:, 0:2, :], ACT.Sigmoid).then_inc(*steps.did("act", "m.sig"))
            nc.scalar.activation(dE, dE0, ACT.Copy).then_inc(*steps.did("act", "dE"))
            S("dg", (0, 1, 2))
            for name, dst, b in (("kT2", kT2, 4), ("kbT", kbT, 2), ("qT2", qT2, 6)):
                act.wait_ge(*after(f"{name}.T"))
                nc.scalar.activation(rows(dst), psum[:, b:b + 2, :], ACT.Copy).then_inc(*steps.did("act", name))
            act_delta_start(act)
            S("dg", (3,))
            act.wait_ge(used, ab_p["dg"] + 4)
            act.wait_ge(*after("dat"))
            nc.scalar.activation(by_t(gtmp), psum[:, 6:8, :], ACT.Silu).then_inc(*steps.did("act", "d.gate"))
            split4(split_hi, act, piece_at("abo", 0))
            act.wait_ge(*after("d.o1"))
            act.wait_ge(*after("d.o0"))
            nc.scalar.activation(by_t(d_sq), mix[:, :, 512:1024], ACT.Square).then_inc(*steps.did("act", "d.osq"))
            act_turn(act, "abo")
            split4(split_hi, act, piece_at("abo", 1))
            act_post(act, "abo", 2 * (first_slot["abo"] + 4))

        def dve_ab(dve):
            dve_norm(dve, "ab")
            for k in range(2):
                split_lo(dve, ab_p["small"] + k, (8, 16))
            S = lambda name, which=(0, 1, 2, 3): split4(split_lo, dve, ab_p[name], which=which)
            S("mqk", (0, 1, 2))
            dve_gates(dve)
            dve_gate_logs(dve)
            S("mqk", (3,))
            S("mv", (0, 1, 2))
            dve_conv_rest(dve, "mqk")
            S("mv", (3,))
            dve_m_v(dve)
            dve_gate_rows(dve)
            S("dk", (0, 1, 2))
            dve_delta_exponents(dve)
            S("dk", (3,))
            S("dq", (0, 1))
            dve_conv_rest(dve, "dk")
            S("dq", (2,))
            dve_m_matrix(dve)
            S("dq", (3,))
            S("dv", (0, 1))
            dve_m_out(dve)
            dve_conv_rest(dve, "dq")
            S("dv", (2, 3))
            S("mo", (0, 1, 2))
            dve_m_norm(dve)
            dve_conv_rest(dve, "dv")
            dve_row_sums(dve, "dk", arena[:, 9216:10240], k_ss)
            dve_row_sums(dve, "dq", arena[:, 10240:11264], q_ss)
            dve_row_scale(dve, "dk", krow, k_r, ["dk.rr"], "krow")
            dve_row_scale(dve, "dq", qrow, q_r, ["dq.rs"], "qrow")
            S("mo", (3,))
            dve.wait_ge(*after("dE"))
            dve.wait_ge(*after("krow"))
            nc.vector.tensor_tensor(heads4(kb), heads4(krow), spread_heads(gbeta), ALU.mult).then_inc(*steps.did("dve", "kb"))
            dve_row_scale(dve, "dv", vb, gbeta, ["dv.R"], "vb")
            dve.wait_ge(*after("m.sig"))
            dve.wait_ge(*after("m.g"))
            nc.vector.tensor_tensor(mix[:, :, 0:512], mix[:, :, 0:512], by_t(arena[:, 9216:10240]), ALU.mult)\
                .then_inc(*steps.did("dve", "m.gate"))
            S("dg", (0, 1, 2))
            dve.wait_ge(*after("m.gate"))
            dve_delta_matrices(dve)
            dve_delta_prep(dve)
            S("dg", (3,))
            for n in range(len(SOLVE)):
                dve_delta_level(dve, n)
            dve_delta_out(dve)
            split4(split_lo, dve, piece_at("abo", 0))
            dve_turn(dve, "abo")
            split4(split_lo, dve, piece_at("abo", 1))
            dve_post(dve, "abo")

        def pool_ab(pool, gains):
            pool_norm(pool, "ab")
            next_gain(pool, gains)
            pool_ab_masks(pool)
            pool_delta(pool)
            next_gain(pool, gains)
            pool_post(pool, "abo")
            next_gain(pool, gains)

        HW = 4 * SEQ
        hq, hk, hb = ([arena[:, (3 * u + n) * HW:(3 * u + n + 1) * HW] for u in range(2)] for n in range(3))
        h_e, h_l = arena[:, 6144:7168], (arena[:, 7168:8192], arena[:, 8192:9216])
        h_at, h_cross = arena[:, 9216:10240], arena[:, 10240:10752]
        h_t1, h_t2 = (arena[:, 6144:7168], arena[:, 8192:9216]), (arena[:, 7168:8192], arena[:, 9216:10240])
        h_sil = (arena[:, 10752:11776], arena[:, 1024:2048])
        h_sq = (arena[:, 0:1024], arena[:, 0:1024])
        lb_d, lb_e, log_lb, log_rest, lb_x = (few.take(8) for _ in range(5))
        h_ss, h_r = (few.take(8), few.take(8)), (few.take(8), few.take(8))
        wide2 = lambda b: psum[:, b:b + 2, :].rearrange("p b n -> p (b n)")
        hu = lambda n: piece_at("hg", n)

        def dve_bounds(dve):
            nc.vector.tensor_tensor(lb_d, lb_logits[:, 8:16], lb_logits[:, 0:8], ALU.subtract).then_inc(*steps.did("dve", "lb.d"))
            dve.wait_ge(*after("lb.ln"))
            nc.vector.scalar_tensor_tensor(log_rest, lb_d, 0.0, lb_e, ALU.max, ALU.add).then_inc(*steps.did("dve", "lb.1"))
            nc.vector.scalar_tensor_tensor(log_lb, lb_d, 0.0, lb_e, ALU.min, ALU.subtract).then_inc(*steps.did("dve", "lb.a"))
            dve.wait_ge(*after("lb.1"))
            nc.vector.tensor_scalar(log_rest, log_rest, -1.0, None, ALU.mult).then_inc(*steps.did("dve", "lb.c"))

        def act_bounds(act):
            act.wait_ge(*after("lb.d"))
            nc.scalar.activation(lb_e, lb_d, ACT.Abs).then_inc(*steps.did("act", "lb.abs"))
            act.wait_ge(*after("lb.abs"))
            nc.scalar.activation(lb_e, lb_e, ACT.Exp, scale=-1.0).then_inc(*steps.did("act", "lb.exp"))
            act.wait_ge(*after("lb.exp"))
            nc.scalar.activation(lb_e, lb_e, ACT.Ln, bias=1.0).then_inc(*steps.did("act", "lb.ln"))

        def act_log1p_exp(act, name, a, src, ready):
            for r in ready:
                act.wait_ge(*after(r))
            nc.scalar.activation(a, src, ACT.Abs).then_inc(*steps.did("act", f"{name}.abs"))
            act.wait_ge(*after(f"{name}.abs"))
            nc.scalar.activation(a, a, ACT.Exp, scale=-1.0).then_inc(*steps.did("act", f"{name}.exp"))
            act.wait_ge(*after(f"{name}.exp"))
            nc.scalar.activation(a, a, ACT.Ln, bias=1.0).then_inc(*steps.did("act", f"{name}.ln"))

        def act_h_forget(act, u):
            act.wait_ge(used, hu(u) + 4)
            act_log1p_exp(act, f"hf{u}", h_t1[u], wide2(2 * u), ())

        def dve_h_forget(dve, u):
            f = wide2(2 * u)
            dve.wait_ge(*after(f"hf{u}.ln"))
            nc.vector.scalar_tensor_tensor(h_t2[u], f, 0.0, h_t1[u], ALU.min, ALU.subtract).then_inc(*steps.did("dve", f"hf{u}.ls"))
            dve.wait_ge(*after(f"hf{u}.ls"))
            dve.wait_ge(*after("lb.c"))
            dve.wait_ge(*after("lb.a"))
            for x in range(4):
                t = slice(x * SEQ, x * SEQ + SEQ)
                a, c = log_lb[:, 4 * u + x:4 * u + x + 1], log_rest[:, 4 * u + x:4 * u + x + 1]
                nc.vector.tensor_scalar(hb[u][:, t], h_t2[u][:, t], c, a, ALU.add, ALU.max)
                nc.vector.tensor_scalar(h_t1[u][:, t], h_t2[u][:, t], c, a, ALU.add, ALU.subtract)
                last = nc.vector.scalar_tensor_tensor(hk[u][:, t], h_t2[u][:, t], c, f[:, t], ALU.add, ALU.subtract)
            last.then_inc(*steps.did("dve", f"hf{u}.x"))

        def act_h_decay(act, u):
            act.wait_ge(*after(f"hf{u}.x"))
            nc.scalar.activation(hk[u], hk[u], ACT.Exp).then_inc(*steps.did("act", f"hk{u}"))
            act_log1p_exp(act, f"hd{u}", h_t1[u], h_t1[u], ())

        def dve_h_decay(dve, u):
            dve.wait_ge(*after(f"hd{u}.ln"))
            nc.vector.tensor_tensor(h_t1[u], h_t1[u], hb[u], ALU.add).then_inc(*steps.did("dve", f"hd{u}.lf"))
            dve.wait_ge(*after(f"hd{u}.lf"))
            for x in range(4):
                t = slice(x * SEQ, x * SEQ + SEQ)
                last = nc.vector.tensor_tensor_scan(hb[u][:, t], ones.broadcast_to([P, SEQ]), h_t1[u][:, t], 0.0, ALU.mult, ALU.add)
            last.then_inc(*steps.did("dve", f"hb{u}"))

        def act_h_q(act, u):
            act.wait_ge(used, hu(2 + u) + 4)
            nc.scalar.activation(hq[u], wide2(4 + 2 * u), ACT.Silu).then_inc(*steps.did("act", f"hq{u}"))

        def act_h_v(act, u):
            act.wait_ge(used, hu(4 + u) + 4)
            act.wait_ge(*after("hg.T11"))
            nc.scalar.activation(mix[:, :, 512 * u:512 * u + 512], psum[:, 4 + 2 * u:6 + 2 * u, :], ACT.Copy, scale=float(P) ** -0.5)\
                .then_inc(*steps.did("act", f"hv{u}"))

        def act_h_gate(act, u):
            act.wait_ge(used, hu(6 + u) + 4)
            if u == 1:
                act.wait_ge(*after("h0.P8"))
            nc.scalar.activation(by_t(h_sil[u]), psum[:, 4:6, :], ACT.Silu).then_inc(*steps.did("act", f"hs{u}"))

        def pe_h_columns(pe, n, b):
            pe_unit(pe, hu(n), columns=[(c * P, bank(b + c // 2, (c % 2) * 256, 256), c % 2 == 0) for c in range(4)])

        def pe_h_piece(pe, n, k, b):
            pe_unit(pe, hu(n), rows=[(0, 512, [bank(b), bank(b + 1)], (True, True))], which=(k,))

        def pe_h_level(pe, u, n):
            X = f"h{u}"
            if n >= 2:
                pe.wait_ge(*after(f"{X}.put{n - 2}"))
            elif u == 1:
                pe.wait_ge(*after(f"h0.put{7 + n}"))
            else:
                pe.wait_ge(*after("hf1.x"))
            if n < len(ALL_LEVELS):
                pe.wait_ge(*after(f"{X}.l{n}"))
                l = r = h_l[n % 2]
            else:
                l, r = hk[u], hq[u]
            if n == 0:
                for x in range(4):
                    last = nc.tensor.matmul(bank(0, x * P, P), head_tok(l)(0, x), head_tok(r)(1, x), start=True, stop=True)
                last.then_inc(*steps.did("pe", f"{X}.P{n}"))
            else:
                per_tile(pe, 2 * (n % 2), head_tok(l), head_tok(r), f"{X}.P{n}")

        def dve_h_put(dve, u, n):
            X = f"h{u}"
            dve.wait_ge(*after(f"{X}.P{n}"))
            if n == 0:
                if u == 1:
                    dve.wait_ge(*after("h0.O"))
                nc.vector.tensor_copy(h_cross, bank(0)).then_inc(*steps.did("dve", f"{X}.put0"))
                return
            dve.wait_ge(*after(f"{X}.put{n - 1}" if n > 1 else f"{X}.at0"))
            mask = cst(f"level{ALL_LEVELS[n]}") if n < len(ALL_LEVELS) else ident
            b = 2 * (n % 2)
            for t in range(NT):
                four = lambda a: a.rearrange("p (m i) -> p m i", m=4)
                last = nc.vector.copy_predicated(four(h_at[:, t * 512:t * 512 + 512]),
                                                 mask.bitcast(U32).unsqueeze(1).broadcast_to([P, 4, P]), four(bank(b + t)))
            last.then_inc(*steps.did("dve", f"{X}.put{n}"))

        def dve_h_levels(dve, u, pieces):
            X = f"h{u}"
            for n, half in enumerate(ALL_LEVELS):
                if n == 0:
                    ready = [f"hb{u}", f"hq{u}", f"hk{u}", "hb1", "hk1"] if u == 0 else ["h0.l7", "hq1"]
                else:
                    ready = [f"{X}.l{n - 1}"]
                dve_level_x(dve, X, n, half, hb[u], h_e, ready)
                split_lo(dve, pieces + n)
                if n >= 1:
                    dve_h_put(dve, u, n - 1)
                if n >= 2:
                    wait = [f"{X}.P{n - 2}"]
                else:
                    wait = [f"h0.P{6 + n}"] if u == 1 else []
                dve_level_l(dve, X, n, half, hq[u], hk[u], h_e, h_l[n % 2], wait)
            for n in (7, 8):
                dve_h_put(dve, u, n)

        def pe_h_out(pe, u):
            X = f"h{u}"
            for r in (f"{X}.put8", "hv1", f"hv{u}") + (("ho0.n",) if u == 1 else ()):
                pe.wait_ge(*after(r))
            for t in range(NT):
                for x in range(4):
                    v = lambda s: mix[:, s, 512 * u + x * P:512 * u + x * P + P]
                    last = nc.tensor.matmul(bank(6 + t, x * P, P), tok_head(h_at)(t, x), v(t), start=True, stop=(t == 0))
                    if t == 1:
                        last = nc.tensor.matmul(bank(7, x * P, P), h_cross[:, x * P:x * P + P], v(0), start=False, stop=True)
            last.then_inc(*steps.did("pe", f"{X}.O"))

        def act_h_square(act, u):
            act.wait_ge(*after(f"h{u}.O"))
            nc.scalar.activation(by_t(h_sq[u]), psum[:, 6:8, :], ACT.Square).then_inc(*steps.did("act", f"ho{u}.sq"))

        def pool_h(pool, u):
            pool.wait_ge(*after(f"ho{u}.ss"))
            pool_rstd(pool, f"ho{u}.r", h_ss[u], 8, P, h_r[u])

        def dve_h_sums(dve, u):
            dve.wait_ge(*after(f"ho{u}.sq"))
            nc.vector.tensor_reduce(h_ss[u], h_sq[u].rearrange("p (k d) -> p k d", d=P), AX_X, ALU.add).then_inc(*steps.did("dve", f"ho{u}.ss"))

        def dve_h_out_norm(dve, u):
            m = mix[:, :, 512 * u:512 * u + 512]
            dve.wait_ge(*after(f"ho{u}.r"))
            nc.vector.tensor_tensor(m.rearrange("p t (k d) -> p t k d", k=4), psum[:, 6:8, :].rearrange("p t (k d) -> p t k d", k=4),
                                    spread_heads(h_r[u]), ALU.mult).then_inc(*steps.did("dve", f"ho{u}.n"))
            g = gain_of(dve, "hgh")
            dve.wait_ge(*after(f"ho{u}.n"))
            nc.vector.tensor_tensor(m, m, g[:, 512 * u:512 * u + 512].unsqueeze(1).broadcast_to([P, NT, 512]), ALU.mult)\
                .then_inc(*steps.did("dve", "hg.last" if u else "ho0.g"))

        def dve_h_out_gate(dve, u):
            m = mix[:, :, 512 * u:512 * u + 512]
            dve.wait_ge(*after("hg.last" if u else "ho0.g"))
            dve.wait_ge(*after(f"hs{u}"))
            nc.vector.tensor_tensor(m, m, by_t(h_sil[u]), ALU.mult).then_inc(*steps.did("dve", f"hgo.m{u}"))

        def pe_hg(pe):
            pe_turn(pe, "hg", nrm)
            pe.wait_ge(*after(turn_end("hg")))
            pe.wait_ge(*after("ffn2.p1"))
            pe_h_columns(pe, 0, 0)
            pe_h_columns(pe, 1, 2)
            pe_h_columns(pe, 2, 4)
            pe_h_columns(pe, 3, 6)
            pe.wait_ge(*after("hq0"))
            for n in range(4):
                pe_h_piece(pe, 4, n, 4)
                pe_h_level(pe, 0, n)
            pe.wait_ge(*after("hq1"))
            for n in range(4, 8):
                pe_h_piece(pe, 5, n - 4, 6)
                pe_h_level(pe, 0, n)
            pe_h_level(pe, 0, 8)
            pe.wait_ge(*after("hv0"))
            pe_h_piece(pe, 6, 0, 4)
            pe_h_level(pe, 1, 0)
            pe_h_out(pe, 0)
            for n in range(1, 4):
                pe_h_piece(pe, 6, n, 4)
                pe_h_level(pe, 1, n)
            pe.wait_ge(*after("hs0"))
            for n in range(4, 8):
                pe_h_piece(pe, 7, n - 4, 4)
                pe_h_level(pe, 1, n)
            pe_h_level(pe, 1, 8)
            pe_h_out(pe, 1)
            pe.wait_ge(*after("hs1"))
            pe_turn(pe, "hgo", mix, ready="hgo.m1")
            pe.wait_ge(*after(turn_end("hgo")))
            out_units(pe, "hgo")

        def act_hg(act, src):
            act_norm(act, "hg", src)
            S = lambda n, which=(0, 1, 2, 3): split4(split_hi, act, hu(n), which=which)
            S(0)
            act_bounds(act)
            S(1, (0, 1))
            act_h_forget(act, 0)
            S(1, (2, 3))
            S(2, (0, 1))
            act_h_decay(act, 0)
            act_h_forget(act, 1)
            S(2, (2, 3))
            S(3, (0, 1))
            act_h_decay(act, 1)
            act_h_q(act, 0)
            S(3, (2, 3))
            for n in range(8):
                S(4 + n // 4, (n % 4,))
                act_level(act, "h0", n, h_e)
                if n == 1:
                    act_h_q(act, 1)
                if n == 5:
                    act_h_v(act, 0)
            for n in range(8):
                S(6 + n // 4, (n % 4,))
                if n == 1:
                    act_h_v(act, 1)
                act_level(act, "h1", n, h_e)
                if n == 2:
                    act_h_square(act, 0)
                if n == 5:
                    act_h_gate(act, 0)
            act_h_gate(act, 1)
            split4(split_hi, act, piece_at("hgo", 0))
            act_h_square(act, 1)
            act_turn(act, "hgo")
            split4(split_hi, act, piece_at("hgo", 1))
            act_post(act, "hgo", 2 * (first_slot["hgo"] + 4))

        def dve_hg(dve):
            dve_norm(dve, "hg")
            S = lambda n, which=(0, 1, 2, 3): split4(split_lo, dve, hu(n), which=which)
            S(0)
            dve_bounds(dve)
            S(1, (0, 1))
            dve_h_forget(dve, 0)
            S(1, (2, 3))
            S(2, (0, 1))
            dve_h_decay(dve, 0)
            dve_h_forget(dve, 1)
            S(2, (2, 3))
            S(3, (0, 1))
            dve_h_decay(dve, 1)
            S(3, (2, 3))
            dve_h_levels(dve, 0, hu(4))
            X, u = "h1", 1
            for n, half in enumerate(ALL_LEVELS):
                dve_level_x(dve, X, n, half, hb[u], h_e, ["h0.l7", "hq1"] if n == 0 else [f"{X}.l{n - 1}"])
                split_lo(dve, hu(6) + n)
                if n >= 1:
                    dve_h_put(dve, u, n - 1)
                dve_level_l(dve, X, n, half, hq[u], hk[u], h_e, h_l[n % 2], [f"{X}.P{n - 2}"] if n >= 2 else [f"h0.P{6 + n}"])
                if n == 2:
                    dve_h_sums(dve, 0)
                if n == 3:
                    dve_h_out_norm(dve, 0)
                if n == 6:
                    dve_h_out_gate(dve, 0)
            for n in (7, 8):
                dve_h_put(dve, u, n)
            split4(split_lo, dve, piece_at("hgo", 0))
            dve_h_sums(dve, 1)
            dve_h_out_norm(dve, 1)
            dve_h_out_gate(dve, 1)
            dve_turn(dve, "hgo")
            split4(split_lo, dve, piece_at("hgo", 1))
            dve_post(dve, "hgo")

        def pool_hg(pool, gains):
            pool_norm(pool, "hg")
            next_gain(pool, gains)
            pool.wait_ge(*after("hd1.ln"))
            nc.gpsimd.memset(h_at, 0.0).then_inc(*steps.did("pool", "h0.at0"))
            pool.wait_ge(*after("h0.O"))
            nc.gpsimd.memset(h_at, 0.0).then_inc(*steps.did("pool", "h1.at0"))
            pool_h(pool, 0)
            pool_h(pool, 1)
            next_gain(pool, gains)
            pool_post(pool, "hgo")
            next_gain(pool, gains)

        staged = arena[:, 4096:4096 + 5 * P].rearrange("p (b n) -> p b n", b=5)
        conv_m, conv_g, lb_logits, gate_bias = few.take(16), few.take(48), few.take(16), few.take(2)
        spread = {}
        SPREAD = [("q_norm", A["q_norm"][0]), ("k_norm", A["k_norm"][0]), ("gla_out_norm", A["gla_out_norm"][0]),
                  ("attn_sinks", A["attn_sinks"][0]), ("ab_m_gate_bias_2", A["ab_m_gate_bias_2"][0].rearrange("a b -> (a b)")),
                  ("ab_g_a_log_2", A["ab_g_a_log_2"][0]), ("ab_g_dt_bias_2", A["ab_g_dt_bias_2"][0])]
        for name, v in SPREAD:
            spread[name] = few.take(v.shape[0])
        gate_up = few.take(256, parts=16)
        p_rows = few.take(NT * 256).rearrange("p (t n) -> p t n", t=NT)

        def act_params(act):
            act.dma_start(h[:, :, :], A["x"][0].rearrange("(t p) d -> p t d", p=P)).then_inc(x_in, 16)
            loads = [(const[:, :], A["const"])]
            for l in range(2):
                w = A["ffn_conv_w_2"][l].rearrange("k (c n) -> (k c) n", n=P)
                loads.append((staged[0:4 * FC, 2 * l, :], w[0:4 * FC]))
                loads.append((staged[0:2 * FC, 2 * l + 1, :], w[4 * FC:6 * FC]))
                loads.append((staged[2 * FC:4 * FC, 2 * l + 1, :], A["ffn_conv_b_2"][l].rearrange("(c n) -> c n", n=P)))
            at = 0
            for v in (A["ab_conv_m_2"][0].rearrange("k (c n) -> (k c) n", n=P),
                      A["ab_conv_g_2"][0].rearrange("k (c n) -> (k c) n", n=P),
                      A["c_lb_logits_2"].rearrange("k (c n) -> (k c) n", n=P),
                      A["gla_b_gate"].rearrange("k (c n) -> (k c) n", n=P)):
                loads.append((staged[at:at + v.shape[0], 4, :], v))
                at += v.shape[0]
            for name, v in SPREAD:
                loads.append((spread[name], v.partition_broadcast(P)))
            loads.append((gate_up, A["gla_w_gate_up"][0]))
            loads.append((p_rows, A["p"][0, 0].rearrange("(t p) n -> p t n", p=P)))
            for dst, src in loads:
                act.dma_start(dst, src).then_inc(params, 16)
            return 16 * len(loads)

        PARAMS = 16 * (1 + 6 + 4 + len(SPREAD) + 2)

        def pe_params(pe):
            pe.wait_ge(params, PARAMS)
            for b in range(5):
                n = 4 * FC if b < 4 else 82
                last = nc.tensor.transpose(psum[:, b // 4, (b % 4) * P:(b % 4) * P + n], staged[0:n, b, :], ident[0:n, 0:n])
            last.then_inc(*steps.did("pe", "params.T"))

        def dve_params(dve):
            nc.vector.memset(zero_r[:, :].bitcast(F32), 0.0).then_inc(*steps.did("dve", "zero_r"))
            nc.vector.memset(ones, 1.0).then_inc(*steps.did("dve", "ones"))
            dve.wait_ge(*after("params.T"))
            for l in range(2):
                for b in range(2):
                    nc.vector.tensor_copy(taps[:, l, 2 * b:2 * b + 2, :],
                                          psum[:, 0, (2 * l + b) * P:(2 * l + b) * P + 4 * FC].rearrange("p (k c) -> p k c", k=2))
            at = 0
            for a, n in ((conv_m, 16), (conv_g, 48), (lb_logits, 16), (gate_bias, 2)):
                last = nc.vector.tensor_copy(a, psum[:, 1, at:at + n])
                at += n
            last.then_inc(*steps.did("dve", "params"))

        STAGES = ["ffn0", "mix0", "ffn1", "ple", "ab", "ffn2", "hg", "ffn3"]
        stages = STAGES[:STAGES.index(stop) + 1] if stop else STAGES
        sources = dict(zip(STAGES, ["x", "ffn0", "mix0", "ffn1", "ple", "abo", "ffn2", "hgo"]))
        final = {"mix0": "mix0", "ab": "abo", "hg": "hgo"}.get(stages[-1], stages[-1])

        block = ctx.enter_context(nc.Block())

        @block.sync
        def _(sp):
            for st in stages:
                if st.startswith("ffn"):
                    sp_ffn(sp, int(st[3]))
                elif st == "mix0":
                    sp_mix0(sp)
                else:
                    for part in {"ple": ("emb", "ple"), "ab": ("ab", "abo"), "hg": ("hg", "hgo")}[st]:
                        sp_proj(sp, part)
            o = out[0].rearrange("(t p) d -> p t d", p=P)
            for t in range(NT):
                sp.wait_ge(*after(f"{final}.h{t}"))
                sp.dma_start(o[:, t, :], h[:, t, :]).then_inc(out_sem, 16)
            sp.wait_ge(out_sem, 32)

        @block.gpsimd
        def _(pool):
            nc.gpsimd.memset(half_power, -0.5).then_inc(*steps.did("pool", "half_power"))
            pool.wait_ge(*after("half_power"))
            gains = iter([g[0] for g in GAINS])
            for _ in range(2):
                next_gain(pool, gains)
            for st in stages:
                if st.startswith("ffn"):
                    pool_norm(pool, st)
                    next_gain(pool, gains)
                    if int(st[3]) >= 2:
                        pool_post(pool, st)
                        next_gain(pool, gains)
                if st == "mix0":
                    pool_mix0(pool)
                    next_gain(pool, gains)
                if st == "ple":
                    pool_ple(pool)
                    next_gain(pool, gains)
                    next_gain(pool, gains)
                if st == "ab":
                    pool_ab(pool, gains)
                if st == "hg":
                    pool_hg(pool, gains)

        @block.scalar
        def _(act):
            act_params(act)
            act.wait_ge(x_in, 16)
            for st in stages:
                if st.startswith("ffn"):
                    act_ffn(act, int(st[3]), sources[st])
                    if int(st[3]) >= 2:
                        act_post(act, st, 2 * (first_slot[st] + 3 * GROUPS))
                if st == "mix0":
                    act_mix0(act, sources[st])
                if st == "ple":
                    act_ple(act)
                if st == "ab":
                    act_ab(act, sources[st])
                if st == "hg":
                    act_hg(act, sources[st])

        @block.vector
        def _(dve):
            dve.wait_ge(x_in, 16)
            nc.vector.tensor_copy(junk, h[:, 0, 0:1]).then_inc(*steps.did("dve", "x.h0"))
            nc.vector.tensor_copy(junk2, h[:, 0, 0:1]).then_inc(*steps.did("dve", "x.h1"))
            dve_params(dve)
            for st in stages:
                if st.startswith("ffn"):
                    dve_ffn(dve, int(st[3]))
                    if int(st[3]) >= 2:
                        dve_post(dve, st)
                if st == "mix0":
                    dve_mix0(dve)
                if st == "ple":
                    dve_ple(dve)
                if st == "ab":
                    dve_ab(dve)
                if st == "hg":
                    dve_hg(dve)

        @block.tensor
        def _(pe):
            pe_params(pe)
            pe.wait_ge(*after("params"))
            for st in stages:
                if st.startswith("ffn"):
                    pe_ffn(pe, int(st[3]))
                if st == "mix0":
                    pe_mix0(pe)
                if st == "ple":
                    pe_ple(pe)
                if st == "ab":
                    pe_ab(pe)
                if st == "hg":
                    pe_hg(pe)

        return steps.made


def kernel(**inputs):
    import numpy as _np
    import concourse.bacc as _bacc
    from concourse import mybir as _mybir
    from concourse.bass_utils import run_bass_kernel_spmd as _run

    arrays = {f"in_{name}": _np.ascontiguousarray(a) for name, a in inputs.items()}
    arrays["in_const"] = shape_constants()[1]

    def program(numbered):
        nc = _bacc.Bacc("TRN2", target_bir_lowering=False, num_devices=1)
        A = {name[3:]: nc.dram_tensor(name, a.shape, _mybir.dt.from_np(a.dtype), kind="ExternalInput").ap()
             for name, a in arrays.items()}
        out = nc.dram_tensor("out_0", (1, SEQ, D), F32, kind="ExternalOutput").ap()
        return nc, build(nc, A, out, numbered)

    _, numbering = program(None)
    nc, _ = program(numbering)
    r = _run(nc, [arrays], core_ids=[0])
    return r.results[0]["out_0"]
```

```python
from contextlib import ExitStack

import numpy as np
import concourse.bass as bass
from concourse import mybir

F32 = mybir.dt.float32
F32R = mybir.dt.float32r
U32 = mybir.dt.uint32
ALU = mybir.AluOpType
ACT = mybir.ActivationFunctionType
AX_X = mybir.AxisListType.X

P = 128
SEQ = 256
NT = SEQ // P
D = 1024
KC = D // P
F = 2816
FC = F // P
GROUP = 256
GROUPS = F // GROUP
BANK = 512
RING = 6
SLOT = 2048
PIECE = SLOT // 2
EPS = 1e-6
BIG = 1.0e30
PARTS = [("ffn0", 3 * GROUPS), ("mix0", 10), ("mix0o", 4), ("ffn1", 3 * GROUPS), ("emb", 1), ("ple", 4),
         ("ab", 15), ("abo", 4), ("ffn2", 3 * GROUPS), ("hg", 16), ("hgo", 4), ("ffn3", 3 * GROUPS)]
LEVELS = [64, 32, 16, 8, 4, 2, 1]

MQ, MV, MO, MI, DQ, DK, DV, DG, DA = 0, 512, 1024, 1536, 1544, 2056, 2568, 3080, 3592
AQ, AK, AV, GQ, GK, GV, GR, GO = 0, 512, 640, 768, 1024, 1280, 1792, 1808


def shape_constants():
    j = np.arange(P)[:, None]
    i = np.arange(P)[None, :]
    parts = {"ident": (j == i), "upper": (j <= i)}
    for h in LEVELS:
        parts[f"level{h}"] = (j // (2 * h) == i // (2 * h)) & (j % (2 * h) < h) & (i % (2 * h) >= h)
    parts["prev"] = np.where(i > j, 0.0, -BIG)
    parts["own"] = np.where(i <= j, 0.0, -BIG)
    freq = np.float32(10000.0) ** (-np.arange(0, 64, 2, dtype=np.float32) / np.float32(64))
    ang = (np.arange(SEQ, dtype=np.float32)[:, None] * freq[None, :]).reshape(NT, P, 32)
    for name, f in (("cos", np.cos), ("sin", np.sin)):
        for t in range(NT):
            parts[f"{name}{t}"] = f(ang[t].astype(np.float64))
    at, cols, n = {}, [], 0
    for name, a in parts.items():
        at[name] = n
        n += a.shape[1]
        cols.append(a.astype(np.float32))
    return at, np.ascontiguousarray(np.concatenate(cols, axis=1))


class Steps:

    def __init__(self, nc, ctx, numbered):
        self.nc, self.ctx, self.numbered = nc, ctx, numbered
        self.sems, self.count, self.made = {}, {}, {}

    def sem(self, name):
        if name not in self.sems:
            self.sems[name] = self.ctx.enter_context(self.nc.semaphore(name))
        return self.sems[name]

    def did(self, engine, name):
        assert name not in self.made, name
        self.count[engine] = self.count.get(engine, 0) + 1
        self.made[name] = (f"{engine}_done", self.count[engine])
        return self.sem(f"{engine}_done"), 1

    def after(self, name):
        if self.numbered is None:
            return self.sem("pe_done"), 1
        s, n = self.numbered[name]
        return self.sem(s), n


def build(nc, A, out, numbered, stop=None):
    const_at, _ = shape_constants()
    ctx = ExitStack()
    with ctx:
        steps = Steps(nc, ctx, numbered)
        after = steps.after

        def sb(name, shape, dt=F32):
            return ctx.enter_context(nc.sbuf_tensor(name, shape, dt))

        def sem(name):
            return ctx.enter_context(nc.semaphore(name))

        raw = sb("raw", [P, RING, SLOT])
        whi = sb("whi", [P, RING, PIECE], F32R)
        wlo = sb("wlo", [P, RING, PIECE], F32R)
        xh = sb("xh", [P, KC, SEQ], F32R)
        xl = sb("xl", [P, KC, SEQ], F32R)
        hidh = sb("hidh", [P, 2, 2, SEQ], F32R)
        hidl = sb("hidl", [P, 2, 2, SEQ], F32R)
        h = sb("h", [P, NT, D])
        gain = sb("gain", [P, 2, D])
        const = sb("const", [P, A["const"].shape[1]])
        small = sb("small", [P, 1792])
        zero_r = sb("zero_r", [P, P], F32R)
        arena = sb("arena", [P, 13824])
        psum = ctx.enter_context(nc.psum_tensor("psum", [P, 8, BANK], F32))

        class Columns:
            def __init__(self, tile):
                self.tile, self.n = tile, 0

            def take(self, n, parts=P):
                a = self.tile[0:parts, self.n:self.n + n]
                self.n += n
                assert self.n <= self.tile.shape[1], self.n
                return a

        few = Columns(small)

        def bank(b, a=0, n=BANK):
            return psum[:, b, a:a + n]

        def cst(name, n=P):
            return const[:, const_at[name]:const_at[name] + n]

        ident = cst("ident")

        sg = arena[:, 0:1024].rearrange("p (a c t) -> p a c t", a=2, c=2)
        hp = arena[:, 1024:2048].rearrange("p (a c t) -> p a c t", a=2, c=2)
        cg = arena[:, 2048:4096].rearrange("p (a g c t) -> p a g c t", a=2, g=2, c=2)
        nrm = arena[:, 11776:13824].rearrange("p (t d) -> p t d", t=NT)
        emb = arena[:, 0:2048].rearrange("p (t d) -> p t d", t=NT)
        sgm = arena[:, 2048:4096].rearrange("p (t d) -> p t d", t=NT)
        taps = sb("taps", [P, 2, 4, 2 * FC])

        loaded = [sem(f"loaded{n}") for n in range(RING)]
        hi_done = sem("hi_done")
        lo_done = sem("lo_done")
        used = sem("used")
        sg_ready = sem("sg_ready")
        hp_ready = sem("hp_ready")
        hid_hi = sem("hid_hi")
        hid_lo = sem("hid_lo")
        conv_mid = sem("conv_mid")
        conv_one = sem("conv_one")
        conv_all = sem("conv_all")
        params = sem("params")
        x_in = [sem(f"x_in{t}") for t in range(NT)]
        ident_in = sem("ident_in")
        gains_in = [sem(f"gain_in{n}") for n in range(2)]
        out_sem = sem("stored")

        ng = A["norm_gains_2"]
        GAINS = [("ffn0", [A["ffn1_norm"][0]], "ffn0.w11"), ("mix0", [A["mix_norm"][0]], "mix0.w11"),
                 ("ffn1", [A["ffn2_norm"][0]], "ffn1.w11"), ("emb", [A["ple_norm"][0]], "emb.e1"),
                 ("ple", [A["ple_gate_norm"][0]], "ple.w11"),
                 ("ab", [ng[0, 0]], "ab.w11"), ("abh", [A["ab_m_norm_2"][0], A["ab_g_norm_2"][0]], "ab.last"),
                 ("abp", [ng[0, 1]], "abo.p11"),
                 ("ffn2", [ng[0, 2]], "ffn2.w11"), ("ffn2p", [ng[0, 3]], "ffn2.p11"),
                 ("hg", [ng[1, 0]], "hg.w11"), ("hgh", [A["c_norm_2"][0]], "hg.last"), ("hgp", [ng[1, 1]], "hgo.p11"),
                 ("ffn3", [ng[1, 2]], "ffn3.w11"), ("ffn3p", [ng[1, 3]], "ffn3.p11")]
        gain_at, counts = {}, [0, 0]
        for n, (name, parts, last_use) in enumerate(GAINS):
            counts[n % 2] += 16 * len(parts)
            gain_at[name] = (n, counts[n % 2])

        def pool_gain(pool, name):
            n, _ = gain_at[name]
            if n >= 2:
                pool.wait_ge(*after(GAINS[n - 2][2]))
            at = 0
            for v in GAINS[n][1]:
                pool.dma_start(gain[:, n % 2, at:at + v.shape[0]], v.partition_broadcast(P)).then_inc(gains_in[n % 2], 16)
                at += v.shape[0]

        def next_gain(pool, gains):
            name = next(gains, None)
            if name:
                pool_gain(pool, name)

        def gain_of(dve, name):
            n, value = gain_at[name]
            dve.wait_ge(gains_in[n % 2], value)
            return gain[:, n % 2, :]

        SWIGLU = [(A["ffn1_w_gate"][0], A["ffn1_w_up"][0], A["ffn1_w_down"][0]),
                  (A["ffn2_w_gate"][0], A["ffn2_w_up"][0], A["ffn2_w_down"][0])]
        CONVFF = [(A["ffn_w_up_2"][l][:, 0:F], A["ffn_w_up_2"][l][:, F:2 * F], A["ffn_w_down_2"][l]) for l in range(2)]
        FFN = SWIGLU + CONVFF

        first_slot, total_slots = {}, 0
        for part, slots in PARTS:
            first_slot[part] = total_slots
            total_slots += slots

        def sp_slot(sp, s, i, shape, parts):
            if not (isinstance(i, int) and s + RING * i < RING):
                sp.wait_ge(lo_done, 2 * (s - RING) + 2 + 2 * RING * i)
            a, b = shape
            view = raw[:, s % RING, 0:a * b].rearrange("p (a b) -> p a b", a=a)
            for where, src in parts:
                dst = view[where] if isinstance(where, tuple) else view[:, where, :]
                sp.dma_start(dst, src).then_inc(loaded[s % RING], 16)

        def sp_gate_up(sp, s, i, n, g):
            wg, wu, _ = FFN[n]
            for k in range(2):
                sp_slot(sp, s + k, i, (4, 512), [
                    ((slice(None), slice(None), slice(256 * j, 256 * j + 256)),
                     w.rearrange("(k p) n -> p k n", p=P)[:, 4 * k:4 * k + 4, bass.ds(g * GROUP, GROUP)])
                    for j, w in enumerate((wg, wu))])

        def sp_down(sp, s, i, n, g):
            wd = FFN[n][2].rearrange("(f p) n -> p f n", p=P)
            sp_slot(sp, s, i, (2, D), [(slice(c, c + 1), wd[:, bass.ds(g * 2 + c, 1), :]) for c in range(2)])

        def sp_ffn(sp, n):
            s = first_slot[f"ffn{n}"] + 2
            sp_gate_up(sp, s - 2, 0, n, 0)

            def body(i):
                for half in range(2):
                    sp_gate_up(sp, s + 3 * half, i, n, i * 2 + half + 1)
                    sp_down(sp, s + 3 * half + 2, i, n, i * 2 + half)
            body(0)
            with sp.Fori(1, GROUPS // 2) as i:
                body(i)
            sp_down(sp, s + 3 * (GROUPS - 1), 0, n, GROUPS - 1)

        def piece_of(p, shape):
            a, b = shape[0] // 2, shape[1]
            r = raw[:, (p // 2) % RING, (p % 2) * a * b:(p % 2 + 1) * a * b]
            return r, whi[:, p % RING, 0:a * b], wlo[:, p % RING, 0:a * b]

        def split_hi(act, p, shape=(4, 512), i=0):
            if p % 2 == 0:
                act.wait_ge(loaded[(p // 2) % RING], 32 * (p // 2 // RING + 1) + 32 * i)
            if not (isinstance(i, int) and p + 2 * RING * i < RING):
                act.wait_ge(used, p - RING + 1 + 2 * RING * i)
            r, hi, _ = piece_of(p, shape)
            nc.scalar.activation(hi, r, ACT.Copy).then_inc(hi_done, 1)

        def split_lo(dve, p, shape=(4, 512), i=0):
            dve.wait_ge(hi_done, p + 1 + 2 * RING * i)
            r, hi, lo = piece_of(p, shape)
            nc.vector.tensor_tensor(lo, r, hi.bitcast(F32), ALU.subtract).then_inc(lo_done, 1)

        def weights(p, a, b):
            return (whi[:, p % RING, 0:a * b].rearrange("p (a b) -> p a b", a=a),
                    wlo[:, p % RING, 0:a * b].rearrange("p (a b) -> p a b", a=a))

        def three(pe_out, sh, sl, mh, ml, start, stop):
            nc.tensor.matmul(pe_out, sh, mh, start=start, stop=False, skip_group_check=True)
            nc.tensor.matmul(pe_out, sh, ml, start=False, stop=False, skip_group_check=True)
            return nc.tensor.matmul(pe_out, sl, mh, start=False, stop=stop, skip_group_check=True)

        def pe_turn(pe, X, t, b, to, tile, ready):
            pe.wait_ge(*after(ready))
            for c in range(4):
                last = nc.tensor.transpose(bank(to, c * P, P), tile[:, t, b * BANK + c * P:b * BANK + c * P + P], ident)
            last.then_inc(*steps.did("pe", f"{X}.T{t}{b}"))

        def turned(t, b, at):
            return (bank(at).rearrange("p (c t) -> p c t", c=4),
                    xh[:, 4 * b:4 * b + 4, t * P:t * P + P], xl[:, 4 * b:4 * b + 4, t * P:t * P + P])

        def act_turn(act, X, t, b, at):
            src, hi, _ = turned(t, b, at)
            act.wait_ge(*after(f"{X}.T{t}{b}"))
            nc.scalar.activation(hi, src, ACT.Copy).then_inc(*steps.did("act", f"{X}.xh{t}{b}"))

        def dve_turn(dve, X, t, b, at):
            src, hi, lo = turned(t, b, at)
            dve.wait_ge(*after(f"{X}.xh{t}{b}"))
            nc.vector.tensor_tensor(lo, src, hi.bitcast(F32), ALU.subtract).then_inc(*steps.did("dve", f"{X}.xl{t}{b}"))

        half_power = few.take(64)
        junk, junk2 = few.take(1), few.take(1)

        def pool_rstd(pool, name, total, n, count, scratch):
            nc.gpsimd.tensor_scalar(scratch, total, 1.0 / count, EPS, ALU.mult, ALU.add)\
                .then_inc(*steps.did("pool", f"{name}.mean"))
            pool.wait_ge(*after(f"{name}.mean"))
            nc.gpsimd.tensor_tensor(scratch, scratch, half_power[:, 0:n], ALU.pow)\
                .then_inc(*steps.did("pool", name))

        ADD = {"ffn0": 0.5, "mix0o": 1.0, "ffn1": 0.5}
        POST = {"abo": "abp", "ffn2": "ffn2p", "hgo": "hgp", "ffn3": "ffn3p"}
        BANKS = [(t, b) for t in range(NT) for b in range(2)]
        sums = {}

        def row_sums(X):
            if X not in sums:
                sums[X] = (few.take(4), few.take(NT), few.take(NT))
            return sums[X]

        def cut(tile, t, b):
            return tile[:, t, b * BANK:b * BANK + BANK]

        def product_ready(prev, t, b):
            if (t, b) == (1, 1):
                return used, 2 * (first_slot[prev] + dict(PARTS)[prev])
            return after(f"{prev}.acc{t}{b}")

        def act_squares(act, src, total, t, b, done):
            nc.scalar.activation(cut(nrm, t, b), src, ACT.Square, accum_out=total[:, 2 * t + b:2 * t + b + 1])\
                .then_inc(*steps.did("act", done))

        def act_between(act, prev, X):
            if prev in POST:
                for t, b in BANKS:
                    act.wait_ge(*product_ready(prev, t, b))
                    act_squares(act, bank(2 * t + b), row_sums(prev)[0], t, b, f"{prev}.ps{t}{b}")
            if prev == "ple":
                for t, b in BANKS:
                    act.wait_ge(*product_ready(prev, t, b))
                    nc.scalar.activation(cut(sgm, t, b), bank(2 * t + b), ACT.Sigmoid).then_inc(*steps.did("act", f"ple.g{t}{b}"))
            if X is None:
                return
            total, _, r = row_sums(X)

            def squares(t):
                for b in range(2):
                    wait_h(act, prev, t, b)
                    act_squares(act, cut(h, t, b), total, t, b, f"{X}.ss{t}{b}")

            def scale(t, b):
                act.wait_ge(*after(f"{X}.r{t}"))
                act.wait_ge(*after(f"{X}.w{t}{b}"))
                nc.scalar.activation(cut(nrm, t, b), cut(nrm, t, b), ACT.Identity, scale=r[:, t:t + 1])\
                    .then_inc(*steps.did("act", f"{X}.n{t}{b}"))
            squares(0)
            scale(0, 0)
            scale(0, 1)
            squares(1)
            act_turn(act, X, 0, 0, 0)
            act_turn(act, X, 0, 1, 1)
            for b in range(2):
                scale(1, b)
            for b in range(2):
                act_turn(act, X, 1, b, 2 + b)

        def wait_h(eng, prev, t, b):
            if prev == "x":
                if b == 0:
                    eng.wait_ge(x_in[t], 16)
            else:
                eng.wait_ge(*after(f"{prev}.h{t}{b}"))

        def pool_between(pool, prev, X):
            for Y_, ss in ((prev, "ps"), (X, "ss")):
                if (ss == "ps" and prev not in POST) or Y_ is None:
                    continue
                total, mean, r = row_sums(Y_)
                for t in range(NT):
                    m = mean[:, t:t + 1]
                    pool.wait_ge(*after(f"{Y_}.{ss}{t}0"))
                    nc.gpsimd.tensor_scalar(m, total[:, 2 * t:2 * t + 1], 1.0 / D, EPS, ALU.mult, ALU.add)\
                        .then_inc(*steps.did("pool", f"{Y_}.{ss}m{t}"))
                    pool.wait_ge(*after(f"{Y_}.{ss}{t}1"))
                    pool.wait_ge(*after(f"{Y_}.{ss}m{t}"))
                    nc.gpsimd.tensor_scalar(m, total[:, 2 * t + 1:2 * t + 2], 1.0 / D, m, ALU.mult, ALU.add)\
                        .then_inc(*steps.did("pool", f"{Y_}.{ss}n{t}"))
                    pool.wait_ge(*after(f"{Y_}.{ss}n{t}"))
                    nc.gpsimd.tensor_tensor(r[:, t:t + 1], m, half_power[:, 0:1], ALU.pow)\
                        .then_inc(*steps.did("pool", f"{Y_}.{'pr' if ss == 'ps' else 'r'}{t}"))

        def dve_between(dve, prev, X):
            def product_gain(t, b):
                g = gain_of(dve, POST[prev])
                dve.wait_ge(*after(f"{prev}.ps{t}{b}"))
                nc.vector.tensor_tensor(cut(nrm, t, b), bank(2 * t + b), g[:, b * BANK:b * BANK + BANK], ALU.mult)\
                    .then_inc(*steps.did("dve", f"{prev}.p{t}{b}"))

            def gated(t, b):
                dve.wait_ge(*after(f"ple.g{t}{b}"))
                nc.vector.tensor_tensor(cut(sgm, t, b), cut(sgm, t, b), cut(emb, t, b), ALU.mult).then_inc(*steps.did("dve", f"ple.m{t}{b}"))

            def prepare(t):
                for b in range(2):
                    if prev in POST:
                        product_gain(t, b)
                    if prev == "ple":
                        gated(t, b)

            def add(t):
                for b in range(2):
                    hh = cut(h, t, b)
                    if prev in ADD:
                        dve.wait_ge(*product_ready(prev, t, b))
                        last = nc.vector.scalar_tensor_tensor(hh, bank(2 * t + b), ADD[prev], hh, ALU.mult, ALU.add)
                    elif prev in POST:
                        dve.wait_ge(*after(f"{prev}.pr{t}"))
                        dve.wait_ge(*after(f"{prev}.p{t}{b}"))
                        last = nc.vector.scalar_tensor_tensor(hh, cut(nrm, t, b), row_sums(prev)[2][:, t:t + 1], hh, ALU.mult, ALU.add)
                    elif prev == "ple":
                        dve.wait_ge(*after(f"ple.m{t}{b}"))
                        last = nc.vector.tensor_tensor(hh, hh, cut(sgm, t, b), ALU.add)
                    else:
                        continue
                    last.then_inc(*steps.did("dve", f"{prev}.h{t}{b}"))

            def gained(t, b):
                g = gain_of(dve, X)
                dve.wait_ge(*after(f"{X}.ss{t}{b}"))
                nc.vector.tensor_tensor(cut(nrm, t, b), cut(h, t, b), g[:, b * BANK:b * BANK + BANK], ALU.mult)\
                    .then_inc(*steps.did("dve", f"{X}.w{t}{b}"))
            prepare(0)
            add(0)
            if X is None:
                prepare(1)
                add(1)
                return
            if prev == "x":
                gained(0, 0)
                gained(0, 1)
                gained(1, 0)
                gained(1, 1)
                for t, b in BANKS:
                    dve_turn(dve, X, t, b, 2 * t + b)
                return
            if prev in POST or prev == "ple":
                prepare(1)
            gained(0, 0)
            gained(0, 1)
            add(1)
            gained(1, 0)
            gained(1, 1)
            dve_turn(dve, X, 0, 0, 0)
            dve_turn(dve, X, 0, 1, 1)
            dve_turn(dve, X, 1, 0, 2)
            dve_turn(dve, X, 1, 1, 3)

        def pe_between(pe, X):
            for t, b in BANKS:
                pe_turn(pe, X, t, b, 2 * t + b, nrm, f"{X}.n{t}{b}")

        def wait_turned(pe, X, b):
            pe.wait_ge(*after(f"{X}.xl1{b}"))

        def pe_piece(pe, p, hi, lo, start, i=0):
            pe.wait_ge(lo_done, p + 1 + 2 * RING * i)
            wh, wl = weights(p, 1, D)
            for t, b in BANKS:
                tok, col = slice(t * P, t * P + P), slice(b * BANK, b * BANK + BANK)
                last = three(bank(2 * t + b), hi[:, tok], lo[:, tok], wh[:, 0, col], wl[:, 0, col], start=start, stop=False)
            last.then_inc(used, 1)

        def pe_last_pieces(pe, X, p, parts, start=False):
            for t, b in BANKS:
                tok, col = slice(t * P, t * P + P), slice(b * BANK, b * BANK + BANK)
                for n, (hi, lo) in enumerate(parts):
                    if (t, b) == (0, 0):
                        pe.wait_ge(lo_done, p + n + 1)
                    wh, wl = weights(p + n, 1, D)
                    last = three(bank(2 * t + b), hi[:, tok], lo[:, tok], wh[:, 0, col], wl[:, 0, col],
                                 start=(start and n == 0), stop=(n == len(parts) - 1))
                    if (t, b) == (1, 1):
                        last.then_inc(used, 1)
                if (t, b) != (1, 1):
                    last.then_inc(*steps.did("pe", f"{X}.acc{t}{b}"))

        def pe_out(pe, part, k):
            if k == 0:
                wait_turned(pe, part, 0)
            pe_piece(pe, 2 * first_slot[part] + k, xh[:, k, :], xl[:, k, :], k == 0)

        def pe_out_last(pe, part):
            wait_turned(pe, part, 1)
            pe_last_pieces(pe, part, 2 * first_slot[part] + 4, [(xh[:, k, :], xl[:, k, :]) for k in range(4, 8)])

        def pe_unit(pe, p, rows=(), columns=(), shape=(4, 512), which=(0, 1, 2, 3), turned=None):
            for k in which:
                if turned and k % 2 == 0:
                    wait_turned(pe, turned, k // 2)
                pe.wait_ge(lo_done, p + k + 1)
                wh, wl = weights(p + k, shape[0] // 2, shape[1])
                for kk in range(2):
                    kc = 2 * k + kk
                    for c0, c1, outs, starts in rows:
                        for t in range(NT):
                            tok = slice(t * P, t * P + P)
                            last = three(outs[t], xh[:, kc, tok], xl[:, kc, tok], wh[:, kk, c0:c1], wl[:, kk, c0:c1],
                                         start=(kc == 0 and starts[t]), stop=(kc == KC - 1))
                    for c0, o, starts in columns:
                        last = three(o, wh[:, kk, c0:c0 + P], wl[:, kk, c0:c0 + P], xh[:, kc, :], xl[:, kc, :],
                                     start=(kc == 0 and starts), stop=(kc == KC - 1))
                last.then_inc(used, 1)

        def out_splits(split, eng, part, which):
            for k in which:
                split(eng, 2 * first_slot[part] + k, (2, D))

        def split4(fn, eng, p, shape=(4, 512), which=(0, 1, 2, 3)):
            for k in which:
                fn(eng, p + k, shape)

        def pe_gate_up(pe, n, g, q, p, i):
            if not isinstance(g, int) or n * GROUPS + g >= 2:
                pe.wait_ge(hid_lo, g + n * GROUPS - 1)
            for k in range(4):
                if isinstance(g, int) and g == 0 and k % 2 == 0:
                    wait_turned(pe, f"ffn{n}", k // 2)
                pe.wait_ge(lo_done, p + k + 1 + 2 * RING * i)
                wh, wl = weights(p + k, 2, 512)
                for kk in range(2):
                    kc = 2 * k + kk
                    for c in range(2):
                        for j in range(2):
                            col = slice(256 * j + 128 * c, 256 * j + 128 * c + 128)
                            last = three(psum[:, 4 + 2 * q + c, 256 * j:256 * j + 256], wh[:, kk, col],
                                         wl[:, kk, col], xh[:, kc, :], xl[:, kc, :],
                                         start=(kc == 0 and j == 0), stop=(kc == KC - 1))
                last.then_inc(used, 1)

        def pe_down(pe, n, g, q, p, i):
            pe.wait_ge(hid_lo, g + n * GROUPS + 1)
            for c in range(2):
                pe_piece(pe, p + c, hidh[:, q, c, :], hidl[:, q, c, :], False, i)

        def ffn_loop(eng, body):
            body(0)
            with eng.Fori(1, GROUPS // 2) as i:
                body(i)

        def pe_ffn(pe, n):
            X = f"ffn{n}"
            pe_between(pe, X)
            p = 2 * first_slot[X]
            pe_gate_up(pe, n, 0, 0, p, 0)
            for b in range(4):
                nc.tensor.matmul(bank(b), zero_r[:, :], xh[:, 0:2, :], start=True, stop=True, skip_group_check=True)

            def body(i):
                for half in range(2):
                    q = p + 4 + 6 * half
                    pe_gate_up(pe, n, i * 2 + half + 1, (half + 1) % 2, q, i)
                    pe_down(pe, n, i * 2 + half, half, q + 4, i)
            ffn_loop(pe, body)
            if n == 1:
                pe.wait_ge(hid_lo, n * GROUPS + GROUPS - 1)
                pe_turn_p(pe)
            pe.wait_ge(hid_lo, n * GROUPS + GROUPS)
            pe_last_pieces(pe, X, p + 4 + 6 * (GROUPS - 1), [(hidh[:, 0, c, :], hidl[:, 0, c, :]) for c in range(2)])

        def act_hidden(act, n, g, q, p, i):
            G0 = n * GROUPS
            first = isinstance(g, int) and g == 0
            act.wait_ge(used, p + 2 * RING * i - (0 if first else 2))
            if n < 2:
                nc.scalar.activation(sg[:, q], psum[:, 4 + 2 * q:6 + 2 * q, 0:256], ACT.Silu).then_inc(sg_ready, 1)
                return
            for j in range(2):
                for c in range(2):
                    f = g * 2 + (FC * j + c)
                    last = nc.scalar.activation(cg[:, q, j, c, :], psum[:, 4 + 2 * q + c, 256 * j:256 * j + 256],
                                                ACT.Identity, scale=tap(n, 2, f), bias=tap(n, 3, f))
            last.then_inc(conv_mid, 1)
            act.wait_ge(conv_all, g + (G0 - 2 * GROUPS) + 1)
            nc.scalar.activation(sg[:, q], cg[:, q, 0], ACT.Silu).then_inc(sg_ready, 1)

        def tap(n, k, f):
            return taps[:, n - 2, k, bass.ds(f, 1)]

        def dve_hidden(dve, n, g, q, i):
            G0 = n * GROUPS
            if n < 2:
                dve.wait_ge(sg_ready, g + G0 + 1)
                nc.vector.tensor_tensor(hp[:, q], psum[:, 4 + 2 * q:6 + 2 * q, 256:512], sg[:, q], ALU.mult)\
                    .then_inc(hp_ready, 1)
                return
            dve.wait_ge(conv_mid, g + (G0 - 2 * GROUPS) + 1)
            for k, done in ((1, conv_one), (0, conv_all)):
                if k == 0:
                    dve.wait_ge(conv_one, g + (G0 - 2 * GROUPS) + 1)
                lag = 2 - k
                for j in range(2):
                    for c in range(2):
                        y = cg[:, q, j, c, lag:SEQ]
                        last = nc.vector.scalar_tensor_tensor(
                            y, psum[:, 4 + 2 * q + c, 256 * j:256 * j + SEQ - lag], tap(n, k, g * 2 + (FC * j + c)), y,
                            ALU.mult, ALU.add)
                last.then_inc(done, 1)
            dve.wait_ge(sg_ready, g + G0 + 1)
            nc.vector.tensor_tensor(hp[:, q], cg[:, q, 1], sg[:, q], ALU.mult).then_inc(hp_ready, 1)

        def act_hid_hi(act, n, g, q, p, i):
            act.wait_ge(hp_ready, g + n * GROUPS + 1)
            if not (isinstance(g, int) and g < 2):
                act.wait_ge(used, p - 6 + 2 * RING * i)
            nc.scalar.activation(hidh[:, q], hp[:, q], ACT.Copy).then_inc(hid_hi, 1)

        def dve_hid_lo(dve, n, g, q):
            dve.wait_ge(hid_hi, g + n * GROUPS + 1)
            nc.vector.tensor_tensor(hidl[:, q], hp[:, q], hidh[:, q].bitcast(F32), ALU.subtract).then_inc(hid_lo, 1)

        def act_ffn(act, n, following):
            p = 2 * first_slot[f"ffn{n}"]

            def body(i):
                for half in range(2):
                    q, g = p + 4 + 6 * half, i * 2 + half
                    for k in range(2):
                        split_hi(act, q + k, i=i)
                    act_hidden(act, n, g, half, q, i)
                    for k in range(2, 4):
                        split_hi(act, q + k, i=i)
                    act_hid_hi(act, n, g, half, q, i)
                    for k in range(4, 6):
                        split_hi(act, q + k, shape=(2, D), i=i)
            ffn_loop(act, body)
            q, g = p + 4 + 6 * (GROUPS - 1), GROUPS - 1
            for k in range(2):
                split_hi(act, q + k, shape=(2, D))
            act_hidden(act, n, g, 0, q, 0)
            first_pieces(split_hi, act, following, (0, 1))
            act_hid_hi(act, n, g, 0, q, 0)
            if n == 1:
                act_turn_p(act)
            first_pieces(split_hi, act, following, (2, 3))

        def dve_ffn(dve, n, following):
            p = 2 * first_slot[f"ffn{n}"]

            def body(i):
                for half in range(2):
                    q, g = p + 4 + 6 * half, i * 2 + half
                    for k in range(2):
                        split_lo(dve, q + k, i=i)
                    dve_hidden(dve, n, g, half, i)
                    for k in range(2, 4):
                        split_lo(dve, q + k, i=i)
                    dve_hid_lo(dve, n, g, half)
                    for k in range(4, 6):
                        split_lo(dve, q + k, shape=(2, D), i=i)
            ffn_loop(dve, body)
            q, g = p + 4 + 6 * (GROUPS - 1), GROUPS - 1
            for k in range(2):
                split_lo(dve, q + k, shape=(2, D))
            dve_hidden(dve, n, g, 0, 0)
            first_pieces(split_lo, dve, following, (0, 1))
            dve_hid_lo(dve, n, g, 0)
            if n == 1:
                dve_turn_p(dve)
            first_pieces(split_lo, dve, following, (2, 3))

        def rows(a):
            return a.rearrange("p (b n) -> p b n", b=2)

        def first_pieces(split, eng, st, which):
            for k in which if st in stages else ():
                if st in ("ple", "ab"):
                    first, shape = (2 * first_slot["emb"], (2, D)) if st == "ple" else (2 * first_slot["ab"], (8, 16))
                    split(eng, first + k, shape if k < 2 else (4, 512) if st == "ab" else (2, D))
                else:
                    split(eng, 2 * first_slot[st] + k)

        ALL = slice(None)

        def unit(w, *cols):
            wv = w.rearrange("(k p) n -> p k n", p=P)
            width = sum(b - a for a, b in cols)
            if len(cols) == 1:
                a, b = cols[0]
                return [((4, width), [(slice(2 * m, 2 * m + 2), wv[:, 4 * k + 2 * m:4 * k + 2 * m + 2, a:b])
                                      for m in range(2)]) for k in range(2)]
            (a, b), (c, d) = cols
            return [((4, width), [((ALL, ALL, slice(0, b - a)), wv[:, 4 * k:4 * k + 4, a:b]),
                                  ((ALL, ALL, slice(b - a, width)), wv[:, 4 * k:4 * k + 4, c:d])]) for k in range(2)]

        def wide(w):
            wv = w.rearrange("(k p) n -> p k n", p=P)
            return [[((2, D), [(slice(c, c + 1), wv[:, k + c:k + c + 1, :]) for c in range(2)])] for k in range(0, wv.shape[1], 2)]

        w_in, w_ple, ab_in, c_in = A["w_in"][0], A["ple_w_gate"][0], A["ab_w_in_2"][0], A["c_w_in_2"][0]
        PROJ = {
            "mix0": [unit(w_in, (AQ, AK)), unit(w_in, (AK, GK)), unit(w_in, (GK, GV), (GR, GO)),
                     unit(w_in, (GV, GR)), unit(w_in, (GO, GO + 512))],
            "mix0o": wide(A["w_out"][0]),
            "emb": wide(A["ple_w_proj"][0]),
            "ple": wide(w_ple),
            "abo": wide(A["ab_w_out_2"][0]),
            "hgo": wide(A["c_w_out_2"][0]),
            "ab": [[((8, 16), [((ALL, ALL, slice(8 * m, 8 * m + 8)), ab_in.rearrange("(k p) n -> p k n", p=P)[:, :, a:a + 8])
                               for m, a in enumerate((MI, DA))])],
                   unit(ab_in, (MQ, MV)), unit(ab_in, (MV, MO)), unit(ab_in, (DK, DV)), unit(ab_in, (DQ, DK)),
                   unit(ab_in, (DV, DG)), unit(ab_in, (MO, MI)), unit(ab_in, (DG, DA))],
            "hg": [unit(c_in, (n, n + 512)) for n in (1024, 1536, 0, 512, 2048, 2560, 3072, 3584)],
        }

        def sp_proj(sp, part):
            s = first_slot[part]
            for slots in PROJ[part]:
                for shape, loads in slots:
                    sp_slot(sp, s, 0, shape, loads)
                    s += 1

        def piece_at(part, u):
            return 2 * (first_slot[part] + 2 * u)

        mix = nrm
        PAIR = 4
        sqa, qn, kn = arena[:, 0:1280], arena[:, 1280:2304], arena[:, 2304:2560]
        qr, kr, kd, tmp = arena[:, 2560:3584], arena[:, 3584:3840], arena[:, 3840:4352], arena[:, 4352:4864]
        av = arena[:, 4992:5248].rearrange("p (t n) -> p t n", t=NT)
        qT, kT = arena[:, 5248:6272], arena[:, 6272:6784]
        s0 = arena[:, 6784:7808].rearrange("p (k n) -> p k n", k=8)
        s1 = arena[:, 7808:9856].rearrange("p (k n) -> p k n", k=8)
        eT = arena[:, 0:3072].rearrange("p (s k n) -> p s k n", s=3, k=8)
        a_ss, a_r = few.take(20), few.take(20)
        a_max, a_neg, a_den, a_exs = few.take(16), few.take(16), few.take(16), few.take(16)

        def pe_a_proj(pe):
            X = "mix0"
            pe_between(pe, X)
            wait_turned(pe, X, 1)
            pe_params(pe)
            pe_unit(pe, piece_at(X, 0), rows=[(0, 512, [bank(0), bank(1)], (True, True))])
            pe.wait_ge(*after("params"))
            pe_unit(pe, piece_at(X, 1), rows=[(0, 256, [bank(2, 0, 256), bank(3, 0, 256)], (True, True))],
                    columns=[(256, bank(4, 0, 256), True), (384, bank(4, 256, 256), False)])
            pe_unit(pe, piece_at(X, 2), columns=[(0, bank(5, 0, 256), True), (128, bank(5, 256, 256), False)],
                    rows=[(256, 272, [bank(6, 0, 16), bank(6, 16, 16)], (True, False))], shape=(4, 272))

        def act_a_rows(act):
            act.wait_ge(used, piece_at("mix0", 2))
            sq = sqa.rearrange("p (t n) -> p t n", t=NT)
            nc.scalar.activation(sq[:, :, 0:512], psum[:, 0:2, :], ACT.Square).then_inc(*steps.did("act", "a.sq"))
            nc.scalar.activation(sq[:, :, 512:640], psum[:, 2:4, 0:128], ACT.Square).then_inc(*steps.did("act", "a.sk"))
            nc.scalar.activation(av, psum[:, 2:4, 128:256], ACT.Copy).then_inc(*steps.did("act", "a.v"))

        def pool_a(pool):
            pool.wait_ge(*after("a.ss"))
            pool_rstd(pool, "a.r", a_ss, 20, 64, a_r)

        def dve_a_sums(dve):
            sq = sqa.rearrange("p (t n) -> p t n", t=NT)
            ss = a_ss.rearrange("p (t k) -> p t k", t=NT)
            dve.wait_ge(*after("a.sk"))
            nc.vector.tensor_reduce(ss, sq.rearrange("p t (k d) -> p t k d", d=64), AX_X, ALU.add)\
                .then_inc(*steps.did("dve", "a.ss"))

        def dve_a_rows(dve):
            r = a_r.rearrange("p (t k) -> p t k", t=NT)
            dve.wait_ge(*after("a.r"))
            dve.wait_ge(*after("a.v"))
            nc.vector.tensor_tensor(kn.rearrange("p (t k d) -> p t k d", t=2, k=2),
                                    psum[:, 2:4, 0:128].rearrange("p t (k d) -> p t k d", k=2),
                                    r[:, :, 8:10].unsqueeze(3).broadcast_to([P, 2, 2, 64]), ALU.mult)\
                .then_inc(*steps.did("dve", "a.kn"))
            nc.vector.tensor_tensor(qn.rearrange("p (t k d) -> p t k d", t=2, k=8),
                                    psum[:, 0:2, :].rearrange("p t (k d) -> p t k d", k=8),
                                    r[:, :, 0:8].unsqueeze(3).broadcast_to([P, 2, 8, 64]), ALU.mult)\
                .then_inc(*steps.did("dve", "a.qn"))
            for name, n, heads, g in (("k", kn, 4, "k_norm"), ("q", qn, 16, "q_norm")):
                v = n.rearrange("p (k d) -> p k d", d=64)
                dve.wait_ge(*after(f"a.{name}n"))
                nc.vector.tensor_tensor(v, v, spread[g].unsqueeze(1).broadcast_to([P, heads, 64]), ALU.mult)\
                    .then_inc(*steps.did("dve", f"a.{name}g"))
            cos, sin = (cst(f"{f}0", 64).rearrange("p (t d) -> p t d", t=2) for f in ("cos", "sin"))
            for name, n, out_, heads in (("k", kn, kr, 2), ("q", qn, qr, 8)):
                v = n.rearrange("p (t k d) -> p t k d", t=2, k=heads)
                o = out_.rearrange("p (t k d) -> p t k d", t=2, k=heads)
                t_ = tmp[:, 0:64 * heads].rearrange("p (t k d) -> p t k d", t=2, k=heads)
                c, s = (a.unsqueeze(2).broadcast_to([P, 2, heads, 32]) for a in (cos, sin))
                lo, hi = slice(0, 32), slice(32, 64)
                dve.wait_ge(*after(f"a.{name}g"))
                nc.vector.tensor_tensor(o[:, :, :, lo], v[:, :, :, lo], c, ALU.mult).then_inc(*steps.did("dve", f"a.{name}1"))
                nc.vector.tensor_tensor(o[:, :, :, hi], v[:, :, :, hi], c, ALU.mult).then_inc(*steps.did("dve", f"a.{name}2"))
                if name == "q":
                    dve.wait_ge(*after("a.kr"))
                nc.vector.tensor_tensor(t_, v[:, :, :, hi], s, ALU.mult).then_inc(*steps.did("dve", f"a.{name}3"))
                dve.wait_ge(*after(f"a.{name}3"))
                nc.vector.tensor_tensor(o[:, :, :, lo], o[:, :, :, lo], t_, ALU.subtract).then_inc(*steps.did("dve", f"a.{name}4"))
                dve.wait_ge(*after(f"a.{name}4"))
                nc.vector.tensor_tensor(t_, v[:, :, :, lo], s, ALU.mult).then_inc(*steps.did("dve", f"a.{name}5"))
                dve.wait_ge(*after(f"a.{name}5"))
                nc.vector.tensor_tensor(o[:, :, :, hi], o[:, :, :, hi], t_, ALU.add).then_inc(*steps.did("dve", f"a.{name}r"))

        def act_a_dup(act):
            act.wait_ge(*after("a.kr"))
            nc.scalar.activation(kd.rearrange("p (k a d) -> p k a d", k=4, a=2),
                                 kr.rearrange("p (k d) -> p k d", k=4).unsqueeze(2).broadcast_to([P, 4, 2, 64]), ACT.Copy)\
                .then_inc(*steps.did("act", "a.kd"))

        def pe_a_turn(pe):
            pe.wait_ge(*after("a.qr"))
            pe.wait_ge(*after("a.kd"))
            for t in range(NT):
                for pair in range(4):
                    nc.tensor.transpose(bank(pair // 2, (pair % 2) * 256 + t * P, P),
                                        qr[:, t * 512 + pair * P:t * 512 + pair * P + P], ident)
                for kv in range(2):
                    last = nc.tensor.transpose(bank(2, kv * 256 + t * P, P),
                                               kd[:, (2 * t + kv) * P:(2 * t + kv) * P + P], ident)
            last.then_inc(*steps.did("pe", "a.T"))

        def act_a_turned(act):
            act.wait_ge(*after("a.T"))
            nc.scalar.activation(rows(qT), psum[:, 0:2, :], ACT.Copy).then_inc(*steps.did("act", "a.qT"))

        def dve_a_turned(dve):
            dve.wait_ge(*after("a.T"))
            nc.vector.tensor_copy(kT, bank(2)).then_inc(*steps.did("dve", "a.kT"))

        SCORE_BANKS = [[2, 4], [5, 6]]

        def pe_a_scores(pe):
            for name in ("a.qT", "a.kT", "g.q", "g.k", "g.glr"):
                pe.wait_ge(*after(name))
            for par in range(2):
                part = slice(64 * par, 64 * par + 64)
                for i in range(4):
                    pair, kv = i, i // 2
                    nc.tensor.matmul(bank(par, i * P, P), qT[part, pair * 256:pair * 256 + P],
                                     kT[part, kv * 256:kv * 256 + P], start=True, stop=True)
                    last = nc.tensor.matmul(bank(SCORE_BANKS[par][i // 2], (i % 2) * 256, 256),
                                            qT[part, pair * 256 + P:pair * 256 + 2 * P],
                                            kT[part, kv * 256:kv * 256 + 256], start=True, stop=True)
            last.then_inc(*steps.did("pe", "a.S"))

        def dve_a_softmax(dve):
            dve.wait_ge(*after("a.S"))
            for par in range(2):
                nc.vector.scalar_tensor_tensor(s0[:, 4 * par:4 * par + 4, :], bank(par).rearrange("p (k n) -> p k n", k=4), 0.125,
                                               cst("own").unsqueeze(1).broadcast_to([P, 4, P]), ALU.mult, ALU.add)
                for m in range(2):
                    last = nc.vector.scalar_tensor_tensor(
                        s1[:, 4 * par + 2 * m:4 * par + 2 * m + 2, :],
                        bank(SCORE_BANKS[par][m]).rearrange("p (k n) -> p k n", k=2), 0.125,
                        cst("prev", 256).unsqueeze(1).broadcast_to([P, 2, 256]), ALU.mult, ALU.add)
            last.then_inc(*steps.did("dve", "a.masked"))
            dve.wait_ge(*after("a.masked"))
            nc.vector.tensor_reduce(a_max[:, 0:8], s0, AX_X, ALU.max).then_inc(*steps.did("dve", "a.m0"))
            nc.vector.tensor_reduce(a_max[:, 8:16], s1, AX_X, ALU.max).then_inc(*steps.did("dve", "a.m1"))
            dve.wait_ge(*after("a.m1"))
            sink = spread["attn_sinks"].rearrange("p (i q) -> p q i", q=2).unsqueeze(1).broadcast_to([P, 2, 2, 4])
            by_head = lambda a: a.rearrange("p (t q i) -> p t q i", t=2, q=2)
            nc.vector.tensor_tensor(by_head(a_max), by_head(a_max), sink, ALU.max).then_inc(*steps.did("dve", "a.m"))
            dve.wait_ge(*after("a.m"))
            nc.vector.tensor_scalar(a_neg, a_max, -1.0, None, ALU.mult).then_inc(*steps.did("dve", "a.neg"))
            nc.vector.tensor_tensor(by_head(a_exs), sink, by_head(a_max), ALU.subtract).then_inc(*steps.did("dve", "a.sm"))

        def act_a_exp(act):
            act.wait_ge(*after("a.neg"))
            for k in range(8):
                nc.scalar.activation(s0[:, k, :], s0[:, k, :], ACT.Exp, bias=a_neg[:, k:k + 1],
                                     accum_out=a_den[:, k:k + 1]).then_inc(*steps.did("act", f"a.e0{k}"))
            act.wait_ge(*after("a.sm"))
            nc.scalar.activation(a_exs, a_exs, ACT.Exp).then_inc(*steps.did("act", "a.exs"))
            for k in range(8):
                nc.scalar.activation(s1[:, k, :], s1[:, k, :], ACT.Exp, bias=a_neg[:, 8 + k:9 + k],
                                     accum_out=a_den[:, 8 + k:9 + k]).then_inc(*steps.did("act", f"a.e1{k}"))

        def dve_a_den(dve):
            dve.wait_ge(*after("a.e17"))
            nc.vector.tensor_tensor(a_den, a_den, a_exs, ALU.add).then_inc(*steps.did("dve", "a.den"))
            dve.wait_ge(*after("a.den"))
            nc.vector.reciprocal(a_den, a_den).then_inc(*steps.did("dve", "a.rden"))

        def pe_a_probs(pe):
            pe.wait_ge(*after("a.masked"))
            for g, (src, at, b) in enumerate(((s0, 0, (0, 1)), (s1, 0, (2, 4)), (s1, P, (5, 6)))):
                pe.wait_ge(*after("a.e07" if g == 0 else "a.e17"))
                for k in range(8):
                    last = nc.tensor.transpose(bank(b[k // 4], (k % 4) * P, P), src[:, k, at:at + P], ident)
                    if k % 4 == 3:
                        last.then_inc(*steps.did("pe", f"a.eT{g}{k // 4}"))

        def act_a_probs(act):
            for g, b in ((0, 0), (1, 2), (2, 5)):
                act.wait_ge(*after(f"a.eT{g}0"))
                nc.scalar.activation(eT[:, g, 0:4, :], bank(b).rearrange("p (k n) -> p k n", k=4), ACT.Copy)\
                    .then_inc(*steps.did("act", f"a.pT{g}0"))

        def dve_a_probs(dve):
            for g, b in ((0, 1), (1, 4), (2, 6)):
                dve.wait_ge(*after(f"a.eT{g}1"))
                nc.vector.tensor_copy(eT[:, g, 4:8, :], bank(b).rearrange("p (k n) -> p k n", k=4))\
                    .then_inc(*steps.did("dve", f"a.pT{g}1"))

        def pe_a_out(pe):
            pe.wait_ge(*after("a.v"))
            for g, t, tv in ((0, 0, 0), (1, 1, 0), (2, 1, 1)):
                for name in ("a.pT00", "a.pT01") if g == 0 else ("a.pT20", "a.pT21"):
                    pe.wait_ge(*after(name))
                if g == 2:
                    continue
                for k in range(8):
                    hd = (k % 4) * 2 + k // 4
                    kv = hd // 4
                    last = nc.tensor.matmul(bank(t, hd * 64, 64), eT[:, g, k, :], av[:, tv, kv * 64:kv * 64 + 64],
                                            start=True, stop=(g == 0))
                    if g == 1:
                        last = nc.tensor.matmul(bank(t, hd * 64, 64), eT[:, 2, k, :], av[:, 1, kv * 64:kv * 64 + 64],
                                                start=False, stop=True)
                if g == 0:
                    pe.wait_ge(*after("a.pT20"))
                    pe.wait_ge(*after("a.pT21"))
            last.then_inc(*steps.did("pe", "a.O"))

        def dve_a_out(dve):
            dve.wait_ge(*after("a.O"))
            for t in range(NT):
                heads = lambda a: a.rearrange("p (i q d) -> p q i d", q=2, d=64)
                nc.vector.tensor_tensor(heads(mix[:, t, 0:512]), heads(bank(t)),
                                        a_den[:, 8 * t:8 * t + 8].rearrange("p (q i) -> p q i", q=2).unsqueeze(3)
                                        .broadcast_to([P, 2, 4, 64]), ALU.mult).then_inc(*steps.did("dve", f"a.mix{t}"))

        gq, gk = arena[:, 9856:10368], arena[:, 10368:10880]
        glr, glrT = arena[:, 10880:10912], arena[0:16, 10912:11168]
        gv = arena[:, 3072:4096].rearrange("p (t n) -> p t n", t=NT)
        sil = arena[:, 8832:9856].rearrange("p (t n) -> p t n", t=NT)
        la, gb = arena[:, 4096:4608], arena[:, 6272:6784]
        lt = arena[:, 9344:9856]
        g_e, g_l = arena[:, 5248:5760], (arena[:, 5760:6272], arena[:, 6784:7296])
        g_at = arena[:, 7296:8320].rearrange("p (q n) -> p q n", q=2)
        g_cross = arena[:, 8320:8832].rearrange("p (q n) -> p q n", q=2)
        osq = arena[:, 0:1024]
        ones = few.take(1)
        g_ss, g_r = few.take(8), few.take(8)

        def act_g_q(act):
            act.wait_ge(used, piece_at("mix0", 2))
            nc.scalar.activation(gq, bank(4), ACT.Copy, scale=0.125).then_inc(*steps.did("act", "g.q"))

        def dve_g_k(dve):
            dve.wait_ge(used, piece_at("mix0", 3))
            nc.vector.tensor_copy(gk, bank(5)).then_inc(*steps.did("dve", "g.k"))
            nc.vector.tensor_copy(glr, bank(6, 0, 32)).then_inc(*steps.did("dve", "g.glr"))

        def pe_g_v(pe, which):
            pe.wait_ge(*after("a.kn"))
            pe_unit(pe, piece_at("mix0", 3), rows=[(0, 512, [bank(3), bank(7)], (True, True))], which=which)

        def act_g_v(act):
            act.wait_ge(used, piece_at("mix0", 4))
            act.wait_ge(*after("a.T"))
            for t, b in ((0, 3), (1, 7)):
                nc.scalar.activation(gv[:, t, :], bank(b), ACT.Copy).then_inc(*steps.did("act", f"g.v{t}"))

        def pe_g_gate(pe):
            pe.wait_ge(*after("g.v1"))
            pe_unit(pe, piece_at("mix0", 4), rows=[(0, 512, [bank(3), bank(7)], (True, True))])

        def pe_g_alpha(pe):
            pe.wait_ge(*after("a.pT21"))
            for t in range(NT):
                last = nc.tensor.transpose(psum[0:16, 6, t * P:t * P + P], glr[:, t * 16:t * 16 + 16], ident)
            last.then_inc(*steps.did("pe", "g.glrT"))
            pe.wait_ge(*after("g.rT"))
            for c in range(2):
                last = nc.tensor.matmul(bank(6, c * 256, 256), gate_up[:, c * P:c * P + P], glrT, start=(c == 0), stop=True,
                                        skip_group_check=True)
            last.then_inc(*steps.did("pe", "g.z"))

        def dve_g_alpha(dve):
            dve.wait_ge(*after("g.glrT"))
            nc.vector.tensor_copy(glrT, psum[0:16, 6, 0:256]).then_inc(*steps.did("dve", "g.rT"))
            dve.wait_ge(*after("g.z"))
            for c in range(2):
                nc.vector.tensor_scalar(la[:, c * 256:c * 256 + 256], bank(6, c * 256, 256), gate_bias[:, c:c + 1], None, ALU.add)\
                    .then_inc(*steps.did("dve", f"g.y{c}"))

        def act_g_alpha(act):
            act.wait_ge(*after("g.y1"))
            act.wait_ge(*after("a.eT21"))
            nc.scalar.activation(lt, la, ACT.Abs).then_inc(*steps.did("act", "g.abs"))
            act.wait_ge(*after("g.abs"))
            nc.scalar.activation(lt, lt, ACT.Exp, scale=-1.0).then_inc(*steps.did("act", "g.exp"))
            act.wait_ge(*after("g.exp"))
            nc.scalar.activation(lt, lt, ACT.Ln, bias=1.0).then_inc(*steps.did("act", "g.ln"))

        def dve_g_sum(dve):
            dve.wait_ge(*after("g.ln"))
            nc.vector.scalar_tensor_tensor(la, la, 0.0, lt, ALU.min, ALU.subtract).then_inc(*steps.did("dve", "g.la"))
            dve.wait_ge(*after("g.la"))
            for c in range(2):
                part = slice(c * 256, c * 256 + 256)
                nc.vector.tensor_tensor_scan(gb[:, part], ones.broadcast_to([P, 256]), la[:, part], 0.0, ALU.mult, ALU.add)\
                    .then_inc(*steps.did("dve", f"g.cum{c}"))
            dve.wait_ge(*after("g.cum1"))
            nc.vector.tensor_scalar(gb, gb, 1.0 / 16.0, None, ALU.mult).then_inc(*steps.did("dve", "g.b"))

        def dve_level_x(dve, X, n, half, b, e, ready):
            blocks = lambda a: a.rearrange("p (m r) -> p m r", r=2 * half)
            left, right = slice(0, half), slice(half, 2 * half)
            for name in ready:
                dve.wait_ge(*after(name))
            ref = blocks(b)[:, :, half - 1:half].broadcast_to([P, b.shape[1] // (2 * half), half])
            nc.vector.tensor_tensor(blocks(e)[:, :, right], blocks(b)[:, :, right], ref, ALU.subtract)\
                .then_inc(*steps.did("dve", f"{X}.x{n}r"))
            nc.vector.tensor_tensor(blocks(e)[:, :, left], ref, blocks(b)[:, :, left], ALU.subtract)\
                .then_inc(*steps.did("dve", f"{X}.x{n}"))

        def dve_level_l(dve, X, n, half, q, k, e, l, ready=()):
            blocks = lambda a: a.rearrange("p (m r) -> p m r", r=2 * half)
            left, right = slice(0, half), slice(half, 2 * half)
            for name in ready:
                dve.wait_ge(*after(name))
            dve.wait_ge(*after(f"{X}.e{n}"))
            nc.vector.tensor_tensor(blocks(l)[:, :, right], blocks(q)[:, :, right], blocks(e)[:, :, right], ALU.mult)\
                .then_inc(*steps.did("dve", f"{X}.l{n}r"))
            nc.vector.tensor_tensor(blocks(l)[:, :, left], blocks(k)[:, :, left], blocks(e)[:, :, left], ALU.mult)\
                .then_inc(*steps.did("dve", f"{X}.l{n}"))

        def act_level(act, X, n, e):
            act.wait_ge(*after(f"{X}.x{n}"))
            nc.scalar.activation(e, e, ACT.Exp).then_inc(*steps.did("act", f"{X}.e{n}"))

        ALL_LEVELS = [P] + LEVELS
        BANKS2 = ((4, 5), (6, 7))

        def pe_g_levels(pe):
            for t in range(NT):
                pe_turn(pe, "mix0o", t, 0, t, mix, "a.mix1")
            for n in range(len(ALL_LEVELS) + 1):
                if n >= 2:
                    pe.wait_ge(*after(f"g.put{n - 2}"))
                if n == 0:
                    pe.wait_ge(*after("g.y1"))
                if n == 1:
                    pe.wait_ge(*after("g.sil1"))
                if n < len(ALL_LEVELS):
                    pe.wait_ge(*after(f"g.l{n}"))
                    l = r = g_l[n % 2]
                else:
                    l, r = gk, gq
                for par in range(2):
                    part = slice(64 * par, 64 * par + 64)
                    for c in range(2):
                        if n == 0:
                            last = nc.tensor.matmul(bank(BANKS2[0][par], c * P, P), l[part, c * 256:c * 256 + P],
                                                    r[part, c * 256 + P:c * 256 + 256], start=True, stop=True)
                            continue
                        for t in range(NT):
                            tok = slice(c * 256 + t * P, c * 256 + t * P + P)
                            last = nc.tensor.matmul(bank(BANKS2[n % 2][par], (2 * c + t) * P, P), l[part, tok], r[part, tok],
                                                    start=True, stop=True)
                last.then_inc(*steps.did("pe", f"g.P{n}"))
                if n in (3, 5):
                    pe_out(pe, "mix0o", n // 2 - 1)

        def dve_g_put(dve, n):
            dve.wait_ge(*after(f"g.P{n}"))
            if n == 0:
                nc.vector.tensor_copy(g_cross, psum[:, 4:6, 0:256]).then_inc(*steps.did("dve", "g.put0"))
                return
            if n == 1:
                dve.wait_ge(*after("g.at0"))
            else:
                dve.wait_ge(*after(f"g.put{n - 1}"))
            mask = cst(f"level{ALL_LEVELS[n]}") if n < len(ALL_LEVELS) else ident
            for par in range(2):
                four = lambda a: a.rearrange("p (m i) -> p m i", m=4)
                last = nc.vector.copy_predicated(four(g_at[:, par, :]), mask.bitcast(U32).unsqueeze(1).broadcast_to([P, 4, P]),
                                                 four(bank(BANKS2[n % 2][par])))
            last.then_inc(*steps.did("dve", f"g.put{n}"))

        def dve_g_levels(dve):
            for n, half in enumerate(ALL_LEVELS):
                ready = ["g.b", "g.q"] if n == 0 else [f"g.l{n - 1}"]
                if n == 0:
                    ready.append("a.S")
                dve_level_x(dve, "g", n, half, gb, g_e, ready)
                if n >= 2:
                    dve_g_put(dve, n - 2)
                if n in (1, 2):
                    dve_turn(dve, "mix0o", n - 1, 0, n - 1)
                if 3 <= n < 7:
                    out_splits(split_lo, dve, "mix0o", (n - 3,))
                dve_level_l(dve, "g", n, half, gq, gk, g_e, g_l[n % 2], ([f"g.P{n - 2}"] if n >= 2 else []) + (["a.eT21"] if n == 1 else []))
            for n in range(len(ALL_LEVELS) - 2, len(ALL_LEVELS) + 1):
                dve_g_put(dve, n)

        def act_g_levels(act):
            for n in range(len(ALL_LEVELS)):
                act_level(act, "g", n, g_e)
                if n < 2:
                    act_turn(act, "mix0o", n, 0, n)
                elif n < 6:
                    out_splits(split_hi, act, "mix0o", (n - 2,))

        def act_g_gate(act):
            act.wait_ge(used, piece_at("mix0o", 0))
            act.wait_ge(*after("a.eT21"))
            act.wait_ge(*after("g.la"))
            for t, b in ((0, 3), (1, 7)):
                nc.scalar.activation(sil[:, t, :], bank(b), ACT.Silu).then_inc(*steps.did("act", f"g.sil{t}"))

        def pe_g_out(pe):
            pe.wait_ge(*after(f"g.put{len(ALL_LEVELS)}"))
            pe.wait_ge(*after("g.v1"))
            for t in range(NT):
                for hd in range(4):
                    par, c = hd % 2, hd // 2
                    o = bank(4 + t, hd * P, P)
                    last = nc.tensor.matmul(o, g_at[:, par, (2 * c + t) * P:(2 * c + t) * P + P], gv[:, t, hd * P:hd * P + P],
                                            start=True, stop=(t == 0))
                    if t == 1:
                        last = nc.tensor.matmul(o, g_cross[:, par, c * P:c * P + P], gv[:, 0, hd * P:hd * P + P],
                                                start=False, stop=True)
            last.then_inc(*steps.did("pe", "g.O"))

        def act_heads(act, X, src, sq, done):
            act.wait_ge(*after(done))
            nc.scalar.activation(sq, src, ACT.Square).then_inc(*steps.did("act", f"{X}.osq"))

        def dve_g_out(dve):
            dve.wait_ge(*after("g.osq"))
            v = osq.rearrange("p (k d) -> p k d", d=P)
            nc.vector.tensor_reduce(g_ss, v, AX_X, ALU.add).then_inc(*steps.did("dve", "g.oss"))
            out_splits(split_lo, dve, "mix0o", (6,))
            dve.wait_ge(*after("g.or"))
            o4 = psum[:, 4:6, :].rearrange("p t (k d) -> p t k d", d=P)
            r4 = g_r.rearrange("p (t k) -> p t k", t=NT).unsqueeze(3).broadcast_to([P, NT, 4, P])
            nc.vector.tensor_tensor(osq.rearrange("p (t k d) -> p t k d", t=NT, d=P), o4, r4, ALU.mult)\
                .then_inc(*steps.did("dve", "g.on"))
            dve.wait_ge(*after("g.on"))
            dve.wait_ge(*after("g.silg"))
            for t in range(NT):
                nc.vector.tensor_tensor(mix[:, t, 512:1024], osq[:, t * 512:t * 512 + 512], sil[:, t, :], ALU.mult)\
                    .then_inc(*steps.did("dve", f"mix0o.n{t}"))

        def sp_mix0(sp):
            sp_proj(sp, "mix0")
            sp_proj(sp, "mix0o")

        def pool_mix0(pool):
            pool_a(pool)
            pool.wait_ge(*after("a.eT21"))
            nc.gpsimd.memset(arena[:, 7296:8320], 0.0).then_inc(*steps.did("pool", "g.at0"))
            pool.wait_ge(*after("g.sil1"))
            pool.wait_ge(*after("params"))
            eight = sil.rearrange("p t (k d) -> p (t k) d", d=P)
            nc.gpsimd.tensor_tensor(eight, eight, spread["gla_out_norm"].unsqueeze(1).broadcast_to([P, 8, P]), ALU.mult)\
                .then_inc(*steps.did("pool", "g.silg"))
            pool.wait_ge(*after("g.oss"))
            pool_rstd(pool, "g.or", g_ss, 8, P, g_r)

        def pe_mix0(pe):
            pe_a_proj(pe)
            pe_g_v(pe, (0, 1))
            pe_a_turn(pe)
            pe_g_v(pe, (2, 3))
            pe_a_scores(pe)
            pe_g_gate(pe)
            pe_a_probs(pe)
            pe_g_alpha(pe)
            pe_a_out(pe)
            pe_g_levels(pe)
            pe_g_out(pe)
            for k in (2, 3):
                pe_out(pe, "mix0o", k)
            for t in range(NT):
                pe_turn(pe, "mix0o", t, 1, 6 + t, mix, f"mix0o.n{t}")
            pe_out_last(pe, "mix0o")

        def act_mix0(act):
            M = lambda u: piece_at("mix0", u)
            split4(split_hi, act, M(1))
            split4(split_hi, act, M(2), (4, 272))
            act_a_rows(act)
            split4(split_hi, act, M(3), which=(0, 1))
            act_g_q(act)
            act_a_dup(act)
            split4(split_hi, act, M(3), which=(2, 3))
            act_a_turned(act)
            split4(split_hi, act, M(4), which=(0, 1, 2))
            act_g_v(act)
            split4(split_hi, act, M(4), which=(3,))
            act_a_exp(act)
            act_a_probs(act)
            act_g_alpha(act)
            act_g_gate(act)
            act_g_levels(act)
            out_splits(split_hi, act, "mix0o", (4, 5))
            act_heads(act, "g", psum[:, 4:6, :], osq.rearrange("p (t n) -> p t n", t=NT), "g.O")
            out_splits(split_hi, act, "mix0o", (6,))
            for t in range(NT):
                act_turn(act, "mix0o", t, 1, 6 + t)
            out_splits(split_hi, act, "mix0o", (7,))
            first_pieces(split_hi, act, "ffn1", (0, 1))

        def dve_mix0(dve):
            M = lambda u: piece_at("mix0", u)
            split4(split_lo, dve, M(1), which=(0, 1))
            dve_params(dve)
            split4(split_lo, dve, M(1), which=(2, 3))
            split4(split_lo, dve, M(2), (4, 272))
            dve_a_sums(dve)
            split4(split_lo, dve, M(3), which=(0, 1))
            dve_a_rows(dve)
            dve_g_k(dve)
            dve_a_turned(dve)
            split4(split_lo, dve, M(3), which=(2, 3))
            split4(split_lo, dve, M(4), which=(0, 1, 2))
            dve_a_softmax(dve)
            split4(split_lo, dve, M(4), which=(3,))
            dve_a_den(dve)
            dve_a_probs(dve)
            dve_g_alpha(dve)
            dve_g_sum(dve)
            dve_a_out(dve)
            dve_g_levels(dve)
            out_splits(split_lo, dve, "mix0o", (4, 5))
            dve_g_out(dve)
            for t in range(NT):
                dve_turn(dve, "mix0o", t, 1, 6 + t)
            out_splits(split_lo, dve, "mix0o", (7,))
            first_pieces(split_lo, dve, "ffn1", (0, 1))


        def pe_turn_p(pe):
            for c in range(2):
                for t in range(NT):
                    last = nc.tensor.transpose(bank(6, c * 256 + t * P, P), p_rows[:, t, c * P:c * P + P], ident)
            last.then_inc(*steps.did("pe", "emb.T"))

        def act_turn_p(act):
            act.wait_ge(*after("emb.T"))
            act.wait_ge(used, 2 * (first_slot["emb"] - 1))
            nc.scalar.activation(hidh[:, 1], bank(6).rearrange("p (c t) -> p c t", c=2), ACT.Copy).then_inc(*steps.did("act", "emb.xh"))

        def dve_turn_p(dve):
            dve.wait_ge(*after("emb.xh"))
            nc.vector.tensor_tensor(hidl[:, 1], bank(6).rearrange("p (c t) -> p c t", c=2), hidh[:, 1].bitcast(F32), ALU.subtract)\
                .then_inc(*steps.did("dve", "emb.xl"))

        def pe_ple(pe):
            pe.wait_ge(*after("emb.xl"))
            p = 2 * first_slot["emb"]
            for c in range(2):
                pe.wait_ge(lo_done, p + c + 1)
                wh, wl = weights(p + c, 1, D)
                for t, b in BANKS:
                    tok, col = slice(t * P, t * P + P), slice(b * BANK, b * BANK + BANK)
                    last = three(bank(4 + 2 * t + b), hidh[:, 1, c, tok], hidl[:, 1, c, tok], wh[:, 0, col], wl[:, 0, col],
                                 start=(c == 0), stop=(c == 1))
                last.then_inc(used, 1)
            pe_between(pe, "ple")
            wait_turned(pe, "ple", 1)
            for k in range(4):
                pe_out(pe, "ple", k)
            pe_out_last(pe, "ple")

        def made(t):
            return psum[:, 4 + 2 * t:6 + 2 * t, :]

        def act_ple(act):
            total = emb_sums[0]
            act.wait_ge(used, 2 * first_slot["ple"])
            for t in range(NT):
                nc.scalar.activation(rows(sgm[:, t, :]), made(t), ACT.Square, accum_out=total[:, t:t + 1])\
                    .then_inc(*steps.did("act", f"emb.ss{t}"))
            out_splits(split_hi, act, "ple", range(2, 8))
            act.wait_ge(*after("emb.ss1"))
            first_pieces(split_hi, act, "ab", (0, 1))

        emb_sums = few.take(NT), few.take(NT)

        def pool_ple(pool):
            total, r = emb_sums
            for t in range(NT):
                pool.wait_ge(*after(f"emb.ss{t}"))
                pool_rstd(pool, f"emb.r{t}", total[:, t:t + 1], 1, D, r[:, t:t + 1])

        def dve_ple(dve):
            _, r = emb_sums
            g = gain_of(dve, "emb")
            out_splits(split_lo, dve, "ple", (2, 3))
            for t in range(NT):
                dve.wait_ge(*after(f"emb.r{t}"))
                nc.vector.scalar_tensor_tensor(rows(emb[:, t, :]), made(t), r[:, t:t + 1], rows(g), ALU.mult, ALU.mult)\
                    .then_inc(*steps.did("dve", f"emb.e{t}"))
            out_splits(split_lo, dve, "ple", (4, 5, 6, 7))
            first_pieces(split_lo, dve, "ab", (0, 1))

        ab_p = {"small": 2 * first_slot["ab"]}
        for n, name in enumerate(("mqk", "mv", "dk", "dq", "dv", "mo", "dg")):
            ab_p[name] = ab_p["small"] + 2 + 4 * n
        Y = {"dk": arena[:, 0:1024], "dq": arena[:, 1024:2048], "dv": arena[:, 2048:3072], "mqk": arena[:, 8192:9216]}
        krow, qrow, vb = arena[:, 3072:4096], arena[:, 4096:5120], arena[:, 5120:6144]
        kb, kbT, kT2, qT2 = arena[:, 6144:7168], arena[:, 7168:8192], arena[:, 0:1024], arena[:, 1024:2048]
        mE, mvE = arena[:, 9216:10752], arena[:, 10752:11776]
        m_sq = arena[:, 8192:9216]
        dE, dNT, dat = arena[:, 8192:9216], arena[:, 9216:10240], arena[:, 2048:3072]
        dN, dXT, dX, dV = arena[:, 6144:7168], arena[:, 7168:8192], arena[:, 4096:5120], arena[:, 9216:10240]
        u0, dS, u1 = arena[:, 10240:10752], arena[:, 10752:11264], arena[:, 11264:11776]
        gtmp, d_sq = arena[:, 8192:9216], arena[:, 6144:7168]
        gz, gth, gcap, gex = few.take(32), few.take(16), few.take(16), few.take(24)
        glog, gcum, gbeta, gei, gt4 = few.take(16), few.take(16), few.take(8), few.take(8), few.take(8)
        m_den, m_ss, m_r, k_ss, k_r, q_ss, q_r, d_ss, d_r = (few.take(8) for _ in range(9))
        exa, glast, kdecay, eg1, beg = (few.take(4) for _ in range(5))
        by_t = lambda a: a.rearrange("p (t n) -> p t n", t=NT)
        heads4 = lambda a: a.rearrange("p (t k d) -> p t k d", t=NT, d=P)
        ones_sq = ones.broadcast_to([P, P])

        def spread_heads(a, t=None):
            return a.rearrange("p (t k) -> p t k", k=4).unsqueeze(3).broadcast_to([P, a.shape[1] // 4, 4, P])

        def conv_banks(name):
            return {"mqk": (0, 1), "dk": (0, 1), "dq": (6, 7), "dv": (0, 1)}[name]

        def conv_tap(name, k, c):
            if name == "mqk":
                return conv_m[:, k * 4 + c:k * 4 + c + 1]
            c += {"dq": 0, "dk": 4, "dv": 8}[name]
            return conv_g[:, k * 12 + c:k * 12 + c + 1]

        def pe_conv_unit(pe, name, ready=()):
            for r in ready:
                pe.wait_ge(*after(r))
            b = conv_banks(name)
            pe_unit(pe, ab_p[name], columns=[(c * P, bank(b[c // 2], (c % 2) * 256, 256), c % 2 == 0) for c in range(4)])

        def act_conv_first(act, name):
            act.wait_ge(used, ab_p[name] + 4)
            b = conv_banks(name)
            for c in range(4):
                last = nc.scalar.activation(Y[name][:, c * 256:c * 256 + 256], bank(b[c // 2], (c % 2) * 256, 256), ACT.Identity,
                                            scale=conv_tap(name, 3, c))
            last.then_inc(*steps.did("act", f"{name}.c3"))

        def dve_conv_rest(dve, name):
            b = conv_banks(name)
            for k in (2, 1, 0):
                dve.wait_ge(*after(f"{name}.c{k + 1}"))
                lag = 3 - k
                for c in range(4):
                    y = Y[name][:, c * 256 + lag:c * 256 + 256]
                    last = nc.vector.scalar_tensor_tensor(y, bank(b[c // 2], (c % 2) * 256, 256 - lag), conv_tap(name, k, c), y,
                                                          ALU.mult, ALU.add)
                last.then_inc(*steps.did("dve", f"{name}.c{k}"))

        def act_conv_silu(act, name):
            act.wait_ge(*after(f"{name}.c0"))
            nc.scalar.activation(Y[name], Y[name], ACT.Silu).then_inc(*steps.did("act", f"{name}.y"))

        def pe_ab_first(pe):
            pe_between(pe, "ab")
            wait_turned(pe, "ab", 1)
            for k in range(2):
                pe.wait_ge(lo_done, ab_p["small"] + k + 1)
                wh, wl = weights(ab_p["small"] + k, 4, 16)
                for kk in range(4):
                    kc = 4 * k + kk
                    for t in range(NT):
                        tok = slice(t * P, t * P + P)
                        last = three(bank(7, t * 16, 16), xh[:, kc, tok], xl[:, kc, tok], wh[:, kk, :], wl[:, kk, :],
                                     start=(kc == 0 and t == 0), stop=(kc == KC - 1))
                last.then_inc(used, 1)
            pe_conv_unit(pe, "mqk")
            pe_unit(pe, ab_p["mv"], rows=[(0, 512, [bank(2), bank(3)], (True, True))])

        def dve_gates(dve):
            dve.wait_ge(used, ab_p["small"] + 2)
            z, src = by_t(gz), bank(7, 0, 32).rearrange("p (t n) -> p t n", t=NT)
            b = spread["ab_m_gate_bias_2"].unsqueeze(1).broadcast_to([P, NT, 8])
            nc.vector.tensor_tensor(z[:, :, 0:8], src[:, :, 0:8], b, ALU.add).then_inc(*steps.did("dve", "gate.if"))
            dt = spread["ab_g_dt_bias_2"].unsqueeze(1).broadcast_to([P, NT, 4])
            nc.vector.tensor_tensor(z[:, :, 8:12], src[:, :, 8:12], dt, ALU.add).then_inc(*steps.did("dve", "gate.a"))
            nc.vector.tensor_copy(z[:, :, 12:16], src[:, :, 12:16]).then_inc(*steps.did("dve", "gate.b"))

        def act_gates(act):
            act.wait_ge(*after("gate.b"))
            nc.scalar.activation(by_t(gth), by_t(gz)[:, :, 0:8], ACT.Tanh, scale=1.0 / 15.0).then_inc(*steps.did("act", "gate.th"))
            e = by_t(gex)
            nc.scalar.activation(e[:, :, 4:8], by_t(gz)[:, :, 8:12], ACT.Abs).then_inc(*steps.did("act", "gate.abs"))
            act.wait_ge(*after("gate.abs"))
            act.wait_ge(*after("gate.cap"))
            nc.scalar.activation(e[:, :, 4:8], e[:, :, 4:8], ACT.Exp, scale=-1.0).then_inc(*steps.did("act", "gate.ea"))
            nc.scalar.activation(e[:, :, 0:4], by_t(gcap)[:, :, 4:8], ACT.Exp, scale=-1.0).then_inc(*steps.did("act", "gate.ef"))
            nc.scalar.activation(e[:, :, 8:12], by_t(gz)[:, :, 12:16], ACT.Exp, scale=-1.0).then_inc(*steps.did("act", "gate.eb"))
            nc.scalar.activation(by_t(gei), by_t(gcap)[:, :, 0:4], ACT.Exp).then_inc(*steps.did("act", "gate.ei"))
            nc.scalar.activation(exa, spread["ab_g_a_log_2"], ACT.Exp).then_inc(*steps.did("act", "gate.exa"))
            act.wait_ge(*after("gate.ef"))
            nc.scalar.activation(e[:, :, 0:8], e[:, :, 0:8], ACT.Ln, bias=1.0).then_inc(*steps.did("act", "gate.ln"))

        def dve_gate_logs(dve):
            dve.wait_ge(*after("gate.th"))
            nc.vector.tensor_scalar(gcap, gth, 15.0, None, ALU.mult).then_inc(*steps.did("dve", "gate.cap"))
            e, l = by_t(gex), by_t(glog)
            dve.wait_ge(*after("gate.ln"))
            nc.vector.tensor_scalar(l[:, :, 0:4], e[:, :, 0:4], -1.0, None, ALU.mult).then_inc(*steps.did("dve", "gate.lf"))
            nc.vector.scalar_tensor_tensor(l[:, :, 4:8], by_t(gz)[:, :, 8:12], 0.0, e[:, :, 4:8], ALU.max, ALU.add)\
                .then_inc(*steps.did("dve", "gate.sp"))
            dve.wait_ge(*after("gate.sp"))
            nc.vector.scalar_tensor_tensor(l[:, :, 4:8], l[:, :, 4:8], -1.0, exa.unsqueeze(1).broadcast_to([P, NT, 4]),
                                           ALU.mult, ALU.mult).then_inc(*steps.did("dve", "gate.g"))
            nc.vector.tensor_scalar(by_t(gbeta), e[:, :, 8:12], 1.0, None, ALU.add).then_inc(*steps.did("dve", "gate.1b"))
            dve.wait_ge(*after("gate.1b"))
            nc.vector.reciprocal(gbeta, gbeta).then_inc(*steps.did("dve", "gate.beta"))

        def pe_gate_sums(pe):
            upper, l = cst("upper"), by_t(glog)
            pe.wait_ge(*after("gate.g"))
            pe.wait_ge(*after("gate.lf"))
            pe.wait_ge(*after("gate.b"))
            nc.tensor.matmul(bank(7, 0, 8), upper, l[:, 0, :], start=True, stop=True, skip_group_check=True)
            nc.tensor.matmul(bank(7, 8, 4), ones_sq, l[:, 0, 0:4], start=False, stop=False, skip_group_check=True)
            nc.tensor.matmul(bank(7, 8, 4), upper, l[:, 1, 0:4], start=False, stop=True, skip_group_check=True)
            nc.tensor.matmul(bank(7, 12, 4), upper, l[:, 1, 4:8], start=False, stop=True, skip_group_check=True)\
                .then_inc(*steps.did("pe", "gate.cum"))
            for x in range(4):
                lf = [l[:, t, x:x + 1].broadcast_to([P, P]) for t in range(NT)]
                o = lambda t: bank(4 + x // 2, (x % 2) * 256 + t * P, P)
                nc.tensor.matmul(o(0), lf[0], upper, start=(x % 2 == 0), stop=True, skip_group_check=True)
                nc.tensor.matmul(o(1), lf[0], ones_sq, start=False, stop=False, skip_group_check=True)
                last = nc.tensor.matmul(o(1), lf[1], upper, start=False, stop=True, skip_group_check=True)
            last.then_inc(*steps.did("pe", "gate.rowm"))
            pe.wait_ge(*after("gate.col"))
            for t in range(NT):
                for x in range(4):
                    last = nc.tensor.matmul(bank(6 + t, x * P, P), l[:, t, 4 + x:5 + x].broadcast_to([P, P]), upper,
                                            start=(x == 0), stop=True, skip_group_check=True)
            last.then_inc(*steps.did("pe", "gate.rowg"))

        def dve_gate_rows(dve):
            dve.wait_ge(*after("gate.cum"))
            nc.vector.tensor_copy(gcum, bank(7, 0, 16)).then_inc(*steps.did("dve", "gate.col"))
            dve.wait_ge(*after("gate.col"))
            dve.wait_ge(*after("gate.rowm"))
            c, x4 = by_t(gcum), mE.rearrange("p (k n) -> p k n", k=4)
            r4 = psum[:, 4:6, :].rearrange("p b (k n) -> p (b k) n", k=2)
            nc.vector.tensor_tensor(x4[:, :, 0:256], r4, c[:, 0, 0:4].unsqueeze(2).broadcast_to([P, 4, 256]), ALU.subtract)\
                .then_inc(*steps.did("dve", "mx0"))
            nc.vector.tensor_tensor(x4[:, :, 256:384], r4[:, :, P:256], c[:, 1, 0:4].unsqueeze(2).broadcast_to([P, 4, P]), ALU.subtract)\
                .then_inc(*steps.did("dve", "mx1"))

        def dve_delta_exponents(dve):
            dve.wait_ge(*after("gate.rowg"))
            c = by_t(gcum)
            nc.vector.tensor_copy(glast, bank(6).rearrange("p (k n) -> p k n", k=4)[:, :, P - 1]).then_inc(*steps.did("dve", "glast"))
            nc.vector.tensor_tensor(heads4(dE0), psum[:, 6:8, :].rearrange("p t (k d) -> p t k d", k=4),
                                    c[:, :, 4:8].unsqueeze(3).broadcast_to([P, NT, 4, P]), ALU.subtract)\
                .then_inc(*steps.did("dve", "dx"))
            dve.wait_ge(*after("glast"))
            nc.vector.tensor_tensor(glast, glast, c[:, 0, 4:8], ALU.subtract).then_inc(*steps.did("dve", "dlast"))

        dE0 = arena[:, 6144:7168]

        def pool_ab_masks(pool):
            pool.wait_ge(*after("mx1"))
            x4 = mE.rearrange("p (k n) -> p k n", k=4)
            for at, name in ((0, "mm0"), (256, "mm1")):
                nc.gpsimd.affine_select(out=x4[:, :, at:at + P], in_=x4[:, :, at:at + P], compare_op=ALU.is_ge, fill=-BIG,
                                        base=0, pattern=[[0, 4], [1, P]], channel_multiplier=-1).then_inc(*steps.did("pool", name))
            pool.wait_ge(*after("dx"))
            v = dE0.rearrange("p (k n) -> p k n", k=8)
            nc.gpsimd.affine_select(out=v, in_=v, compare_op=ALU.is_ge, fill=-BIG, base=0, pattern=[[0, 8], [1, P]],
                                    channel_multiplier=-1).then_inc(*steps.did("pool", "dm"))

        def act_ab_decays(act):
            act.wait_ge(*after("mm1"))
            nc.scalar.activation(mE, mE, ACT.Exp).then_inc(*steps.did("act", "mE"))
            act.wait_ge(*after("dm"))
            nc.scalar.activation(dE0, dE0, ACT.Exp).then_inc(*steps.did("act", "dE0"))
            act.wait_ge(*after("dlast"))
            nc.scalar.activation(kdecay, glast, ACT.Exp).then_inc(*steps.did("act", "kdecay"))
            nc.scalar.activation(eg1, by_t(gcum)[:, 1, 4:8], ACT.Exp).then_inc(*steps.did("act", "eg1"))

        def dve_m_v(dve):
            dve.wait_ge(used, ab_p["mv"] + 4)
            dve.wait_ge(*after("gate.ei"))
            nc.vector.tensor_tensor(heads4(mvE), psum[:, 2:4, :].rearrange("p t (k d) -> p t k d", k=4), spread_heads(gei), ALU.mult)\
                .then_inc(*steps.did("dve", "mvE"))

        M_BANKS = (2, 4, 3, 5)

        def pe_m_scores(pe):
            for name in ("mqk.y", "mvE", "mx1"):
                pe.wait_ge(*after(name))
            y = Y["mqk"]
            for par in range(2):
                part = slice(64 * par, 64 * par + 64)
                for c in range(2):
                    x = 2 * c + par
                    q, k = y[part, c * 256:c * 256 + 256], y[part, 512 + c * 256:512 + c * 256 + 256]
                    nc.tensor.matmul(bank(M_BANKS[x], 0, 256), k[:, 0:P], q, start=True, stop=True)
                    last = nc.tensor.matmul(bank(M_BANKS[x], 256, P), k[:, P:256], q[:, P:256], start=True, stop=True)
            last.then_inc(*steps.did("pe", "mS"))

        def dve_m_matrix(dve):
            dve.wait_ge(*after("mS"))
            dve.wait_ge(*after("mE"))
            for x in range(4):
                e = mE[:, x * 384:x * 384 + 384]
                last = nc.vector.scalar_tensor_tensor(e, bank(M_BANKS[x], 0, 384), 0.125, e, ALU.mult, ALU.mult)
            last.then_inc(*steps.did("dve", "mA"))

        def pe_m_out(pe):
            pe.wait_ge(*after("mA"))
            last = None
            for den in range(2):
                for x in range(4):
                    a = mE[:, x * 384:x * 384 + 384]
                    for t in range(NT):
                        o = bank(4, t * 4 + x, 1) if den else bank(2 + t, x * P, P)
                        rhs = lambda s: by_t(gei)[:, s, x:x + 1] if den else mvE[:, s * 512 + x * P:s * 512 + x * P + P]
                        nc.tensor.matmul(o, a[:, t * P:t * P + P], rhs(0), start=True, stop=(t == 0))
                        if t == 1:
                            last = nc.tensor.matmul(o, a[:, 256:384], rhs(1), start=False, stop=True)
            last.then_inc(*steps.did("pe", "mO"))

        def dve_m_out(dve):
            dve.wait_ge(*after("mO"))
            nc.vector.tensor_scalar(m_den, bank(4, 0, 8), -1.0, None, ALU.mult).then_inc(*steps.did("dve", "m.nden"))
            dve.wait_ge(*after("m.nden"))
            nc.vector.scalar_tensor_tensor(m_den, bank(4, 0, 8), 1.0, m_den, ALU.max, ALU.max).then_inc(*steps.did("dve", "m.den"))
            dve.wait_ge(*after("m.den"))
            nc.vector.reciprocal(m_den, m_den).then_inc(*steps.did("dve", "m.rden"))
            dve.wait_ge(*after("m.rden"))
            m4 = mix[:, :, 0:512].rearrange("p t (k d) -> p t k d", k=4)
            nc.vector.tensor_tensor(m4, psum[:, 2:4, :].rearrange("p t (k d) -> p t k d", k=4), spread_heads(m_den), ALU.mult)\
                .then_inc(*steps.did("dve", "m.h"))

        def act_m_square(act):
            act.wait_ge(*after("m.h"))
            nc.scalar.activation(by_t(m_sq), mix[:, :, 0:512], ACT.Square).then_inc(*steps.did("act", "m.sq"))

        def dve_m_norm(dve):
            dve.wait_ge(*after("m.sq"))
            nc.vector.tensor_reduce(m_ss, m_sq.rearrange("p (k d) -> p k d", d=P), AX_X, ALU.add).then_inc(*steps.did("dve", "m.ss"))
            dve.wait_ge(*after("m.r"))
            m4 = mix[:, :, 0:512].rearrange("p t (k d) -> p t k d", k=4)
            nc.vector.tensor_tensor(m4, m4, spread_heads(m_r), ALU.mult).then_inc(*steps.did("dve", "m.n"))

        ROW_BANKS = {"dk": 4, "dq": 2, "dv": 0}

        def pe_rows(pe, name, ready):
            for r in ready:
                pe.wait_ge(*after(r))
            for t in range(NT):
                for c in range(4):
                    last = nc.tensor.transpose(bank(ROW_BANKS[name] + t, c * P, P), Y[name][:, c * 256 + t * P:c * 256 + t * P + P], ident)
            last.then_inc(*steps.did("pe", f"{name}.R"))

        def act_row_squares(act, name, sq):
            act.wait_ge(*after(f"{name}.R"))
            b = ROW_BANKS[name]
            nc.scalar.activation(by_t(sq), psum[:, b:b + 2, :], ACT.Square).then_inc(*steps.did("act", f"{name}.sq"))

        def dve_row_sums(dve, name, sq, ss):
            dve.wait_ge(*after(f"{name}.sq"))
            nc.vector.tensor_reduce(ss, sq.rearrange("p (k d) -> p k d", d=P), AX_X, ALU.add).then_inc(*steps.did("dve", f"{name}.ss"))

        def dve_row_scale(dve, name, dst, r, ready, done):
            b = ROW_BANKS[name]
            for x in ready:
                dve.wait_ge(*after(x))
            nc.vector.tensor_tensor(heads4(dst), psum[:, b:b + 2, :].rearrange("p t (k d) -> p t k d", k=4), spread_heads(r), ALU.mult)\
                .then_inc(*steps.did("dve", done))

        def pool_delta(pool):
            pool.wait_ge(*after("m.ss"))
            pool_rstd(pool, "m.r", m_ss, 8, P, m_r)
            for name, ss, r in (("dk", k_ss, k_r), ("dq", q_ss, q_r)):
                pool.wait_ge(*after(f"{name}.ss"))
                pool_rstd(pool, f"{name}.rr", ss, 8, 1, r)
            pool.wait_ge(*after("dq.rr"))
            nc.gpsimd.tensor_scalar(q_r, q_r, float(P) ** -0.5, None, ALU.mult).then_inc(*steps.did("pool", "dq.rs"))
            g = gain_of(pool, "abh")
            for name, a, at, done in (("m.sig", arena[:, 9216:10240], 0, "m.sigg"), ("d.gate", gtmp, 512, "ab.last")):
                pool.wait_ge(*after(name))
                nc.gpsimd.tensor_tensor(by_t(a), by_t(a), g[:, at:at + 512].unsqueeze(1).broadcast_to([P, NT, 512]), ALU.mult)\
                    .then_inc(*steps.did("pool", done))
            pool.wait_ge(*after("d.ss"))
            pool_rstd(pool, "d.r", d_ss, 8, P, d_r)

        def pe_cols(pe, name, src, b, ready):
            for r in ready:
                pe.wait_ge(*after(r))
            for x in range(4):
                for t in range(NT):
                    last = nc.tensor.transpose(bank(b + x // 2, (x % 2) * 256 + t * P, P), src[:, t * 512 + x * P:t * 512 + x * P + P], ident)
            last.then_inc(*steps.did("pe", name))

        def per_tile(pe, b, lhs, rhs, name):
            for t in range(NT):
                for x in range(4):
                    last = nc.tensor.matmul(bank(b + t, x * P, P), lhs(t, x), rhs(t, x), start=True, stop=True)
            last.then_inc(*steps.did("pe", name))

        tok_head = lambda a: lambda t, x: a[:, t * 512 + x * P:t * 512 + x * P + P]
        head_tok = lambda a: lambda t, x: a[:, x * 256 + t * P:x * 256 + t * P + P]

        def pe_delta_matrices(pe):
            pe.wait_ge(*after("kT2"))
            pe.wait_ge(*after("qT2"))
            pe.wait_ge(*after("kbT"))
            per_tile(pe, 2, head_tok(kT2), head_tok(kbT), "dNT.p")
            per_tile(pe, 4, head_tok(kT2), head_tok(qT2), "dat.p")

        def dve_delta_matrices(dve):
            dve.wait_ge(*after("dE"))
            for name, b, dst in (("dNT", 2, dNT), ("dat", 4, dat)):
                dve.wait_ge(*after(f"{name}.p"))
                nc.vector.tensor_tensor(by_t(dst), psum[:, b:b + 2, :], by_t(dE), ALU.mult).then_inc(*steps.did("dve", name))
            dve.wait_ge(*after("dNT"))
            eight = lambda a: a.rearrange("p (k n) -> p k n", k=8)
            nc.vector.tensor_tensor(eight(dXT), eight(dNT), cst("level1").unsqueeze(1).broadcast_to([P, 8, P]), ALU.mult)\
                .then_inc(*steps.did("dve", "dXT.m"))
            dve.wait_ge(*after("dXT.m"))
            nc.vector.tensor_tensor(eight(dXT), ident.unsqueeze(1).broadcast_to([P, 8, P]), eight(dXT), ALU.subtract)\
                .then_inc(*steps.did("dve", "dXT"))

        SOLVE = LEVELS[::-1][1:]

        def pe_delta_start(pe):
            pe.wait_ge(*after("dNT"))
            for t in range(NT):
                for x in range(4):
                    last = nc.tensor.transpose(bank(t, x * P, P), tok_head(dNT)(t, x), ident)
            last.then_inc(*steps.did("pe", "dN.T"))
            pe.wait_ge(*after("dXT"))
            pe.wait_ge(*after("dat"))
            for t in range(NT):
                for x in range(4):
                    last = nc.tensor.transpose(bank(2 + t, x * P, P), tok_head(dXT)(t, x), ident)
            last.then_inc(*steps.did("pe", "dX.T"))

        def act_delta_start(act):
            for name, dst, b in (("dN", dN, 0), ("dX", dX, 2)):
                act.wait_ge(*after(f"{name}.T"))
                nc.scalar.activation(by_t(dst), psum[:, b:b + 2, :], ACT.Copy).then_inc(*steps.did("act", name))

        def solved(n, t):
            return f"dX.{n}{t}"

        def pe_delta_level(pe, n, part):
            for t in range(NT):
                if part == 0:
                    for name in ("dN", "dX") if n == 0 else (f"dXTn{n - 1}{t}",):
                        pe.wait_ge(*after(name))
                    for x in range(4):
                        last = nc.tensor.matmul(bank(t, x * P, P), tok_head(dN)(t, x), tok_head(dXT)(t, x), start=True, stop=True)
                    last.then_inc(*steps.did("pe", f"dV.p{n}{t}"))
                    continue
                pe.wait_ge(*after(f"dV{n}{t}"))
                if n > 0:
                    pe.wait_ge(*after(f"dXn{n - 1}{t}"))
                for x in range(4):
                    last = nc.tensor.matmul(bank(2 + t, x * P, P), tok_head(dX)(t, x), tok_head(dV)(t, x), start=True, stop=True)
                last.then_inc(*steps.did("pe", f"dXT.p{n}{t}"))
                if n < len(SOLVE) - 1:
                    for x in range(4):
                        last = nc.tensor.matmul(bank(4 + t, x * P, P), tok_head(dV)(t, x), tok_head(dX)(t, x), start=True, stop=True)
                    last.then_inc(*steps.did("pe", f"dX.p{n}{t}"))

        def dve_delta_level(dve, n):
            four = lambda a: a.rearrange("p (k n) -> p k n", k=4)
            mask = cst(f"level{SOLVE[n]}").unsqueeze(1).broadcast_to([P, 4, P])
            half = lambda a, t: a[:, t * 512:t * 512 + 512]
            for t in range(NT):
                dve.wait_ge(*after(f"dV.p{n}{t}"))
                nc.vector.tensor_tensor(four(half(dV, t)), four(bank(t)), mask, ALU.mult).then_inc(*steps.did("dve", f"dV{n}{t}"))
            for t in range(NT):
                dve.wait_ge(*after(f"dXT.p{n}{t}"))
                if n > 0:
                    dve.wait_ge(*after(f"dXTn{n - 1}{t}"))
                nc.vector.tensor_tensor(half(dXT, t), half(dXT, t), bank(2 + t), ALU.subtract).then_inc(*steps.did("dve", f"dXTn{n}{t}"))
                if n < len(SOLVE) - 1:
                    dve.wait_ge(*after(f"dX.p{n}{t}"))
                    nc.vector.tensor_tensor(half(dX, t), half(dX, t), bank(4 + t), ALU.subtract).then_inc(*steps.did("dve", f"dXn{n}{t}"))

        def four_heads(pe, b, lhs, rhs, name):
            for x in range(4):
                last = nc.tensor.matmul(bank(b, x * P, P), lhs(x), rhs(x), start=True, stop=True)
            last.then_inc(*steps.did("pe", name))

        head = lambda a: lambda x: a[:, x * P:x * P + P]

        def pe_delta_out(pe):
            n = len(SOLVE) - 1
            pe.wait_ge(*after(f"dXTn{n}0"))
            four_heads(pe, 0, head(dXT[:, 0:512]), head(vb[:, 0:512]), "d.u0p")
            pe.wait_ge(*after("d.u0"))
            pe.wait_ge(*after("d.kdec"))
            four_heads(pe, 1, head(krow[:, 0:512]), head(u0), "d.Sp")
            four_heads(pe, 5, head(dat[:, 0:512]), head(u0), "d.o0p")
            pe.wait_ge(*after("d.S"))
            pe.wait_ge(*after(f"dXTn{n}1"))
            four_heads(pe, 2, lambda x: head_tok(kT2)(1, x), head(dS), "d.kSp")
            four_heads(pe, 3, lambda x: head_tok(qT2)(1, x), head(dS), "d.qSp")
            pe.wait_ge(*after("d.rhs"))
            four_heads(pe, 0, head(dXT[:, 512:1024]), head(u1), "d.u1p")
            pe.wait_ge(*after("d.u1"))
            four_heads(pe, 1, head(dat[:, 512:1024]), head(u1), "d.o1p")

        def dve_delta_prep(dve):
            four = lambda a: a.rearrange("p (k n) -> p k n", k=4)
            dve.wait_ge(*after("kdecay"))
            dve.wait_ge(*after("kT2.T"))
            nc.vector.tensor_tensor(four(krow[:, 0:512]), four(krow[:, 0:512]), kdecay.unsqueeze(2).broadcast_to([P, 4, P]), ALU.mult)\
                .then_inc(*steps.did("dve", "d.kdec"))
            dve.wait_ge(*after("eg1"))
            nc.vector.tensor_tensor(beg, eg1, gbeta[:, 4:8], ALU.mult).then_inc(*steps.did("dve", "beg"))

        def dve_delta_out(dve):
            four = lambda a: a.rearrange("p (k n) -> p k n", k=4)
            wide = lambda a: a.unsqueeze(2).broadcast_to([P, 4, P])
            dve.wait_ge(*after("d.u0p"))
            nc.vector.tensor_copy(u0, bank(0)).then_inc(*steps.did("dve", "d.u0"))
            dve.wait_ge(*after("d.Sp"))
            nc.vector.tensor_copy(dS, bank(1)).then_inc(*steps.did("dve", "d.S"))
            out_splits(split_lo, dve, "abo", (2,))
            dve.wait_ge(*after("d.kSp"))
            dve.wait_ge(*after("beg"))
            nc.vector.tensor_tensor(four(u1), four(bank(2)), wide(beg), ALU.mult).then_inc(*steps.did("dve", "d.ks"))
            dve.wait_ge(*after("d.ks"))
            nc.vector.tensor_tensor(u1, vb[:, 512:1024], u1, ALU.subtract).then_inc(*steps.did("dve", "d.rhs"))
            m = mix[:, 1, 512:1024]
            dve.wait_ge(*after("d.qSp"))
            nc.vector.tensor_tensor(four(m), four(bank(3)), wide(eg1), ALU.mult).then_inc(*steps.did("dve", "d.qs"))
            dve.wait_ge(*after("d.u1p"))
            nc.vector.tensor_copy(u1, bank(0)).then_inc(*steps.did("dve", "d.u1"))
            nc.vector.tensor_copy(mix[:, 0, 512:1024], bank(5)).then_inc(*steps.did("dve", "d.o0"))
            out_splits(split_lo, dve, "abo", (3,))
            dve.wait_ge(*after("d.o1p"))
            dve.wait_ge(*after("d.qs"))
            nc.vector.tensor_tensor(m, m, bank(1), ALU.add).then_inc(*steps.did("dve", "d.o1"))
            out_splits(split_lo, dve, "abo", (4,))
            dve.wait_ge(*after("d.osq"))
            nc.vector.tensor_reduce(d_ss, d_sq.rearrange("p (k d) -> p k d", d=P), AX_X, ALU.add).then_inc(*steps.did("dve", "d.ss"))
            out_splits(split_lo, dve, "abo", (5,))
            dve.wait_ge(*after("d.r"))
            m4 = mix[:, :, 512:1024].rearrange("p t (k d) -> p t k d", k=4)
            nc.vector.tensor_tensor(m4, m4, spread_heads(d_r), ALU.mult).then_inc(*steps.did("dve", "d.n"))
            dve.wait_ge(*after("d.n"))
            dve.wait_ge(*after("ab.last"))
            for t in range(NT):
                nc.vector.tensor_tensor(mix[:, t, 512:1024], mix[:, t, 512:1024], gtmp[:, t * 512:t * 512 + 512], ALU.mult)\
                    .then_inc(*steps.did("dve", f"abo.n{t}"))

        def pe_ab(pe):
            pe_ab_first(pe)
            pe_gate_sums(pe)
            pe_conv_unit(pe, "dk", ["mqk.c0"])
            pe_m_scores(pe)
            pe_conv_unit(pe, "dq", ["dx", "glast"])
            pe_m_out(pe)
            pe_conv_unit(pe, "dv", ["dk.c0"])
            pe_rows(pe, "dk", ["dk.y", "m.h"])
            pe_rows(pe, "dq", ["dq.y"])
            pe.wait_ge(*after("dq.c0"))
            pe_unit(pe, ab_p["mo"], rows=[(0, 512, [bank(6), bank(7)], (True, True))])
            pe_rows(pe, "dv", ["dv.y"])
            pe_cols(pe, "kT2.T", krow, 4, ["krow"])
            pe_cols(pe, "kbT.T", kb, 2, ["kb", "qrow"])
            pe_cols(pe, "qT2.T", qrow, 6, ["m.sig"])
            pe.wait_ge(*after("m.gate"))
            pe_delta_matrices(pe)
            pe_delta_start(pe)
            for n in range(len(SOLVE)):
                pe_delta_level(pe, n, 0)
                if n < 4:
                    if n == 0:
                        pe.wait_ge(*after("qT2"))
                    pe_unit(pe, ab_p["dg"], rows=[(0, 512, [bank(6), bank(7)], (True, True))], which=(n,))
                pe_delta_level(pe, n, 1)
                if n == 4:
                    for t in range(NT):
                        pe_turn(pe, "abo", t, 0, 6 + t, mix, "d.gate")
            pe_delta_out(pe)
            pe_turn_after(pe)

        def pe_turn_after(pe):
            for k in range(4):
                if k == 0:
                    pe.wait_ge(*after("d.o1"))
                pe_out(pe, "abo", k)
            for t in range(NT):
                pe_turn(pe, "abo", t, 1, 6 + t, mix, f"abo.n{t}")
            pe_out_last(pe, "abo")

        def act_ab(act):
            S = lambda name, which=(0, 1, 2, 3): split4(split_hi, act, ab_p[name], which=which)
            S("mqk", (2,))
            act_gates(act)
            S("mqk", (3,))
            S("mv", (0, 1, 2))
            act_conv_first(act, "mqk")
            S("mv", (3,))
            S("dk", (0,))
            act_conv_silu(act, "mqk")
            S("dk", (1, 2, 3))
            act_ab_decays(act)
            S("dq", (0, 1))
            act_conv_first(act, "dk")
            S("dq", (2,))
            act_conv_silu(act, "dk")
            S("dq", (3,))
            S("dv", (0, 1))
            act_conv_first(act, "dq")
            S("dv", (2, 3))
            act_conv_silu(act, "dq")
            act_m_square(act)
            S("mo", (0, 1, 2))
            act_conv_first(act, "dv")
            S("mo", (3,))
            act_row_squares(act, "dk", arena[:, 9216:10240])
            act_conv_silu(act, "dv")
            act_row_squares(act, "dq", arena[:, 10240:11264])
            act.wait_ge(*after("krow"))
            act.wait_ge(*after("m.ss"))
            act.wait_ge(*after("m.n"))
            act.wait_ge(used, ab_p["mo"] + 4)
            act.wait_ge(*after("dk.ss"))
            nc.scalar.activation(by_t(arena[:, 9216:10240]), psum[:, 6:8, :], ACT.Sigmoid).then_inc(*steps.did("act", "m.sig"))
            nc.scalar.activation(dE, dE0, ACT.Copy).then_inc(*steps.did("act", "dE"))
            S("dg", (0, 1, 2))
            for name, dst, b in (("kT2", kT2, 4), ("kbT", kbT, 2), ("qT2", qT2, 6)):
                act.wait_ge(*after(f"{name}.T"))
                nc.scalar.activation(rows(dst), psum[:, b:b + 2, :], ACT.Copy).then_inc(*steps.did("act", name))
            act_delta_start(act)
            S("dg", (3,))
            out_splits(split_hi, act, "abo", (0, 1))
            act.wait_ge(used, ab_p["dg"] + 4)
            act.wait_ge(*after("dat"))
            nc.scalar.activation(by_t(gtmp), psum[:, 6:8, :], ACT.Silu).then_inc(*steps.did("act", "d.gate"))
            for t in range(NT):
                act_turn(act, "abo", t, 0, 6 + t)
            out_splits(split_hi, act, "abo", (2, 3, 4))
            act.wait_ge(*after("d.o1"))
            act.wait_ge(*after("d.o0"))
            nc.scalar.activation(by_t(d_sq), mix[:, :, 512:1024], ACT.Square).then_inc(*steps.did("act", "d.osq"))
            out_splits(split_hi, act, "abo", (5,))
            for t in range(NT):
                act_turn(act, "abo", t, 1, 6 + t)
            out_splits(split_hi, act, "abo", (6, 7))
            first_pieces(split_hi, act, "ffn2", (0, 1))

        def dve_ab(dve):
            S = lambda name, which=(0, 1, 2, 3): split4(split_lo, dve, ab_p[name], which=which)
            S("mqk", (2,))
            dve_gates(dve)
            dve_gate_logs(dve)
            S("mqk", (3,))
            S("mv", (0, 1, 2))
            dve_conv_rest(dve, "mqk")
            S("mv", (3,))
            dve_m_v(dve)
            dve_gate_rows(dve)
            S("dk", (0, 1, 2))
            dve_delta_exponents(dve)
            S("dk", (3,))
            S("dq", (0, 1))
            dve_conv_rest(dve, "dk")
            S("dq", (2,))
            dve_m_matrix(dve)
            S("dq", (3,))
            S("dv", (0, 1))
            dve_m_out(dve)
            S("dv", (2, 3))
            dve_conv_rest(dve, "dq")
            S("mo", (0, 1, 2))
            dve_conv_rest(dve, "dv")
            S("mo", (3,))
            dve_m_norm(dve)
            dve_row_sums(dve, "dk", arena[:, 9216:10240], k_ss)
            dve_row_sums(dve, "dq", arena[:, 10240:11264], q_ss)
            dve_row_scale(dve, "dk", krow, k_r, ["dk.rr"], "krow")
            dve_row_scale(dve, "dq", qrow, q_r, ["dq.rs"], "qrow")
            dve.wait_ge(*after("dE"))
            dve.wait_ge(*after("krow"))
            nc.vector.tensor_tensor(heads4(kb), heads4(krow), spread_heads(gbeta), ALU.mult).then_inc(*steps.did("dve", "kb"))
            dve_row_scale(dve, "dv", vb, gbeta, ["dv.R"], "vb")
            dve.wait_ge(*after("m.sigg"))
            dve.wait_ge(*after("m.n"))
            nc.vector.tensor_tensor(mix[:, :, 0:512], mix[:, :, 0:512], by_t(arena[:, 9216:10240]), ALU.mult)\
                .then_inc(*steps.did("dve", "m.gate"))
            S("dg", (0, 1, 2))
            dve.wait_ge(*after("m.gate"))
            dve_delta_matrices(dve)
            dve_delta_prep(dve)
            S("dg", (3,))
            for n in range(len(SOLVE)):
                dve_delta_level(dve, n)
                if n in (3, 4):
                    out_splits(split_lo, dve, "abo", (n - 3,))
            for t in range(NT):
                dve_turn(dve, "abo", t, 0, 6 + t)
            dve_delta_out(dve)
            for t in range(NT):
                dve_turn(dve, "abo", t, 1, 6 + t)
            out_splits(split_lo, dve, "abo", (6, 7))
            first_pieces(split_lo, dve, "ffn2", (0, 1))

        def pool_ab(pool, gains):
            next_gain(pool, gains)
            pool_ab_masks(pool)
            pool_delta(pool)
            next_gain(pool, gains)

        HW = 4 * SEQ
        hq, hk, hb = ([arena[:, (3 * u + n) * HW:(3 * u + n + 1) * HW] for u in range(2)] for n in range(3))
        h_e, h_l = arena[:, 6144:7168], (arena[:, 7168:8192], arena[:, 8192:9216])
        h_at, h_cross = arena[:, 9216:10240], arena[:, 10240:10752]
        h_t1, h_t2 = (arena[:, 6144:7168], arena[:, 8192:9216]), (arena[:, 7168:8192], arena[:, 9216:10240])
        h_sil = (arena[:, 10752:11776], arena[:, 1024:2048])
        h_sq = (arena[:, 0:1024], arena[:, 0:1024])
        lb_d, lb_e, log_lb, log_rest, lb_x = (few.take(8) for _ in range(5))
        h_ss, h_r = (few.take(8), few.take(8)), (few.take(8), few.take(8))
        wide2 = lambda b: psum[:, b:b + 2, :].rearrange("p b n -> p (b n)")
        hu = lambda n: piece_at("hg", n)

        def dve_bounds(dve):
            nc.vector.tensor_tensor(lb_d, lb_logits[:, 8:16], lb_logits[:, 0:8], ALU.subtract).then_inc(*steps.did("dve", "lb.d"))
            dve.wait_ge(*after("lb.ln"))
            nc.vector.scalar_tensor_tensor(log_rest, lb_d, 0.0, lb_e, ALU.max, ALU.add).then_inc(*steps.did("dve", "lb.1"))
            nc.vector.scalar_tensor_tensor(log_lb, lb_d, 0.0, lb_e, ALU.min, ALU.subtract).then_inc(*steps.did("dve", "lb.a"))
            dve.wait_ge(*after("lb.1"))
            nc.vector.tensor_scalar(log_rest, log_rest, -1.0, None, ALU.mult).then_inc(*steps.did("dve", "lb.c"))

        def act_bounds(act):
            act.wait_ge(*after("lb.d"))
            nc.scalar.activation(lb_e, lb_d, ACT.Abs).then_inc(*steps.did("act", "lb.abs"))
            act.wait_ge(*after("lb.abs"))
            nc.scalar.activation(lb_e, lb_e, ACT.Exp, scale=-1.0).then_inc(*steps.did("act", "lb.exp"))
            act.wait_ge(*after("lb.exp"))
            nc.scalar.activation(lb_e, lb_e, ACT.Ln, bias=1.0).then_inc(*steps.did("act", "lb.ln"))

        def act_log1p_exp(act, name, a, src, ready):
            for r in ready:
                act.wait_ge(*after(r))
            nc.scalar.activation(a, src, ACT.Abs).then_inc(*steps.did("act", f"{name}.abs"))
            act.wait_ge(*after(f"{name}.abs"))
            nc.scalar.activation(a, a, ACT.Exp, scale=-1.0).then_inc(*steps.did("act", f"{name}.exp"))
            act.wait_ge(*after(f"{name}.exp"))
            nc.scalar.activation(a, a, ACT.Ln, bias=1.0).then_inc(*steps.did("act", f"{name}.ln"))

        def act_h_forget(act, u):
            act.wait_ge(used, hu(u) + 4)
            act_log1p_exp(act, f"hf{u}", h_t1[u], wide2(2 * u), ())

        def dve_h_forget(dve, u):
            f = wide2(2 * u)
            dve.wait_ge(*after(f"hf{u}.ln"))
            nc.vector.scalar_tensor_tensor(h_t2[u], f, 0.0, h_t1[u], ALU.min, ALU.subtract).then_inc(*steps.did("dve", f"hf{u}.ls"))
            dve.wait_ge(*after(f"hf{u}.ls"))
            dve.wait_ge(*after("lb.c"))
            dve.wait_ge(*after("lb.a"))
            for x in range(4):
                t = slice(x * SEQ, x * SEQ + SEQ)
                a, c = log_lb[:, 4 * u + x:4 * u + x + 1], log_rest[:, 4 * u + x:4 * u + x + 1]
                nc.vector.tensor_scalar(hb[u][:, t], h_t2[u][:, t], c, a, ALU.add, ALU.max)
                nc.vector.tensor_scalar(h_t1[u][:, t], h_t2[u][:, t], c, a, ALU.add, ALU.subtract)
                last = nc.vector.scalar_tensor_tensor(hk[u][:, t], h_t2[u][:, t], c, f[:, t], ALU.add, ALU.subtract)
            last.then_inc(*steps.did("dve", f"hf{u}.x"))

        def act_h_decay(act, u):
            act.wait_ge(*after(f"hf{u}.x"))
            nc.scalar.activation(hk[u], hk[u], ACT.Exp).then_inc(*steps.did("act", f"hk{u}"))
            act_log1p_exp(act, f"hd{u}", h_t1[u], h_t1[u], ())

        def dve_h_decay(dve, u):
            dve.wait_ge(*after(f"hd{u}.ln"))
            nc.vector.tensor_tensor(h_t1[u], h_t1[u], hb[u], ALU.add).then_inc(*steps.did("dve", f"hd{u}.lf"))
            dve.wait_ge(*after(f"hd{u}.lf"))
            for x in range(4):
                t = slice(x * SEQ, x * SEQ + SEQ)
                last = nc.vector.tensor_tensor_scan(hb[u][:, t], ones.broadcast_to([P, SEQ]), h_t1[u][:, t], 0.0, ALU.mult, ALU.add)
            last.then_inc(*steps.did("dve", f"hb{u}"))

        def act_h_q(act, u):
            act.wait_ge(used, hu(2 + u) + 4)
            nc.scalar.activation(hq[u], wide2(4 + 2 * u), ACT.Silu).then_inc(*steps.did("act", f"hq{u}"))

        def act_h_v(act, u):
            act.wait_ge(used, hu(4 + u) + 4)
            act.wait_ge(*after("hg.T11"))
            nc.scalar.activation(mix[:, :, 512 * u:512 * u + 512], psum[:, 4 + 2 * u:6 + 2 * u, :], ACT.Copy, scale=float(P) ** -0.5)\
                .then_inc(*steps.did("act", f"hv{u}"))

        def act_h_gate(act, u):
            act.wait_ge(used, hu(6 + u) + 4)
            if u == 1:
                act.wait_ge(*after("h0.P8"))
            nc.scalar.activation(by_t(h_sil[u]), psum[:, 4:6, :], ACT.Silu).then_inc(*steps.did("act", f"hs{u}"))

        def pe_h_columns(pe, n, b):
            pe_unit(pe, hu(n), columns=[(c * P, bank(b + c // 2, (c % 2) * 256, 256), c % 2 == 0) for c in range(4)])

        def pe_h_piece(pe, n, k, b):
            pe_unit(pe, hu(n), rows=[(0, 512, [bank(b), bank(b + 1)], (True, True))], which=(k,))

        def pe_h_level(pe, u, n):
            X = f"h{u}"
            if n >= 2:
                pe.wait_ge(*after(f"{X}.put{n - 2}"))
            elif u == 1:
                pe.wait_ge(*after(f"h0.put{7 + n}"))
            else:
                pe.wait_ge(*after("hf1.x"))
            if n < len(ALL_LEVELS):
                pe.wait_ge(*after(f"{X}.l{n}"))
                l = r = h_l[n % 2]
            else:
                l, r = hk[u], hq[u]
            if n == 0:
                for x in range(4):
                    last = nc.tensor.matmul(bank(0, x * P, P), head_tok(l)(0, x), head_tok(r)(1, x), start=True, stop=True)
                last.then_inc(*steps.did("pe", f"{X}.P{n}"))
            else:
                per_tile(pe, 2 * (n % 2), head_tok(l), head_tok(r), f"{X}.P{n}")

        def dve_h_put(dve, u, n):
            X = f"h{u}"
            dve.wait_ge(*after(f"{X}.P{n}"))
            if n == 0:
                if u == 1:
                    dve.wait_ge(*after("h0.O"))
                nc.vector.tensor_copy(h_cross, bank(0)).then_inc(*steps.did("dve", f"{X}.put0"))
                return
            dve.wait_ge(*after(f"{X}.put{n - 1}" if n > 1 else f"{X}.at0"))
            mask = cst(f"level{ALL_LEVELS[n]}") if n < len(ALL_LEVELS) else ident
            b = 2 * (n % 2)
            for t in range(NT):
                four = lambda a: a.rearrange("p (m i) -> p m i", m=4)
                last = nc.vector.copy_predicated(four(h_at[:, t * 512:t * 512 + 512]),
                                                 mask.bitcast(U32).unsqueeze(1).broadcast_to([P, 4, P]), four(bank(b + t)))
            last.then_inc(*steps.did("dve", f"{X}.put{n}"))

        def dve_h_levels(dve, u, pieces):
            X = f"h{u}"
            for n, half in enumerate(ALL_LEVELS):
                if n == 0:
                    ready = [f"hb{u}", f"hq{u}", f"hk{u}", "hb1", "hk1"] if u == 0 else ["h0.l7", "hq1"]
                else:
                    ready = [f"{X}.l{n - 1}"]
                dve_level_x(dve, X, n, half, hb[u], h_e, ready)
                split_lo(dve, pieces + n)
                if n >= 2:
                    dve_h_put(dve, u, n - 2)
                if n >= 2:
                    wait = [f"{X}.P{n - 2}"]
                else:
                    wait = [f"h0.P{6 + n}"] if u == 1 else []
                dve_level_l(dve, X, n, half, hq[u], hk[u], h_e, h_l[n % 2], wait)
            for n in (6, 7, 8):
                dve_h_put(dve, u, n)

        def pe_h_out(pe, u):
            X = f"h{u}"
            for r in (f"{X}.put8", "hv1", f"hv{u}") + (("ho0.n",) if u == 1 else ()):
                pe.wait_ge(*after(r))
            for t in range(NT):
                for x in range(4):
                    v = lambda s: mix[:, s, 512 * u + x * P:512 * u + x * P + P]
                    last = nc.tensor.matmul(bank(6 + t, x * P, P), tok_head(h_at)(t, x), v(t), start=True, stop=(t == 0))
                    if t == 1:
                        last = nc.tensor.matmul(bank(7, x * P, P), h_cross[:, x * P:x * P + P], v(0), start=False, stop=True)
            last.then_inc(*steps.did("pe", f"{X}.O"))

        def act_h_square(act, u):
            act.wait_ge(*after(f"h{u}.O"))
            nc.scalar.activation(by_t(h_sq[u]), psum[:, 6:8, :], ACT.Square).then_inc(*steps.did("act", f"ho{u}.sq"))

        def pool_h(pool, u):
            pool.wait_ge(*after(f"ho{u}.ss"))
            pool_rstd(pool, f"ho{u}.r", h_ss[u], 8, P, h_r[u])

        def dve_h_sums(dve, u):
            dve.wait_ge(*after(f"ho{u}.sq"))
            nc.vector.tensor_reduce(h_ss[u], h_sq[u].rearrange("p (k d) -> p k d", d=P), AX_X, ALU.add).then_inc(*steps.did("dve", f"ho{u}.ss"))

        def dve_h_out_norm(dve, u):
            m = mix[:, :, 512 * u:512 * u + 512]
            dve.wait_ge(*after(f"ho{u}.r"))
            nc.vector.tensor_tensor(m.rearrange("p t (k d) -> p t k d", k=4), psum[:, 6:8, :].rearrange("p t (k d) -> p t k d", k=4),
                                    spread_heads(h_r[u]), ALU.mult).then_inc(*steps.did("dve", f"ho{u}.n"))

        def dve_h_out_gate(dve, u):
            m = mix[:, :, 512 * u:512 * u + 512]
            dve.wait_ge(*after(f"ho{u}.n"))
            dve.wait_ge(*after("hg.last" if u else "hs0.g"))
            nc.vector.tensor_tensor(m, m, by_t(h_sil[u]), ALU.mult).then_inc(*steps.did("dve", f"hgo.m{u}"))

        def pe_hg(pe):
            pe_between(pe, "hg")
            wait_turned(pe, "hg", 1)
            pe_h_columns(pe, 0, 0)
            pe_h_columns(pe, 1, 2)
            pe_h_columns(pe, 2, 4)
            pe_h_columns(pe, 3, 6)
            pe.wait_ge(*after("hq0"))
            for n in range(4):
                pe_h_piece(pe, 4, n, 4)
                pe_h_level(pe, 0, n)
            pe.wait_ge(*after("hq1"))
            for n in range(4, 8):
                pe_h_piece(pe, 5, n - 4, 6)
                pe_h_level(pe, 0, n)
            pe_h_level(pe, 0, 8)
            pe.wait_ge(*after("hv0"))
            pe_h_piece(pe, 6, 0, 4)
            pe_h_level(pe, 1, 0)
            pe_h_out(pe, 0)
            for n in range(1, 4):
                pe_h_piece(pe, 6, n, 4)
                pe_h_level(pe, 1, n)
            pe.wait_ge(*after("hs0"))
            for n in range(4, 8):
                pe_h_piece(pe, 7, n - 4, 4)
                pe_h_level(pe, 1, n)
            pe_h_level(pe, 1, 8)
            pe.wait_ge(*after("hs1"))
            for t in range(NT):
                pe_turn(pe, "hgo", t, 0, 4 + t, mix, "hgo.m0")
            pe_h_out(pe, 1)
            for k in range(4):
                pe_out(pe, "hgo", k)
            for t in range(NT):
                pe_turn(pe, "hgo", t, 1, 4 + t, mix, "hgo.m1")
            pe_out_last(pe, "hgo")

        def act_hg(act):
            S = lambda n, which=(0, 1, 2, 3): split4(split_hi, act, hu(n), which=which)
            S(1, (0,))
            act_bounds(act)
            S(1, (1, 2, 3))
            S(2, (0,))
            act_h_forget(act, 0)
            S(2, (1, 2))
            act_h_decay(act, 0)
            S(2, (3,))
            S(3, (0,))
            act_h_forget(act, 1)
            S(3, (1,))
            act_h_decay(act, 1)
            act_h_q(act, 0)
            S(3, (2, 3))
            for n in range(8):
                S(4 + n // 4, (n % 4,))
                act_level(act, "h0", n, h_e)
                if n == 1:
                    act_h_q(act, 1)
                if n == 5:
                    act_h_v(act, 0)
            for n in range(8):
                S(6 + n // 4, (n % 4,))
                if n == 1:
                    act_h_v(act, 1)
                act_level(act, "h1", n, h_e)
                if n == 2:
                    act_h_square(act, 0)
                if n == 5:
                    act_h_gate(act, 0)
            act_h_gate(act, 1)
            for t in range(NT):
                act_turn(act, "hgo", t, 0, 4 + t)
            out_splits(split_hi, act, "hgo", (0, 1))
            act_h_square(act, 1)
            out_splits(split_hi, act, "hgo", (2, 3, 4, 5))
            for t in range(NT):
                act_turn(act, "hgo", t, 1, 4 + t)
            out_splits(split_hi, act, "hgo", (6, 7))
            first_pieces(split_hi, act, "ffn3", (0, 1))

        def dve_hg(dve):
            S = lambda n, which=(0, 1, 2, 3): split4(split_lo, dve, hu(n), which=which)
            S(1, (0,))
            dve_bounds(dve)
            S(1, (1, 2, 3))
            S(2, (0,))
            dve_h_forget(dve, 0)
            S(2, (1, 2))
            dve_h_decay(dve, 0)
            S(2, (3,))
            S(3, (0,))
            dve_h_forget(dve, 1)
            S(3, (1,))
            dve_h_decay(dve, 1)
            S(3, (2, 3))
            dve_h_levels(dve, 0, hu(4))
            X, u = "h1", 1
            for n, half in enumerate(ALL_LEVELS):
                dve_level_x(dve, X, n, half, hb[u], h_e, ["h0.l7", "hq1"] if n == 0 else [f"{X}.l{n - 1}"])
                split_lo(dve, hu(6) + n)
                if n >= 2:
                    dve_h_put(dve, u, n - 2)
                dve_level_l(dve, X, n, half, hq[u], hk[u], h_e, h_l[n % 2], [f"{X}.P{n - 2}"] if n >= 2 else [f"h0.P{6 + n}"])
                if n == 2:
                    dve_h_sums(dve, 0)
                if n == 3:
                    dve_h_out_norm(dve, 0)
                if n == 6:
                    dve_h_out_gate(dve, 0)
            for n in (6, 7, 8):
                dve_h_put(dve, u, n)
            for t in range(NT):
                dve_turn(dve, "hgo", t, 0, 4 + t)
            out_splits(split_lo, dve, "hgo", (0, 1))
            dve_h_sums(dve, 1)
            out_splits(split_lo, dve, "hgo", (2, 3))
            dve_h_out_norm(dve, 1)
            dve_h_out_gate(dve, 1)
            out_splits(split_lo, dve, "hgo", (4, 5))
            for t in range(NT):
                dve_turn(dve, "hgo", t, 1, 4 + t)
            out_splits(split_lo, dve, "hgo", (6, 7))
            first_pieces(split_lo, dve, "ffn3", (0, 1))

        def pool_hg(pool, gains):
            pool.wait_ge(*after("hd1.ln"))
            nc.gpsimd.memset(h_at, 0.0).then_inc(*steps.did("pool", "h0.at0"))
            pool.wait_ge(*after("h0.O"))
            nc.gpsimd.memset(h_at, 0.0).then_inc(*steps.did("pool", "h1.at0"))
            pool_h(pool, 0)
            g = gain_of(pool, "hgh")
            for u in range(2):
                a = by_t(h_sil[u])
                pool.wait_ge(*after(f"hs{u}"))
                nc.gpsimd.tensor_tensor(a, a, g[:, 512 * u:512 * u + 512].unsqueeze(1).broadcast_to([P, NT, 512]), ALU.mult)\
                    .then_inc(*steps.did("pool", "hg.last" if u else "hs0.g"))
            pool_h(pool, 1)
            next_gain(pool, gains)

        staged = arena[:, 4096:4096 + 5 * P].rearrange("p (b n) -> p b n", b=5)
        conv_m, conv_g, lb_logits, gate_bias = few.take(16), few.take(48), few.take(16), few.take(2)
        spread = {}
        SPREAD = [("q_norm", A["q_norm"][0]), ("k_norm", A["k_norm"][0]), ("gla_out_norm", A["gla_out_norm"][0]),
                  ("attn_sinks", A["attn_sinks"][0]), ("ab_m_gate_bias_2", A["ab_m_gate_bias_2"][0].rearrange("a b -> (a b)")),
                  ("ab_g_a_log_2", A["ab_g_a_log_2"][0]), ("ab_g_dt_bias_2", A["ab_g_dt_bias_2"][0])]
        for name, v in SPREAD:
            spread[name] = few.take(v.shape[0])
        gate_up = few.take(256, parts=16)
        p_rows = few.take(NT * 256).rearrange("p (t n) -> p t n", t=NT)

        def act_loads(act):
            x = A["x"][0].rearrange("(t p) d -> p t d", p=P)
            act.dma_start(h[:, 0, :], x[:, 0, :]).then_inc(x_in[0], 16)
            act.dma_start(const[:, 0:P], A["const"][:, 0:P]).then_inc(ident_in, 16)
            act.dma_start(h[:, 1, :], x[:, 1, :]).then_inc(x_in[1], 16)

        def pool_params(pool):
            loads = [(const[:, P:], A["const"][:, P:])]
            for l in range(2):
                w = A["ffn_conv_w_2"][l].rearrange("k (c n) -> (k c) n", n=P)
                loads.append((staged[0:4 * FC, 2 * l, :], w[0:4 * FC]))
                loads.append((staged[0:2 * FC, 2 * l + 1, :], w[4 * FC:6 * FC]))
                loads.append((staged[2 * FC:4 * FC, 2 * l + 1, :], A["ffn_conv_b_2"][l].rearrange("(c n) -> c n", n=P)))
            at = 0
            for v in (A["ab_conv_m_2"][0].rearrange("k (c n) -> (k c) n", n=P),
                      A["ab_conv_g_2"][0].rearrange("k (c n) -> (k c) n", n=P),
                      A["c_lb_logits_2"].rearrange("k (c n) -> (k c) n", n=P),
                      A["gla_b_gate"].rearrange("k (c n) -> (k c) n", n=P)):
                loads.append((staged[at:at + v.shape[0], 4, :], v))
                at += v.shape[0]
            for name, v in SPREAD:
                loads.append((spread[name], v.partition_broadcast(P)))
            loads.append((gate_up, A["gla_w_gate_up"][0]))
            loads.append((p_rows, A["p"][0, 0].rearrange("(t p) n -> p t n", p=P)))
            for dst, src in loads:
                pool.dma_start(dst, src).then_inc(params, 16)
            assert 16 * len(loads) == PARAMS

        PARAMS = 16 * (1 + 6 + 4 + len(SPREAD) + 2)

        def pe_params(pe):
            pe.wait_ge(params, PARAMS)
            for b in range(5):
                n = 4 * FC if b < 4 else 82
                last = nc.tensor.transpose(bank(2 + b // 4, (b % 4) * P, n), staged[0:n, b, :], ident[0:n, 0:n])
            last.then_inc(*steps.did("pe", "params.T"))

        def dve_params(dve):
            dve.wait_ge(*after("params.T"))
            for l in range(2):
                for b in range(2):
                    nc.vector.tensor_copy(taps[:, l, 2 * b:2 * b + 2, :],
                                          bank(2, (2 * l + b) * P, 4 * FC).rearrange("p (k c) -> p k c", k=2))
            at = 0
            for a, n in ((conv_m, 16), (conv_g, 48), (lb_logits, 16), (gate_bias, 2)):
                last = nc.vector.tensor_copy(a, bank(3, at, n))
                at += n
            last.then_inc(*steps.did("dve", "params"))

        STAGES = ["ffn0", "mix0", "ffn1", "ple", "ab", "ffn2", "hg", "ffn3"]
        stages = STAGES[:STAGES.index(stop) + 1] if stop else STAGES
        ENDS = dict(zip(STAGES, ["ffn0", "mix0o", "ffn1", "ple", "abo", "ffn2", "hgo", "ffn3"]))
        steps_of = list(zip(["x"] + [ENDS[st] for st in stages], stages + [None]))
        LATE = ("x", "mix0o", "ple", "abo", "hgo")
        following = dict(zip(stages, stages[1:] + [None]))

        block = ctx.enter_context(nc.Block())

        @block.sync
        def _(sp):
            for st in stages:
                if st.startswith("ffn"):
                    sp_ffn(sp, int(st[3]))
                elif st == "mix0":
                    sp_mix0(sp)
                else:
                    for part in {"ple": ("emb", "ple"), "ab": ("ab", "abo"), "hg": ("hg", "hgo")}[st]:
                        sp_proj(sp, part)
            o = out[0].rearrange("(t p) d -> p t d", p=P)
            last = ENDS[stages[-1]]
            for t, b in BANKS:
                sp.wait_ge(*after(f"{last}.h{t}{b}"))
                sp.dma_start(cut(o, t, b), cut(h, t, b)).then_inc(out_sem, 16)
            sp.wait_ge(out_sem, 64)

        @block.gpsimd
        def _(pool):
            nc.gpsimd.memset(half_power, -0.5).then_inc(*steps.did("pool", "half_power"))
            gains = iter([g[0] for g in GAINS])
            next_gain(pool, gains)
            pool.wait_ge(*after("half_power"))
            for prev, st in steps_of:
                pool_between(pool, prev, st)
                if st == "ffn0":
                    next_gain(pool, gains)
                    pool_params(pool)
                    next_gain(pool, gains)
                elif st in ("mix0", "ffn1", "ffn3"):
                    next_gain(pool, gains)
                elif st in ("ffn2", "hg"):
                    next_gain(pool, gains)
                    next_gain(pool, gains)
                if st == "mix0":
                    pool_mix0(pool)
                if st == "ple":
                    pool_ple(pool)
                    next_gain(pool, gains)
                    next_gain(pool, gains)
                if st == "ab":
                    pool_ab(pool, gains)
                if st == "hg":
                    pool_hg(pool, gains)

        @block.scalar
        def _(act):
            act_loads(act)
            first_pieces(split_hi, act, "ffn0", (0, 1))
            for prev, st in steps_of:
                act_between(act, prev, st)
                if prev in LATE:
                    first_pieces(split_hi, act, st, (2, 3))
                if st and st.startswith("ffn"):
                    act_ffn(act, int(st[3]), following[st])
                if st == "mix0":
                    act_mix0(act)
                if st == "ple":
                    act_ple(act)
                if st == "ab":
                    act_ab(act)
                if st == "hg":
                    act_hg(act)

        @block.vector
        def _(dve):
            nc.vector.memset(zero_r[:, :].bitcast(F32), 0.0).then_inc(*steps.did("dve", "zero_r"))
            nc.vector.memset(ones, 1.0).then_inc(*steps.did("dve", "ones"))
            first_pieces(split_lo, dve, "ffn0", (0, 1))
            for prev, st in steps_of:
                dve_between(dve, prev, st)
                if prev in LATE:
                    first_pieces(split_lo, dve, st, (2, 3))
                if st and st.startswith("ffn"):
                    dve_ffn(dve, int(st[3]), following[st])
                if st == "mix0":
                    dve_mix0(dve)
                if st == "ple":
                    dve_ple(dve)
                if st == "ab":
                    dve_ab(dve)
                if st == "hg":
                    dve_hg(dve)

        @block.tensor
        def _(pe):
            pe.wait_ge(ident_in, 16)
            pe.wait_ge(*after("ones"))
            for st in stages:
                if st.startswith("ffn"):
                    pe_ffn(pe, int(st[3]))
                if st == "mix0":
                    pe_mix0(pe)
                if st == "ple":
                    pe_ple(pe)
                if st == "ab":
                    pe_ab(pe)
                if st == "hg":
                    pe_hg(pe)

        return steps.made


def kernel(**inputs):
    import numpy as _np
    import concourse.bacc as _bacc
    from concourse import mybir as _mybir
    from concourse.bass_utils import run_bass_kernel_spmd as _run

    arrays = {f"in_{name}": _np.ascontiguousarray(a) for name, a in inputs.items()}
    arrays["in_const"] = shape_constants()[1]

    def program(numbered):
        nc = _bacc.Bacc("TRN2", target_bir_lowering=False, num_devices=1)
        A = {name[3:]: nc.dram_tensor(name, a.shape, _mybir.dt.from_np(a.dtype), kind="ExternalInput").ap()
             for name, a in arrays.items()}
        out = nc.dram_tensor("out_0", (1, SEQ, D), F32, kind="ExternalOutput").ap()
        return nc, build(nc, A, out, numbered)

    _, numbering = program(None)
    nc, _ = program(numbering)
    r = _run(nc, [arrays], core_ids=[0])
    return r.results[0]["out_0"]
```

```python
from contextlib import ExitStack

import numpy as np
import concourse.bass as bass
from concourse import mybir

F32 = mybir.dt.float32
F32R = mybir.dt.float32r
U32 = mybir.dt.uint32
ALU = mybir.AluOpType
ACT = mybir.ActivationFunctionType
AX_X = mybir.AxisListType.X

P = 128
SEQ = 256
NT = SEQ // P
D = 1024
KC = D // P
F = 2816
FC = F // P
GROUP = 256
GROUPS = F // GROUP
BANK = 512
RING = 6
SLOT = 2048
PIECE = SLOT // 2
EPS = 1e-6
BIG = 1.0e30
PARTS = [("ffn0", 3 * GROUPS), ("mix0", 10), ("mix0o", 4), ("ffn1", 3 * GROUPS), ("emb", 1), ("ple", 4),
         ("ab", 15), ("abo", 4), ("ffn2", 3 * GROUPS), ("hg", 16), ("hgo", 4), ("ffn3", 3 * GROUPS)]
LEVELS = [64, 32, 16, 8, 4, 2, 1]

MQ, MV, MO, MI, DQ, DK, DV, DG, DA = 0, 512, 1024, 1536, 1544, 2056, 2568, 3080, 3592
AQ, AK, AV, GQ, GK, GV, GR, GO = 0, 512, 640, 768, 1024, 1280, 1792, 1808


def shape_constants():
    j = np.arange(P)[:, None]
    i = np.arange(P)[None, :]
    parts = {"ident": (j == i), "upper": (j <= i)}
    for h in LEVELS:
        parts[f"level{h}"] = (j // (2 * h) == i // (2 * h)) & (j % (2 * h) < h) & (i % (2 * h) >= h)
    parts["prev"] = np.where(i > j, 0.0, -BIG)
    parts["own"] = np.where(i <= j, 0.0, -BIG)
    freq = np.float32(10000.0) ** (-np.arange(0, 64, 2, dtype=np.float32) / np.float32(64))
    ang = (np.arange(SEQ, dtype=np.float32)[:, None] * freq[None, :]).reshape(NT, P, 32)
    for name, f in (("cos", np.cos), ("sin", np.sin)):
        for t in range(NT):
            parts[f"{name}{t}"] = f(ang[t].astype(np.float64))
    at, cols, n = {}, [], 0
    for name, a in parts.items():
        at[name] = n
        n += a.shape[1]
        cols.append(a.astype(np.float32))
    return at, np.ascontiguousarray(np.concatenate(cols, axis=1))


class Steps:

    def __init__(self, nc, ctx, numbered):
        self.nc, self.ctx, self.numbered = nc, ctx, numbered
        self.sems, self.count, self.made = {}, {}, {}

    def sem(self, name):
        if name not in self.sems:
            self.sems[name] = self.ctx.enter_context(self.nc.semaphore(name))
        return self.sems[name]

    def did(self, engine, name):
        assert name not in self.made, name
        self.count[engine] = self.count.get(engine, 0) + 1
        self.made[name] = (f"{engine}_done", self.count[engine])
        return self.sem(f"{engine}_done"), 1

    def after(self, name):
        if self.numbered is None:
            return self.sem("pe_done"), 1
        s, n = self.numbered[name]
        return self.sem(s), n


def build(nc, A, out, numbered, stop=None):
    const_at, _ = shape_constants()
    ctx = ExitStack()
    with ctx:
        steps = Steps(nc, ctx, numbered)
        after = steps.after

        def sb(name, shape, dt=F32):
            return ctx.enter_context(nc.sbuf_tensor(name, shape, dt))

        def sem(name):
            return ctx.enter_context(nc.semaphore(name))

        raw = sb("raw", [P, RING, SLOT])
        whi = sb("whi", [P, RING, PIECE], F32R)
        wlo = sb("wlo", [P, RING, PIECE], F32R)
        xh = sb("xh", [P, KC, SEQ], F32R)
        xl = sb("xl", [P, KC, SEQ], F32R)
        hidh = sb("hidh", [P, 2, 2, SEQ], F32R)
        hidl = sb("hidl", [P, 2, 2, SEQ], F32R)
        h = sb("h", [P, NT, D])
        gain = sb("gain", [P, 2, D])
        const = sb("const", [P, A["const"].shape[1]])
        small = sb("small", [P, 1792])
        zero_r = sb("zero_r", [P, P], F32R)
        arena = sb("arena", [P, 13824])
        psum = ctx.enter_context(nc.psum_tensor("psum", [P, 8, BANK], F32))

        class Columns:
            def __init__(self, tile):
                self.tile, self.n = tile, 0

            def take(self, n, parts=P):
                a = self.tile[0:parts, self.n:self.n + n]
                self.n += n
                assert self.n <= self.tile.shape[1], self.n
                return a

        few = Columns(small)

        def bank(b, a=0, n=BANK):
            return psum[:, b, a:a + n]

        def cst(name, n=P):
            return const[:, const_at[name]:const_at[name] + n]

        ident = cst("ident")

        sg = arena[:, 0:1024].rearrange("p (a c t) -> p a c t", a=2, c=2)
        hp = arena[:, 1024:2048].rearrange("p (a c t) -> p a c t", a=2, c=2)
        cg = arena[:, 2048:4096].rearrange("p (a g c t) -> p a g c t", a=2, g=2, c=2)
        nrm = arena[:, 11776:13824].rearrange("p (t d) -> p t d", t=NT)
        emb = arena[:, 0:2048].rearrange("p (t d) -> p t d", t=NT)
        sgm = arena[:, 2048:4096].rearrange("p (t d) -> p t d", t=NT)
        taps = sb("taps", [P, 2, 4, 2 * FC])

        loaded = [sem(f"loaded{n}") for n in range(RING)]
        hi_done = sem("hi_done")
        lo_done = sem("lo_done")
        used = sem("used")
        sg_ready = sem("sg_ready")
        hp_ready = sem("hp_ready")
        hid_hi = sem("hid_hi")
        hid_lo = sem("hid_lo")
        conv_mid = sem("conv_mid")
        conv_one = sem("conv_one")
        conv_all = sem("conv_all")
        params = sem("params")
        x_in = [sem(f"x_in{t}") for t in range(NT)]
        ident_in = sem("ident_in")
        gains_in = [sem(f"gain_in{n}") for n in range(2)]
        out_sem = sem("stored")

        ng = A["norm_gains_2"]
        GAINS = [("ffn0", [A["ffn1_norm"][0]], "ffn0.w11"), ("mix0", [A["mix_norm"][0]], "mix0.w11"),
                 ("ffn1", [A["ffn2_norm"][0]], "ffn1.w11"), ("emb", [A["ple_norm"][0]], "emb.e1"),
                 ("ple", [A["ple_gate_norm"][0]], "ple.w11"),
                 ("ab", [ng[0, 0]], "ab.w11"), ("abh", [A["ab_m_norm_2"][0], A["ab_g_norm_2"][0]], "ab.last"),
                 ("abp", [ng[0, 1]], "abo.p11"),
                 ("ffn2", [ng[0, 2]], "ffn2.w11"), ("ffn2p", [ng[0, 3]], "ffn2.p11"),
                 ("hg", [ng[1, 0]], "hg.w11"), ("hgh", [A["c_norm_2"][0]], "hg.last"), ("hgp", [ng[1, 1]], "hgo.p11"),
                 ("ffn3", [ng[1, 2]], "ffn3.w11"), ("ffn3p", [ng[1, 3]], "ffn3.p11")]
        gain_at, counts = {}, [0, 0]
        for n, (name, parts, last_use) in enumerate(GAINS):
            counts[n % 2] += 16 * len(parts)
            gain_at[name] = (n, counts[n % 2])

        def pool_gain(pool, name):
            n, _ = gain_at[name]
            if n >= 2:
                pool.wait_ge(*after(GAINS[n - 2][2]))
            at = 0
            for v in GAINS[n][1]:
                pool.dma_start(gain[:, n % 2, at:at + v.shape[0]], v.partition_broadcast(P)).then_inc(gains_in[n % 2], 16)
                at += v.shape[0]

        def next_gain(pool, gains):
            name = next(gains, None)
            if name:
                pool_gain(pool, name)

        def gain_of(dve, name):
            n, value = gain_at[name]
            dve.wait_ge(gains_in[n % 2], value)
            return gain[:, n % 2, :]

        SWIGLU = [(A["ffn1_w_gate"][0], A["ffn1_w_up"][0], A["ffn1_w_down"][0]),
                  (A["ffn2_w_gate"][0], A["ffn2_w_up"][0], A["ffn2_w_down"][0])]
        CONVFF = [(A["ffn_w_up_2"][l][:, 0:F], A["ffn_w_up_2"][l][:, F:2 * F], A["ffn_w_down_2"][l]) for l in range(2)]
        FFN = SWIGLU + CONVFF

        first_slot, total_slots = {}, 0
        for part, slots in PARTS:
            first_slot[part] = total_slots
            total_slots += slots

        def sp_slot(sp, s, i, shape, parts):
            if not (isinstance(i, int) and s + RING * i < RING):
                sp.wait_ge(lo_done, 2 * (s - RING) + 2 + 2 * RING * i)
            a, b = shape
            view = raw[:, s % RING, 0:a * b].rearrange("p (a b) -> p a b", a=a)
            for where, src in parts:
                dst = view[where] if isinstance(where, tuple) else view[:, where, :]
                sp.dma_start(dst, src).then_inc(loaded[s % RING], 16)

        def sp_gate_up(sp, s, i, n, g):
            wg, wu, _ = FFN[n]
            for k in range(2):
                sp_slot(sp, s + k, i, (4, 512), [
                    ((slice(None), slice(None), slice(256 * j, 256 * j + 256)),
                     w.rearrange("(k p) n -> p k n", p=P)[:, 4 * k:4 * k + 4, bass.ds(g * GROUP, GROUP)])
                    for j, w in enumerate((wg, wu))])

        def sp_down(sp, s, i, n, g):
            wd = FFN[n][2].rearrange("(f p) n -> p f n", p=P)
            sp_slot(sp, s, i, (2, D), [(slice(c, c + 1), wd[:, bass.ds(g * 2 + c, 1), :]) for c in range(2)])

        def sp_ffn(sp, n):
            s = first_slot[f"ffn{n}"] + 2
            sp_gate_up(sp, s - 2, 0, n, 0)

            def body(i):
                for half in range(2):
                    sp_gate_up(sp, s + 3 * half, i, n, i * 2 + half + 1)
                    sp_down(sp, s + 3 * half + 2, i, n, i * 2 + half)
            ffn_loop(sp, body)
            s += 3 * (GROUPS - 3)
            for m in (0, 1):
                sp_gate_up(sp, s + 2 * m, 0, n, GROUPS - 2 + m)
            for m in range(3):
                sp_down(sp, s + 4 + m, 0, n, GROUPS - 3 + m)

        def ffn_loop(eng, body):
            body(0)
            with eng.Fori(1, GROUPS // 2 - 1) as i:
                body(i)

        def piece_of(p, shape):
            a, b = shape[0] // 2, shape[1]
            r = raw[:, (p // 2) % RING, (p % 2) * a * b:(p % 2 + 1) * a * b]
            return r, whi[:, p % RING, 0:a * b], wlo[:, p % RING, 0:a * b]

        def split_hi(act, p, shape=(4, 512), i=0):
            if p % 2 == 0:
                act.wait_ge(loaded[(p // 2) % RING], 32 * (p // 2 // RING + 1) + 32 * i)
            if not (isinstance(i, int) and p + 2 * RING * i < RING):
                act.wait_ge(used, p - RING + 1 + 2 * RING * i)
            r, hi, _ = piece_of(p, shape)
            nc.scalar.activation(hi, r, ACT.Copy).then_inc(hi_done, 1)

        def split_lo(dve, p, shape=(4, 512), i=0):
            dve.wait_ge(hi_done, p + 1 + 2 * RING * i)
            r, hi, lo = piece_of(p, shape)
            nc.vector.tensor_tensor(lo, r, hi.bitcast(F32), ALU.subtract).then_inc(lo_done, 1)

        def pool_split_lo(pool, p, shape=(4, 512)):
            pool.wait_ge(lo_done, p)
            pool.wait_ge(hi_done, p + 1)
            r, hi, lo = piece_of(p, shape)
            nc.gpsimd.tensor_tensor(lo, r, hi.bitcast(F32), ALU.subtract).then_inc(lo_done, 1)

        def weights(p, a, b):
            return (whi[:, p % RING, 0:a * b].rearrange("p (a b) -> p a b", a=a),
                    wlo[:, p % RING, 0:a * b].rearrange("p (a b) -> p a b", a=a))

        def three(pe_out, sh, sl, mh, ml, start, stop):
            nc.tensor.matmul(pe_out, sh, mh, start=start, stop=False, skip_group_check=True)
            nc.tensor.matmul(pe_out, sh, ml, start=False, stop=False, skip_group_check=True)
            return nc.tensor.matmul(pe_out, sl, mh, start=False, stop=stop, skip_group_check=True)

        def pe_turn(pe, X, t, b, to, tile, ready):
            pe.wait_ge(*after(ready))
            for c in range(4):
                last = nc.tensor.transpose(bank(to, c * P, P), tile[:, t, b * BANK + c * P:b * BANK + c * P + P], ident)
            last.then_inc(*steps.did("pe", f"{X}.T{t}{b}"))

        def turned(t, b, at):
            return (bank(at).rearrange("p (c t) -> p c t", c=4),
                    xh[:, 4 * b:4 * b + 4, t * P:t * P + P], xl[:, 4 * b:4 * b + 4, t * P:t * P + P])

        def act_turn(act, X, t, b, at):
            src, hi, _ = turned(t, b, at)
            act.wait_ge(*after(f"{X}.T{t}{b}"))
            nc.scalar.activation(hi, src, ACT.Copy).then_inc(*steps.did("act", f"{X}.xh{t}{b}"))

        def dve_turn(dve, X, t, b, at):
            src, hi, lo = turned(t, b, at)
            dve.wait_ge(*after(f"{X}.xh{t}{b}"))
            nc.vector.tensor_tensor(lo, src, hi.bitcast(F32), ALU.subtract).then_inc(*steps.did("dve", f"{X}.xl{t}{b}"))

        half_power = few.take(64)

        def pool_rstd(pool, name, total, n, count, scratch):
            nc.gpsimd.tensor_scalar(scratch, total, 1.0 / count, EPS, ALU.mult, ALU.add)\
                .then_inc(*steps.did("pool", f"{name}.mean"))
            pool.wait_ge(*after(f"{name}.mean"))
            nc.gpsimd.tensor_tensor(scratch, scratch, half_power[:, 0:n], ALU.pow)\
                .then_inc(*steps.did("pool", name))

        ADD = {"ffn0": 0.5, "mix0o": 1.0, "ffn1": 0.5}
        POST = {"abo": "abp", "ffn2": "ffn2p", "hgo": "hgp", "ffn3": "ffn3p"}
        TILE_FIRST = ("mix0", "ple", "ab")
        BANKS = [(t, b) for t in range(NT) for b in range(2)]
        sums = {}

        def row_sums(X):
            if X not in sums:
                sums[X] = (few.take(4), few.take(NT), few.take(NT))
            return sums[X]

        def cut(tile, t, b):
            return tile[:, t, b * BANK:b * BANK + BANK]

        def product_ready(prev, t, b):
            if (t, b) == (1, 1):
                return used, 2 * (first_slot[prev] + dict(PARTS)[prev])
            return after(f"{prev}.acc{t}{b}")

        def act_squares(act, src, total, t, b, done):
            nc.scalar.activation(cut(nrm, t, b), src, ACT.Square, accum_out=total[:, 2 * t + b:2 * t + b + 1])\
                .then_inc(*steps.did("act", done))

        def act_between(act, prev, X):
            def product_squares(t, b):
                if prev in POST:
                    act.wait_ge(*product_ready(prev, t, b))
                    act_squares(act, bank(2 * t + b), row_sums(prev)[0], t, b, f"{prev}.ps{t}{b}")
            for t, b in BANKS[:3]:
                product_squares(t, b)
            if prev == "ple":
                for t, b in BANKS:
                    act.wait_ge(*product_ready(prev, t, b))
                    nc.scalar.activation(cut(sgm, t, b), bank(2 * t + b), ACT.Sigmoid).then_inc(*steps.did("act", f"ple.g{t}{b}"))
            if X is None:
                product_squares(1, 1)
                return
            total, _, r = row_sums(X)

            def squares(t):
                for b in range(2):
                    wait_h(act, prev, t, b)
                    act_squares(act, cut(h, t, b), total, t, b, f"{X}.ss{t}{b}")

            def scale(t, b):
                act.wait_ge(*after(f"{X}.r{t}"))
                act.wait_ge(*after(f"{X}.w{t}{b}"))
                nc.scalar.activation(cut(nrm, t, b), cut(nrm, t, b), ACT.Identity, scale=r[:, t:t + 1])\
                    .then_inc(*steps.did("act", f"{X}.n{t}{b}"))
            product_squares(1, 1)
            squares(0)
            scale(0, 0)
            scale(0, 1)
            squares(1)
            act_turn(act, X, 0, 0, 0)
            act_turn(act, X, 0, 1, 1)
            more_pieces(split_hi, act, X)
            for b in range(2):
                scale(1, b)
            for b in range(2):
                act_turn(act, X, 1, b, 2 + b)

        def wait_h(eng, prev, t, b):
            if prev == "x":
                if b == 0:
                    eng.wait_ge(x_in[t], 16)
            else:
                eng.wait_ge(*after(f"{prev}.h{t}{b}"))

        def pool_between(pool, prev, X):
            for part, ss in ((prev, "ps"), (X, "ss")):
                if (ss == "ps" and prev not in POST) or part is None:
                    continue
                total, mean, r = row_sums(part)
                for t in range(NT):
                    m = mean[:, t:t + 1]
                    pool.wait_ge(*after(f"{part}.{ss}{t}0"))
                    nc.gpsimd.tensor_scalar(m, total[:, 2 * t:2 * t + 1], 1.0 / D, EPS, ALU.mult, ALU.add)\
                        .then_inc(*steps.did("pool", f"{part}.{ss}m{t}"))
                    pool.wait_ge(*after(f"{part}.{ss}{t}1"))
                    pool.wait_ge(*after(f"{part}.{ss}m{t}"))
                    nc.gpsimd.tensor_scalar(m, total[:, 2 * t + 1:2 * t + 2], 1.0 / D, m, ALU.mult, ALU.add)\
                        .then_inc(*steps.did("pool", f"{part}.{ss}n{t}"))
                    pool.wait_ge(*after(f"{part}.{ss}n{t}"))
                    nc.gpsimd.tensor_tensor(r[:, t:t + 1], m, half_power[:, 0:1], ALU.pow)\
                        .then_inc(*steps.did("pool", f"{part}.{'pr' if ss == 'ps' else 'r'}{t}"))

        def dve_between(dve, prev, X):
            def product_gain(t, b):
                g = gain_of(dve, POST[prev])
                dve.wait_ge(*after(f"{prev}.ps{t}{b}"))
                nc.vector.tensor_tensor(cut(nrm, t, b), bank(2 * t + b), g[:, b * BANK:b * BANK + BANK], ALU.mult)\
                    .then_inc(*steps.did("dve", f"{prev}.p{t}{b}"))

            def gated(t, b):
                dve.wait_ge(*after(f"ple.g{t}{b}"))
                nc.vector.tensor_tensor(cut(sgm, t, b), cut(sgm, t, b), cut(emb, t, b), ALU.mult).then_inc(*steps.did("dve", f"ple.m{t}{b}"))

            def prepare(t):
                for b in range(2):
                    if prev in POST:
                        product_gain(t, b)
                    if prev == "ple":
                        gated(t, b)

            def add(t):
                for b in range(2):
                    hh = cut(h, t, b)
                    if prev in ADD:
                        dve.wait_ge(*product_ready(prev, t, b))
                        last = nc.vector.scalar_tensor_tensor(hh, bank(2 * t + b), ADD[prev], hh, ALU.mult, ALU.add)
                    elif prev in POST:
                        dve.wait_ge(*after(f"{prev}.pr{t}"))
                        dve.wait_ge(*after(f"{prev}.p{t}{b}"))
                        last = nc.vector.scalar_tensor_tensor(hh, cut(nrm, t, b), row_sums(prev)[2][:, t:t + 1], hh, ALU.mult, ALU.add)
                    elif prev == "ple":
                        dve.wait_ge(*after(f"ple.m{t}{b}"))
                        last = nc.vector.tensor_tensor(hh, hh, cut(sgm, t, b), ALU.add)
                    else:
                        continue
                    last.then_inc(*steps.did("dve", f"{prev}.h{t}{b}"))

            def gained(t, b):
                g = gain_of(dve, X)
                dve.wait_ge(*after(f"{X}.ss{t}{b}"))
                nc.vector.tensor_tensor(cut(nrm, t, b), cut(h, t, b), g[:, b * BANK:b * BANK + BANK], ALU.mult)\
                    .then_inc(*steps.did("dve", f"{X}.w{t}{b}"))
            prepare(0)
            add(0)
            if X is None:
                prepare(1)
                add(1)
                return
            if prev == "x":
                gained(0, 0)
                gained(0, 1)
                gained(1, 0)
                gained(1, 1)
                for t, b in BANKS:
                    dve_turn(dve, X, t, b, 2 * t + b)
                return
            if prev in POST or prev == "ple":
                prepare(1)
            gained(0, 0)
            gained(0, 1)
            add(1)
            if X in TILE_FIRST:
                dve_turn(dve, X, 0, 0, 0)
                dve_turn(dve, X, 0, 1, 1)
            gained(1, 0)
            gained(1, 1)
            if X not in TILE_FIRST:
                dve_turn(dve, X, 0, 0, 0)
                dve_turn(dve, X, 0, 1, 1)
            more_pieces(split_lo, dve, X)
            dve_turn(dve, X, 1, 0, 2)
            dve_turn(dve, X, 1, 1, 3)

        def pe_between(pe, X, piece=None):
            for b in range(2):
                pe_turn(pe, X, 0, b, b, nrm, f"{X}.n0{b}")
            if piece:
                pe.wait_ge(*after(f"{X}.xl01"))
                for k in range(3):
                    piece(0, k)
            for b in range(2):
                pe_turn(pe, X, 1, b, 2 + b, nrm, f"{X}.n1{b}")
            if piece:
                piece(0, 3)
                wait_turned(pe, X, 1)
                for k in range(4):
                    piece(1, k)

        def wait_turned(pe, X, b):
            pe.wait_ge(*after(f"{X}.xl1{b}"))

        def pe_piece(pe, p, hi, lo, start, i=0, tile=None):
            pe.wait_ge(lo_done, p + 1 + 2 * RING * i)
            wh, wl = weights(p, 1, D)
            for t, b in BANKS:
                if tile in (None, t):
                    tok, col = slice(t * P, t * P + P), slice(b * BANK, b * BANK + BANK)
                    last = three(bank(2 * t + b), hi[:, tok], lo[:, tok], wh[:, 0, col], wl[:, 0, col], start=start, stop=False)
            if tile != 0:
                last.then_inc(used, 1)

        def pe_last_pieces(pe, X, p, parts, start=False):
            for t, b in BANKS:
                tok, col = slice(t * P, t * P + P), slice(b * BANK, b * BANK + BANK)
                for n, (hi, lo) in enumerate(parts):
                    if (t, b) == (0, 0):
                        pe.wait_ge(lo_done, p + n + 1)
                    wh, wl = weights(p + n, 1, D)
                    last = three(bank(2 * t + b), hi[:, tok], lo[:, tok], wh[:, 0, col], wl[:, 0, col],
                                 start=(start and n == 0), stop=(n == len(parts) - 1))
                    if (t, b) == (1, 1):
                        last.then_inc(used, 1)
                if (t, b) != (1, 1):
                    last.then_inc(*steps.did("pe", f"{X}.acc{t}{b}"))

        def pe_out(pe, part, k, tile=None):
            if k == 0 and tile is None:
                wait_turned(pe, part, 0)
            pe_piece(pe, 2 * first_slot[part] + k, xh[:, k, :], xl[:, k, :], k == 0, tile=tile)

        def pe_out_last(pe, part):
            wait_turned(pe, part, 1)
            first = 6 if part == "ple" else 4
            for k in range(4, first):
                pe_out(pe, part, k)
            pe_last_pieces(pe, part, 2 * first_slot[part] + first, [(xh[:, k, :], xl[:, k, :]) for k in range(first, 8)])

        def pe_unit(pe, p, rows=(), columns=(), shape=(4, 512), which=(0, 1, 2, 3), tile=None):
            for k in which:
                pe.wait_ge(lo_done, p + k + 1)
                wh, wl = weights(p + k, shape[0] // 2, shape[1])
                for kk in range(2):
                    kc = 2 * k + kk
                    for c0, c1, outs, starts in rows:
                        for t in range(NT) if tile is None else (tile,):
                            tok = slice(t * P, t * P + P)
                            last = three(outs[t], xh[:, kc, tok], xl[:, kc, tok], wh[:, kk, c0:c1], wl[:, kk, c0:c1],
                                         start=(kc == 0 and starts[t]), stop=(kc == KC - 1))
                    for c0, o, starts in columns:
                        last = three(o, wh[:, kk, c0:c0 + P], wl[:, kk, c0:c0 + P], xh[:, kc, :], xl[:, kc, :],
                                     start=(kc == 0 and starts), stop=(kc == KC - 1))
                if tile != 0:
                    last.then_inc(used, 1)

        def out_splits(split, eng, part, which):
            for k in which:
                split(eng, 2 * first_slot[part] + k, (2, D))

        def splits(split, eng, p, shape=(4, 512), which=(0, 1, 2, 3)):
            for k in which:
                split(eng, p + k, shape)

        def pe_gate_up(pe, n, g, q, p, i):
            if not isinstance(g, int) or n * GROUPS + g >= 2:
                pe.wait_ge(hid_lo, g + n * GROUPS - 1)
            for k in range(4):
                if isinstance(g, int) and g == 0 and k % 2 == 0:
                    wait_turned(pe, f"ffn{n}", k // 2)
                pe.wait_ge(lo_done, p + k + 1 + 2 * RING * i)
                wh, wl = weights(p + k, 2, 512)
                for kk in range(2):
                    kc = 2 * k + kk
                    for c in range(2):
                        for j in range(2):
                            col = slice(256 * j + 128 * c, 256 * j + 128 * c + 128)
                            last = three(psum[:, 4 + 2 * q + c, 256 * j:256 * j + 256], wh[:, kk, col],
                                         wl[:, kk, col], xh[:, kc, :], xl[:, kc, :],
                                         start=(kc == 0 and j == 0), stop=(kc == KC - 1))
                last.then_inc(used, 1)

        def pe_down(pe, n, g, q, p, i):
            pe.wait_ge(hid_lo, g + n * GROUPS + 1)
            for c in range(2):
                pe_piece(pe, p + c, hidh[:, q, c, :], hidl[:, q, c, :], False, i)

        def pe_ffn(pe, n):
            X = f"ffn{n}"
            p = 2 * first_slot[X]
            pe_between(pe, X)
            pe_gate_up(pe, n, 0, 0, p, 0)
            for b in range(4):
                nc.tensor.matmul(bank(b), zero_r[:, :], xh[:, 0:2, :], start=True, stop=True, skip_group_check=True)

            def body(i):
                for half in range(2):
                    q = p + 4 + 6 * half
                    pe_gate_up(pe, n, i * 2 + half + 1, (half + 1) % 2, q, i)
                    pe_down(pe, n, i * 2 + half, half, q + 4, i)
            ffn_loop(pe, body)
            b = tail_at(p)
            for m in range(2):
                pe_gate_up(pe, n, GROUPS - 2 + m, 1 - m, b + 4 * m, 0)
            for m in range(2):
                pe_down(pe, n, GROUPS - 3 + m, m, b + 8 + 2 * m, 0)
            if n == 1:
                pe_turn_p(pe)
            pe.wait_ge(hid_lo, n * GROUPS + GROUPS)
            pe_last_pieces(pe, X, b + 12, [(hidh[:, 0, c, :], hidl[:, 0, c, :]) for c in range(2)])

        def tail_at(p):
            return p + 4 + 6 * (GROUPS - 3)

        def act_hidden(act, n, g, q, p, i):
            G0 = n * GROUPS
            first = isinstance(g, int) and g == 0
            act.wait_ge(used, p + 2 * RING * i - (0 if first else 2))
            if n < 2:
                nc.scalar.activation(sg[:, q], psum[:, 4 + 2 * q:6 + 2 * q, 0:256], ACT.Silu).then_inc(sg_ready, 1)
                return
            for j in range(2):
                for c in range(2):
                    f = g * 2 + (FC * j + c)
                    last = nc.scalar.activation(cg[:, q, j, c, :], psum[:, 4 + 2 * q + c, 256 * j:256 * j + 256],
                                                ACT.Identity, scale=tap(n, 2, f), bias=tap(n, 3, f))
            last.then_inc(conv_mid, 1)
            act.wait_ge(conv_all, g + (G0 - 2 * GROUPS) + 1)
            nc.scalar.activation(sg[:, q], cg[:, q, 0], ACT.Silu).then_inc(sg_ready, 1)

        def tap(n, k, f):
            return taps[:, n - 2, k, bass.ds(f, 1)]

        def dve_hidden(dve, n, g, q, i):
            G0 = n * GROUPS
            if n < 2:
                dve.wait_ge(sg_ready, g + G0 + 1)
                nc.vector.tensor_tensor(hp[:, q], psum[:, 4 + 2 * q:6 + 2 * q, 256:512], sg[:, q], ALU.mult)\
                    .then_inc(hp_ready, 1)
                return
            dve.wait_ge(conv_mid, g + (G0 - 2 * GROUPS) + 1)
            for k, done in ((1, conv_one), (0, conv_all)):
                if k == 0:
                    dve.wait_ge(conv_one, g + (G0 - 2 * GROUPS) + 1)
                lag = 2 - k
                for j in range(2):
                    for c in range(2):
                        y = cg[:, q, j, c, lag:SEQ]
                        last = nc.vector.scalar_tensor_tensor(
                            y, psum[:, 4 + 2 * q + c, 256 * j:256 * j + SEQ - lag], tap(n, k, g * 2 + (FC * j + c)), y,
                            ALU.mult, ALU.add)
                last.then_inc(done, 1)
            dve.wait_ge(sg_ready, g + G0 + 1)
            nc.vector.tensor_tensor(hp[:, q], cg[:, q, 1], sg[:, q], ALU.mult).then_inc(hp_ready, 1)

        def act_hid_hi(act, n, g, q, p, i):
            act.wait_ge(hp_ready, g + n * GROUPS + 1)
            if not (isinstance(g, int) and g < 2):
                act.wait_ge(used, p - 6 + 2 * RING * i)
            nc.scalar.activation(hidh[:, q], hp[:, q], ACT.Copy).then_inc(hid_hi, 1)

        def dve_hid_lo(dve, n, g, q):
            dve.wait_ge(hid_hi, g + n * GROUPS + 1)
            nc.vector.tensor_tensor(hidl[:, q], hp[:, q], hidh[:, q].bitcast(F32), ALU.subtract).then_inc(hid_lo, 1)

        def act_ffn(act, n, following):
            p = 2 * first_slot[f"ffn{n}"]

            def body(i):
                for half in range(2):
                    q, g = p + 4 + 6 * half, i * 2 + half
                    early = 4 if isinstance(g, int) and g == 0 else 2
                    for k in range(early):
                        split_hi(act, q + k, i=i)
                    act_hidden(act, n, g, half, q, i)
                    for k in range(early, 4):
                        split_hi(act, q + k, i=i)
                    act_hid_hi(act, n, g, half, q, i)
                    for k in range(4, 6):
                        split_hi(act, q + k, shape=(2, D), i=i)
            ffn_loop(act, body)
            b, g = tail_at(p), GROUPS - 1
            tail_splits = lambda *which: [split_hi(act, b + k) for k in which]
            tail_splits(0, 1)
            act_hidden(act, n, g - 2, 0, b, 0)
            tail_splits(2, 3)
            act_hid_hi(act, n, g - 2, 0, b, 0)
            tail_splits(4, 5, 6, 7)
            act_hidden(act, n, g - 1, 1, b + 6, 0)
            act_hid_hi(act, n, g - 1, 1, b + 6, 0)
            tail_splits(8, 9, 10, 11, 12)
            act_hidden(act, n, g, 0, b + 10, 0)
            tail_splits(13)
            act_hid_hi(act, n, g, 0, b + 16, 0)
            first_pieces(split_hi, act, following, (0, 1))
            if n == 1:
                act_turn_p(act)
            first_pieces(split_hi, act, following, (2,) if n == 2 else (2, 3))

        def dve_ffn(dve, n, following):
            p = 2 * first_slot[f"ffn{n}"]

            def body(i):
                for half in range(2):
                    q, g = p + 4 + 6 * half, i * 2 + half
                    early = 4 if isinstance(g, int) and g == 0 else 2
                    for k in range(early):
                        split_lo(dve, q + k, i=i)
                    dve_hidden(dve, n, g, half, i)
                    for k in range(early, 4):
                        split_lo(dve, q + k, i=i)
                    dve_hid_lo(dve, n, g, half)
                    for k in range(4, 6):
                        split_lo(dve, q + k, shape=(2, D), i=i)
            ffn_loop(dve, body)
            b, g = tail_at(p), GROUPS - 1
            tail_splits = lambda *which: [split_lo(dve, b + k) for k in which]
            tail_splits(0, 1)
            dve_hidden(dve, n, g - 2, 0, 0)
            tail_splits(2, 3)
            dve_hid_lo(dve, n, g - 2, 0)
            tail_splits(4, 5, 6, 7)
            dve_hidden(dve, n, g - 1, 1, 0)
            dve_hid_lo(dve, n, g - 1, 1)
            tail_splits(8, 9, 10, 11, 12)
            dve_hidden(dve, n, g, 0, 0)
            tail_splits(13)
            dve_hid_lo(dve, n, g, 0)
            first_pieces(split_lo, dve, following, (0, 1))
            if n == 1:
                dve_turn_p(dve)
            first_pieces(split_lo, dve, following, (2,) if n == 2 else (2, 3))

        def rows(a):
            return a.rearrange("p (b n) -> p b n", b=2)

        def more_pieces(split, eng, st):
            if st in ("ple", "ab"):
                first_pieces(split, eng, st, (4, 5))

        def first_pieces(split, eng, st, which):
            for k in which if st in stages else ():
                if st in ("ple", "ab"):
                    first, shape = (2 * first_slot["emb"], (2, D)) if st == "ple" else (2 * first_slot["ab"], (8, 16))
                    split(eng, first + k, shape if k < 2 else (4, 512) if st == "ab" else (2, D))
                else:
                    split(eng, 2 * first_slot[st] + k)

        ALL = slice(None)

        def unit(w, *cols):
            wv = w.rearrange("(k p) n -> p k n", p=P)
            width = sum(b - a for a, b in cols)
            if len(cols) == 1:
                a, b = cols[0]
                return [((4, width), [(slice(2 * m, 2 * m + 2), wv[:, 4 * k + 2 * m:4 * k + 2 * m + 2, a:b])
                                      for m in range(2)]) for k in range(2)]
            (a, b), (c, d) = cols
            return [((4, width), [((ALL, ALL, slice(0, b - a)), wv[:, 4 * k:4 * k + 4, a:b]),
                                  ((ALL, ALL, slice(b - a, width)), wv[:, 4 * k:4 * k + 4, c:d])]) for k in range(2)]

        def wide(w):
            wv = w.rearrange("(k p) n -> p k n", p=P)
            return [[((2, D), [(slice(c, c + 1), wv[:, k + c:k + c + 1, :]) for c in range(2)])] for k in range(0, wv.shape[1], 2)]

        w_in, w_ple, ab_in, c_in = A["w_in"][0], A["ple_w_gate"][0], A["ab_w_in_2"][0], A["c_w_in_2"][0]
        PROJ = {
            "mix0": [unit(w_in, (AQ, AK)), unit(w_in, (AK, GK)), unit(w_in, (GK, GV), (GR, GO)),
                     unit(w_in, (GV, GR)), unit(w_in, (GO, GO + 512))],
            "mix0o": wide(A["w_out"][0]),
            "emb": wide(A["ple_w_proj"][0]),
            "ple": wide(w_ple),
            "abo": wide(A["ab_w_out_2"][0]),
            "hgo": wide(A["c_w_out_2"][0]),
            "ab": [[((8, 16), [((ALL, ALL, slice(8 * m, 8 * m + 8)), ab_in.rearrange("(k p) n -> p k n", p=P)[:, :, a:a + 8])
                               for m, a in enumerate((MI, DA))])],
                   unit(ab_in, (MV, MO)), unit(ab_in, (MQ, MV)), unit(ab_in, (DK, DV)), unit(ab_in, (DQ, DK)),
                   unit(ab_in, (DV, DG)), unit(ab_in, (MO, MI)), unit(ab_in, (DG, DA))],
            "hg": [unit(c_in, (n, n + 512)) for n in (1024, 1536, 0, 512, 2048, 2560, 3072, 3584)],
        }

        def sp_proj(sp, part):
            s = first_slot[part]
            for slots in PROJ[part]:
                for shape, loads in slots:
                    sp_slot(sp, s, 0, shape, loads)
                    s += 1

        def piece_at(part, u):
            return 2 * (first_slot[part] + 2 * u)

        mix = nrm
        PAIR = 4
        sqa, qn, kn = arena[:, 0:1280], arena[:, 1280:2304], arena[:, 2304:2560]
        qr, kr, kd, tmp = arena[:, 2560:3584], arena[:, 3584:3840], arena[:, 3840:4352], arena[:, 4352:4864]
        av = arena[:, 4992:5248].rearrange("p (t n) -> p t n", t=NT)
        qT, kT = arena[:, 5248:6272], arena[:, 6272:6784]
        s0 = arena[:, 6784:7808].rearrange("p (k n) -> p k n", k=8)
        s1 = arena[:, 7808:9856].rearrange("p (k n) -> p k n", k=8)
        eT = arena[:, 0:3072].rearrange("p (s k n) -> p s k n", s=3, k=8)
        a_ss, a_r = few.take(20), few.take(20)
        a_max, a_neg, a_den, a_exs = few.take(16), few.take(16), few.take(16), few.take(16)

        def pe_a_proj(pe):
            X = "mix0"
            pe_between(pe, X, lambda t, k: pe_unit(pe, piece_at(X, 0), rows=[(0, 512, [bank(0), bank(1)], (True, True))],
                                                   which=(k,), tile=t))
            pe_params(pe)
            pe_unit(pe, piece_at(X, 1), rows=[(0, 256, [bank(2, 0, 256), bank(3, 0, 256)], (True, True))],
                    columns=[(256, bank(4, 0, 256), True), (384, bank(4, 256, 256), False)])
            pe.wait_ge(*after("params"))
            pe_unit(pe, piece_at(X, 2), columns=[(0, bank(5, 0, 256), True), (128, bank(5, 256, 256), False)],
                    rows=[(256, 272, [bank(6, 0, 16), bank(6, 16, 16)], (True, False))], shape=(4, 272))

        def act_a_rows(act):
            act.wait_ge(used, piece_at("mix0", 2))
            sq = sqa.rearrange("p (t n) -> p t n", t=NT)
            nc.scalar.activation(sq[:, :, 0:512], psum[:, 0:2, :], ACT.Square).then_inc(*steps.did("act", "a.sq"))
            nc.scalar.activation(sq[:, :, 512:640], psum[:, 2:4, 0:128], ACT.Square).then_inc(*steps.did("act", "a.sk"))
            nc.scalar.activation(av, psum[:, 2:4, 128:256], ACT.Copy).then_inc(*steps.did("act", "a.v"))

        def pool_a(pool):
            pool.wait_ge(*after("a.ss"))
            pool_rstd(pool, "a.r", a_ss, 20, 64, a_r)

        def dve_a_sums(dve):
            sq = sqa.rearrange("p (t n) -> p t n", t=NT)
            ss = a_ss.rearrange("p (t k) -> p t k", t=NT)
            dve.wait_ge(*after("a.sk"))
            nc.vector.tensor_reduce(ss, sq.rearrange("p t (k d) -> p t k d", d=64), AX_X, ALU.add)\
                .then_inc(*steps.did("dve", "a.ss"))

        def dve_a_rows(dve):
            r = a_r.rearrange("p (t k) -> p t k", t=NT)
            dve.wait_ge(*after("a.r"))
            dve.wait_ge(*after("a.v"))
            nc.vector.tensor_tensor(kn.rearrange("p (t k d) -> p t k d", t=2, k=2),
                                    psum[:, 2:4, 0:128].rearrange("p t (k d) -> p t k d", k=2),
                                    r[:, :, 8:10].unsqueeze(3).broadcast_to([P, 2, 2, 64]), ALU.mult)\
                .then_inc(*steps.did("dve", "a.kn"))
            nc.vector.tensor_tensor(qn.rearrange("p (t k d) -> p t k d", t=2, k=8),
                                    psum[:, 0:2, :].rearrange("p t (k d) -> p t k d", k=8),
                                    r[:, :, 0:8].unsqueeze(3).broadcast_to([P, 2, 8, 64]), ALU.mult)\
                .then_inc(*steps.did("dve", "a.qn"))
            for name, n, heads, g in (("k", kn, 4, "k_norm"), ("q", qn, 16, "q_norm")):
                v = n.rearrange("p (k d) -> p k d", d=64)
                dve.wait_ge(*after(f"a.{name}n"))
                nc.vector.tensor_tensor(v, v, spread[g].unsqueeze(1).broadcast_to([P, heads, 64]), ALU.mult)\
                    .then_inc(*steps.did("dve", f"a.{name}g"))
            cos, sin = (cst(f"{f}0", 64).rearrange("p (t d) -> p t d", t=2) for f in ("cos", "sin"))
            for name, n, out_, heads in (("k", kn, kr, 2), ("q", qn, qr, 8)):
                v = n.rearrange("p (t k d) -> p t k d", t=2, k=heads)
                o = out_.rearrange("p (t k d) -> p t k d", t=2, k=heads)
                t_ = tmp[:, 0:64 * heads].rearrange("p (t k d) -> p t k d", t=2, k=heads)
                c, s = (a.unsqueeze(2).broadcast_to([P, 2, heads, 32]) for a in (cos, sin))
                lo, hi = slice(0, 32), slice(32, 64)
                dve.wait_ge(*after(f"a.{name}g"))
                nc.vector.tensor_tensor(o[:, :, :, lo], v[:, :, :, lo], c, ALU.mult).then_inc(*steps.did("dve", f"a.{name}1"))
                nc.vector.tensor_tensor(o[:, :, :, hi], v[:, :, :, hi], c, ALU.mult).then_inc(*steps.did("dve", f"a.{name}2"))
                if name == "q":
                    dve.wait_ge(*after("a.kr"))
                nc.vector.tensor_tensor(t_, v[:, :, :, hi], s, ALU.mult).then_inc(*steps.did("dve", f"a.{name}3"))
                dve.wait_ge(*after(f"a.{name}3"))
                nc.vector.tensor_tensor(o[:, :, :, lo], o[:, :, :, lo], t_, ALU.subtract).then_inc(*steps.did("dve", f"a.{name}4"))
                dve.wait_ge(*after(f"a.{name}4"))
                nc.vector.tensor_tensor(t_, v[:, :, :, lo], s, ALU.mult).then_inc(*steps.did("dve", f"a.{name}5"))
                dve.wait_ge(*after(f"a.{name}5"))
                nc.vector.tensor_tensor(o[:, :, :, hi], o[:, :, :, hi], t_, ALU.add).then_inc(*steps.did("dve", f"a.{name}r"))

        def act_a_dup(act):
            act.wait_ge(*after("a.kr"))
            nc.scalar.activation(kd.rearrange("p (k a d) -> p k a d", k=4, a=2),
                                 kr.rearrange("p (k d) -> p k d", k=4).unsqueeze(2).broadcast_to([P, 4, 2, 64]), ACT.Copy)\
                .then_inc(*steps.did("act", "a.kd"))

        def pe_a_turn(pe):
            pe.wait_ge(*after("a.qr"))
            pe.wait_ge(*after("a.kd"))
            for t in range(NT):
                for pair in range(4):
                    nc.tensor.transpose(bank(pair // 2, (pair % 2) * 256 + t * P, P),
                                        qr[:, t * 512 + pair * P:t * 512 + pair * P + P], ident)
                for kv in range(2):
                    last = nc.tensor.transpose(bank(2, kv * 256 + t * P, P),
                                               kd[:, (2 * t + kv) * P:(2 * t + kv) * P + P], ident)
            last.then_inc(*steps.did("pe", "a.T"))

        def act_a_turned(act):
            act.wait_ge(*after("a.T"))
            nc.scalar.activation(rows(qT), psum[:, 0:2, :], ACT.Copy).then_inc(*steps.did("act", "a.qT"))

        def dve_a_turned(dve):
            dve.wait_ge(*after("a.T"))
            nc.vector.tensor_copy(kT, bank(2)).then_inc(*steps.did("dve", "a.kT"))

        SCORE_BANKS = [[2, 4], [5, 6]]

        def pe_a_scores(pe):
            for name in ("a.qT", "a.kT", "g.q", "g.k", "g.y1"):
                pe.wait_ge(*after(name))
            for par in range(2):
                part = slice(64 * par, 64 * par + 64)
                for i in range(4):
                    pair, kv = i, i // 2
                    nc.tensor.matmul(bank(par, i * P, P), qT[part, pair * 256:pair * 256 + P],
                                     kT[part, kv * 256:kv * 256 + P], start=True, stop=True)
                    last = nc.tensor.matmul(bank(SCORE_BANKS[par][i // 2], (i % 2) * 256, 256),
                                            qT[part, pair * 256 + P:pair * 256 + 2 * P],
                                            kT[part, kv * 256:kv * 256 + 256], start=True, stop=True)
            last.then_inc(*steps.did("pe", "a.S"))

        def dve_a_softmax(dve):
            dve.wait_ge(*after("a.S"))
            sink = spread["attn_sinks"].rearrange("p (i q) -> p q i", q=2)
            for t, (scores, mask, banks, width) in enumerate(((s0, cst("own"), [[0], [1]], P),
                                                              (s1, cst("prev", 256), SCORE_BANKS, 256))):
                k = BANK // width
                for par in range(2):
                    for m, b in enumerate(banks[par]):
                        last = nc.vector.scalar_tensor_tensor(
                            scores[:, 4 * par + k * m:4 * par + k * m + k, :], bank(b).rearrange("p (k n) -> p k n", k=k), 0.125,
                            mask.unsqueeze(1).broadcast_to([P, k, width]), ALU.mult, ALU.add)
                last.then_inc(*steps.did("dve", f"a.masked{t}"))
                at = slice(8 * t, 8 * t + 8)
                by_head = lambda a: a[:, at].rearrange("p (q i) -> p q i", q=2)
                dve.wait_ge(*after(f"a.masked{t}"))
                nc.vector.tensor_reduce(a_max[:, at], scores, AX_X, ALU.max).then_inc(*steps.did("dve", f"a.m{t}"))
                dve.wait_ge(*after(f"a.m{t}"))
                nc.vector.tensor_tensor(by_head(a_max), by_head(a_max), sink, ALU.max).then_inc(*steps.did("dve", f"a.ms{t}"))
                dve.wait_ge(*after(f"a.ms{t}"))
                nc.vector.tensor_scalar(a_neg[:, at], a_max[:, at], -1.0, None, ALU.mult).then_inc(*steps.did("dve", f"a.neg{t}"))
                nc.vector.tensor_tensor(by_head(a_exs), sink, by_head(a_max), ALU.subtract).then_inc(*steps.did("dve", f"a.sm{t}"))

        def act_a_exp(act):
            act.wait_ge(*after("a.neg0"))
            for k in range(8):
                nc.scalar.activation(s0[:, k, :], s0[:, k, :], ACT.Exp, bias=a_neg[:, k:k + 1],
                                     accum_out=a_den[:, k:k + 1]).then_inc(*steps.did("act", f"a.e0{k}"))
            act.wait_ge(*after("a.sm1"))
            nc.scalar.activation(a_exs, a_exs, ACT.Exp).then_inc(*steps.did("act", "a.exs"))
            for k in range(8):
                nc.scalar.activation(s1[:, k, :], s1[:, k, :], ACT.Exp, bias=a_neg[:, 8 + k:9 + k],
                                     accum_out=a_den[:, 8 + k:9 + k]).then_inc(*steps.did("act", f"a.e1{k}"))

        def dve_a_den(dve):
            dve.wait_ge(*after("a.e17"))
            nc.vector.tensor_tensor(a_den, a_den, a_exs, ALU.add).then_inc(*steps.did("dve", "a.den"))
            dve.wait_ge(*after("a.den"))
            nc.vector.reciprocal(a_den, a_den).then_inc(*steps.did("dve", "a.rden"))

        def pe_a_probs(pe, groups):
            for g, (src, at, b) in enumerate(((s0, 0, (0, 1)), (s1, 0, (2, 4)), (s1, P, (5, 6)))):
                if g not in groups:
                    continue
                pe.wait_ge(*after(f"a.masked{min(g, 1)}"))
                pe.wait_ge(*after("a.e07" if g == 0 else "a.e17"))
                for k in range(8):
                    last = nc.tensor.transpose(bank(b[k // 4], (k % 4) * P, P), src[:, k, at:at + P], ident)
                    if k % 4 == 3:
                        last.then_inc(*steps.did("pe", f"a.eT{g}{k // 4}"))

        def act_a_probs(act):
            for g, b in ((0, 0), (1, 2), (2, 5)):
                act.wait_ge(*after(f"a.eT{g}0"))
                nc.scalar.activation(eT[:, g, 0:4, :], bank(b).rearrange("p (k n) -> p k n", k=4), ACT.Copy)\
                    .then_inc(*steps.did("act", f"a.pT{g}0"))

        def dve_a_probs(dve):
            for g, b in ((0, 1), (1, 4), (2, 6)):
                dve.wait_ge(*after(f"a.eT{g}1"))
                nc.vector.tensor_copy(eT[:, g, 4:8, :], bank(b).rearrange("p (k n) -> p k n", k=4))\
                    .then_inc(*steps.did("dve", f"a.pT{g}1"))

        def pe_a_out(pe):
            def products(t, groups):
                for k in range(8):
                    hd = (k % 4) * 2 + k // 4
                    kv = hd // 4
                    for g, tv in groups:
                        last = nc.tensor.matmul(bank(t, hd * 64, 64), eT[:, g, k, :], av[:, tv, kv * 64:kv * 64 + 64],
                                                start=(g < 2), stop=(g != 1))
                return last
            for name in ("a.v", "a.pT00", "a.pT01"):
                pe.wait_ge(*after(name))
            products(0, ((0, 0),))
            for name in ("a.pT20", "a.pT21"):
                pe.wait_ge(*after(name))
            products(1, ((1, 0), (2, 1))).then_inc(*steps.did("pe", "a.O"))

        def dve_a_out(dve):
            dve.wait_ge(*after("a.O"))
            for t in range(NT):
                heads = lambda a: a.rearrange("p (i q d) -> p q i d", q=2, d=64)
                nc.vector.tensor_tensor(heads(mix[:, t, 0:512]), heads(bank(t)),
                                        a_den[:, 8 * t:8 * t + 8].rearrange("p (q i) -> p q i", q=2).unsqueeze(3)
                                        .broadcast_to([P, 2, 4, 64]), ALU.mult).then_inc(*steps.did("dve", f"a.mix{t}"))

        gq, gk = arena[:, 9856:10368], arena[:, 10368:10880]
        glr, glrT = arena[:, 10880:10912], arena[0:16, 10912:11168]
        gv = arena[:, 3072:4096].rearrange("p (t n) -> p t n", t=NT)
        sil = arena[:, 8832:9856].rearrange("p (t n) -> p t n", t=NT)
        la, gb = arena[:, 4096:4608], arena[:, 6272:6784]
        lt = arena[:, 9344:9856]
        g_e = (arena[:, 5248:5760], la)
        g_l = (arena[:, 5760:6272], arena[:, 6784:7296])
        g_at = arena[:, 7296:8320].rearrange("p (q n) -> p q n", q=2)
        g_cross = arena[:, 8320:8832].rearrange("p (q n) -> p q n", q=2)
        osq = arena[:, 0:1024]
        ones = few.take(1)
        g_ss, g_r = few.take(8), few.take(8)

        def act_g_q(act):
            act.wait_ge(used, piece_at("mix0", 2))
            nc.scalar.activation(gq, bank(4), ACT.Copy, scale=0.125).then_inc(*steps.did("act", "g.q"))

        def dve_g_k(dve):
            dve.wait_ge(used, piece_at("mix0", 3))
            nc.vector.tensor_copy(gk, bank(5)).then_inc(*steps.did("dve", "g.k"))
            nc.vector.tensor_copy(glr, bank(6, 0, 32)).then_inc(*steps.did("dve", "g.glr"))

        def pe_g_v(pe, which):
            pe.wait_ge(*after("a.kn"))
            pe_unit(pe, piece_at("mix0", 3), rows=[(0, 512, [bank(3), bank(7)], (True, True))], which=which)

        def act_g_v(act):
            act.wait_ge(used, piece_at("mix0", 4))
            act.wait_ge(*after("a.T"))
            for t, b in ((0, 3), (1, 7)):
                nc.scalar.activation(gv[:, t, :], bank(b), ACT.Copy).then_inc(*steps.did("act", f"g.v{t}"))

        def pe_g_gate(pe, which):
            pe.wait_ge(*after("g.v1"))
            pe_unit(pe, piece_at("mix0", 4), rows=[(0, 512, [bank(3), bank(7)], (True, True))], which=which)

        def pe_g_rank(pe):
            pe.wait_ge(*after("g.glr"))
            for t in range(NT):
                last = nc.tensor.transpose(psum[0:16, 6, t * P:t * P + P], glr[:, t * 16:t * 16 + 16], ident)
            last.then_inc(*steps.did("pe", "g.glrT"))

        def pe_g_alpha(pe):
            pe.wait_ge(*after("g.rT"))
            for c in range(2):
                last = nc.tensor.matmul(bank(6, c * 256, 256), gate_up[:, c * P:c * P + P], glrT, start=(c == 0), stop=True,
                                        skip_group_check=True)
            last.then_inc(*steps.did("pe", "g.z"))

        def dve_g_rank(dve):
            dve.wait_ge(*after("g.glrT"))
            nc.vector.tensor_copy(glrT, psum[0:16, 6, 0:256]).then_inc(*steps.did("dve", "g.rT"))

        def dve_g_alpha(dve):
            dve.wait_ge(*after("g.z"))
            for c in range(2):
                nc.vector.tensor_scalar(la[:, c * 256:c * 256 + 256], bank(6, c * 256, 256), gate_bias[:, c:c + 1], None, ALU.add)\
                    .then_inc(*steps.did("dve", f"g.y{c}"))

        def act_g_alpha(act):
            act.wait_ge(*after("g.y1"))
            nc.scalar.activation(lt, la, ACT.Abs).then_inc(*steps.did("act", "g.abs"))
            act.wait_ge(*after("g.abs"))
            nc.scalar.activation(lt, lt, ACT.Exp, scale=-1.0).then_inc(*steps.did("act", "g.exp"))
            act.wait_ge(*after("g.exp"))
            nc.scalar.activation(lt, lt, ACT.Ln, bias=1.0).then_inc(*steps.did("act", "g.ln"))

        def dve_g_log(dve):
            dve.wait_ge(*after("g.ln"))
            nc.vector.scalar_tensor_tensor(la, la, 0.0, lt, ALU.min, ALU.subtract).then_inc(*steps.did("dve", "g.la"))

        def dve_g_sum(dve):
            dve.wait_ge(*after("g.la"))
            dve.wait_ge(*after("a.S"))
            for c in range(2):
                part = slice(c * 256, c * 256 + 256)
                nc.vector.tensor_tensor_scan(gb[:, part], ones.broadcast_to([P, 256]), la[:, part], 0.0, ALU.mult, ALU.add)\
                    .then_inc(*steps.did("dve", f"g.cum{c}"))
            dve.wait_ge(*after("g.cum1"))
            nc.vector.tensor_scalar(gb, gb, 1.0 / 16.0, None, ALU.mult).then_inc(*steps.did("dve", "g.b"))

        def dve_level_x(dve, X, n, half, b, e, ready):
            blocks = lambda a: a.rearrange("p (m r) -> p m r", r=2 * half)
            left, right = slice(0, half), slice(half, 2 * half)
            for name in ready:
                dve.wait_ge(*after(name))
            ref = blocks(b)[:, :, half - 1:half].broadcast_to([P, b.shape[1] // (2 * half), half])
            nc.vector.tensor_tensor(blocks(e)[:, :, right], blocks(b)[:, :, right], ref, ALU.subtract)\
                .then_inc(*steps.did("dve", f"{X}.x{n}r"))
            nc.vector.tensor_tensor(blocks(e)[:, :, left], ref, blocks(b)[:, :, left], ALU.subtract)\
                .then_inc(*steps.did("dve", f"{X}.x{n}"))

        def dve_level_l(dve, X, n, half, q, k, e, l, ready=()):
            blocks = lambda a: a.rearrange("p (m r) -> p m r", r=2 * half)
            left, right = slice(0, half), slice(half, 2 * half)
            for name in ready:
                dve.wait_ge(*after(name))
            dve.wait_ge(*after(f"{X}.e{n}"))
            nc.vector.tensor_tensor(blocks(l)[:, :, right], blocks(q)[:, :, right], blocks(e)[:, :, right], ALU.mult)\
                .then_inc(*steps.did("dve", f"{X}.l{n}r"))
            nc.vector.tensor_tensor(blocks(l)[:, :, left], blocks(k)[:, :, left], blocks(e)[:, :, left], ALU.mult)\
                .then_inc(*steps.did("dve", f"{X}.l{n}"))

        def act_level(act, X, n, e):
            act.wait_ge(*after(f"{X}.x{n}"))
            nc.scalar.activation(e, e, ACT.Exp).then_inc(*steps.did("act", f"{X}.e{n}"))

        ALL_LEVELS = [P] + LEVELS
        BANKS2 = ((4, 5), (6, 7))

        def pe_g_levels(pe):
            for n in range(len(ALL_LEVELS) + 1):
                if n == 2:
                    for t in range(NT):
                        pe_turn(pe, "mix0o", t, 0, t, mix, "a.mix1")
                for name in (("a.pT11", "a.pT20"), ("a.pT21", "g.sil1"))[n] if n < 2 else (f"g.put{n - 2}",):
                    pe.wait_ge(*after(name))
                if n < len(ALL_LEVELS):
                    pe.wait_ge(*after(f"g.l{n}"))
                    l = r = g_l[n % 2]
                else:
                    l, r = gk, gq
                for par in range(2):
                    part = slice(64 * par, 64 * par + 64)
                    for c in range(2):
                        if n == 0:
                            last = nc.tensor.matmul(bank(BANKS2[0][par], c * P, P), l[part, c * 256:c * 256 + P],
                                                    r[part, c * 256 + P:c * 256 + 256], start=True, stop=True)
                            continue
                        for t in range(NT):
                            tok = slice(c * 256 + t * P, c * 256 + t * P + P)
                            last = nc.tensor.matmul(bank(BANKS2[n % 2][par], (2 * c + t) * P, P), l[part, tok], r[part, tok],
                                                    start=True, stop=True)
                last.then_inc(*steps.did("pe", f"g.P{n}"))

        def dve_g_put(dve, n):
            dve.wait_ge(*after(f"g.P{n}"))
            if n == 0:
                nc.vector.tensor_copy(g_cross, psum[:, 4:6, 0:256]).then_inc(*steps.did("dve", "g.put0"))
                return
            if n == 1:
                dve.wait_ge(*after("g.at0"))
            else:
                dve.wait_ge(*after(f"g.put{n - 1}"))
            mask = cst(f"level{ALL_LEVELS[n]}") if n < len(ALL_LEVELS) else ident
            for par in range(2):
                four = lambda a: a.rearrange("p (m i) -> p m i", m=4)
                last = nc.vector.copy_predicated(four(g_at[:, par, :]), mask.bitcast(U32).unsqueeze(1).broadcast_to([P, 4, P]),
                                                 four(bank(BANKS2[n % 2][par])))
            last.then_inc(*steps.did("dve", f"g.put{n}"))

        def dve_g_exponents(dve, n):
            dve_level_x(dve, "g", n, ALL_LEVELS[n], gb, g_e[n % 2], [f"g.l{n - 2}"] if n >= 2 else ["g.b"])

        def dve_g_decayed(dve, n):
            ready = [f"g.P{n - 2}"] if n >= 2 else ["a.eT21"] if n == 1 else ["g.q"]
            dve_level_l(dve, "g", n, ALL_LEVELS[n], gq, gk, g_e[n % 2], g_l[n % 2], ready)

        def dve_g_levels(dve):
            levels = len(ALL_LEVELS)
            for n in range(2, levels):
                dve_g_put(dve, n - 2)
                dve_g_decayed(dve, n)
                if n + 2 < levels:
                    dve_g_exponents(dve, n + 2)
                if n in (5, 6):
                    dve_turn(dve, "mix0o", n - 5, 0, n - 5)
            for n in range(levels - 2, levels + 1):
                dve_g_put(dve, n)

        def act_g_levels(act):
            for n in range(2, len(ALL_LEVELS)):
                act_level(act, "g", n, g_e[n % 2])
                if n == 3:
                    for t in range(NT):
                        act_turn(act, "mix0o", t, 0, t)
                if 3 <= n < 7:
                    out_splits(split_hi, act, "mix0o", (n - 3,))

        def act_g_gate(act):
            act.wait_ge(used, piece_at("mix0o", 0))
            act.wait_ge(*after("a.eT21"))
            for t, b in ((0, 3), (1, 7)):
                nc.scalar.activation(sil[:, t, :], bank(b), ACT.Silu).then_inc(*steps.did("act", f"g.sil{t}"))

        def pe_g_out(pe):
            pe.wait_ge(*after(f"g.put{len(ALL_LEVELS)}"))
            pe.wait_ge(*after("g.v1"))
            for t in range(NT):
                for hd in range(4):
                    par, c = hd % 2, hd // 2
                    o = bank(4 + t, hd * P, P)
                    last = nc.tensor.matmul(o, g_at[:, par, (2 * c + t) * P:(2 * c + t) * P + P], gv[:, t, hd * P:hd * P + P],
                                            start=True, stop=(t == 0))
                    if t == 1:
                        last = nc.tensor.matmul(o, g_cross[:, par, c * P:c * P + P], gv[:, 0, hd * P:hd * P + P],
                                                start=False, stop=True)
            last.then_inc(*steps.did("pe", "g.O"))

        def act_g_square(act):
            act.wait_ge(*after("g.O"))
            nc.scalar.activation(osq.rearrange("p (t n) -> p t n", t=NT), psum[:, 4:6, :], ACT.Square)\
                .then_inc(*steps.did("act", "g.osq"))

        def dve_g_out(dve):
            dve.wait_ge(*after("g.osq"))
            v = osq.rearrange("p (k d) -> p k d", d=P)
            nc.vector.tensor_reduce(g_ss, v, AX_X, ALU.add).then_inc(*steps.did("dve", "g.oss"))
            out_splits(split_lo, dve, "mix0o", (6,))
            dve.wait_ge(*after("g.or"))
            o4 = psum[:, 4:6, :].rearrange("p t (k d) -> p t k d", d=P)
            r4 = g_r.rearrange("p (t k) -> p t k", t=NT).unsqueeze(3).broadcast_to([P, NT, 4, P])
            nc.vector.tensor_tensor(osq.rearrange("p (t k d) -> p t k d", t=NT, d=P), o4, r4, ALU.mult)\
                .then_inc(*steps.did("dve", "g.on"))
            dve.wait_ge(*after("g.on"))
            dve.wait_ge(*after("g.silg"))
            for t in range(NT):
                nc.vector.tensor_tensor(mix[:, t, 512:1024], osq[:, t * 512:t * 512 + 512], sil[:, t, :], ALU.mult)\
                    .then_inc(*steps.did("dve", f"mix0o.n{t}"))

        def sp_mix0(sp):
            sp_proj(sp, "mix0")
            sp_proj(sp, "mix0o")

        def pool_mix0(pool):
            pool_a(pool)
            for k in (2, 3):
                pool_split_lo(pool, piece_at("mix0", 3) + k)
            pool.wait_ge(*after("a.eT21"))
            nc.gpsimd.memset(arena[:, 7296:8320], 0.0).then_inc(*steps.did("pool", "g.at0"))
            pool.wait_ge(*after("g.sil1"))
            pool.wait_ge(*after("params"))
            eight = sil.rearrange("p t (k d) -> p (t k) d", d=P)
            nc.gpsimd.tensor_tensor(eight, eight, spread["gla_out_norm"].unsqueeze(1).broadcast_to([P, 8, P]), ALU.mult)\
                .then_inc(*steps.did("pool", "g.silg"))
            for k in range(4):
                pool_split_lo(pool, piece_at("mix0o", 0) + k, (2, D))
            pool.wait_ge(*after("g.oss"))
            pool_rstd(pool, "g.or", g_ss, 8, P, g_r)

        def pe_mix0(pe):
            pe_a_proj(pe)
            pe_g_v(pe, (0, 1))
            pe_a_turn(pe)
            pe_g_rank(pe)
            pe_g_v(pe, (2,))
            pe_g_alpha(pe)
            pe_g_v(pe, (3,))
            pe_a_scores(pe)
            pe_g_gate(pe, (0, 1, 2))
            pe_a_probs(pe, (0,))
            pe_g_gate(pe, (3,))
            pe_a_probs(pe, (1, 2))
            pe_a_out(pe)
            pe_g_levels(pe)
            pe_out(pe, "mix0o", 0)
            pe_g_out(pe)
            for k in (1, 2, 3):
                pe_out(pe, "mix0o", k)
            for t in range(NT):
                pe_turn(pe, "mix0o", t, 1, 6 + t, mix, f"mix0o.n{t}")
            pe_out_last(pe, "mix0o")

        def act_mix0(act):
            M = lambda u: piece_at("mix0", u)
            splits(split_hi, act, M(1))
            splits(split_hi, act, M(2), (4, 272))
            act_a_rows(act)
            splits(split_hi, act, M(3), which=(0, 1))
            act_g_q(act)
            act_a_dup(act)
            splits(split_hi, act, M(3), which=(2, 3))
            act_a_turned(act)
            splits(split_hi, act, M(4), which=(0, 1))
            act_g_alpha(act)
            act_g_v(act)
            splits(split_hi, act, M(4), which=(2, 3))
            act_a_exp(act)
            act_a_probs(act)
            for n in range(2):
                act_level(act, "g", n, g_e[n])
            act_g_gate(act)
            act_g_levels(act)
            out_splits(split_hi, act, "mix0o", (4, 5))
            act_g_square(act)
            out_splits(split_hi, act, "mix0o", (6,))
            for t in range(NT):
                act_turn(act, "mix0o", t, 1, 6 + t)
            out_splits(split_hi, act, "mix0o", (7,))
            first_pieces(split_hi, act, "ffn1", (0, 1))

        def dve_mix0(dve):
            M = lambda u: piece_at("mix0", u)
            splits(split_lo, dve, M(1), which=(0, 1))
            dve_params(dve)
            splits(split_lo, dve, M(1), which=(2, 3))
            splits(split_lo, dve, M(2), (4, 272))
            dve_a_sums(dve)
            splits(split_lo, dve, M(3), which=(0, 1))
            dve_a_rows(dve)
            dve_g_k(dve)
            dve_a_turned(dve)
            dve_g_rank(dve)
            dve.wait_ge(lo_done, M(4))
            splits(split_lo, dve, M(4), which=(0,))
            dve_g_alpha(dve)
            splits(split_lo, dve, M(4), which=(1,))
            dve_g_log(dve)
            splits(split_lo, dve, M(4), which=(2,))
            dve_a_softmax(dve)
            splits(split_lo, dve, M(4), which=(3,))
            dve_g_sum(dve)
            dve_g_exponents(dve, 0)
            dve_a_den(dve)
            dve_g_exponents(dve, 1)
            dve_a_probs(dve)
            for n in range(2):
                dve_g_decayed(dve, n)
                dve_g_exponents(dve, n + 2)
            dve_a_out(dve)
            dve_g_levels(dve)
            dve.wait_ge(lo_done, piece_at("mix0o", 0) + 4)
            out_splits(split_lo, dve, "mix0o", (4, 5))
            dve_g_out(dve)
            for t in range(NT):
                dve_turn(dve, "mix0o", t, 1, 6 + t)
            out_splits(split_lo, dve, "mix0o", (7,))
            first_pieces(split_lo, dve, "ffn1", (0, 1))


        def pe_turn_p(pe):
            for c in range(2):
                for t in range(NT):
                    last = nc.tensor.transpose(bank(6, c * 256 + t * P, P), p_rows[:, t, c * P:c * P + P], ident)
            last.then_inc(*steps.did("pe", "emb.T"))

        def act_turn_p(act):
            act.wait_ge(*after("emb.T"))
            act.wait_ge(used, 2 * (first_slot["emb"] - 1))
            nc.scalar.activation(hidh[:, 1], bank(6).rearrange("p (c t) -> p c t", c=2), ACT.Copy).then_inc(*steps.did("act", "emb.xh"))

        def dve_turn_p(dve):
            dve.wait_ge(*after("emb.xh"))
            nc.vector.tensor_tensor(hidl[:, 1], bank(6).rearrange("p (c t) -> p c t", c=2), hidh[:, 1].bitcast(F32), ALU.subtract)\
                .then_inc(*steps.did("dve", "emb.xl"))

        def pe_ple(pe):
            pe.wait_ge(*after("emb.xl"))
            p = 2 * first_slot["emb"]
            for c in range(2):
                pe.wait_ge(lo_done, p + c + 1)
                wh, wl = weights(p + c, 1, D)
                for t, b in BANKS:
                    tok, col = slice(t * P, t * P + P), slice(b * BANK, b * BANK + BANK)
                    last = three(bank(4 + 2 * t + b), hidh[:, 1, c, tok], hidl[:, 1, c, tok], wh[:, 0, col], wl[:, 0, col],
                                 start=(c == 0), stop=(c == 1))
                last.then_inc(used, 1)
            pe_between(pe, "ple", lambda t, k: pe_out(pe, "ple", k, tile=t))
            pe_out_last(pe, "ple")

        def made(t):
            return psum[:, 4 + 2 * t:6 + 2 * t, :]

        def act_ple(act):
            total = emb_sums[0]
            act.wait_ge(used, 2 * first_slot["ple"])
            for t in range(NT):
                nc.scalar.activation(rows(sgm[:, t, :]), made(t), ACT.Square, accum_out=total[:, t:t + 1])\
                    .then_inc(*steps.did("act", f"emb.ss{t}"))
            out_splits(split_hi, act, "ple", range(4, 8))
            act.wait_ge(*after("emb.ss1"))
            first_pieces(split_hi, act, "ab", (0, 1, 2, 3))

        emb_sums = few.take(NT), few.take(NT)

        def pool_ple(pool):
            total, r = emb_sums
            for t in range(NT):
                pool.wait_ge(*after(f"emb.ss{t}"))
                pool_rstd(pool, f"emb.r{t}", total[:, t:t + 1], 1, D, r[:, t:t + 1])

        def dve_ple(dve):
            _, r = emb_sums
            g = gain_of(dve, "emb")
            for t in range(NT):
                dve.wait_ge(*after(f"emb.r{t}"))
                nc.vector.scalar_tensor_tensor(rows(emb[:, t, :]), made(t), r[:, t:t + 1], rows(g), ALU.mult, ALU.mult)\
                    .then_inc(*steps.did("dve", f"emb.e{t}"))
            out_splits(split_lo, dve, "ple", (4, 5, 6, 7))
            first_pieces(split_lo, dve, "ab", (0, 1, 2, 3))

        ab_p = {"small": 2 * first_slot["ab"]}
        for n, name in enumerate(("mv", "mqk", "dk", "dq", "dv", "mo", "dg")):
            ab_p[name] = ab_p["small"] + 2 + 4 * n
        Y = {"dk": arena[:, 0:1024], "dq": arena[:, 1024:2048], "dv": arena[:, 2048:3072], "mqk": arena[:, 8192:9216]}
        krow, qrow, vb = arena[:, 3072:4096], arena[:, 4096:5120], arena[:, 5120:6144]
        kb, kbT, kT2, qT2 = arena[:, 6144:7168], arena[:, 7168:8192], arena[:, 0:1024], arena[:, 1024:2048]
        mE, mvE = arena[:, 9216:10752], arena[:, 10752:11776]
        m_sq = arena[:, 8192:9216]
        dE, dNT, dat = arena[:, 8192:9216], arena[:, 9216:10240], arena[:, 2048:3072]
        dN, dXT, dX, dV = arena[:, 6144:7168], arena[:, 7168:8192], arena[:, 4096:5120], arena[:, 9216:10240]
        u0, dS, u1 = arena[:, 10240:10752], arena[:, 10752:11264], arena[:, 11264:11776]
        gtmp, d_sq = arena[:, 8192:9216], arena[:, 6144:7168]
        gz, gth, gcap, gex = few.take(32), few.take(16), few.take(16), few.take(24)
        glog, gcum, gbeta, gei, gt4 = few.take(16), few.take(16), few.take(8), few.take(8), few.take(8)
        m_den, m_ss, m_r, k_ss, k_r, q_ss, q_r, d_ss, d_r = (few.take(8) for _ in range(9))
        exa, glast, kdecay, eg1, beg = (few.take(4) for _ in range(5))
        by_t = lambda a: a.rearrange("p (t n) -> p t n", t=NT)
        heads4 = lambda a: a.rearrange("p (t k d) -> p t k d", t=NT, d=P)
        ones_sq = ones.broadcast_to([P, P])

        def spread_heads(a, t=None):
            return a.rearrange("p (t k) -> p t k", k=4).unsqueeze(3).broadcast_to([P, a.shape[1] // 4, 4, P])

        def conv_banks(name):
            return {"mqk": (2, 3), "dk": (0, 1), "dq": (6, 7), "dv": (0, 1)}[name]

        def conv_tap(name, k, c):
            if name == "mqk":
                return conv_m[:, k * 4 + c:k * 4 + c + 1]
            c += {"dq": 0, "dk": 4, "dv": 8}[name]
            return conv_g[:, k * 12 + c:k * 12 + c + 1]

        def pe_conv_unit(pe, name, ready=()):
            for r in ready:
                pe.wait_ge(*after(r))
            b = conv_banks(name)
            pe_unit(pe, ab_p[name], columns=[(c * P, bank(b[c // 2], (c % 2) * 256, 256), c % 2 == 0) for c in range(4)])

        def act_conv_first(act, name):
            act.wait_ge(used, ab_p[name] + 4)
            b = conv_banks(name)
            for c in range(4):
                last = nc.scalar.activation(Y[name][:, c * 256:c * 256 + 256], bank(b[c // 2], (c % 2) * 256, 256), ACT.Identity,
                                            scale=conv_tap(name, 3, c))
            last.then_inc(*steps.did("act", f"{name}.c3"))

        def dve_conv_rest(dve, name):
            b = conv_banks(name)
            for k in (2, 1, 0):
                dve.wait_ge(*after(f"{name}.c{k + 1}"))
                lag = 3 - k
                for c in range(4):
                    y = Y[name][:, c * 256 + lag:c * 256 + 256]
                    last = nc.vector.scalar_tensor_tensor(y, bank(b[c // 2], (c % 2) * 256, 256 - lag), conv_tap(name, k, c), y,
                                                          ALU.mult, ALU.add)
                last.then_inc(*steps.did("dve", f"{name}.c{k}"))

        def act_conv_silu(act, name):
            act.wait_ge(*after(f"{name}.c0"))
            nc.scalar.activation(Y[name], Y[name], ACT.Silu).then_inc(*steps.did("act", f"{name}.y"))

        def pe_ab_first(pe):
            def piece(t, k):
                if k == 0:
                    for m in range(2):
                        pe.wait_ge(lo_done, ab_p["small"] + m + 1)
                        wh, wl = weights(ab_p["small"] + m, 4, 16)
                        for kk in range(4):
                            kc = 4 * m + kk
                            tok = slice(t * P, t * P + P)
                            last = three(bank(7, t * 16, 16), xh[:, kc, tok], xl[:, kc, tok], wh[:, kk, :], wl[:, kk, :],
                                         start=(kc == 0 and t == 0), stop=(kc == KC - 1))
                        if t == 1:
                            last.then_inc(used, 1)
                pe_unit(pe, ab_p["mv"], rows=[(0, 512, [bank(0), bank(1)], (True, True))], which=(k,), tile=t)
            pe_between(pe, "ab", piece)
            pe_conv_unit(pe, "mqk")

        def dve_gates(dve):
            dve.wait_ge(used, ab_p["small"] + 2)
            z, src = by_t(gz), bank(7, 0, 32).rearrange("p (t n) -> p t n", t=NT)
            b = spread["ab_m_gate_bias_2"].unsqueeze(1).broadcast_to([P, NT, 8])
            nc.vector.tensor_tensor(z[:, :, 0:8], src[:, :, 0:8], b, ALU.add).then_inc(*steps.did("dve", "gate.if"))
            dt = spread["ab_g_dt_bias_2"].unsqueeze(1).broadcast_to([P, NT, 4])
            nc.vector.tensor_tensor(z[:, :, 8:12], src[:, :, 8:12], dt, ALU.add).then_inc(*steps.did("dve", "gate.a"))
            nc.vector.tensor_copy(z[:, :, 12:16], src[:, :, 12:16]).then_inc(*steps.did("dve", "gate.b"))

        def act_gates(act):
            act.wait_ge(*after("gate.b"))
            nc.scalar.activation(by_t(gth), by_t(gz)[:, :, 0:8], ACT.Tanh, scale=1.0 / 15.0).then_inc(*steps.did("act", "gate.th"))
            e = by_t(gex)
            nc.scalar.activation(e[:, :, 4:8], by_t(gz)[:, :, 8:12], ACT.Abs).then_inc(*steps.did("act", "gate.abs"))
            act.wait_ge(*after("gate.abs"))
            act.wait_ge(*after("gate.cap"))
            nc.scalar.activation(e[:, :, 4:8], e[:, :, 4:8], ACT.Exp, scale=-1.0).then_inc(*steps.did("act", "gate.ea"))
            nc.scalar.activation(e[:, :, 0:4], by_t(gcap)[:, :, 4:8], ACT.Exp, scale=-1.0).then_inc(*steps.did("act", "gate.ef"))
            nc.scalar.activation(e[:, :, 8:12], by_t(gz)[:, :, 12:16], ACT.Exp, scale=-1.0).then_inc(*steps.did("act", "gate.eb"))
            nc.scalar.activation(by_t(gei), by_t(gcap)[:, :, 0:4], ACT.Exp).then_inc(*steps.did("act", "gate.ei"))
            nc.scalar.activation(exa, spread["ab_g_a_log_2"], ACT.Exp).then_inc(*steps.did("act", "gate.exa"))
            act.wait_ge(*after("gate.ef"))
            nc.scalar.activation(e[:, :, 0:8], e[:, :, 0:8], ACT.Ln, bias=1.0).then_inc(*steps.did("act", "gate.ln"))

        def dve_gate_logs(dve):
            dve.wait_ge(*after("gate.th"))
            nc.vector.tensor_scalar(gcap, gth, 15.0, None, ALU.mult).then_inc(*steps.did("dve", "gate.cap"))
            e, l = by_t(gex), by_t(glog)
            dve.wait_ge(*after("gate.ln"))
            nc.vector.tensor_scalar(l[:, :, 0:4], e[:, :, 0:4], -1.0, None, ALU.mult).then_inc(*steps.did("dve", "gate.lf"))
            nc.vector.scalar_tensor_tensor(l[:, :, 4:8], by_t(gz)[:, :, 8:12], 0.0, e[:, :, 4:8], ALU.max, ALU.add)\
                .then_inc(*steps.did("dve", "gate.sp"))
            dve.wait_ge(*after("gate.sp"))
            nc.vector.scalar_tensor_tensor(l[:, :, 4:8], l[:, :, 4:8], -1.0, exa.unsqueeze(1).broadcast_to([P, NT, 4]),
                                           ALU.mult, ALU.mult).then_inc(*steps.did("dve", "gate.g"))
            nc.vector.tensor_scalar(by_t(gbeta), e[:, :, 8:12], 1.0, None, ALU.add).then_inc(*steps.did("dve", "gate.1b"))
            dve.wait_ge(*after("gate.1b"))
            nc.vector.reciprocal(gbeta, gbeta).then_inc(*steps.did("dve", "gate.beta"))

        def pe_gate_sums(pe):
            upper, l = cst("upper"), by_t(glog)
            pe.wait_ge(*after("gate.g"))
            pe.wait_ge(*after("gate.lf"))
            pe.wait_ge(*after("gate.b"))
            nc.tensor.matmul(bank(7, 0, 8), upper, l[:, 0, :], start=True, stop=True, skip_group_check=True)
            nc.tensor.matmul(bank(7, 8, 4), ones_sq, l[:, 0, 0:4], start=False, stop=False, skip_group_check=True)
            nc.tensor.matmul(bank(7, 8, 4), upper, l[:, 1, 0:4], start=False, stop=True, skip_group_check=True)
            nc.tensor.matmul(bank(7, 12, 4), upper, l[:, 1, 4:8], start=False, stop=True, skip_group_check=True)\
                .then_inc(*steps.did("pe", "gate.cum"))
            for x in range(4):
                lf = [l[:, t, x:x + 1].broadcast_to([P, P]) for t in range(NT)]
                o = lambda t: bank(4 + x // 2, (x % 2) * 256 + t * P, P)
                nc.tensor.matmul(o(0), lf[0], upper, start=(x % 2 == 0), stop=True, skip_group_check=True)
                nc.tensor.matmul(o(1), lf[0], ones_sq, start=False, stop=False, skip_group_check=True)
                last = nc.tensor.matmul(o(1), lf[1], upper, start=False, stop=True, skip_group_check=True)
            last.then_inc(*steps.did("pe", "gate.rowm"))
            pe.wait_ge(*after("gate.col"))
            for t in range(NT):
                for x in range(4):
                    last = nc.tensor.matmul(bank(6 + t, x * P, P), l[:, t, 4 + x:5 + x].broadcast_to([P, P]), upper,
                                            start=(x == 0), stop=True, skip_group_check=True)
            last.then_inc(*steps.did("pe", "gate.rowg"))

        def dve_gate_rows(dve):
            dve.wait_ge(*after("gate.col"))
            dve.wait_ge(*after("gate.rowm"))
            c, x4 = by_t(gcum), mE.rearrange("p (k n) -> p k n", k=4)
            r4 = psum[:, 4:6, :].rearrange("p b (k n) -> p (b k) n", k=2)
            nc.vector.tensor_tensor(x4[:, :, 0:256], r4, c[:, 0, 0:4].unsqueeze(2).broadcast_to([P, 4, 256]), ALU.subtract)\
                .then_inc(*steps.did("dve", "mx0"))
            nc.vector.tensor_tensor(x4[:, :, 256:384], r4[:, :, P:256], c[:, 1, 0:4].unsqueeze(2).broadcast_to([P, 4, P]), ALU.subtract)\
                .then_inc(*steps.did("dve", "mx1"))

        def dve_delta_exponents(dve):
            dve.wait_ge(*after("gate.rowg"))
            c = by_t(gcum)
            nc.vector.tensor_copy(glast, bank(6).rearrange("p (k n) -> p k n", k=4)[:, :, P - 1]).then_inc(*steps.did("dve", "glast"))
            nc.vector.tensor_tensor(heads4(dE0), psum[:, 6:8, :].rearrange("p t (k d) -> p t k d", k=4),
                                    c[:, :, 4:8].unsqueeze(3).broadcast_to([P, NT, 4, P]), ALU.subtract)\
                .then_inc(*steps.did("dve", "dx"))
            dve.wait_ge(*after("glast"))
            nc.vector.tensor_tensor(glast, glast, c[:, 0, 4:8], ALU.subtract).then_inc(*steps.did("dve", "dlast"))

        dE0 = arena[:, 6144:7168]

        def pool_ab_masks(pool):
            pool.wait_ge(*after("mx1"))
            x4 = mE.rearrange("p (k n) -> p k n", k=4)
            for at, name in ((0, "mm0"), (256, "mm1")):
                nc.gpsimd.affine_select(out=x4[:, :, at:at + P], in_=x4[:, :, at:at + P], compare_op=ALU.is_ge, fill=-BIG,
                                        base=0, pattern=[[0, 4], [1, P]], channel_multiplier=-1).then_inc(*steps.did("pool", name))
            pool.wait_ge(*after("dx"))
            v = dE0.rearrange("p (k n) -> p k n", k=8)
            nc.gpsimd.affine_select(out=v, in_=v, compare_op=ALU.is_ge, fill=-BIG, base=0, pattern=[[0, 8], [1, P]],
                                    channel_multiplier=-1).then_inc(*steps.did("pool", "dm"))

        def act_ab_decays(act):
            act.wait_ge(*after("mm1"))
            nc.scalar.activation(mE, mE, ACT.Exp).then_inc(*steps.did("act", "mE"))
            act.wait_ge(*after("dm"))
            nc.scalar.activation(dE0, dE0, ACT.Exp).then_inc(*steps.did("act", "dE0"))
            act.wait_ge(*after("dlast"))
            nc.scalar.activation(kdecay, glast, ACT.Exp).then_inc(*steps.did("act", "kdecay"))
            nc.scalar.activation(eg1, by_t(gcum)[:, 1, 4:8], ACT.Exp).then_inc(*steps.did("act", "eg1"))

        def dve_m_v(dve):
            dve.wait_ge(used, ab_p["mv"] + 4)
            dve.wait_ge(*after("gate.ei"))
            nc.vector.tensor_tensor(heads4(mvE), psum[:, 0:2, :].rearrange("p t (k d) -> p t k d", k=4), spread_heads(gei), ALU.mult)\
                .then_inc(*steps.did("dve", "mvE"))

        M_BANKS = (2, 4, 3, 5)

        def pe_m_scores(pe):
            for name in ("mqk.y", "mvE", "mx1"):
                pe.wait_ge(*after(name))
            y = Y["mqk"]
            for par in range(2):
                part = slice(64 * par, 64 * par + 64)
                for c in range(2):
                    x = 2 * c + par
                    q, k = y[part, c * 256:c * 256 + 256], y[part, 512 + c * 256:512 + c * 256 + 256]
                    nc.tensor.matmul(bank(M_BANKS[x], 0, 256), k[:, 0:P], q, start=True, stop=True)
                    last = nc.tensor.matmul(bank(M_BANKS[x], 256, P), k[:, P:256], q[:, P:256], start=True, stop=True)
            last.then_inc(*steps.did("pe", "mS"))

        def dve_m_matrix(dve):
            dve.wait_ge(*after("mS"))
            dve.wait_ge(*after("mE"))
            for x in range(4):
                e = mE[:, x * 384:x * 384 + 384]
                last = nc.vector.scalar_tensor_tensor(e, bank(M_BANKS[x], 0, 384), 0.125, e, ALU.mult, ALU.mult)
            last.then_inc(*steps.did("dve", "mA"))

        def pe_m_out(pe):
            pe.wait_ge(*after("mA"))
            last = None
            for den in range(2):
                for x in range(4):
                    a = mE[:, x * 384:x * 384 + 384]
                    for t in range(NT):
                        o = bank(4, t * 4 + x, 1) if den else bank(2 + t, x * P, P)
                        rhs = lambda s: by_t(gei)[:, s, x:x + 1] if den else mvE[:, s * 512 + x * P:s * 512 + x * P + P]
                        nc.tensor.matmul(o, a[:, t * P:t * P + P], rhs(0), start=True, stop=(t == 0))
                        if t == 1:
                            last = nc.tensor.matmul(o, a[:, 256:384], rhs(1), start=False, stop=True)
            last.then_inc(*steps.did("pe", "mO"))

        def dve_m_out(dve):
            dve.wait_ge(*after("mO"))
            nc.vector.tensor_scalar(m_den, bank(4, 0, 8), -1.0, None, ALU.mult).then_inc(*steps.did("dve", "m.nden"))
            dve.wait_ge(*after("m.nden"))
            nc.vector.scalar_tensor_tensor(m_den, bank(4, 0, 8), 1.0, m_den, ALU.max, ALU.max).then_inc(*steps.did("dve", "m.den"))
            dve.wait_ge(*after("m.den"))
            nc.vector.reciprocal(m_den, m_den).then_inc(*steps.did("dve", "m.rden"))
            dve.wait_ge(*after("m.rden"))
            m4 = mix[:, :, 0:512].rearrange("p t (k d) -> p t k d", k=4)
            nc.vector.tensor_tensor(m4, psum[:, 2:4, :].rearrange("p t (k d) -> p t k d", k=4), spread_heads(m_den), ALU.mult)\
                .then_inc(*steps.did("dve", "m.h"))

        def act_m_square(act):
            act.wait_ge(*after("m.h"))
            nc.scalar.activation(by_t(m_sq), mix[:, :, 0:512], ACT.Square).then_inc(*steps.did("act", "m.sq"))

        def dve_m_sums(dve):
            dve.wait_ge(*after("m.sq"))
            nc.vector.tensor_reduce(m_ss, m_sq.rearrange("p (k d) -> p k d", d=P), AX_X, ALU.add).then_inc(*steps.did("dve", "m.ss"))

        def dve_m_norm(dve):
            dve.wait_ge(*after("m.rr"))
            m4 = mix[:, :, 0:512].rearrange("p t (k d) -> p t k d", k=4)
            nc.vector.tensor_tensor(m4, m4, spread_heads(m_r), ALU.mult).then_inc(*steps.did("dve", "m.n"))

        ROW_BANKS = {"dk": 4, "dq": 2, "dv": 0}

        def pe_rows(pe, name, ready):
            for r in ready:
                pe.wait_ge(*after(r))
            for t in range(NT):
                for c in range(4):
                    last = nc.tensor.transpose(bank(ROW_BANKS[name] + t, c * P, P), Y[name][:, c * 256 + t * P:c * 256 + t * P + P], ident)
            last.then_inc(*steps.did("pe", f"{name}.R"))

        def act_row_squares(act, name, sq):
            act.wait_ge(*after(f"{name}.R"))
            b = ROW_BANKS[name]
            nc.scalar.activation(by_t(sq), psum[:, b:b + 2, :], ACT.Square).then_inc(*steps.did("act", f"{name}.sq"))

        def dve_row_sums(dve, name, sq, ss):
            dve.wait_ge(*after(f"{name}.sq"))
            nc.vector.tensor_reduce(ss, sq.rearrange("p (k d) -> p k d", d=P), AX_X, ALU.add).then_inc(*steps.did("dve", f"{name}.ss"))

        def dve_row_scale(dve, name, dst, r, ready, done):
            b = ROW_BANKS[name]
            for x in ready:
                dve.wait_ge(*after(x))
            nc.vector.tensor_tensor(heads4(dst), psum[:, b:b + 2, :].rearrange("p t (k d) -> p t k d", k=4), spread_heads(r), ALU.mult)\
                .then_inc(*steps.did("dve", done))

        def pool_delta(pool):
            for k in range(3):
                pool_split_lo(pool, ab_p["mo"] + k)
            for name, ss, count, r in (("m", m_ss, P, m_r), ("dk", k_ss, 1, k_r), ("dq", q_ss, 1, q_r)):
                pool.wait_ge(*after(f"{name}.ss"))
                pool_rstd(pool, f"{name}.rr", ss, 8, count, r)
                if name == "dq":
                    pool.wait_ge(*after("dq.rr"))
                    nc.gpsimd.tensor_scalar(q_r, q_r, float(P) ** -0.5, None, ALU.mult).then_inc(*steps.did("pool", "dq.rs"))
            g = gain_of(pool, "abh")
            for name, a, at, done in (("m.sig", arena[:, 9216:10240], 0, "m.sigg"), ("d.gate", gtmp, 512, "ab.last")):
                pool.wait_ge(*after(name))
                nc.gpsimd.tensor_tensor(by_t(a), by_t(a), g[:, at:at + 512].unsqueeze(1).broadcast_to([P, NT, 512]), ALU.mult)\
                    .then_inc(*steps.did("pool", done))
                if name == "m.sig":
                    for k in range(3):
                        pool_split_lo(pool, ab_p["dg"] + k)
            for k in range(6):
                pool_split_lo(pool, 2 * first_slot["abo"] + k, (2, D))
            pool.wait_ge(*after("d.ss"))
            pool_rstd(pool, "d.r", d_ss, 8, P, d_r)

        def pe_cols(pe, name, src, b, ready):
            for r in ready:
                pe.wait_ge(*after(r))
            for x in range(4):
                for t in range(NT):
                    last = nc.tensor.transpose(bank(b + x // 2, (x % 2) * 256 + t * P, P), src[:, t * 512 + x * P:t * 512 + x * P + P], ident)
            last.then_inc(*steps.did("pe", name))

        def per_tile(pe, b, lhs, rhs, name):
            for t in range(NT):
                for x in range(4):
                    last = nc.tensor.matmul(bank(b + t, x * P, P), lhs(t, x), rhs(t, x), start=True, stop=True)
            last.then_inc(*steps.did("pe", name))

        tok_head = lambda a: lambda t, x: a[:, t * 512 + x * P:t * 512 + x * P + P]
        head_tok = lambda a: lambda t, x: a[:, x * 256 + t * P:x * 256 + t * P + P]

        def pe_delta_matrices(pe):
            pe.wait_ge(*after("kT2"))
            pe.wait_ge(*after("kbT"))
            per_tile(pe, 4, head_tok(kT2), head_tok(kbT), "dNT.p")
            pe.wait_ge(*after("qT2"))
            per_tile(pe, 2, head_tok(kT2), head_tok(qT2), "dat.p")

        def dve_delta_matrices(dve):
            dve.wait_ge(*after("dE"))
            def decayed(name, b, dst):
                dve.wait_ge(*after(f"{name}.p"))
                nc.vector.tensor_tensor(by_t(dst), psum[:, b:b + 2, :], by_t(dE), ALU.mult).then_inc(*steps.did("dve", name))
            decayed("dNT", 4, dNT)
            dve.wait_ge(*after("dNT"))
            eight = lambda a: a.rearrange("p (k n) -> p k n", k=8)
            nc.vector.tensor_tensor(eight(dXT), eight(dNT), cst("level1").unsqueeze(1).broadcast_to([P, 8, P]), ALU.mult)\
                .then_inc(*steps.did("dve", "dXT.m"))
            dve.wait_ge(*after("dXT.m"))
            nc.vector.tensor_tensor(eight(dXT), ident.unsqueeze(1).broadcast_to([P, 8, P]), eight(dXT), ALU.subtract)\
                .then_inc(*steps.did("dve", "dXT"))
            decayed("dat", 2, dat)

        SOLVE = LEVELS[::-1][1:]

        def pe_delta_start(pe):
            pe.wait_ge(*after("dNT"))
            for t in range(NT):
                for x in range(4):
                    last = nc.tensor.transpose(bank(t, x * P, P), tok_head(dNT)(t, x), ident)
            last.then_inc(*steps.did("pe", "dN.T"))
            pe.wait_ge(*after("dXT"))
            for t in range(NT):
                for x in range(4):
                    last = nc.tensor.transpose(bank(4 + t, x * P, P), tok_head(dXT)(t, x), ident)
            last.then_inc(*steps.did("pe", "dX.T"))

        def act_delta_start(act):
            for name, dst, b in (("dN", dN, 0), ("dX", dX, 4)):
                act.wait_ge(*after(f"{name}.T"))
                nc.scalar.activation(by_t(dst), psum[:, b:b + 2, :], ACT.Copy).then_inc(*steps.did("act", name))

        def solved(n, t):
            return f"dX.{n}{t}"

        def pe_delta_level(pe, n, part):
            for t in range(NT):
                if part == 0:
                    for name in ("dN", "dX") if n == 0 else (f"dXTn{n - 1}{t}",):
                        pe.wait_ge(*after(name))
                    for x in range(4):
                        last = nc.tensor.matmul(bank(t, x * P, P), tok_head(dN)(t, x), tok_head(dXT)(t, x), start=True, stop=True)
                    last.then_inc(*steps.did("pe", f"dV.p{n}{t}"))
                    continue
                pe.wait_ge(*after(f"dV{n}{t}"))
                if n > 0:
                    pe.wait_ge(*after(f"dXn{n - 1}{t}"))
                for x in range(4):
                    last = nc.tensor.matmul(bank(2 + t, x * P, P), tok_head(dX)(t, x), tok_head(dV)(t, x), start=True, stop=True)
                last.then_inc(*steps.did("pe", f"dXT.p{n}{t}"))
                if n < len(SOLVE) - 1:
                    for x in range(4):
                        last = nc.tensor.matmul(bank(4 + t, x * P, P), tok_head(dV)(t, x), tok_head(dX)(t, x), start=True, stop=True)
                    last.then_inc(*steps.did("pe", f"dX.p{n}{t}"))

        def dve_delta_level(dve, n):
            four = lambda a: a.rearrange("p (k n) -> p k n", k=4)
            mask = cst(f"level{SOLVE[n]}").unsqueeze(1).broadcast_to([P, 4, P])
            half = lambda a, t: a[:, t * 512:t * 512 + 512]
            for t in range(NT):
                dve.wait_ge(*after(f"dV.p{n}{t}"))
                nc.vector.tensor_tensor(four(half(dV, t)), four(bank(t)), mask, ALU.mult).then_inc(*steps.did("dve", f"dV{n}{t}"))
            for t in range(NT):
                dve.wait_ge(*after(f"dXT.p{n}{t}"))
                if n > 0:
                    dve.wait_ge(*after(f"dXTn{n - 1}{t}"))
                nc.vector.tensor_tensor(half(dXT, t), half(dXT, t), bank(2 + t), ALU.subtract).then_inc(*steps.did("dve", f"dXTn{n}{t}"))
                if n < len(SOLVE) - 1:
                    dve.wait_ge(*after(f"dX.p{n}{t}"))
                    nc.vector.tensor_tensor(half(dX, t), half(dX, t), bank(4 + t), ALU.subtract).then_inc(*steps.did("dve", f"dXn{n}{t}"))

        def four_heads(pe, b, lhs, rhs, name):
            for x in range(4):
                last = nc.tensor.matmul(bank(b, x * P, P), lhs(x), rhs(x), start=True, stop=True)
            last.then_inc(*steps.did("pe", name))

        head = lambda a: lambda x: a[:, x * P:x * P + P]

        def pe_delta_out(pe):
            n = len(SOLVE) - 1
            pe.wait_ge(*after(f"dXTn{n}0"))
            four_heads(pe, 0, head(dXT[:, 0:512]), head(vb[:, 0:512]), "d.u0p")
            pe.wait_ge(*after("d.u0"))
            pe.wait_ge(*after("d.kdec"))
            four_heads(pe, 1, head(krow[:, 0:512]), head(u0), "d.Sp")
            four_heads(pe, 5, head(dat[:, 0:512]), head(u0), "d.o0p")
            pe.wait_ge(*after("d.S"))
            pe.wait_ge(*after(f"dXTn{n}1"))
            four_heads(pe, 2, lambda x: head_tok(kT2)(1, x), head(dS), "d.kSp")
            four_heads(pe, 3, lambda x: head_tok(qT2)(1, x), head(dS), "d.qSp")
            pe.wait_ge(*after("d.rhs"))
            four_heads(pe, 0, head(dXT[:, 512:1024]), head(u1), "d.u1p")
            pe.wait_ge(*after("d.u1"))
            four_heads(pe, 4, head(dat[:, 512:1024]), head(u1), "d.o1p")

        def dve_delta_prep(dve):
            four = lambda a: a.rearrange("p (k n) -> p k n", k=4)
            dve.wait_ge(*after("kdecay"))
            dve.wait_ge(*after("kT2.T"))
            nc.vector.tensor_tensor(four(krow[:, 0:512]), four(krow[:, 0:512]), kdecay.unsqueeze(2).broadcast_to([P, 4, P]), ALU.mult)\
                .then_inc(*steps.did("dve", "d.kdec"))
            dve.wait_ge(*after("eg1"))
            nc.vector.tensor_tensor(beg, eg1, gbeta[:, 4:8], ALU.mult).then_inc(*steps.did("dve", "beg"))

        def dve_delta_out(dve):
            four = lambda a: a.rearrange("p (k n) -> p k n", k=4)
            wide = lambda a: a.unsqueeze(2).broadcast_to([P, 4, P])
            dve.wait_ge(*after("d.u0p"))
            nc.vector.tensor_copy(u0, bank(0)).then_inc(*steps.did("dve", "d.u0"))
            dve.wait_ge(*after("d.Sp"))
            nc.vector.tensor_copy(dS, bank(1)).then_inc(*steps.did("dve", "d.S"))
            for t in range(NT):
                dve_turn(dve, "abo", t, 0, 6 + t)
            dve.wait_ge(*after("d.kSp"))
            dve.wait_ge(*after("beg"))
            nc.vector.tensor_tensor(four(u1), four(bank(2)), wide(beg), ALU.mult).then_inc(*steps.did("dve", "d.ks"))
            dve.wait_ge(*after("d.ks"))
            nc.vector.tensor_tensor(u1, vb[:, 512:1024], u1, ALU.subtract).then_inc(*steps.did("dve", "d.rhs"))
            m = mix[:, 1, 512:1024]
            dve.wait_ge(*after("d.qSp"))
            nc.vector.tensor_tensor(four(m), four(bank(3)), wide(eg1), ALU.mult).then_inc(*steps.did("dve", "d.qs"))
            dve.wait_ge(*after("d.u1p"))
            nc.vector.tensor_copy(u1, bank(0)).then_inc(*steps.did("dve", "d.u1"))
            nc.vector.tensor_copy(mix[:, 0, 512:1024], bank(5)).then_inc(*steps.did("dve", "d.o0"))
            dve.wait_ge(*after("d.o1p"))
            dve.wait_ge(*after("d.qs"))
            nc.vector.tensor_tensor(m, m, bank(4), ALU.add).then_inc(*steps.did("dve", "d.o1"))
            dve.wait_ge(*after("d.osq"))
            nc.vector.tensor_reduce(d_ss, d_sq.rearrange("p (k d) -> p k d", d=P), AX_X, ALU.add).then_inc(*steps.did("dve", "d.ss"))
            dve.wait_ge(*after("d.r"))
            m4 = mix[:, :, 512:1024].rearrange("p t (k d) -> p t k d", k=4)
            nc.vector.tensor_tensor(m4, m4, spread_heads(d_r), ALU.mult).then_inc(*steps.did("dve", "d.n"))
            dve.wait_ge(*after("d.n"))
            dve.wait_ge(*after("ab.last"))
            for t in range(NT):
                nc.vector.tensor_tensor(mix[:, t, 512:1024], mix[:, t, 512:1024], gtmp[:, t * 512:t * 512 + 512], ALU.mult)\
                    .then_inc(*steps.did("dve", f"abo.n{t}"))

        def pe_ab(pe):
            pe_ab_first(pe)
            pe_gate_sums(pe)
            pe_conv_unit(pe, "dk", ["mvE"])
            pe_m_scores(pe)
            pe_conv_unit(pe, "dq", ["dx", "glast"])
            pe_m_out(pe)
            pe_conv_unit(pe, "dv", ["dk.c0"])
            pe_rows(pe, "dk", ["dk.y", "m.h"])
            pe_rows(pe, "dq", ["dq.y"])
            pe.wait_ge(*after("dq.c0"))
            pe_unit(pe, ab_p["mo"], rows=[(0, 512, [bank(6), bank(7)], (True, True))])
            pe_rows(pe, "dv", ["dv.y"])
            pe_cols(pe, "kT2.T", krow, 4, ["krow"])
            pe_cols(pe, "kbT.T", kb, 6, ["kb", "m.sig"])
            pe_cols(pe, "qT2.T", qrow, 2, ["qrow"])
            dg_piece = lambda k: pe_unit(pe, ab_p["dg"], rows=[(0, 512, [bank(6), bank(7)], (True, True))], which=(k,))
            pe_delta_matrices(pe)
            pe.wait_ge(*after("qT2"))
            dg_piece(0)
            pe_delta_start(pe)
            for n in range(len(SOLVE)):
                pe_delta_level(pe, n, 0)
                if n < 3:
                    dg_piece(n + 1)
                if n == 0:
                    pe.wait_ge(*after("dat"))
                pe_delta_level(pe, n, 1)
                if n == 3:
                    for t in range(NT):
                        pe_turn(pe, "abo", t, 0, 6 + t, mix, "d.gate")
            pe_delta_out(pe)
            pe_turn_after(pe)

        def pe_turn_after(pe):
            for k in range(4):
                if k == 0:
                    pe.wait_ge(*after("d.u1"))
                if k == 3:
                    for t in range(NT):
                        pe_turn(pe, "abo", t, 1, 6 + t, mix, f"abo.n{t}")
                pe_out(pe, "abo", k)
            pe_out_last(pe, "abo")

        def act_ab(act):
            S = lambda name, which=(0, 1, 2, 3): splits(split_hi, act, ab_p[name], which=which)
            S("mqk", (0, 1))
            act_gates(act)
            S("mqk", (2, 3))
            S("dk", (0, 1))
            act_conv_first(act, "mqk")
            S("dk", (2,))
            act_conv_silu(act, "mqk")
            S("dk", (3,))
            act_ab_decays(act)
            S("dq", (0, 1))
            act_conv_first(act, "dk")
            S("dq", (2,))
            act_conv_silu(act, "dk")
            S("dq", (3,))
            S("dv", (0, 1))
            act_conv_first(act, "dq")
            S("dv", (2, 3))
            S("mo", (0, 1))
            act_m_square(act)
            S("mo", (2,))
            act_conv_silu(act, "dq")
            act_conv_first(act, "dv")
            S("mo", (3,))
            act_row_squares(act, "dk", arena[:, 9216:10240])
            act_conv_silu(act, "dv")
            act_row_squares(act, "dq", arena[:, 10240:11264])
            act.wait_ge(*after("m.ss"))
            nc.scalar.activation(dE, dE0, ACT.Copy).then_inc(*steps.did("act", "dE"))
            S("dg", (0, 1))
            act.wait_ge(used, ab_p["mo"] + 4)
            act.wait_ge(*after("dk.ss"))
            nc.scalar.activation(by_t(arena[:, 9216:10240]), psum[:, 6:8, :], ACT.Sigmoid).then_inc(*steps.did("act", "m.sig"))
            S("dg", (2,))
            for name, dst, b in (("kT2", kT2, 4), ("kbT", kbT, 6), ("qT2", qT2, 2)):
                act.wait_ge(*after(f"{name}.T"))
                nc.scalar.activation(rows(dst), psum[:, b:b + 2, :], ACT.Copy).then_inc(*steps.did("act", name))
            act_delta_start(act)
            S("dg", (3,))
            out_splits(split_hi, act, "abo", (0, 1))
            act.wait_ge(used, ab_p["dg"] + 4)
            act.wait_ge(*after("dat"))
            nc.scalar.activation(by_t(gtmp), psum[:, 6:8, :], ACT.Silu).then_inc(*steps.did("act", "d.gate"))
            for t in range(NT):
                act_turn(act, "abo", t, 0, 6 + t)
            out_splits(split_hi, act, "abo", (2, 3, 4, 5))
            act.wait_ge(*after("d.o1"))
            act.wait_ge(*after("d.o0"))
            nc.scalar.activation(by_t(d_sq), mix[:, :, 512:1024], ACT.Square).then_inc(*steps.did("act", "d.osq"))
            for t in range(NT):
                act_turn(act, "abo", t, 1, 6 + t)
            out_splits(split_hi, act, "abo", (6, 7))
            first_pieces(split_hi, act, "ffn2", (0, 1))

        def dve_ab(dve):
            S = lambda name, which=(0, 1, 2, 3): splits(split_lo, dve, ab_p[name], which=which)
            S("mqk", (0, 1))
            dve_gates(dve)
            dve_gate_logs(dve)
            S("mqk", (2, 3))
            dve_m_v(dve)
            S("dk", (0, 1))
            dve.wait_ge(*after("gate.cum"))
            nc.vector.tensor_copy(gcum, bank(7, 0, 16)).then_inc(*steps.did("dve", "gate.col"))
            dve_conv_rest(dve, "mqk")
            dve_gate_rows(dve)
            S("dk", (2,))
            dve_delta_exponents(dve)
            S("dk", (3,))
            S("dq", (0, 1))
            dve_conv_rest(dve, "dk")
            S("dq", (2,))
            dve_m_matrix(dve)
            S("dq", (3,))
            S("dv", (0, 1))
            dve_m_out(dve)
            S("dv", (2, 3))
            dve_conv_rest(dve, "dq")
            dve_m_sums(dve)
            dve_conv_rest(dve, "dv")
            dve.wait_ge(lo_done, ab_p["mo"] + 3)
            S("mo", (3,))
            dve_row_sums(dve, "dk", arena[:, 9216:10240], k_ss)
            dve_m_norm(dve)
            dve_row_sums(dve, "dq", arena[:, 10240:11264], q_ss)
            dve_row_scale(dve, "dk", krow, k_r, ["dk.rr"], "krow")
            dve.wait_ge(*after("dE"))
            dve.wait_ge(*after("krow"))
            nc.vector.tensor_tensor(heads4(kb), heads4(krow), spread_heads(gbeta), ALU.mult).then_inc(*steps.did("dve", "kb"))
            dve_row_scale(dve, "dq", qrow, q_r, ["dq.rs"], "qrow")
            dve_row_scale(dve, "dv", vb, gbeta, ["dv.R"], "vb")
            dve.wait_ge(*after("m.sigg"))
            dve.wait_ge(*after("m.n"))
            nc.vector.tensor_tensor(mix[:, :, 0:512], mix[:, :, 0:512], by_t(arena[:, 9216:10240]), ALU.mult)\
                .then_inc(*steps.did("dve", "m.gate"))
            dve.wait_ge(*after("m.gate"))
            dve_delta_matrices(dve)
            dve_delta_prep(dve)
            dve.wait_ge(lo_done, ab_p["dg"] + 3)
            S("dg", (3,))
            for n in range(len(SOLVE)):
                dve_delta_level(dve, n)
            dve_delta_out(dve)
            for t in range(NT):
                dve_turn(dve, "abo", t, 1, 6 + t)
            dve.wait_ge(lo_done, 2 * first_slot["abo"] + 6)
            out_splits(split_lo, dve, "abo", (6, 7))
            first_pieces(split_lo, dve, "ffn2", (0, 1))

        def pool_ab(pool, gains):
            next_gain(pool, gains)
            pool_ab_masks(pool)
            pool_delta(pool)
            next_gain(pool, gains)

        HW = 4 * SEQ
        hq, hk, hb = ([arena[:, (3 * u + n) * HW:(3 * u + n + 1) * HW] for u in range(2)] for n in range(3))
        h_e = ((arena[:, 6144:7168], arena[:, 10752:11776]),
               (arena[:, 6144:7168], arena[:, 2048:3072]))
        h_l = (arena[:, 7168:8192], arena[:, 8192:9216])
        h_at, h_cross = arena[:, 9216:10240], arena[:, 10240:10752]
        h_t1, h_t2 = (arena[:, 6144:7168], arena[:, 8192:9216]), (arena[:, 7168:8192], arena[:, 9216:10240])
        h_sil = (arena[:, 10752:11776], arena[:, 1024:2048])
        h_sq = arena[:, 0:1024]
        lb_d, lb_e, log_lb, log_rest, lb_x = (few.take(8) for _ in range(5))
        h_ss, h_r = (few.take(8), few.take(8)), (few.take(8), few.take(8))
        wide2 = lambda b: psum[:, b:b + 2, :].rearrange("p b n -> p (b n)")
        hu = lambda n: piece_at("hg", n)

        def dve_bounds(dve):
            nc.vector.tensor_tensor(lb_d, lb_logits[:, 8:16], lb_logits[:, 0:8], ALU.subtract).then_inc(*steps.did("dve", "lb.d"))
            dve.wait_ge(*after("lb.ln"))
            nc.vector.scalar_tensor_tensor(log_rest, lb_d, 0.0, lb_e, ALU.max, ALU.add).then_inc(*steps.did("dve", "lb.1"))
            nc.vector.scalar_tensor_tensor(log_lb, lb_d, 0.0, lb_e, ALU.min, ALU.subtract).then_inc(*steps.did("dve", "lb.a"))
            dve.wait_ge(*after("lb.1"))
            nc.vector.tensor_scalar(log_rest, log_rest, -1.0, None, ALU.mult).then_inc(*steps.did("dve", "lb.c"))

        def act_bounds(act):
            act.wait_ge(*after("lb.d"))
            nc.scalar.activation(lb_e, lb_d, ACT.Abs).then_inc(*steps.did("act", "lb.abs"))
            act.wait_ge(*after("lb.abs"))
            nc.scalar.activation(lb_e, lb_e, ACT.Exp, scale=-1.0).then_inc(*steps.did("act", "lb.exp"))
            act.wait_ge(*after("lb.exp"))
            nc.scalar.activation(lb_e, lb_e, ACT.Ln, bias=1.0).then_inc(*steps.did("act", "lb.ln"))

        def act_log1p_exp(act, name, a, src, ready):
            for r in ready:
                act.wait_ge(*after(r))
            nc.scalar.activation(a, src, ACT.Abs).then_inc(*steps.did("act", f"{name}.abs"))
            act.wait_ge(*after(f"{name}.abs"))
            nc.scalar.activation(a, a, ACT.Exp, scale=-1.0).then_inc(*steps.did("act", f"{name}.exp"))
            act.wait_ge(*after(f"{name}.exp"))
            nc.scalar.activation(a, a, ACT.Ln, bias=1.0).then_inc(*steps.did("act", f"{name}.ln"))

        def act_h_forget(act, u):
            act.wait_ge(used, hu(u) + 4)
            act_log1p_exp(act, f"hf{u}", h_t1[u], wide2(2 * u), ())

        def dve_h_forget(dve, u, between=None):
            f = wide2(2 * u)
            dve.wait_ge(*after(f"hf{u}.ln"))
            nc.vector.scalar_tensor_tensor(h_t2[u], f, 0.0, h_t1[u], ALU.min, ALU.subtract).then_inc(*steps.did("dve", f"hf{u}.ls"))
            dve.wait_ge(*after(f"hf{u}.ls"))
            dve.wait_ge(*after("lb.c"))
            dve.wait_ge(*after("lb.a"))
            for x in range(4):
                if between and x in (0, 2):
                    between(x // 2)
                t = slice(x * SEQ, x * SEQ + SEQ)
                a, c = log_lb[:, 4 * u + x:4 * u + x + 1], log_rest[:, 4 * u + x:4 * u + x + 1]
                nc.vector.tensor_scalar(hb[u][:, t], h_t2[u][:, t], c, a, ALU.add, ALU.max)
                nc.vector.tensor_scalar(h_t1[u][:, t], h_t2[u][:, t], c, a, ALU.add, ALU.subtract)
                last = nc.vector.scalar_tensor_tensor(hk[u][:, t], h_t2[u][:, t], c, f[:, t], ALU.add, ALU.subtract)
            last.then_inc(*steps.did("dve", f"hf{u}.x"))

        def act_h_decay(act, u, between=None):
            act.wait_ge(*after(f"hf{u}.x"))
            nc.scalar.activation(hk[u], hk[u], ACT.Exp).then_inc(*steps.did("act", f"hk{u}"))
            if between:
                between()
            act_log1p_exp(act, f"hd{u}", h_t1[u], h_t1[u], ())

        def dve_h_decay(dve, u):
            dve.wait_ge(*after(f"hd{u}.ln"))
            nc.vector.tensor_tensor(h_t1[u], h_t1[u], hb[u], ALU.add).then_inc(*steps.did("dve", f"hd{u}.lf"))
            dve.wait_ge(*after(f"hd{u}.lf"))
            for x in range(4):
                t = slice(x * SEQ, x * SEQ + SEQ)
                last = nc.vector.tensor_tensor_scan(hb[u][:, t], ones.broadcast_to([P, SEQ]), h_t1[u][:, t], 0.0, ALU.mult, ALU.add)
            last.then_inc(*steps.did("dve", f"hb{u}"))

        def act_h_q(act, u):
            act.wait_ge(used, hu(2 + u) + 4)
            nc.scalar.activation(hq[u], wide2(4 + 2 * u), ACT.Silu).then_inc(*steps.did("act", f"hq{u}"))

        def act_h_v(act, u):
            act.wait_ge(used, hu(4 + u) + 4)
            act.wait_ge(*after("hg.T11"))
            nc.scalar.activation(mix[:, :, 512 * u:512 * u + 512], psum[:, 4 + 2 * u:6 + 2 * u, :], ACT.Copy, scale=float(P) ** -0.5)\
                .then_inc(*steps.did("act", f"hv{u}"))

        def act_h_gate(act, u):
            act.wait_ge(used, hu(6 + u) + 4)
            act.wait_ge(*after("h0.P8" if u else "h0.l7"))
            nc.scalar.activation(by_t(h_sil[u]), psum[:, 4:6, :], ACT.Silu).then_inc(*steps.did("act", f"hs{u}"))

        def pe_h_columns(pe, n, b):
            pe_unit(pe, hu(n), columns=[(c * P, bank(b + c // 2, (c % 2) * 256, 256), c % 2 == 0) for c in range(4)])

        def pe_h_piece(pe, n, k, b):
            pe_unit(pe, hu(n), rows=[(0, 512, [bank(b), bank(b + 1)], (True, True))], which=(k,))

        def pe_h_level(pe, u, n):
            X = f"h{u}"
            if n >= 2:
                pe.wait_ge(*after(f"{X}.put{n - 2}"))
            elif u == 1:
                pe.wait_ge(*after(f"h0.put{7 + n}"))
            else:
                pe.wait_ge(*after("hf1.x"))
            if n < len(ALL_LEVELS):
                pe.wait_ge(*after(f"{X}.l{n}"))
                l = r = h_l[n % 2]
            else:
                l, r = hk[u], hq[u]
            if n == 0:
                for x in range(4):
                    last = nc.tensor.matmul(bank(0, x * P, P), head_tok(l)(0, x), head_tok(r)(1, x), start=True, stop=True)
                last.then_inc(*steps.did("pe", f"{X}.P{n}"))
            else:
                per_tile(pe, 2 * (n % 2), head_tok(l), head_tok(r), f"{X}.P{n}")

        def dve_h_put(dve, u, n):
            X = f"h{u}"
            dve.wait_ge(*after(f"{X}.P{n}"))
            if n == 0:
                if u == 1:
                    dve.wait_ge(*after("h0.O"))
                nc.vector.tensor_copy(h_cross, bank(0)).then_inc(*steps.did("dve", f"{X}.put0"))
                return
            dve.wait_ge(*after(f"{X}.put{n - 1}" if n > 1 else f"{X}.at0"))
            mask = cst(f"level{ALL_LEVELS[n]}") if n < len(ALL_LEVELS) else ident
            b = 2 * (n % 2)
            for t in range(NT):
                four = lambda a: a.rearrange("p (m i) -> p m i", m=4)
                last = nc.vector.copy_predicated(four(h_at[:, t * 512:t * 512 + 512]),
                                                 mask.bitcast(U32).unsqueeze(1).broadcast_to([P, 4, P]), four(bank(b + t)))
            last.then_inc(*steps.did("dve", f"{X}.put{n}"))

        def dve_h_exponents(dve, m):
            u, n = divmod(m, 8)
            ready = [f"hb{u}"] + ([f"h{(m - 2) // 8}.l{(m - 2) % 8}"] if m >= 2 else [])
            dve_level_x(dve, f"h{u}", n, ALL_LEVELS[n], hb[u], h_e[u][n % 2], ready)

        def dve_h_levels(dve, levels, between={}):
            for m in levels:
                u, n = divmod(m, 8)
                if n >= 2:
                    dve_h_put(dve, u, n - 2)
                    ready = [f"h{u}.P{n - 2}"]
                else:
                    ready = [f"h0.P{6 + n}"] if u == 1 else ["hb1"] if n == 1 else []
                dve_level_l(dve, f"h{u}", n, ALL_LEVELS[n], hq[u], hk[u], h_e[u][n % 2], h_l[n % 2],
                            ready + [f"hq{u}", f"hk{u}"] * (n == 0))
                if m + 2 < 16:
                    dve_h_exponents(dve, m + 2)
                if m in between:
                    between[m](dve, 0)
                if n == 7:
                    for last in (6, 7, 8):
                        dve_h_put(dve, u, last)

        def pe_h_out(pe, u):
            X = f"h{u}"
            for r in (f"{X}.put8", "hv1", f"hv{u}") + (("ho0.n",) if u == 1 else ()):
                pe.wait_ge(*after(r))
            for t in range(NT):
                for x in range(4):
                    v = lambda s: mix[:, s, 512 * u + x * P:512 * u + x * P + P]
                    last = nc.tensor.matmul(bank(6 + t, x * P, P), tok_head(h_at)(t, x), v(t), start=True, stop=(t == 0))
                    if t == 1:
                        last = nc.tensor.matmul(bank(7, x * P, P), h_cross[:, x * P:x * P + P], v(0), start=False, stop=True)
            last.then_inc(*steps.did("pe", f"{X}.O"))

        def act_h_square(act, u):
            act.wait_ge(*after(f"h{u}.O"))
            nc.scalar.activation(by_t(h_sq), psum[:, 6:8, :], ACT.Square).then_inc(*steps.did("act", f"ho{u}.sq"))

        def pool_h(pool, u):
            pool.wait_ge(*after(f"ho{u}.ss"))
            pool_rstd(pool, f"ho{u}.r", h_ss[u], 8, P, h_r[u])

        def dve_h_sums(dve, u):
            dve.wait_ge(*after(f"ho{u}.sq"))
            nc.vector.tensor_reduce(h_ss[u], h_sq.rearrange("p (k d) -> p k d", d=P), AX_X, ALU.add).then_inc(*steps.did("dve", f"ho{u}.ss"))

        def dve_h_out_norm(dve, u):
            m = mix[:, :, 512 * u:512 * u + 512]
            dve.wait_ge(*after(f"ho{u}.r"))
            nc.vector.tensor_tensor(m.rearrange("p t (k d) -> p t k d", k=4), psum[:, 6:8, :].rearrange("p t (k d) -> p t k d", k=4),
                                    spread_heads(h_r[u]), ALU.mult).then_inc(*steps.did("dve", f"ho{u}.n"))

        def dve_h_out_gate(dve, u):
            m = mix[:, :, 512 * u:512 * u + 512]
            dve.wait_ge(*after(f"ho{u}.n"))
            dve.wait_ge(*after("hg.last" if u else "hs0.g"))
            nc.vector.tensor_tensor(m, m, by_t(h_sil[u]), ALU.mult).then_inc(*steps.did("dve", f"hgo.m{u}"))

        def pe_hg(pe):
            pe_between(pe, "hg")
            wait_turned(pe, "hg", 1)
            pe_h_columns(pe, 0, 0)
            pe_h_columns(pe, 1, 2)
            pe_h_columns(pe, 2, 4)
            pe_h_columns(pe, 3, 6)
            banks_read = {0: "hq0", 4: "hq1", 8: "hv0", 12: "hs0"}

            def piece(k):
                if k in banks_read:
                    pe.wait_ge(*after(banks_read[k]))
                pe_h_piece(pe, 4 + k // 4, k % 4, 6 if k // 4 == 1 else 4)
            for k in range(3):
                piece(k)
            for m in range(18):
                pe_h_level(pe, m // 9, m % 9)
                if m == 9:
                    pe_h_out(pe, 0)
                if m + 3 < 16:
                    piece(m + 3)
            pe.wait_ge(*after("hs1"))
            for t in range(NT):
                pe_turn(pe, "hgo", t, 0, 4 + t, mix, "hgo.m0")
            pe_h_out(pe, 1)
            for k in range(4):
                if k == 3:
                    for t in range(NT):
                        pe_turn(pe, "hgo", t, 1, 4 + t, mix, "hgo.m1")
                pe_out(pe, "hgo", k)
            pe_out_last(pe, "hgo")

        def act_hg(act):
            S = lambda n, which=(0, 1, 2, 3): splits(split_hi, act, hu(n), which=which)
            S(1, (0,))
            act_bounds(act)
            S(1, (1, 2, 3))
            S(2, (0, 1))
            act_h_forget(act, 0)
            S(2, (2, 3))
            S(3, (0,))
            act_h_decay(act, 0)
            S(3, (1,))
            act_h_forget(act, 1)
            S(3, (2, 3))
            act_h_q(act, 0)
            split_hi(act, hu(4))
            split_hi(act, hu(4) + 1)
            split_hi(act, hu(4) + 2)
            act_h_decay(act, 1, between=lambda: act_level(act, "h0", 0, h_e[0][0]))
            split_hi(act, hu(4) + 3)
            act_level(act, "h0", 1, h_e[0][1])
            for n in range(8):
                split_hi(act, hu(5) + n)
                if n > 1:
                    act_level(act, "h0", n, h_e[0][n % 2])
                if n == 0:
                    act_h_q(act, 1)
                if n == 2:
                    act_h_v(act, 0)
                if n == 6:
                    act_h_v(act, 1)
            for n in range(8):
                split_hi(act, hu(7) + n)
                act_level(act, "h1", n, h_e[1][n % 2])
                if n == 0:
                    act_h_gate(act, 0)
                if n == 2:
                    act_h_square(act, 0)
                if n == 6:
                    act_h_gate(act, 1)
            for t in range(NT):
                act_turn(act, "hgo", t, 0, 4 + t)
            act_h_square(act, 1)
            out_splits(split_hi, act, "hgo", (4, 5))
            for t in range(NT):
                act_turn(act, "hgo", t, 1, 4 + t)
            out_splits(split_hi, act, "hgo", (6, 7))
            first_pieces(split_hi, act, "ffn3", (0, 1))

        def dve_hg(dve):
            S = lambda n, which=(0, 1, 2, 3): splits(split_lo, dve, hu(n), which=which)
            S(1, (0,))
            dve_bounds(dve)
            S(1, (1, 2, 3))
            S(2, (0, 1))
            dve_h_forget(dve, 0)
            S(2, (2, 3))
            S(3, (0,))
            dve_h_decay(dve, 0)
            S(3, (1,))
            dve_h_forget(dve, 1, between=lambda m: S(3, (2 + m,)))
            dve_h_exponents(dve, 0)
            dve_h_exponents(dve, 1)
            dve_h_levels(dve, (0,))
            dve_h_decay(dve, 1)
            dve_h_levels(dve, range(1, 16), {10: dve_h_sums, 11: dve_h_out_norm, 15: dve_h_out_gate})
            for t in range(NT):
                dve_turn(dve, "hgo", t, 0, 4 + t)
            dve_h_sums(dve, 1)
            dve.wait_ge(lo_done, 2 * first_slot["hgo"] + 2)
            out_splits(split_lo, dve, "hgo", (2, 3))
            dve_h_out_norm(dve, 1)
            dve_h_out_gate(dve, 1)
            out_splits(split_lo, dve, "hgo", (4, 5))
            for t in range(NT):
                dve_turn(dve, "hgo", t, 1, 4 + t)
            out_splits(split_lo, dve, "hgo", (6, 7))
            first_pieces(split_lo, dve, "ffn3", (0, 1))

        def pool_hg(pool, gains):
            for n in range(2):
                pool_split_lo(pool, hu(4) + n)
            pool.wait_ge(*after("hf1.x"))
            nc.gpsimd.memset(h_at, 0.0).then_inc(*steps.did("pool", "h0.at0"))
            for n in range(2, 13):
                pool_split_lo(pool, hu(4) + n)
            g = gain_of(pool, "hgh")

            def gate_gain(u):
                a = by_t(h_sil[u])
                pool.wait_ge(*after(f"hs{u}"))
                nc.gpsimd.tensor_tensor(a, a, g[:, 512 * u:512 * u + 512].unsqueeze(1).broadcast_to([P, NT, 512]), ALU.mult)\
                    .then_inc(*steps.did("pool", "hg.last" if u else "hs0.g"))
            pool.wait_ge(*after("h0.O"))
            nc.gpsimd.memset(h_at, 0.0).then_inc(*steps.did("pool", "h1.at0"))
            pool_split_lo(pool, hu(4) + 13)
            pool_split_lo(pool, hu(4) + 14)
            pool_h(pool, 0)
            gate_gain(0)
            for n in range(15, 18):
                pool_split_lo(pool, hu(4) + n)
            gate_gain(1)
            pool_h(pool, 1)
            next_gain(pool, gains)

        staged = arena[:, 4096:4096 + 5 * P].rearrange("p (b n) -> p b n", b=5)
        conv_m, conv_g, lb_logits, gate_bias = few.take(16), few.take(48), few.take(16), few.take(2)
        spread = {}
        SPREAD = [("q_norm", A["q_norm"][0]), ("k_norm", A["k_norm"][0]), ("gla_out_norm", A["gla_out_norm"][0]),
                  ("attn_sinks", A["attn_sinks"][0]), ("ab_m_gate_bias_2", A["ab_m_gate_bias_2"][0].rearrange("a b -> (a b)")),
                  ("ab_g_a_log_2", A["ab_g_a_log_2"][0]), ("ab_g_dt_bias_2", A["ab_g_dt_bias_2"][0])]
        for name, v in SPREAD:
            spread[name] = few.take(v.shape[0])
        gate_up = few.take(256, parts=16)
        p_rows = few.take(NT * 256).rearrange("p (t n) -> p t n", t=NT)

        def act_loads(act):
            x = A["x"][0].rearrange("(t p) d -> p t d", p=P)
            act.dma_start(const[:, 0:P], A["const"][:, 0:P]).then_inc(ident_in, 16)
            act.dma_start(h[:, 1, :], x[:, 1, :]).then_inc(x_in[1], 16)

        def pool_params(pool):
            loads = [(const[:, P:], A["const"][:, P:])]
            for l in range(2):
                w = A["ffn_conv_w_2"][l].rearrange("k (c n) -> (k c) n", n=P)
                loads.append((staged[0:4 * FC, 2 * l, :], w[0:4 * FC]))
                loads.append((staged[0:2 * FC, 2 * l + 1, :], w[4 * FC:6 * FC]))
                loads.append((staged[2 * FC:4 * FC, 2 * l + 1, :], A["ffn_conv_b_2"][l].rearrange("(c n) -> c n", n=P)))
            at = 0
            for v in (A["ab_conv_m_2"][0].rearrange("k (c n) -> (k c) n", n=P),
                      A["ab_conv_g_2"][0].rearrange("k (c n) -> (k c) n", n=P),
                      A["c_lb_logits_2"].rearrange("k (c n) -> (k c) n", n=P),
                      A["gla_b_gate"].rearrange("k (c n) -> (k c) n", n=P)):
                loads.append((staged[at:at + v.shape[0], 4, :], v))
                at += v.shape[0]
            for name, v in SPREAD:
                loads.append((spread[name], v.partition_broadcast(P)))
            loads.append((gate_up, A["gla_w_gate_up"][0]))
            loads.append((p_rows, A["p"][0, 0].rearrange("(t p) n -> p t n", p=P)))
            for dst, src in loads:
                pool.dma_start(dst, src).then_inc(params, 16)
            assert 16 * len(loads) == PARAMS

        PARAMS = 16 * (1 + 6 + 4 + len(SPREAD) + 2)

        def pe_params(pe):
            pe.wait_ge(params, PARAMS)
            for b in range(5):
                n = 4 * FC if b < 4 else 82
                last = nc.tensor.transpose(bank(6 + b // 4, (b % 4) * P, n), staged[0:n, b, :], ident[0:n, 0:n])
            last.then_inc(*steps.did("pe", "params.T"))

        def dve_params(dve):
            dve.wait_ge(*after("params.T"))
            for l in range(2):
                for b in range(2):
                    nc.vector.tensor_copy(taps[:, l, 2 * b:2 * b + 2, :],
                                          bank(6, (2 * l + b) * P, 4 * FC).rearrange("p (k c) -> p k c", k=2))
            at = 0
            for a, n in ((conv_m, 16), (conv_g, 48), (lb_logits, 16), (gate_bias, 2)):
                last = nc.vector.tensor_copy(a, bank(7, at, n))
                at += n
            last.then_inc(*steps.did("dve", "params"))

        STAGES = ["ffn0", "mix0", "ffn1", "ple", "ab", "ffn2", "hg", "ffn3"]
        stages = STAGES[:STAGES.index(stop) + 1] if stop else STAGES
        ENDS = dict(zip(STAGES, ["ffn0", "mix0o", "ffn1", "ple", "abo", "ffn2", "hgo", "ffn3"]))
        steps_of = list(zip(["x"] + [ENDS[st] for st in stages], stages + [None]))
        LATE = {"x": (0, 1, 2, 3), "mix0o": (2, 3), "abo": (2, 3), "ffn2": (3,), "hgo": (2, 3)}
        following = dict(zip(stages, stages[1:] + [None]))

        block = ctx.enter_context(nc.Block())

        @block.sync
        def _(sp):
            sp.dma_start(h[:, 0, :], A["x"][0, 0:P, :]).then_inc(x_in[0], 16)
            for st in stages:
                if st.startswith("ffn"):
                    sp_ffn(sp, int(st[3]))
                elif st == "mix0":
                    sp_mix0(sp)
                else:
                    for part in {"ple": ("emb", "ple"), "ab": ("ab", "abo"), "hg": ("hg", "hgo")}[st]:
                        sp_proj(sp, part)
            o = out[0].rearrange("(t p) d -> p t d", p=P)
            last = ENDS[stages[-1]]
            for t, b in BANKS:
                sp.wait_ge(*after(f"{last}.h{t}{b}"))
                sp.dma_start(cut(o, t, b), cut(h, t, b)).then_inc(out_sem, 16)
            sp.wait_ge(out_sem, 64)

        @block.gpsimd
        def _(pool):
            nc.gpsimd.memset(half_power, -0.5).then_inc(*steps.did("pool", "half_power"))
            gains = iter([g[0] for g in GAINS])
            next_gain(pool, gains)
            pool.wait_ge(*after("half_power"))
            for prev, st in steps_of:
                pool_between(pool, prev, st)
                if st == "ffn0":
                    next_gain(pool, gains)
                    pool_params(pool)
                    next_gain(pool, gains)
                elif st in ("mix0", "ffn1", "ffn3"):
                    next_gain(pool, gains)
                elif st in ("ffn2", "hg"):
                    next_gain(pool, gains)
                    next_gain(pool, gains)
                if st == "mix0":
                    pool_mix0(pool)
                if st == "ple":
                    pool_ple(pool)
                    next_gain(pool, gains)
                    next_gain(pool, gains)
                if st == "ab":
                    pool_ab(pool, gains)
                if st == "hg":
                    pool_hg(pool, gains)

        @block.scalar
        def _(act):
            act_loads(act)
            for prev, st in steps_of:
                act_between(act, prev, st)
                first_pieces(split_hi, act, st, LATE.get(prev, ()))
                if st and st.startswith("ffn"):
                    act_ffn(act, int(st[3]), following[st])
                if st == "mix0":
                    act_mix0(act)
                if st == "ple":
                    act_ple(act)
                if st == "ab":
                    act_ab(act)
                if st == "hg":
                    act_hg(act)

        @block.vector
        def _(dve):
            nc.vector.memset(zero_r[:, :].bitcast(F32), 0.0).then_inc(*steps.did("dve", "zero_r"))
            nc.vector.memset(ones, 1.0).then_inc(*steps.did("dve", "ones"))
            for prev, st in steps_of:
                dve_between(dve, prev, st)
                first_pieces(split_lo, dve, st, LATE.get(prev, ()))
                if st and st.startswith("ffn"):
                    dve_ffn(dve, int(st[3]), following[st])
                if st == "mix0":
                    dve_mix0(dve)
                if st == "ple":
                    dve_ple(dve)
                if st == "ab":
                    dve_ab(dve)
                if st == "hg":
                    dve_hg(dve)

        @block.tensor
        def _(pe):
            pe.wait_ge(ident_in, 16)
            pe.wait_ge(*after("ones"))
            for st in stages:
                if st.startswith("ffn"):
                    pe_ffn(pe, int(st[3]))
                if st == "mix0":
                    pe_mix0(pe)
                if st == "ple":
                    pe_ple(pe)
                if st == "ab":
                    pe_ab(pe)
                if st == "hg":
                    pe_hg(pe)

        return steps.made


def kernel(**inputs):
    import numpy as _np
    import concourse.bacc as _bacc
    from concourse import mybir as _mybir
    from concourse.bass_utils import run_bass_kernel_spmd as _run

    arrays = {f"in_{name}": _np.ascontiguousarray(a) for name, a in inputs.items()}
    arrays["in_const"] = shape_constants()[1]

    def program(numbered):
        nc = _bacc.Bacc("TRN2", target_bir_lowering=False, num_devices=1)
        A = {name[3:]: nc.dram_tensor(name, a.shape, _mybir.dt.from_np(a.dtype), kind="ExternalInput").ap()
             for name, a in arrays.items()}
        out = nc.dram_tensor("out_0", (1, SEQ, D), F32, kind="ExternalOutput").ap()
        return nc, build(nc, A, out, numbered)

    _, numbering = program(None)
    nc, _ = program(numbering)
    r = _run(nc, [arrays], core_ids=[0])
    return r.results[0]["out_0"]
```
